# Optimizing a Trainium2 kernel written in Bass

```python
import jax
import jax.numpy as jnp
from jax import lax
import numpy as np
import math
import jax, jax.numpy as jnp

D_MODEL = 1024
BATCH = 1
SEQ = 1024
DEPTH = 1

D_MIX = D_MODEL
GLA_HEADS = 4
GLA_DV = (D_MIX // 2) // GLA_HEADS
GLA_DK = GLA_DV // 2
GLA_LOWRANK = 16
GLA_TAU = 16.0
GLA_CHUNK = 16
ATT_HEADS = 8
ATT_HD = (D_MIX - GLA_HEADS * GLA_DV) // ATT_HEADS
DILATIONS = ((128, 1), (512, 4), (2048, 16))
ATT_BLOCK = 128
N_GROUPS = 4
EXPERTS_PER_GROUP = 8
N_EXPERTS = N_GROUPS * EXPERTS_PER_GROUP
TOP_K = 2
D_FF_EXPERT = 512
MOE_BLOCK = 128
EPS = 1e-6

GLA_QK = GLA_HEADS * GLA_DK
GLA_V = GLA_HEADS * GLA_DV
ATT_W = ATT_HEADS * ATT_HD
IN_SIZES = (GLA_QK, GLA_QK, GLA_V, GLA_V, GLA_LOWRANK, ATT_W, ATT_W, ATT_W)
IN_SPLITS = tuple(sum(IN_SIZES[:i + 1]) for i in range(len(IN_SIZES) - 1))
IN_COLS = sum(IN_SIZES)


def rmsnorm(x, g):
    xf = x.astype(jnp.float32)
    y = xf * lax.rsqrt(jnp.mean(xf * xf, axis=-1, keepdims=True) + EPS)
    return (y * g.astype(jnp.float32)).astype(x.dtype)

def gla_chunked(q, k, v, log_a):
    B, T, H, DK = q.shape
    DV = v.shape[-1]
    C = GLA_CHUNK
    N = T // C

    def chunks(t):
        return t.astype(jnp.float32).reshape(B, N, C, H, t.shape[-1]).transpose(0, 3, 1, 2, 4)

    q = chunks(q) * (DK ** -0.5)
    k, v, la = chunks(k), chunks(v), chunks(log_a)
    G = jnp.cumsum(la, axis=3)
    causal = jnp.tril(jnp.ones((C, C), dtype=bool))[:, :, None]
    diff = G[:, :, :, :, None, :] - G[:, :, :, None, :, :]
    decay = jnp.where(causal, jnp.exp(jnp.where(causal, diff, 0.0)), 0.0)
    A = jnp.einsum('bhnid,bhnjd,bhnijd->bhnij', q, k, decay)
    o_intra = jnp.einsum('bhnij,bhnjv->bhniv', A, v)
    G_last = G[:, :, :, -1:, :]
    U = jnp.einsum('bhncd,bhncv->bhndv', k * jnp.exp(G_last - G), v)
    a_chunk = jnp.exp(G_last[:, :, :, 0, :])

    def step(S, inp):
        a, u = inp
        return a[..., None] * S + u, S

    S0 = jnp.zeros((B, H, DK, DV), jnp.float32)
    _, S_prev = lax.scan(step, S0, (jnp.moveaxis(a_chunk, 2, 0), jnp.moveaxis(U, 2, 0)))
    S_prev = jnp.moveaxis(S_prev, 0, 2)
    o_inter = jnp.einsum('bhncd,bhndv->bhncv', q * jnp.exp(G), S_prev)
    o = o_intra + o_inter
    return o.transpose(0, 2, 3, 1, 4).reshape(B, T, H, DV)

def dilated_branch(q, k, v, window, dilation):
    B, H, T, D = q.shape
    d = dilation
    L = T // d
    n_back = window // d
    P = ATT_BLOCK
    nb = -(-L // P)
    Lp = nb * P

    def phase(t):
        t = t.reshape(B, H, L, d, D).transpose(0, 1, 3, 2, 4)
        t = jnp.pad(t, ((0, 0), (0, 0), (0, 0), (0, Lp - L), (0, 0)))
        return t.reshape(B, H, d, nb, P, D)

    def with_prev(t):
        prev = jnp.concatenate([jnp.zeros_like(t[:, :, :, :1]), t[:, :, :, :-1]], axis=3)
        return jnp.concatenate([prev, t], axis=4)

    qb = phase(q)
    kb, vb = with_prev(phase(k)), with_prev(phase(v))
    s = jnp.einsum('bhrnqd,bhrnkd->bhrnqk', qb, kb) * (D ** -0.5)
    blk = jnp.arange(nb)[:, None, None]
    qpos = jnp.arange(P)[None, :, None] + P
    kpos = jnp.arange(2 * P)[None, None, :]
    dist = qpos - kpos
    valid = (dist >= 0) & (dist <= n_back) & (blk * P + kpos - P >= 0)
    s = jnp.where(valid, s, -jnp.inf)
    m = jnp.max(s, axis=-1)
    p = jnp.exp(s - m[..., None])
    den = jnp.sum(p, axis=-1)
    o = jnp.einsum('bhrnqk,bhrnkd->bhrnqd', p, vb) / den[..., None]

    def unphase(t):
        rest = t.shape[5:]
        t = t.reshape((B, H, d, Lp) + rest)[:, :, :, :L]
        t = jnp.moveaxis(t, 2, 3)
        return t.reshape((B, H, T) + rest)

    return unphase(o), unphase(m), unphase(den)

def hybrid_mixer(n, w_in, gla_gate_w2, gla_gate_b, gla_norm_g, w_out):
    B, T, _ = n.shape
    proj = n @ w_in
    gq, gk, gv, gr, glr, aq, ak, av = jnp.split(proj, IN_SPLITS, axis=-1)
    log_a = jax.nn.log_sigmoid((glr @ gla_gate_w2 + gla_gate_b).astype(jnp.float32)) / GLA_TAU
    heads = lambda t: t.reshape(B, T, GLA_HEADS, -1)
    o_gla = gla_chunked(heads(gq), heads(gk), heads(gv), heads(log_a))
    o_gla = o_gla * lax.rsqrt(jnp.mean(o_gla * o_gla, axis=-1, keepdims=True) + EPS) * gla_norm_g.astype(jnp.float32)
    o_gla = o_gla.reshape(B, T, GLA_V) * jax.nn.silu(gr.astype(jnp.float32))
    to_bhtd = lambda t: t.astype(jnp.float32).reshape(B, T, ATT_HEADS, ATT_HD).transpose(0, 2, 1, 3)
    q, k, v = to_bhtd(aq), to_bhtd(ak), to_bhtd(av)
    branches = [dilated_branch(q, k, v, w, d) for (w, d) in DILATIONS]
    o_all = jnp.stack([br[0] for br in branches])
    m_all = jnp.stack([br[1] for br in branches])
    den_all = jnp.stack([br[2] for br in branches])
    wts = den_all * jnp.exp(m_all - jnp.max(m_all, axis=0, keepdims=True))
    o_att = jnp.sum(wts[..., None] * o_all, axis=0) / jnp.sum(wts, axis=0)[..., None]
    o_att = o_att.transpose(0, 2, 1, 3).reshape(B, T, ATT_W)
    o = jnp.concatenate([o_gla, o_att], axis=-1).astype(n.dtype)
    return o @ w_out

def hier_moe(n, w_grp, b_grp, w_exp, b_exp, w1, w3, w2):
    B, T, D = n.shape
    M = B * T
    x = n.reshape(M, D)
    g_logits = (x @ w_grp).astype(jnp.float32) + b_grp.astype(jnp.float32)
    g_idx = jnp.argmax(g_logits, axis=-1).astype(jnp.int32)
    g_prob = jnp.take_along_axis(jax.nn.softmax(g_logits, axis=-1), g_idx[:, None], axis=-1)
    e_logits = ((x @ w_exp).astype(jnp.float32) + b_exp.astype(jnp.float32)).reshape(M, N_GROUPS, EXPERTS_PER_GROUP)
    e_logits = jnp.take_along_axis(e_logits, g_idx[:, None, None], axis=1)[:, 0]
    top_v, top_i = lax.top_k(e_logits, TOP_K)
    gate = jax.nn.softmax(top_v, axis=-1) * g_prob
    expert_id = g_idx[:, None] * EXPERTS_PER_GROUP + top_i.astype(jnp.int32)
    A = M * TOP_K
    e_flat = expert_id.reshape(A)
    tok_flat = jnp.repeat(jnp.arange(M, dtype=jnp.int32), TOP_K)
    order = jnp.argsort(e_flat)
    e_s, tok_s, w_s = e_flat[order], tok_flat[order], gate.reshape(A)[order]
    counts = jnp.bincount(e_flat, length=N_EXPERTS)
    start = jnp.cumsum(counts) - counts
    padded = (counts + MOE_BLOCK - 1) // MOE_BLOCK * MOE_BLOCK
    p_end = jnp.cumsum(padded)
    dest = (p_end - padded)[e_s] + jnp.arange(A) - start[e_s]
    R = (-(-A // MOE_BLOCK) + N_EXPERTS) * MOE_BLOCK
    n_blk = R // MOE_BLOCK
    row_tok = jnp.zeros((R,), jnp.int32).at[dest].set(tok_s)
    row_w = jnp.zeros((R,), jnp.float32).at[dest].set(w_s)
    blk_exp = jnp.minimum(jnp.searchsorted(p_end, jnp.arange(n_blk) * MOE_BLOCK, side='right'), N_EXPERTS - 1)

    def expert_block(args):
        toks, e = args
        xb = x[toks]
        hb = jax.nn.silu(xb @ w1[e]) * (xb @ w3[e])
        return hb @ w2[e]

    y = lax.map(expert_block, (row_tok.reshape(n_blk, MOE_BLOCK), blk_exp))
    y = y.reshape(R, D).astype(jnp.float32) * row_w[:, None]
    out = jnp.zeros((M, D), jnp.float32).at[row_tok].add(y)
    return out.astype(n.dtype).reshape(B, T, D)

def first_inputs(seed: int = 0) -> dict:
    key = jax.random.key(seed)
    ks = jax.random.split(key, 17)
    nrm = jax.random.normal
    f = jnp.float32
    return {
        'x': nrm(ks[0], (BATCH, SEQ, D_MODEL), f),
        'norm1_g': 1.0 + 0.02 * nrm(ks[1], (DEPTH, D_MODEL), f),
        'w_in': nrm(ks[2], (DEPTH, D_MODEL, IN_COLS), f) * D_MODEL ** -0.5,
        'gla_gate_w2': nrm(ks[3], (DEPTH, GLA_LOWRANK, GLA_QK), f) * GLA_LOWRANK ** -0.5,
        'gla_gate_b': 0.1 * nrm(ks[4], (DEPTH, GLA_QK), f),
        'gla_norm_g': 1.0 + 0.02 * nrm(ks[5], (DEPTH, GLA_DV), f),
        'w_out': nrm(ks[6], (DEPTH, D_MIX, D_MODEL), f) * D_MIX ** -0.5,
        'norm2_g': 1.0 + 0.02 * nrm(ks[7], (DEPTH, D_MODEL), f),
        'router_group_w': nrm(ks[8], (DEPTH, D_MODEL, N_GROUPS), f) * D_MODEL ** -0.5,
        'router_group_b': 0.01 * nrm(ks[9], (DEPTH, N_GROUPS), f),
        'router_expert_w': nrm(ks[10], (DEPTH, D_MODEL, N_EXPERTS), f) * D_MODEL ** -0.5,
        'router_expert_b': 0.01 * nrm(ks[11], (DEPTH, N_EXPERTS), f),
        'expert_w1': nrm(ks[12], (DEPTH, N_EXPERTS, D_MODEL, D_FF_EXPERT), f) * D_MODEL ** -0.5,
        'expert_w3': nrm(ks[13], (DEPTH, N_EXPERTS, D_MODEL, D_FF_EXPERT), f) * D_MODEL ** -0.5,
        'expert_w2': nrm(ks[14], (DEPTH, N_EXPERTS, D_FF_EXPERT, D_MODEL), f) * D_FF_EXPERT ** -0.5,
        'final_norm_g': 1.0 + 0.02 * nrm(ks[15], (D_MODEL,), f),
    }

def first_block(x, norm1_g, w_in, gla_gate_w2, gla_gate_b, gla_norm_g, w_out, norm2_g,
              router_group_w, router_group_b, router_expert_w, router_expert_b,
              expert_w1, expert_w3, expert_w2, final_norm_g):
    h = x
    for l in range(DEPTH):
        h = h + hybrid_mixer(rmsnorm(h, norm1_g[l]), w_in[l], gla_gate_w2[l], gla_gate_b[l],
                             gla_norm_g[l], w_out[l])
        h = h + hier_moe(rmsnorm(h, norm2_g[l]), router_group_w[l], router_group_b[l],
                         router_expert_w[l], router_expert_b[l],
                         expert_w1[l], expert_w3[l], expert_w2[l])
    return rmsnorm(h, final_norm_g)


LRU_WIDTH = 1024
LRU_HEADS = 16
LRU_HEAD_DIM = LRU_WIDTH // LRU_HEADS
LRU_CONV = 4
LRU_C = 8.0
HYENA_WIDTH = 1024
HYENA_ORDER = 2
HYENA_CONV = 3
FILTER_EMB = 33
FILTER_BANDS = (FILTER_EMB - 1) // 2
FILTER_HIDDEN = 64
DECAY_FAST = 0.3
DECAY_SLOW = 1.5
DECAY_TARGET = 1e-2
N_BRANCHES = 2
IN_COLS_2 = 2 * LRU_WIDTH + (HYENA_ORDER + 1) * HYENA_WIDTH + N_BRANCHES * D_MODEL
N_EXPERTS_2 = 16
CAPACITY_FACTOR = 2
D_FF_EXPERT_2 = 2 * D_MODEL


def rmsnorm_2(x, g):
    xf = x.astype(jnp.float32)
    y = xf * lax.rsqrt(jnp.mean(xf * xf, axis=-1, keepdims=True) + EPS)
    return (y * g.astype(jnp.float32)).astype(x.dtype)

def dwconv(x, w, b, pad):
    C = x.shape[-1]
    y = lax.conv_general_dilated(x, w[:, None, :].astype(x.dtype), window_strides=(1,), padding=[pad],
                                 dimension_numbers=("NWC", "WIO", "NWC"), feature_group_count=C)
    return y + b.astype(x.dtype)

def rg_lru(xa, w_r, b_r, w_i, b_i, lam, reverse):
    B, S, W = xa.shape
    xh = xa.reshape(B, S, LRU_HEADS, LRU_HEAD_DIM)
    r = jax.nn.sigmoid(jnp.einsum('bshi,hij->bshj', xh, w_r.astype(jnp.float32)).reshape(B, S, W) + b_r.astype(jnp.float32))
    i = jax.nn.sigmoid(jnp.einsum('bshi,hij->bshj', xh, w_i.astype(jnp.float32)).reshape(B, S, W) + b_i.astype(jnp.float32))
    log_a = -LRU_C * r * jax.nn.softplus(-lam.astype(jnp.float32))
    a = jnp.exp(log_a)
    mult = jnp.sqrt(jnp.maximum(1.0 - jnp.exp(2.0 * log_a), 0.0))
    pos = jnp.arange(S)[None, :, None]
    start = S - 1 if reverse else 0
    mult = jnp.where(pos == start, 1.0, mult)
    bx = mult * (i * xa)

    def combine(e1, e2):
        a1, b1 = e1
        a2, b2 = e2
        return a1 * a2, a2 * b1 + b2

    _, h = lax.associative_scan(combine, (a, bx), axis=1, reverse=reverse)
    return h

def hyena_filters(L, w1, b1, w2, b2, w3, freq):
    f32 = jnp.float32
    t = jnp.linspace(0.0, 1.0, L, dtype=f32)[:, None]
    w = (2.0 * math.pi / L) * jnp.arange(L, dtype=f32)[:, None]
    f = jnp.linspace(1e-4, FILTER_BANDS - 1, FILTER_BANDS, dtype=f32)[None, :]
    z = jnp.concatenate([t, jnp.cos(w * f), -jnp.sin(w * f)], axis=-1)
    freq = freq.astype(f32)
    h = jnp.sin(freq[0] * (z @ w1.astype(f32) + b1.astype(f32)))
    h = jnp.sin(freq[1] * (h @ w2.astype(f32) + b2.astype(f32)))
    h = (h @ w3.astype(f32)).reshape(L, HYENA_ORDER, 2, HYENA_WIDTH)
    min_decay = math.log(DECAY_TARGET) / DECAY_SLOW
    max_decay = math.log(DECAY_TARGET) / DECAY_FAST
    deltas = jnp.abs(jnp.linspace(min_decay, max_decay, HYENA_WIDTH, dtype=f32))
    decay = jnp.exp(-t * deltas[None, :])
    return h * decay[:, None, None, :]

def bidir_kernel(hf, hb):
    zero = jnp.zeros((1, hf.shape[1]), hf.dtype)
    return jnp.concatenate([hf, zero, hb[:0:-1]], axis=0)

def fftconv(u, k, bias):
    L = u.shape[1]
    U = jnp.fft.rfft(u, n=2 * L, axis=1)
    K = jnp.fft.rfft(k, axis=0)
    y = jnp.fft.irfft(U * K[None], n=2 * L, axis=1)[:, :L]
    return y + u * bias.astype(jnp.float32)

def second_inputs(seed: int = 0) -> dict:
    key = jax.random.key(seed)
    ks = jax.random.split(key, 32)
    f32 = jnp.float32
    nrm = lambda k, shape, s: (jax.random.normal(k, shape, f32) * s).astype(f32)
    Dp = DEPTH
    u = jax.random.uniform(ks[9], (Dp, 2, LRU_WIDTH), f32, 0.9, 0.999)
    a0 = u ** (1.0 / LRU_C)
    lam = jnp.log(a0) - jnp.log1p(-a0)
    return {
        "x": nrm(ks[0], (BATCH, SEQ, D_MODEL), 1.0),
        "g_mix": 1.0 + nrm(ks[1], (Dp, D_MODEL), 0.01),
        "w_in": nrm(ks[2], (Dp, D_MODEL, IN_COLS_2), D_MODEL ** -0.5),
        "conv_a_w": nrm(ks[3], (Dp, LRU_CONV, LRU_WIDTH), LRU_CONV ** -0.5),
        "conv_a_b": nrm(ks[4], (Dp, LRU_WIDTH), 0.01),
        "lru_w_r": nrm(ks[5], (Dp, 2, LRU_HEADS, LRU_HEAD_DIM, LRU_HEAD_DIM), LRU_HEAD_DIM ** -0.5),
        "lru_b_r": nrm(ks[6], (Dp, 2, LRU_WIDTH), 0.01),
        "lru_w_i": nrm(ks[7], (Dp, 2, LRU_HEADS, LRU_HEAD_DIM, LRU_HEAD_DIM), LRU_HEAD_DIM ** -0.5),
        "lru_b_i": nrm(ks[8], (Dp, 2, LRU_WIDTH), 0.01),
        "lru_lambda": lam,
        "w_a_out": nrm(ks[10], (Dp, LRU_WIDTH, D_MODEL), LRU_WIDTH ** -0.5),
        "conv_b_w": nrm(ks[11], (Dp, HYENA_CONV, (HYENA_ORDER + 1) * HYENA_WIDTH), HYENA_CONV ** -0.5),
        "conv_b_b": nrm(ks[12], (Dp, (HYENA_ORDER + 1) * HYENA_WIDTH), 0.01),
        "filt_w1": nrm(ks[13], (Dp, FILTER_EMB, FILTER_HIDDEN), FILTER_EMB ** -0.5),
        "filt_b1": nrm(ks[14], (Dp, FILTER_HIDDEN), 0.1),
        "filt_w2": nrm(ks[15], (Dp, FILTER_HIDDEN, FILTER_HIDDEN), FILTER_HIDDEN ** -0.5),
        "filt_b2": nrm(ks[16], (Dp, FILTER_HIDDEN), 0.1),
        "filt_w3": nrm(ks[17], (Dp, FILTER_HIDDEN, HYENA_ORDER * 2 * HYENA_WIDTH), 0.005),
        "filt_freq": 1.0 + nrm(ks[18], (Dp, 2, FILTER_HIDDEN), 0.01),
        "filt_bias": nrm(ks[19], (Dp, HYENA_ORDER, HYENA_WIDTH), 0.5),
        "w_b_out": nrm(ks[20], (Dp, HYENA_WIDTH, D_MODEL), HYENA_WIDTH ** -0.5),
        "w_o": nrm(ks[21], (Dp, D_MODEL, D_MODEL), D_MODEL ** -0.5),
        "g_ffn": 1.0 + nrm(ks[22], (Dp, D_MODEL), 0.01),
        "w_router": nrm(ks[23], (Dp, D_MODEL, N_EXPERTS_2), D_MODEL ** -0.5),
        "w_gate": nrm(ks[24], (Dp, N_EXPERTS_2, D_MODEL, D_FF_EXPERT_2), D_MODEL ** -0.5),
        "w_up": nrm(ks[25], (Dp, N_EXPERTS_2, D_MODEL, D_FF_EXPERT_2), D_MODEL ** -0.5),
        "w_down": nrm(ks[26], (Dp, N_EXPERTS_2, D_FF_EXPERT_2, D_MODEL), D_FF_EXPERT_2 ** -0.5),
        "g_final": 1.0 + nrm(ks[27], (D_MODEL,), 0.01),
    }

def second_block(x, g_mix, w_in, conv_a_w, conv_a_b, lru_w_r, lru_b_r, lru_w_i, lru_b_i, lru_lambda, w_a_out,
              conv_b_w, conv_b_b, filt_w1, filt_b1, filt_w2, filt_b2, filt_w3, filt_freq, filt_bias, w_b_out,
              w_o, g_ffn, w_router, w_gate, w_up, w_down, g_final):
    f32 = jnp.float32
    dt = x.dtype
    B, S, D = x.shape
    bidx = jnp.arange(B)[:, None, None]
    cap = CAPACITY_FACTOR * S // N_EXPERTS_2
    for l in range(DEPTH):
        h = rmsnorm_2(x, g_mix[l])
        proj = h @ w_in[l]
        a_x, a_gate, hy, gates = jnp.split(
            proj, [LRU_WIDTH, 2 * LRU_WIDTH, 2 * LRU_WIDTH + (HYENA_ORDER + 1) * HYENA_WIDTH], axis=-1)

        xa = dwconv(a_x, conv_a_w[l], conv_a_b[l], (LRU_CONV // 2, LRU_CONV - 1 - LRU_CONV // 2)).astype(f32)
        h_a = (rg_lru(xa, lru_w_r[l, 0], lru_b_r[l, 0], lru_w_i[l, 0], lru_b_i[l, 0], lru_lambda[l, 0], False)
               + rg_lru(xa, lru_w_r[l, 1], lru_b_r[l, 1], lru_w_i[l, 1], lru_b_i[l, 1], lru_lambda[l, 1], True))
        y_a = (h_a * jax.nn.gelu(a_gate.astype(f32))).astype(dt) @ w_a_out[l]

        hy = dwconv(hy, conv_b_w[l], conv_b_b[l], (HYENA_CONV // 2, HYENA_CONV - 1 - HYENA_CONV // 2))
        v, x1, x2 = jnp.split(hy, HYENA_ORDER + 1, axis=-1)
        filt = hyena_filters(S, filt_w1[l], filt_b1[l], filt_w2[l], filt_b2[l], filt_w3[l], filt_freq[l])
        z = v.astype(f32)
        for n, gate in enumerate((x1, x2)):
            k = bidir_kernel(filt[:, n, 0], filt[:, n, 1])
            z = gate.astype(f32) * fftconv(z, k, filt_bias[l, n])
        y_b = z.astype(dt) @ w_b_out[l]

        g_a, g_b = jnp.split(jax.nn.sigmoid(gates.astype(f32)), N_BRANCHES, axis=-1)
        merged = (g_a * y_a.astype(f32) + g_b * y_b.astype(f32)).astype(dt)
        x = x + merged @ w_o[l]

        h = rmsnorm_2(x, g_ffn[l])
        aff = jax.nn.softmax((h @ w_router[l]).astype(f32), axis=-1)
        vals, idx = lax.top_k(jnp.swapaxes(aff, 1, 2), cap)
        xe = h[bidx, idx]
        gt = jnp.einsum('becd,edf->becf', xe, w_gate[l])
        up = jnp.einsum('becd,edf->becf', xe, w_up[l])
        ye = jnp.einsum('becf,efd->becd', jax.nn.silu(gt) * up, w_down[l])
        ye = ye * vals[..., None].astype(ye.dtype)
        x = x + jnp.zeros_like(x).at[bidx, idx].add(ye.astype(dt))
    return rmsnorm_2(x, g_final)


def setup_inputs(seed=0):
    out = dict(first_inputs(seed))
    for name, value in second_inputs(seed + 1).items():
        if name != "x":
            out[name + "_2"] = value
    return out


def reference(
    x, norm1_g, w_in, gla_gate_w2, gla_gate_b, gla_norm_g, w_out, norm2_g, router_group_w,
    router_group_b, router_expert_w, router_expert_b, expert_w1, expert_w3, expert_w2,
    final_norm_g, g_mix_2, w_in_2, conv_a_w_2, conv_a_b_2, lru_w_r_2, lru_b_r_2, lru_w_i_2,
    lru_b_i_2, lru_lambda_2, w_a_out_2, conv_b_w_2, conv_b_b_2, filt_w1_2, filt_b1_2, filt_w2_2,
    filt_b2_2, filt_w3_2, filt_freq_2, filt_bias_2, w_b_out_2, w_o_2, g_ffn_2, w_router_2,
    w_gate_2, w_up_2, w_down_2, g_final_2,
):
    x = first_block(
        x, norm1_g, w_in, gla_gate_w2, gla_gate_b, gla_norm_g, w_out, norm2_g, router_group_w,
        router_group_b, router_expert_w, router_expert_b, expert_w1, expert_w3, expert_w2,
        final_norm_g,
    )
    return second_block(
        x, g_mix_2, w_in_2, conv_a_w_2, conv_a_b_2, lru_w_r_2, lru_b_r_2, lru_w_i_2, lru_b_i_2,
        lru_lambda_2, w_a_out_2, conv_b_w_2, conv_b_b_2, filt_w1_2, filt_b1_2, filt_w2_2,
        filt_b2_2, filt_w3_2, filt_freq_2, filt_bias_2, w_b_out_2, w_o_2, g_ffn_2, w_router_2,
        w_gate_2, w_up_2, w_down_2, g_final_2,
    )


_drawn_inputs = setup_inputs


def setup_inputs(seed=0):
    import zlib

    import numpy as np

    out = dict(_drawn_inputs(seed))
    spreads = {}
    factors = {'router_group_b': 4.757,
     'router_expert_b': 3.283,
     'g_mix_2': 6.521,
     'lru_b_r_2': 64.0,
     'lru_b_i_2': 64.0,
     'conv_b_b_2': 18.638,
     'filt_b1_2': 3.148,
     'filt_freq_2': 8.0,
     'g_ffn_2': 41.744,
     'g_final_2': 31.478,
     'conv_a_b_2': 8.0}
    for name, (base, spread) in spreads.items():
        noise = np.random.default_rng([zlib.crc32(name.encode()), seed]).standard_normal(out[name].shape)
        drawn = base * np.exp(spread * noise) if base else spread * noise
        out[name] = jnp.asarray(drawn.astype(out[name].dtype))
    for name, factor in factors.items():
        out[name] = (out[name] * factor).astype(out[name].dtype)
    return out
```

```python
from contextlib import ExitStack

import numpy as np

import concourse.bass as bass
from concourse import mybir

F32 = mybir.dt.float32
I32 = mybir.dt.int32
U32 = mybir.dt.uint32
ACT = mybir.ActivationFunctionType
ALU = mybir.AluOpType
AXX = mybir.AxisListType.X

P = 128
T = 1024
D = 1024
NT = T // P
ND = D // P
EPS = 1e-6
BANK = 512


class Store:

    used = []

    def __init__(self, nc, name):
        self.nc, self.name, self.stack = nc, name, ExitStack()

    def __enter__(self):
        self.stack.__enter__()
        return self

    def __exit__(self, *a):
        return self.stack.__exit__(*a)

    def sb(self, name, shape, dt=F32):
        return self.stack.enter_context(self.nc.sbuf_tensor(f"{self.name}_{name}", shape, dt))

    def ps(self, name, shape, dt=F32):
        return self.stack.enter_context(self.nc.psum_tensor(f"{self.name}_{name}", shape, dt))

    def sem(self, name):
        Store.used.append(self.nc.alloc_semaphore(f"{self.name}_{name}"))
        return Store.used[-1]

    @staticmethod
    def give_back_semaphores(nc):
        nc.clear_and_free_semaphores(Store.used)
        nc.all_engine_barrier()
        Store.used = []


def first(i):
    return isinstance(i, int) and i == 0


def repeat(engine, n, body):
    body(0)
    with engine.Fori(1, n) as i:
        body(i)


def tile(t):
    return bass.ds(t, 1)


def row(vec):
    return vec.rearrange("(o n) -> o n", o=1)


def setup_constants(nc, ident, ones_col):
    cleared = nc.alloc_semaphore("ident_cleared")
    with nc.Block() as block:
        @block.gpsimd
        def _(pool):
            pool.memset(ident[:, :], 0.0).then_inc(cleared, 1)
            pool.memset(ones_col[:, :], 1.0)
            pool.wait_ge(cleared, 1)
            pool.affine_select(out=ident[:, :], in_=ident[:, :], compare_op=ALU.not_equal, fill=1.0,
                               base=0, pattern=[[-1, P]], channel_multiplier=1)


def norm_phase(nc, name, src, gain, ident, natural=None, transposed=None):
    with Store(nc, name) as m:
        xt = [m.sb(f"x{b}", [P, D]) for b in range(2)]
        xn = [m.sb(f"xn{b}", [P, D]) for b in range(2)]
        squares = m.sb("squares", [P, D])
        gain_b = m.sb("gain", [P, D])
        ssum = m.sb("ssum", [P, 2])
        rms = m.sb("rms", [P, 2])
        rstd = m.sb("rstd", [P, 2])
        eps = m.sb("eps", [P, 1])
        turned = [m.ps(f"turned{b}", [P, 2, BANK]) for b in range(2)]
        eps_set = m.sem("eps_set")
        x_loaded = [m.sem(f"x_loaded{b}") for b in range(2)]
        gain_loaded = m.sem("gain_loaded")
        ssum_ready = m.sem("ssum_ready")
        rms_ready = m.sem("rms_ready")
        rstd_ready = m.sem("rstd_ready")
        xn_ready = m.sem("xn_ready")
        xn_turned = m.sem("xn_turned")
        turned_copied = m.sem("turned_copied")
        stored = [m.sem(f"stored{b}") for b in range(2)]
        src_t = src.rearrange("(t p) d -> t p d", p=P)
        nat_t = natural.rearrange("(t p) d -> t p d", p=P) if natural is not None else None
        with nc.Block() as block:
            @block.sync
            def _(sp):
                sp.dma_start(gain_b[:, :], row(gain).partition_broadcast(P)).then_inc(gain_loaded, 16)

                def load(i):
                    for b in range(2):
                        if not first(i):
                            sp.wait_ge(xn_ready, 2 * i + b - 1)
                        sp.dma_start(xt[b][:, :], src_t[tile(2 * i + b), :, :]).then_inc(x_loaded[b], 16)
                repeat(sp, NT // 2, load)

            @block.gpsimd
            def _(pool):
                if natural is None:
                    return
                with pool.Fori(0, NT // 2) as i:
                    for b in range(2):
                        pool.wait_ge(xn_ready, 2 * i + b + 1)
                        pool.dma_start(nat_t[tile(2 * i + b), :, :], xn[b][:, :]).then_inc(stored[b], 16)
                for b in range(2):
                    pool.wait_ge(stored[b], 16 * (NT // 2))

            @block.scalar
            def _(act):
                act.wait_ge(eps_set, 1)
                with act.Fori(0, NT // 2) as i:
                    for b in range(2):
                        act.wait_ge(x_loaded[b], 16 * (i + 1))
                        act.activation(squares[:, :], xt[b][:, :], ACT.Square, accum_out=ssum[:, b:b + 1]).then_inc(ssum_ready, 1)
                        act.wait_ge(ssum_ready, 2 * i + b + 1)
                        act.activation(rms[:, b:b + 1], ssum[:, b:b + 1], ACT.Sqrt, scale=1.0 / D, bias=eps[:, :]).then_inc(rms_ready, 1)
                    for b in range(2 if transposed is not None else 0):
                        act.wait_ge(xn_turned, 2 * i + b + 1)
                        act.activation(transposed[:, :, bass.ds((2 * i + b) * P, P)],
                                       turned[b][:, :, :].rearrange("p a (k t) -> p (a k) t", t=P), ACT.Copy).then_inc(turned_copied, 1)

            @block.vector
            def _(dve):
                dve.memset(eps[:, :], EPS).then_inc(eps_set, 1)
                dve.wait_ge(gain_loaded, 16)

                def norm(i):
                    for b in range(2):
                        dve.wait_ge(rms_ready, 2 * i + b + 1)
                        dve.reciprocal(rstd[:, b:b + 1], rms[:, b:b + 1]).then_inc(rstd_ready, 1)
                        dve.wait_ge(rstd_ready, 2 * i + b + 1)
                        if not first(i):
                            if transposed is not None:
                                dve.wait_ge(xn_turned, 2 * i + b - 1)
                            if natural is not None:
                                dve.wait_ge(stored[b], 16 * i)
                        dve.scalar_tensor_tensor(xn[b][:, :], xt[b][:, :], rstd[:, b:b + 1], gain_b[:, :],
                                                 ALU.mult, ALU.mult).then_inc(xn_ready, 1)
                repeat(dve, NT // 2, norm)

            @block.tensor
            def _(pe):
                if transposed is None:
                    return

                def turn(i):
                    for b in range(2):
                        pe.wait_ge(xn_ready, 2 * i + b + 1)
                        if not first(i):
                            pe.wait_ge(turned_copied, 2 * i + b - 1)
                        for k in range(ND):
                            last = nc.tensor.transpose(turned[b][:, k // 4, bass.ts(k % 4, P)], xn[b][:, bass.ts(k, P)], ident[:, :])
                        last.then_inc(xn_turned, 1)
                repeat(pe, NT // 2, turn)


def residual_phase(nc, name, act_T, w, res, outs):
    RING = 4
    with Store(nc, name) as m:
        w_sb = m.sb("w", [P, ND, D])
        res_sb = m.sb("res", [P, NT, D])
        out_sb = [m.sb(f"out{r}", [P, BANK]) for r in range(RING)]
        prod = [m.ps(f"prod{r}", [P, BANK]) for r in range(RING)]
        w_loaded = [m.sem(f"w_loaded{h}") for h in range(2)]
        res_loaded = m.sem("res_loaded")
        prod_ready = m.sem("prod_ready")
        sum_ready = m.sem("sum_ready")
        stored = [m.sem(f"stored{r}") for r in range(RING)]
        w_k = w.rearrange("(k p) n -> p k n", p=P)
        groups = [(h, t) for h in range(2) for t in range(NT)]
        with nc.Block() as block:
            @block.sync
            def _(sp):
                for h in range(2):
                    sp.dma_start(w_sb[:, :, bass.ts(h, BANK)], w_k[:, :, bass.ts(h, BANK)]).then_inc(w_loaded[h], 16)
                    if h == 0:
                        sp.dma_start(res_sb[:, :, :], res.rearrange("(t p) d -> p t d", p=P)).then_inc(res_loaded, 16)
                for g, (h, t) in enumerate(groups):
                    sp.wait_ge(sum_ready, g + 1)
                    for o in outs:
                        sp.dma_start(o[bass.ts(t, P), bass.ts(h, BANK)], out_sb[g % RING][:, :]).then_inc(stored[g % RING], 16)
                for r in range(RING):
                    sp.wait_ge(stored[r], 16 * len(outs) * (len(groups) // RING))

            @block.tensor
            def _(pe):
                for g, (h, t) in enumerate(groups):
                    if t == 0:
                        pe.wait_ge(w_loaded[h], 16)
                    if g >= RING:
                        pe.wait_ge(sum_ready, g - RING + 1)
                    for k in range(ND):
                        last = nc.tensor.matmul(prod[g % RING][:, :], act_T[:, k, bass.ts(t, P)], w_sb[:, k, bass.ts(h, BANK)],
                                                start=(k == 0), stop=(k == ND - 1))
                    last.then_inc(prod_ready, 1)

            @block.vector
            def _(dve):
                dve.wait_ge(res_loaded, 16)
                for g, (h, t) in enumerate(groups):
                    dve.wait_ge(prod_ready, g + 1)
                    if g >= RING:
                        dve.wait_ge(stored[g % RING], 16 * len(outs) * (g // RING))
                    dve.tensor_tensor(out_sb[g % RING][:, :], prod[g % RING][:, :], res_sb[:, t, bass.ts(h, BANK)], ALU.add).then_inc(sum_ready, 1)


GLA_H, GLA_K, GLA_V, GLA_LOW = 4, 64, 128, 16
GLA_QK = GLA_H * GLA_K
GLA_VW = GLA_H * GLA_V
GLA_TAU = 16.0
ATT_H, ATT_D = 8, 64
ATT_W = ATT_H * ATT_D
COL_GQ, COL_GK, COL_GV, COL_GR = 0, GLA_QK, 2 * GLA_QK, 2 * GLA_QK + GLA_VW
COL_LOW = COL_GR + GLA_VW
COL_AQ = COL_LOW + GLA_LOW
COL_AK, COL_AV = COL_AQ + ATT_W, COL_AQ + 2 * ATT_W
LEVELS = [1 << s for s in range(7)]


def gla_level_masks():
    key, query = np.arange(P)[:, None], np.arange(P)[None, :]
    masks = [(key // (2 * s) == query // (2 * s)) & (key // s % 2 == 0) & (query // s % 2 == 1) for s in LEVELS]
    masks.append(key == query)
    return np.ascontiguousarray(np.stack(masks, axis=1).astype(np.uint32))


def gla_phase(nc, n_T, w_in, gate_w2, gate_b, norm_g, masks, ident, o_T):
    NQ = GLA_QK // P
    RING = 4
    with Store(nc, "gla") as m:
        wqk = m.sb("wqk", [P, ND, 2 * GLA_QK])
        wv = m.sb("wv", [P, ND, GLA_VW])
        wr = m.sb("wr", [P, ND, GLA_VW])
        wlow = m.sb("wlow", [P, ND, GLA_LOW])
        w2 = m.sb("w2", [GLA_LOW, GLA_QK])
        bias = m.sb("bias", [P, NQ])
        ng_b = m.sb("ng", [P, GLA_V])
        mask = m.sb("mask", [P, len(LEVELS) + 1, P], U32)
        q_T = m.sb("q", [P, NQ, T])
        k_T = m.sb("k", [P, NQ, T])
        cum = m.sb("cum", [P, NQ, T])
        t1 = m.sb("t1", [P, NQ, T])
        mix = [m.sb(f"mix{b}", [P, NQ, T]) for b in range(2)]
        v = m.sb("v", [P, NT, GLA_VW])
        gate = m.sb("gate", [P, NT, GLA_VW])
        low_T = mix[1][0:GLA_LOW, 0, :]
        t2 = mix[0]
        score_T = wqk[:, :, :].rearrange("p t (h q) -> p t h q", q=P)
        kd = wv[:, 0:NT // 2, :].rearrange("p a (b c) -> p (a b) c", c=GLA_QK)
        state = wr[:, :, :].rearrange("p a (t v) -> p (a t) v", v=2 * GLA_V).rearrange("p (j t) v -> p j t v", j=NQ)
        a_tile = m.sb("a_tile", [P, NQ, NT])
        o_n = [m.sb(f"o_n{b}", [P, GLA_VW]) for b in range(2)]
        osq = m.sb("osq", [P, GLA_VW])
        ssum = m.sb("ssum", [P, NT, GLA_H])
        rms = m.sb("rms", [P, NT, GLA_H])
        rstd = m.sb("rstd", [P, NT, GLA_H])
        eps = m.sb("eps", [P, 1])
        one = m.sb("one", [P, P])
        two_banks = [m.ps(f"banks{r}", [P, 2, BANK]) for r in range(4)]
        bank = [two_banks[r // 2][:, r % 2, :] for r in range(8)]
        w_loaded = {n: m.sem(n + "_loaded") for n in ("low", "small", "qk", "v", "r", "mask")}
        proj_ready = m.sem("proj_ready")
        proj_read = m.sem("proj_read")
        low_ready = m.sem("low_ready")
        la_step = m.sem("la_step")
        ln_ready = m.sem("ln_ready")
        dve_step = m.sem("dve_step")
        diff_ready = m.sem("diff_ready")
        decay_ready = m.sem("decay_ready")
        mix_ready = m.sem("mix_ready")
        scored = m.sem("scored")
        picked = m.sem("picked")
        kd_turned = m.sem("kd_turned")
        kd_ready = m.sem("kd_ready")
        update_ready = m.sem("update_ready")
        state_ready = m.sem("state_ready")
        o_ready = m.sem("o_ready")
        osq_ready = m.sem("osq_ready")
        osum_ready = m.sem("osum_ready")
        rms_ready = m.sem("rms_ready")
        on_ready = m.sem("on_ready")
        on_turned = m.sem("on_turned")
        o_stored = m.sem("o_stored")
        w_k = w_in.rearrange("(k p) n -> p k n", p=P)
        PROJ = [("low", 0, h) for h in range(2)] + [("z", j, h) for j in range(NQ) for h in range(2)]
        PROJ += [(n, j, h) for n in ("q", "k") for j in range(NQ) for h in range(2)]
        PROJ += [("v", t, 0) for t in range(NT)] + [("r", t, 0) for t in range(NT)]
        N_LOW, N_Z, N_QK = 2, 2 + 2 * NQ, 2 + 6 * NQ
        N_V, N_PROJ = N_QK + NT, N_QK + 2 * NT
        NL = len(LEVELS)
        with nc.Block() as block:
            @block.sync
            def _(sp):
                sp.dma_start(wlow[:, :, :], w_k[:, :, COL_LOW:COL_LOW + GLA_LOW]).then_inc(w_loaded["low"], 16)
                sp.dma_start(w2[:, :], gate_w2).then_inc(w_loaded["small"], 16)
                with nc.allow_non_contiguous_dma(reason="a bias per partition"):
                    sp.dma_start(bias[:, :], gate_b.rearrange("(j p) -> p j", p=P)).then_inc(w_loaded["small"], 16)
                sp.dma_start(ng_b[:, :], row(norm_g).partition_broadcast(P)).then_inc(w_loaded["small"], 16)
                sp.dma_start(wqk[:, :, :], w_k[:, :, COL_GQ:COL_GQ + 2 * GLA_QK]).then_inc(w_loaded["qk"], 16)
                sp.dma_start(wv[:, :, :], w_k[:, :, COL_GV:COL_GV + GLA_VW]).then_inc(w_loaded["v"], 16)
                sp.dma_start(wr[:, :, :], w_k[:, :, COL_GR:COL_GR + GLA_VW]).then_inc(w_loaded["r"], 16)
                sp.dma_start(mask[:, :, :], masks).then_inc(w_loaded["mask"], 16)

            @block.tensor
            def _(pe):
                pe.wait_ge(w_loaded["low"], 16)
                for g, (what, j, h) in enumerate(PROJ):
                    out = bank[g % RING]
                    if g >= RING + N_LOW:
                        pe.wait_ge(proj_read, g - RING - N_LOW + 1)
                    elif g >= RING:
                        pe.wait_ge(low_ready, g - RING + 1)
                    if what == "z":
                        if g == N_LOW:
                            pe.wait_ge(w_loaded["small"], 48)
                            pe.wait_ge(low_ready, 2)
                        last = nc.tensor.matmul(out[:, :], w2[:, bass.ts(j, P)], low_T[:, bass.ts(h, BANK)], start=True, stop=True)
                    else:
                        if g == N_Z:
                            pe.wait_ge(w_loaded["qk"], 16)
                        if g == N_QK:
                            pe.wait_ge(w_loaded["v"], 16)
                        if g == N_V:
                            pe.wait_ge(w_loaded["r"], 16)
                        for k in range(ND):
                            if what == "low":
                                o, lhsT, rhs = out[0:GLA_LOW, :], wlow[:, k, :], n_T[:, k, bass.ts(h, BANK)]
                            elif what in "qk":
                                o, lhsT, rhs = out[:, :], wqk[:, k, bass.ds((what == "k") * GLA_QK + j * P, P)], n_T[:, k, bass.ts(h, BANK)]
                            else:
                                o, lhsT, rhs = out[:, :], n_T[:, k, bass.ts(j, P)], (wv if what == "v" else wr)[:, k, :]
                            last = nc.tensor.matmul(o, lhsT, rhs, start=(k == 0), stop=(k == ND - 1))
                    last.then_inc(proj_ready, 1)

                s = 0
                for level in range(NL + 1):
                    if level < NL:
                        pe.wait_ge(mix_ready, 2 * (level + 1))
                    if level == 0:
                        pe.wait_ge(proj_read, N_PROJ - N_LOW)
                    for t in range(NT):
                        if s >= 2:
                            pe.wait_ge(picked, s - 1)
                        for odd in range(2):
                            part = slice(odd * GLA_K, (odd + 1) * GLA_K)
                            for j in range(NQ):
                                lhsT = (k_T if level == NL else mix[level % 2])[part, j, bass.ts(t, P)]
                                rhs = (q_T if level == NL else mix[level % 2])[part, j, bass.ts(t, P)]
                                last = nc.tensor.matmul(two_banks[s % 2][:, odd, bass.ts(j, P)], lhsT, rhs, start=True, stop=True)
                        last.then_inc(scored, 1)
                        s += 1

                pe.wait_ge(mix_ready, 2 * NL + 1)
                for t in range(NT):
                    if t >= 2:
                        pe.wait_ge(kd_ready, t - 1)
                    for j in range(NQ):
                        last = nc.tensor.transpose(bank[4 + t % 2][:, bass.ts(j, P)], mix[NL % 2][:, j, bass.ts(t, P)], ident[:, :])
                    last.then_inc(kd_turned, 1)

                pe.wait_ge(picked, NT * (NL + 1))
                pe.wait_ge(mix_ready, 2 * NL + 2)
                for t in range(NT):
                    b = t % 2
                    pe.wait_ge(kd_ready, t + 1)
                    if t >= 1:
                        pe.wait_ge(state_ready, GLA_H * t)
                    for j in range(NQ):
                        last = nc.tensor.matmul(bank[6][:, bass.ts(j, 2 * GLA_V)], kd[:, t, bass.ts(j, P)], v[:, t, bass.ts(j, 2 * GLA_V)],
                                                start=True, stop=True)
                    last.then_inc(update_ready, 1)
                    if t >= 2:
                        pe.wait_ge(on_ready, t - 1)
                    for j in range(NQ):
                        if t > 0:
                            nc.tensor.matmul(bank[b][:, bass.ts(j, 2 * GLA_V)], mix[(NL + 1) % 2][:, j, bass.ts(t, P)], state[:, j, t, :],
                                             start=True, stop=False)
                        for odd in range(2):
                            hd = 2 * j + odd
                            last = nc.tensor.matmul(bank[b][:, bass.ts(hd, GLA_V)], score_T[:, t, odd * NQ + j, :], v[:, t, bass.ts(hd, GLA_V)],
                                                    start=(t == 0), stop=(t == 0 or odd == 1))
                    last.then_inc(o_ready, 1)
                    for u in ([t - 1] if t else []) + ([t] if t == NT - 1 else []):
                        pe.wait_ge(on_ready, u + 1)
                        if u >= 2:
                            pe.wait_ge(o_stored, u - 1)
                        for hd in range(GLA_H):
                            last = nc.tensor.transpose(bank[2 + u % 2][:, bass.ts(hd, P)], o_n[u % 2][:, bass.ts(hd, P)], ident[:, :])
                        last.then_inc(on_turned, 1)

            @block.scalar
            def _(act):
                act.wait_ge(w_loaded["small"], 48)
                for g in range(N_LOW, N_Z):
                    j, h = PROJ[g][1:]
                    act.wait_ge(proj_ready, g + 1)
                    act.activation(t1[:, j, bass.ts(h, BANK)], bank[g % RING][:, :], ACT.Identity, bias=bias[:, j:j + 1]).then_inc(proj_read, 1)
                act.wait_ge(proj_read, N_Z - N_LOW)
                act.activation(t2[:, :, :], t1[:, :, :], ACT.Abs).then_inc(la_step, 1)
                act.wait_ge(la_step, 1)
                act.activation(t2[:, :, :], t2[:, :, :], ACT.Exp, scale=-1.0).then_inc(la_step, 1)
                act.wait_ge(la_step, 2)
                act.activation(t2[:, :, :], t2[:, :, :], ACT.Ln, bias=one[:, 0:1]).then_inc(ln_ready, 1)
                for g in range(N_Z, N_PROJ):
                    what, j, h = PROJ[g]
                    act.wait_ge(proj_ready, g + 1)
                    if what in "qk":
                        act.activation((q_T if what == "q" else k_T)[:, j, bass.ts(h, BANK)], bank[g % RING][:, :], ACT.Copy,
                                       scale=GLA_K ** -0.5 if what == "q" else 1.0).then_inc(proj_read, 1)
                    elif what == "v":
                        act.activation(v[:, j, :], bank[g % RING][:, :], ACT.Copy).then_inc(proj_read, 1)
                    else:
                        act.activation(gate[:, j, :], bank[g % RING][:, :], ACT.Silu).then_inc(proj_read, 1)
                for level, s in enumerate(LEVELS):
                    act.wait_ge(diff_ready, level + 1)
                    halves = t1[:, :, :].rearrange("p j (n two s) -> p (j n) two s", two=2, s=s)
                    act.activation(halves[:, :, 0, :], halves[:, :, 0, :], ACT.Exp, scale=-1.0).then_inc(decay_ready, 1)
                    act.activation(halves[:, :, 1, :], halves[:, :, 1, :], ACT.Exp).then_inc(decay_ready, 1)
                act.wait_ge(diff_ready, NL + 1)
                act.activation(t1[:, :, :], t1[:, :, :], ACT.Exp, scale=-1.0).then_inc(decay_ready, 1)
                ends = cum[:, :, :].rearrange("p j (t c) -> p j t c", c=P)[:, :, :, P - 1]
                act.activation(a_tile[:, :, :], ends, ACT.Exp).then_inc(decay_ready, 1)
                act.wait_ge(decay_ready, 2 * NL + 2)
                act.activation(cum[:, :, :], cum[:, :, :], ACT.Exp).then_inc(decay_ready, 1)
                for t in range(NT):
                    act.wait_ge(kd_turned, t + 1)
                    act.activation(kd[:, t, :], bank[4 + t % 2][:, 0:GLA_QK], ACT.Copy).then_inc(kd_ready, 1)
                for t in range(NT):
                    act.wait_ge(osum_ready, t + 1)
                    act.activation(rms[:, t, :], ssum[:, t, :], ACT.Sqrt, scale=1.0 / GLA_V, bias=eps[:, :]).then_inc(rms_ready, 1)
                    for u in ([t - 1] if t else []) + ([t] if t == NT - 1 else []):
                        act.wait_ge(on_turned, u + 1)
                        act.activation(o_T[:, 0:GLA_H, bass.ts(u, P)], bank[2 + u % 2][:, :].rearrange("p (h t) -> p h t", t=P),
                                       ACT.Copy).then_inc(o_stored, 1)

            @block.vector
            def _(dve):
                dve.memset(eps[:, :], EPS).then_inc(dve_step, 1)
                dve.memset(one[:, :], 1.0).then_inc(dve_step, 1)
                n = 2
                for h in range(N_LOW):
                    dve.wait_ge(proj_ready, h + 1)
                    dve.tensor_copy(low_T[:, bass.ts(h, BANK)], bank[h][0:GLA_LOW, :]).then_inc(low_ready, 1)
                dve.wait_ge(proj_ready, N_QK)
                dve.memset(wqk[:, :, :], 0.0).then_inc(dve_step, 1)
                n += 1
                dve.wait_ge(ln_ready, 1)
                dve.tensor_scalar(t1[:, :, :], t1[:, :, :], 0.0, None, ALU.min).then_inc(dve_step, 1)
                n += 1
                dve.wait_ge(dve_step, n)
                dve.tensor_tensor(t1[:, :, :], t1[:, :, :], t2[:, :, :], ALU.subtract).then_inc(dve_step, 1)
                n += 1
                dve.wait_ge(dve_step, n)
                dve.tensor_scalar(t2[:, :, :], t1[:, :, :], 1.0 / GLA_TAU, None, ALU.mult).then_inc(dve_step, 1)
                n += 1
                dve.wait_ge(dve_step, n)
                for j in range(NQ):
                    for t in range(NT):
                        dve.tensor_tensor_scan(cum[:, j, bass.ts(t, P)], one[:, :], t2[:, j, bass.ts(t, P)], 0.0, ALU.mult, ALU.add).then_inc(dve_step, 1)
                        n += 1
                dve.wait_ge(dve_step, n)
                dve.wait_ge(w_loaded["mask"], 16)
                dve.wait_ge(proj_read, N_PROJ - N_LOW)
                dve.memset(wr[:, :, :], 0.0).then_inc(dve_step, 1)
                n += 1
                dve.wait_ge(dve_step, n)

                def level_diff(s):
                    blocks = cum[:, :, :].rearrange("p j (n b) -> p (j n) b", b=2 * s)
                    middle = blocks[:, :, s - 1:s].to_broadcast([P, NQ * T // (2 * s), 2 * s])
                    dve.tensor_tensor(t1[:, :, :].rearrange("p j (n b) -> p (j n) b", b=2 * s), blocks, middle, ALU.subtract).then_inc(diff_ready, 1)

                def pick(level):
                    for t in range(NT):
                        g = level * NT + t
                        dve.wait_ge(scored, g + 1)
                        dve.copy_predicated(score_T[:, t, :, :].rearrange("p (o j) q -> p o j q", o=2),
                            mask[:, level:level + 1, :].unsqueeze(1).to_broadcast([P, 2, NQ, P]),
                                            two_banks[g % 2][:, :, 0:NQ * P].rearrange("p o (j q) -> p o j q", q=P)).then_inc(picked, 1)

                for level, s in enumerate(LEVELS):
                    if level:
                        dve.wait_ge(mix_ready, 2 * level)
                    level_diff(s)
                    if level:
                        pick(level - 1)
                    dve.wait_ge(decay_ready, 2 * (level + 1))
                    out = mix[level % 2][:, :, :].rearrange("p j (n two s) -> p (j n) two s", two=2, s=s)
                    dec = t1[:, :, :].rearrange("p j (n two s) -> p (j n) two s", two=2, s=s)
                    if level >= 2:
                        dve.wait_ge(scored, NT * (level - 1))
                    for half, src in enumerate((k_T, q_T)):
                        dve.tensor_tensor(out[:, :, half, :], src[:, :, :].rearrange("p j (n two s) -> p (j n) two s", two=2, s=s)[:, :, half, :],
                                          dec[:, :, half, :], ALU.mult).then_inc(mix_ready, 1)
                dve.wait_ge(mix_ready, 2 * NL)
                tiles = cum[:, :, :].rearrange("p j (t c) -> p (j t) c", c=P)
                dve.tensor_tensor(t1[:, :, :].rearrange("p j (t c) -> p (j t) c", c=P), tiles,
                                  tiles[:, :, P - 1:P].to_broadcast([P, NQ * NT, P]), ALU.subtract).then_inc(diff_ready, 1)
                pick(NL - 1)
                pick(NL)
                dve.wait_ge(decay_ready, 2 * NL + 3)
                dve.tensor_tensor(mix[NL % 2][:, :, :], k_T[:, :, :], t1[:, :, :], ALU.mult).then_inc(mix_ready, 1)
                dve.tensor_tensor(mix[(NL + 1) % 2][:, :, :], q_T[:, :, :], cum[:, :, :], ALU.mult).then_inc(mix_ready, 1)
                dve.tensor_tensor(gate[:, :, :].rearrange("p t (h v) -> p (t h) v", v=GLA_V), gate[:, :, :].rearrange("p t (h v) -> p (t h) v", v=GLA_V),
                                  ng_b[:, :].rearrange("p (o v) -> p o v", o=1).to_broadcast([P, NT * GLA_H, GLA_V]), ALU.mult).then_inc(dve_step, 1)
                n += 1
                for t in range(NT):
                    dve.wait_ge(update_ready, t + 1)
                    if t:
                        dve.wait_ge(state_ready, GLA_H * t)
                    for hd in range(GLA_H):
                        j, part, cols = hd // 2, slice((hd % 2) * GLA_K, (hd % 2 + 1) * GLA_K), slice((hd % 2) * GLA_V, (hd % 2 + 1) * GLA_V)
                        new = bank[6][part, bass.ts(hd, GLA_V)]
                        if t == 0:
                            dve.tensor_copy(state[part, j, 1, cols], new).then_inc(state_ready, 1)
                        elif t + 1 < NT:
                            dve.scalar_tensor_tensor(state[part, j, t + 1, cols], state[part, j, t, cols], a_tile[part, j, t:t + 1], new,
                                                     ALU.mult, ALU.add).then_inc(state_ready, 1)
                    dve.wait_ge(o_ready, t + 1)
                    o = bank[t % 2][:, :]
                    if t >= 2:
                        dve.wait_ge(on_turned, t - 1)
                    dve.tensor_copy(o_n[t % 2][:, :], o).then_inc(dve_step, 1)
                    n += 1
                    dve.wait_ge(dve_step, n)
                    dve.tensor_tensor(osq[:, :], o_n[t % 2][:, :], o_n[t % 2][:, :], ALU.mult).then_inc(dve_step, 1)
                    n += 1
                    dve.wait_ge(dve_step, n)
                    dve.reduce_sum(ssum[:, t, :], osq[:, :].rearrange("p (h v) -> p h v", v=GLA_V), axis=AXX).then_inc(osum_ready, 1)
                    dve.wait_ge(rms_ready, t + 1)
                    dve.reciprocal(rstd[:, t, :], rms[:, t, :]).then_inc(dve_step, 1)
                    n += 1
                    dve.tensor_tensor(o_n[t % 2][:, :], o_n[t % 2][:, :], gate[:, t, :], ALU.mult).then_inc(dve_step, 1)
                    n += 1
                    dve.wait_ge(dve_step, n)
                    dve.tensor_tensor(o_n[t % 2][:, :].rearrange("p (h v) -> p h v", v=GLA_V), o_n[t % 2][:, :].rearrange("p (h v) -> p h v", v=GLA_V),
                                      rstd[:, t, :].unsqueeze(2).to_broadcast([P, GLA_H, GLA_V]), ALU.mult).then_inc(on_ready, 1)


DILATIONS = ((128, 1), (512, 4), (2048, 16))
MASKED = -1e30


def attention_bias():
    q = np.arange(P)[:, None, None]
    back = (np.arange(NT - 1, -1, -1)[None, :, None] * P + q - np.arange(P)[None, None, :])
    count = sum(((back >= 0) & (back <= w) & (back % d == 0)).astype(np.int64) for w, d in DILATIONS)
    return np.where(count > 0, np.log(np.maximum(count, 1)), MASKED).astype(np.float32).reshape(P, T)


def attention_phase(nc, n_T, w_in, bias, ident, o_T):
    PAIRS = ATT_H // 2
    NSTEP = 2 * NT
    NEED = [n % NT + 1 for n in range(NSTEP)]
    with Store(nc, "att") as m:
        w = {n: m.sb("w" + n, [P, ND, P]) for n in "qkv"}
        proj = {n: m.sb(n + "T", [P, T]) for n in "qkv"}
        v = m.sb("v", [P, NT, P])
        bias_sb = m.sb("bias", [P, T])
        logit = [m.sb(f"logit{b}", [P, T]) for b in range(2)]
        prob = [m.sb(f"prob{b}", [P, T]) for b in range(2)]
        prob_T = [m.sb(f"probT{b}", [P, NT, P]) for b in range(2)]
        top = m.sb("top", [P, NSTEP])
        neg_top = m.sb("neg_top", [P, NSTEP])
        den = m.sb("den", [P, NSTEP])
        rden = m.sb("rden", [P, NSTEP])
        o_rows = m.sb("o_rows", [P, NT, P])
        score = [m.ps(f"score{b}", [P, 2, BANK]) for b in range(2)]
        turned = m.ps("turned", [P, 2, BANK])
        o_ps = [m.ps(f"o{b}", [P, BANK]) for b in range(2)]
        w_loaded = m.sem("w_loaded")
        bias_loaded = m.sem("bias_loaded")
        proj_ready = m.sem("proj_ready")
        proj_read = m.sem("proj_read")
        v_turned = m.sem("v_turned")
        v_ready = m.sem("v_ready")
        score_ready = m.sem("score_ready")
        top_found = m.sem("top_found")
        top_ready = m.sem("top_ready")
        prob_ready = m.sem("prob_ready")
        prob_turned = m.sem("prob_turned")
        probT_ready = m.sem("probT_ready")
        o_ready = m.sem("o_ready")
        rden_ready = m.sem("rden_ready")
        o_normed = m.sem("o_normed")
        o_turned = m.sem("o_turned")
        o_stored = m.sem("o_stored")
        w_k = w_in.rearrange("(k p) n -> p k n", p=P)
        PROJ = [(n, h) for n in "qkv" for h in range(2)]
        proj_bank = [score[g // 2 % 2][:, g % 2, :] for g in range(len(PROJ))]
        NP = len(PROJ)
        with nc.Block() as block:
            @block.sync
            def _(sp):
                sp.dma_start(bias_sb[:, :], bias).then_inc(bias_loaded, 16)

                def load(i):
                    if not first(i):
                        sp.wait_ge(proj_ready, NP * i)
                    for n, col in (("q", COL_AQ), ("k", COL_AK), ("v", COL_AV)):
                        sp.dma_start(w[n][:, :, :], w_k[:, :, bass.ds(i * P + col, P)]).then_inc(w_loaded, 16)
                repeat(sp, PAIRS, load)

            @block.tensor
            def _(pe):
                def pair(i):
                    base = NSTEP * i
                    pe.wait_ge(w_loaded, 48 * (i + 1))
                    if not first(i):
                        pe.wait_ge(top_found, base)
                    for g, (n, h) in enumerate(PROJ):
                        if g >= 4:
                            pe.wait_ge(proj_read, NP * i + g - 3)
                        for k in range(ND):
                            last = nc.tensor.matmul(proj_bank[g], w[n][:, k, :], n_T[:, k, bass.ts(h, BANK)], start=(k == 0), stop=(k == ND - 1))
                        last.then_inc(proj_ready, 1)
                    pe.wait_ge(proj_read, NP * (i + 1))
                    if not first(i):
                        pe.wait_ge(o_stored, 2 * i)
                    for c in range(2):
                        for j in range(4):
                            last = nc.tensor.transpose(turned[:, c, bass.ts(j, P)], proj["v"][:, bass.ts(4 * c + j, P)], ident[:, :])
                        last.then_inc(v_turned, 1)

                    def scores(n):
                        hd, t = n // NT, n % NT
                        part = slice(hd * ATT_D, (hd + 1) * ATT_D)
                        if n >= 2:
                            pe.wait_ge(top_found, base + n - 1)
                        for c in range(2):
                            width = min(max(NEED[n] * P - c * BANK, 0), BANK)
                            if width:
                                last = nc.tensor.matmul(score[n % 2][:, c, 0:width], proj["q"][part, bass.ts(t, P)],
                                                        proj["k"][part, c * BANK:c * BANK + width], start=True, stop=True)
                        last.then_inc(score_ready, 1)

                    def turn(n):
                        pe.wait_ge(prob_ready, base + n + 1)
                        if n == 0:
                            pe.wait_ge(v_ready, 2 * (i + 1))
                        else:
                            pe.wait_ge(probT_ready, base + n)
                        for j in range(NEED[n]):
                            last = nc.tensor.transpose(turned[:, j // 4, bass.ts(j % 4, P)], prob[n % 2][:, bass.ts(j, P)], ident[:, :])
                        last.then_inc(prob_turned, 1)

                    def weigh(n):
                        hd = n // NT
                        pe.wait_ge(probT_ready, base + n + 1)
                        if not (first(i) and n < 2):
                            pe.wait_ge(o_normed, base + n - 1)
                        for j in range(NEED[n]):
                            last = nc.tensor.matmul(o_ps[n % 2][:, 0:ATT_D], prob_T[n % 2][:, j, :], v[:, j, bass.ts(hd, ATT_D)],
                                                    start=(j == 0), stop=(j == NEED[n] - 1))
                        last.then_inc(o_ready, 1)

                    for n in range(NSTEP + 2):
                        if n < NSTEP:
                            scores(n)
                        if 1 <= n <= NSTEP:
                            turn(n - 1)
                        if n >= 2:
                            weigh(n - 2)
                    pe.wait_ge(o_normed, base + NSTEP)
                    for c in range(2):
                        for j in range(4):
                            last = nc.tensor.transpose(turned[:, c, bass.ts(j, P)], o_rows[:, 4 * c + j, :], ident[:, :])
                        last.then_inc(o_turned, 1)
                repeat(pe, PAIRS, pair)

            @block.scalar
            def _(act):
                def pair(i):
                    base = NSTEP * i
                    for g, (n, h) in enumerate(PROJ):
                        act.wait_ge(proj_ready, NP * i + g + 1)
                        act.activation(proj[n][:, bass.ts(h, BANK)], proj_bank[g], ACT.Copy,
                                       scale=ATT_D ** -0.5 if n == "q" else 1.0).then_inc(proj_read, 1)
                    for c in range(2):
                        act.wait_ge(v_turned, 2 * i + c + 1)
                        act.activation(v[:, bass.ts(c, 4), :], turned[:, c, :].rearrange("p (j d) -> p j d", d=P), ACT.Copy).then_inc(v_ready, 1)

                    def copy_probs(n):
                        act.wait_ge(prob_turned, base + n + 1)
                        if not (first(i) and n < 2):
                            act.wait_ge(o_ready, base + n - 1)
                        act.activation(prob_T[n % 2][:, 0:NEED[n], :], turned[:, :, :].rearrange("p c (j q) -> p (c j) q", q=P)[:, 0:NEED[n], :],
                                       ACT.Copy).then_inc(probT_ready, 1)

                    for n in range(NSTEP):
                        act.wait_ge(top_ready, base + n + 1)
                        if not (first(i) and n < 2):
                            act.wait_ge(prob_turned, base + n - 1)
                        act.activation(prob[n % 2][:, 0:NEED[n] * P], logit[n % 2][:, 0:NEED[n] * P], ACT.Exp, bias=neg_top[:, n:n + 1],
                                       accum_out=den[:, n:n + 1]).then_inc(prob_ready, 1)
                        if n >= 1:
                            copy_probs(n - 1)
                    copy_probs(NSTEP - 1)
                    for c in range(2):
                        act.wait_ge(o_turned, 2 * i + c + 1)
                        act.activation(o_T[:, tile(i + GLA_VW // P), bass.ts(c, BANK)], turned[:, c, :], ACT.Copy).then_inc(o_stored, 1)
                repeat(act, PAIRS, pair)

            @block.vector
            def _(dve):
                dve.wait_ge(bias_loaded, 16)

                def pair(i):
                    base = NSTEP * i

                    def normed(n):
                        hd, t = n // NT, n % NT
                        dve.wait_ge(prob_ready, base + n + 1)
                        dve.reciprocal(rden[:, n:n + 1], den[:, n:n + 1]).then_inc(rden_ready, 1)
                        dve.wait_ge(rden_ready, base + n + 1)
                        dve.wait_ge(o_ready, base + n + 1)
                        if n == 0 and not first(i):
                            dve.wait_ge(o_turned, 2 * i)
                        dve.tensor_scalar(o_rows[:, t, bass.ts(hd, ATT_D)], o_ps[n % 2][:, 0:ATT_D], rden[:, n:n + 1], None, ALU.mult).then_inc(o_normed, 1)

                    for n in range(NSTEP):
                        cols = NEED[n] * P
                        dve.wait_ge(score_ready, base + n + 1)
                        if not (first(i) and n < 2):
                            dve.wait_ge(prob_ready, base + n - 1)
                        dve.memset(neg_top[:, n:n + 1], 0.0)
                        dve.tensor_tensor_reduce(out=logit[n % 2][:, 0:cols], in0=score[n % 2][:, :, :].rearrange("p c k -> p (c k)")[:, 0:cols],
                                                 in1=bias_sb[:, T - cols:T], scale=1.0, scalar=MASKED, op0=ALU.add, op1=ALU.max,
                                                 accum_out=top[:, n:n + 1]).then_inc(top_found, 1)
                        dve.wait_ge(top_found, base + n + 1)
                        dve.tensor_scalar(neg_top[:, n:n + 1], top[:, n:n + 1], -1.0, None, ALU.mult).then_inc(top_ready, 1)
                        if n >= 2:
                            normed(n - 2)
                    normed(NSTEP - 2)
                    normed(NSTEP - 1)
                repeat(dve, PAIRS, pair)


N_EXP, N_GRP, F_EXP = 32, 4, 512
PER_GRP = N_EXP // N_GRP
SLOTS = P
N_OVER = 2 * T // SLOTS - 1
N_BLK = N_EXP + N_OVER
BIG = 1e30


class Chain:

    def __init__(self, engine, sem):
        self.engine, self.sem, self.n = engine, sem, 0

    def then(self, instruction):
        instruction.then_inc(self.sem, 1)
        self.n += 1
        self.engine.wait_ge(self.sem, self.n)


def router_phase(nc, h_T, w_grp, b_grp, w_exp, b_exp, tables, row_tok, y_rows):
    gates, dest, idx_all, over_exp, n_over = (tables[n] for n in ("gates", "dest", "idx_all", "over_exp", "n_over"))
    NG4, NE = N_GRP, N_EXP
    with Store(nc, "router") as m:
        w = m.sb("w", [P, ND, NG4 + NE])
        bias = m.sb("bias", [P, NG4 + NE])
        g = m.sb("g", [P, NT, NG4])
        e = m.sb("e", [P, NT, NE])
        g_hot = m.sb("g_hot", [P, NT, NG4])
        gt = m.sb("gt", [P, NT, NG4])
        best = m.sb("best", [P, NT])
        where = m.sb("where", [P, NT])
        g_sum = m.sb("g_sum", [P, NT])
        hot = [m.sb(f"hot{j}", [P, NT, NE]) for j in range(2)]
        value = [m.sb(f"value{j}", [P, NT]) for j in range(2)]
        te = m.sb("te", [P, NT, NE])
        ratio = m.sb("ratio", [P, NT])
        both = m.sb("both", [P, NT, NE])
        pos = m.sb("pos", [P, NT, NE])
        total = m.sb("total", [P, NE])
        over = m.sb("over", [P, NE])
        over_end = m.sb("over_end", [P, NE])
        jump = m.sb("jump", [P, NE])
        ones_e = m.sb("ones_e", [P, NE])
        ones_sq = m.sb("ones_sq", [P, P])
        before = m.sb("before", [P, P])
        down4 = m.sb("down4", [P, NG4])
        down32 = m.sb("down32", [P, NE])
        first_row = m.sb("first_row", [P, NE])
        blk = m.sb("blk", [1, N_OVER])
        cmp = m.sb("cmp", [1, N_OVER, NE])
        cnt = m.sb("cnt", [1, N_OVER])
        dest_f = m.sb("dest_f", [P, NT, 2])
        tok = m.sb("tok", [P, NT], I32)
        zero = m.sb("zero", [P, N_BLK], I32)
        zero_rows = m.sb("zero_rows", [P, D])
        rows_cleared = m.sem("rows_cleared")
        y_cleared = m.sem("y_cleared")
        logit_ps = m.ps("logit", [P, BANK])
        pos_ps = m.ps("pos_ps", [P, BANK])
        tot_ps = m.ps("tot_ps", [P, BANK])
        loaded = m.sem("loaded")
        made = m.sem("made")
        zeroed = m.sem("zeroed")
        logits_ready = m.sem("logits_ready")
        diff_ready = m.sem("diff_ready")
        exp_ready = m.sem("exp_ready")
        both_ready = m.sem("both_ready")
        pos_ready = m.sem("pos_ready")
        step = m.sem("step")
        dest_ready = m.sem("dest_ready")
        listed = m.sem("listed")
        idx_loaded = m.sem("idx_loaded")

        def over_e(x):
            return x.unsqueeze(2).to_broadcast([P, NT, NE])

        def over_t(x, n):
            return x.unsqueeze(1).to_broadcast([P, NT, n])

        with nc.Block() as block:
            @block.sync
            def _(sp):
                for cols, src in ((slice(0, NG4), w_grp), (slice(NG4, NG4 + NE), w_exp)):
                    sp.dma_start(w[:, :, cols], src.rearrange("(k p) n -> p k n", p=P)).then_inc(loaded, 16)
                for cols, src in ((slice(0, NG4), b_grp), (slice(NG4, NG4 + NE), b_exp)):
                    sp.dma_start(bias[:, cols], row(src).partition_broadcast(P)).then_inc(loaded, 16)
                sp.wait_ge(rows_cleared, 1)
                sp.dma_start(y_rows[N_EXP * SLOTS:, :].rearrange("(b p) d -> p b d", p=P),
                             zero_rows[:, :].unsqueeze(1).to_broadcast([P, N_OVER, D])).then_inc(y_cleared, 16)
                sp.wait_ge(y_cleared, 16)

            @block.gpsimd
            def _(pool):
                pool.memset(zero_rows[:, :], 0.0).then_inc(rows_cleared, 1)
                pool.iota(down4[:, :], pattern=[[-1, NG4]], base=NG4, channel_multiplier=0, allow_small_or_imprecise_dtypes=True).then_inc(made, 1)
                pool.iota(down32[:, :], pattern=[[-1, NE]], base=NE, channel_multiplier=0, allow_small_or_imprecise_dtypes=True).then_inc(made, 1)
                pool.iota(first_row[:, :], pattern=[[SLOTS, NE]], base=0, channel_multiplier=0, allow_small_or_imprecise_dtypes=True).then_inc(made, 1)
                pool.iota(blk[:, :], pattern=[[1, N_OVER]], base=0, channel_multiplier=0, allow_small_or_imprecise_dtypes=True).then_inc(made, 1)
                pool.iota(tok[:, :], pattern=[[P, NT]], base=0, channel_multiplier=1).then_inc(made, 1)
                pool.memset(ones_e[:, :], 1.0).then_inc(made, 1)
                pool.memset(ones_sq[:, :], 1.0).then_inc(made, 1)
                pool.memset(zero[:, :], 0).then_inc(made, 1)
                pool.wait_ge(made, 8)
                pool.affine_select(out=before[:, :], in_=ones_sq[:, :], compare_op=ALU.is_gt, fill=0.0, base=0, pattern=[[1, P]],
                                   channel_multiplier=-1).then_inc(made, 1)
                pool.dma_start(row_tok.rearrange("(p b) o -> p (b o)", p=P), zero[:, :]).then_inc(zeroed, 16)
                pool.wait_ge(zeroed, 16)
                pool.wait_ge(dest_ready, 1)
                for t in range(NT):
                    for j in range(2):
                        pool.indirect_dma_start(out=row_tok, out_offset=bass.IndirectOffsetOnAxis(ap=dest[:, 2 * t + j:2 * t + j + 1], axis=0),
                                                in_=tok[:, t:t + 1], in_offset=None).then_inc(listed, 16)
                pool.wait_ge(listed, 16 * 2 * NT)
                with nc.allow_non_contiguous_dma(reason="a row number per partition"):
                    pool.dma_start(idx_all[:, :], row_tok.rearrange("(b p) o -> p (b o)", p=P)).then_inc(idx_loaded, 16)
                pool.wait_ge(idx_loaded, 16)

            @block.tensor
            def _(pe):
                pe.wait_ge(loaded, 64)
                for t in range(NT):
                    for k in range(ND):
                        last = nc.tensor.matmul(logit_ps[:, bass.ts(t, NG4 + NE)], h_T[:, k, bass.ts(t, P)], w[:, k, :], start=(k == 0), stop=(k == ND - 1))
                last.then_inc(logits_ready, 1)
                pe.wait_ge(both_ready, 1)
                pe.wait_ge(made, 9)
                for t in range(NT):
                    for u in range(t):
                        nc.tensor.matmul(pos_ps[:, bass.ts(t, NE)], ones_sq[:, :], both[:, u, :], start=(u == 0), stop=False)
                    nc.tensor.matmul(pos_ps[:, bass.ts(t, NE)], before[:, :], both[:, t, :], start=(t == 0), stop=True)
                for u in range(NT):
                    last = nc.tensor.matmul(tot_ps[:, 0:NE], ones_sq[:, :], both[:, u, :], start=(u == 0), stop=(u == NT - 1))
                last.then_inc(pos_ready, 1)

            @block.scalar
            def _(act):
                act.wait_ge(diff_ready, 1)
                act.activation(gt[:, :, :], gt[:, :, :], ACT.Exp).then_inc(exp_ready, 1)
                act.wait_ge(diff_ready, 2)
                act.activation(ratio[:, :], ratio[:, :], ACT.Exp).then_inc(exp_ready, 1)

            @block.vector
            def _(dve):
                c = Chain(dve, step)
                dve.wait_ge(loaded, 64)
                dve.wait_ge(made, 9)
                dve.wait_ge(logits_ready, 1)
                logits = logit_ps[:, 0:NT * (NG4 + NE)].rearrange("p (t n) -> p t n", n=NG4 + NE)
                c.then(dve.tensor_tensor(g[:, :, :], logits[:, :, 0:NG4], over_t(bias[:, 0:NG4], NG4), ALU.add))
                c.then(dve.tensor_tensor(e[:, :, :], logits[:, :, NG4:], over_t(bias[:, NG4:], NE), ALU.add))
                c.then(dve.reduce_max(best[:, :], g[:, :, :], axis=AXX))
                b4 = best[:, :].unsqueeze(2).to_broadcast([P, NT, NG4])
                dve.tensor_tensor(gt[:, :, :], g[:, :, :], b4, ALU.subtract).then_inc(diff_ready, 1)
                c.then(dve.tensor_tensor(g_hot[:, :, :], g[:, :, :], b4, ALU.is_ge))
                c.then(dve.tensor_tensor(g_hot[:, :, :], g_hot[:, :, :], over_t(down4[:, :], NG4), ALU.mult))
                c.then(dve.reduce_max(where[:, :], g_hot[:, :, :], axis=AXX))
                c.then(dve.tensor_tensor(g_hot[:, :, :], over_t(down4[:, :], NG4), where[:, :].unsqueeze(2).to_broadcast([P, NT, NG4]), ALU.is_equal))
                dve.wait_ge(exp_ready, 1)
                c.then(dve.reduce_sum(g_sum[:, :], gt[:, :, :], axis=AXX))
                hot8 = g_hot[:, :, :].rearrange("p t g -> p (t g)").unsqueeze(2).to_broadcast([P, NT * NG4, PER_GRP])
                e8 = e[:, :, :].rearrange("p t (g n) -> p (t g) n", n=PER_GRP)
                c.then(dve.tensor_tensor(e8, e8, hot8, ALU.mult))
                c.then(dve.tensor_scalar(g_hot[:, :, :], g_hot[:, :, :], 1.0, BIG, ALU.subtract, ALU.mult))
                c.then(dve.tensor_tensor(e8, e8, hot8, ALU.add))
                for j in range(2):
                    c.then(dve.reduce_max(value[j][:, :], e[:, :, :], axis=AXX))
                    c.then(dve.tensor_tensor(te[:, :, :], e[:, :, :], over_e(value[j][:, :]), ALU.is_ge))
                    c.then(dve.tensor_tensor(te[:, :, :], te[:, :, :], over_t(down32[:, :], NE), ALU.mult))
                    c.then(dve.reduce_max(where[:, :], te[:, :, :], axis=AXX))
                    c.then(dve.tensor_tensor(hot[j][:, :, :], over_t(down32[:, :], NE), over_e(where[:, :]), ALU.is_equal))
                    if j == 0:
                        c.then(dve.scalar_tensor_tensor(e[:, :, :], hot[0][:, :, :], -BIG, e[:, :, :], ALU.mult, ALU.add))
                dve.tensor_tensor(both[:, :, :], hot[0][:, :, :], hot[1][:, :, :], ALU.add).then_inc(both_ready, 1)
                dve.tensor_tensor(ratio[:, :], value[1][:, :], value[0][:, :], ALU.subtract).then_inc(diff_ready, 1)
                dve.wait_ge(exp_ready, 2)
                c.then(dve.tensor_scalar(best[:, :], ratio[:, :], 1.0, None, ALU.add))
                c.then(dve.tensor_tensor(best[:, :], best[:, :], g_sum[:, :], ALU.mult))
                c.then(dve.reciprocal(gates[:, 0, :], best[:, :]))
                c.then(dve.tensor_tensor(gates[:, 1, :], gates[:, 0, :], ratio[:, :], ALU.mult))
                dve.wait_ge(pos_ready, 1)
                c.then(dve.tensor_copy(pos[:, :, :], pos_ps[:, 0:NT * NE].rearrange("p (t n) -> p t n", n=NE)))
                c.then(dve.tensor_copy(total[:, :], tot_ps[:, 0:NE]))
                c.then(dve.tensor_scalar(over[:, :], total[:, :], float(SLOTS), None, ALU.is_gt))
                for n in range(2, T // SLOTS):
                    c.then(dve.scalar_tensor_tensor(over[:, :], total[:, :], float(n * SLOTS), over[:, :], ALU.is_gt, ALU.add))
                c.then(dve.tensor_tensor_scan(over_end[:, :], ones_e[:, :], over[:, :], 0.0, ALU.mult, ALU.add))
                c.then(dve.tensor_tensor(jump[:, :], over_end[:, :], over[:, :], ALU.subtract))
                c.then(dve.tensor_scalar(jump[:, :], jump[:, :], float(SLOTS), float((N_EXP - 1) * SLOTS), ALU.mult, ALU.add))
                c.then(dve.tensor_tensor(jump[:, :], jump[:, :], first_row[:, :], ALU.subtract))
                c.then(dve.tensor_scalar(te[:, :, :], pos[:, :, :], float(SLOTS), None, ALU.is_ge))
                c.then(dve.tensor_tensor(te[:, :, :], te[:, :, :], over_t(jump[:, :], NE), ALU.mult))
                c.then(dve.tensor_tensor(te[:, :, :], te[:, :, :], pos[:, :, :], ALU.add))
                c.then(dve.tensor_tensor(te[:, :, :], te[:, :, :], over_t(first_row[:, :], NE), ALU.add))
                for j in range(2):
                    c.then(dve.tensor_tensor(hot[j][:, :, :], hot[j][:, :, :], te[:, :, :], ALU.mult))
                    c.then(dve.reduce_sum(dest_f[:, :, j], hot[j][:, :, :], axis=AXX))
                dve.tensor_copy(dest[:, :], dest_f[:, :, :].rearrange("p t j -> p (t j)")).then_inc(dest_ready, 1)
                c.then(dve.tensor_tensor(cmp[:, :, :], over_end[0:1, :].unsqueeze(1).to_broadcast([1, N_OVER, NE]),
                                         blk[:, :].unsqueeze(2).to_broadcast([1, N_OVER, NE]), ALU.is_le))
                c.then(dve.reduce_sum(cnt[:, :], cmp[:, :, :], axis=AXX))
                c.then(dve.tensor_scalar(over_exp[:, :], cnt[:, :], float(N_EXP - 1), None, ALU.min))
                c.then(dve.tensor_copy(n_over[:, :], over_end[0:1, NE - 1:NE]))


CHUNK = F_EXP
PER_STEP = 4


class ExpertStore(Store):

    def __init__(self, nc, name, n_x):
        super().__init__(nc, name)
        self.n_x = n_x

    def __enter__(m):
        super().__enter__()
        m.w1 = [m.sb(f"w1_{b}", [P, ND, CHUNK]) for b in range(2)]
        m.w3 = [m.sb(f"w3_{b}", [P, ND, CHUNK]) for b in range(2)]
        m.w2 = [m.sb(f"w2_{b}", [P, CHUNK // P, D]) for b in range(2)]
        m.idx = m.sb("idx", [P, 1], I32)
        m.rows = [m.sb(f"rows{b}", [P, D]) for b in range(m.n_x)]
        m.x_T = [m.sb(f"xT{b}", [P, ND, SLOTS]) for b in range(m.n_x)]
        m.silu = m.sb("silu", [P, CHUNK])
        m.hid = m.sb("hid", [P, CHUNK])
        m.hid_T = m.sb("hidT", [P, CHUNK // P, SLOTS])
        m.y = [m.sb(f"y{b}", [P, D]) for b in range(2)]
        m.gate_ps = m.ps("gate_ps", [P, CHUNK])
        m.up_ps = m.ps("up_ps", [P, CHUNK])
        m.hT_ps = m.ps("hT_ps", [P, BANK])
        m.xT_ps = m.ps("xT_ps", [P, 2, BANK])
        m.y_ps = m.ps("y_ps", [P, 2, BANK])
        m.w1_loaded = [m.sem(f"w1_loaded{b}") for b in range(2)]
        m.w3_loaded = [m.sem(f"w3_loaded{b}") for b in range(2)]
        m.w2_loaded = [m.sem(f"w2_loaded{b}") for b in range(2)]
        m.idx_ready = m.sem("idx_ready")
        m.lists_taken = m.sem("lists_taken")
        m.x_turned = m.sem("x_turned")
        m.xT_ready = m.sem("xT_ready")
        m.gate_ready = m.sem("gate_ready")
        m.up_ready = m.sem("up_ready")
        m.silu_ready = m.sem("silu_ready")
        m.hid_ready = m.sem("hid_ready")
        m.hid_turned = m.sem("hid_turned")
        m.hidT_ready = m.sem("hidT_ready")
        m.y_ready = m.sem("y_ready")
        m.y_read = m.sem("y_read")
        m.rows_loaded = [m.sem(f"rows_loaded{b}") for b in range(m.n_x)]
        m.y_stored = [m.sem(f"y_stored{b}") for b in range(2)]
        return m


def up_product(nc, w, x_T, out):
    for k in range(ND):
        last = nc.tensor.matmul(out[:, :], x_T[:, k, :], w[:, k, :], start=(k == 0), stop=(k == ND - 1))
    return last


def turn_rows(nc, rows, out, ident):
    for k in range(ND):
        last = nc.tensor.transpose(out[:, k // 4, bass.ts(k % 4, P)], rows[:, bass.ts(k, P)], ident[:, :])
    return last


def turn_hidden(nc, m, ident):
    for k in range(CHUNK // P):
        last = nc.tensor.transpose(m.hT_ps[:, bass.ts(k, P)], m.hid[:, bass.ts(k, P)], ident[:, :])
    return last


def down_product(nc, w2, m, start, stop):
    for h in range(2):
        for k in range(CHUNK // P):
            last = nc.tensor.matmul(m.y_ps[:, h, :], m.hid_T[:, k, :], w2[:, k, bass.ts(h, BANK)],
                                    start=(start and k == 0), stop=(stop and k == CHUNK // P - 1))
    return last


def expert_phase(nc, name, n_steps, w1_of, w3_of, w2_of, idx_all, src, ident, shared_x, y_rows=None, scale=None, add_to=None):
    n_chunks = n_steps * PER_STEP
    n_groups = n_steps if shared_x else n_chunks
    with ExpertStore(nc, name, 1 if shared_x else 2) as m:
        nx = m.n_x

        def group(i, c):
            return i if shared_x else PER_STEP * i + c

        with nc.Block() as block:
            @block.sync
            def _(sp):
                def step(i):
                    for c in range(PER_STEP):
                        q, b = PER_STEP * i + c, c % 2
                        for w, src_w, loaded, used in ((m.w1, w1_of, m.w1_loaded, m.gate_ready), (m.w3, w3_of, m.w3_loaded, m.up_ready)):
                            if not (first(i) and c < 2):
                                sp.wait_ge(used, q - 1)
                            sp.dma_start(w[b][:, :, :], src_w(i, c)).then_inc(loaded[b], 16)
                        if not (first(i) and c < 2):
                            sp.wait_ge(m.y_ready, q - 1)
                        sp.dma_start(m.w2[b][:, :, :], w2_of(i, c)).then_inc(m.w2_loaded[b], 16)
                        if not shared_x and not (first(i) and c < 2):
                            store_y(PER_STEP * i + c - 2, c % 2)

                def store_y(q, b):
                    sp.wait_ge(m.y_read, q + 1)
                    sp.dma_start(y_rows[bass.ds(q * SLOTS, SLOTS), :], m.y[b][:, :]).then_inc(m.y_stored[b], 16)

                repeat(sp, n_steps, step)
                if not shared_x:
                    for q in range(n_chunks - 2, n_chunks):
                        store_y(q, q % 2)
                    for b in range(2):
                        sp.wait_ge(m.y_stored[b], 16 * n_chunks // 2)

            @block.gpsimd
            def _(pool):
                def gather(g, b, nth):
                    if not (isinstance(g, int) and g < nx):
                        pool.wait_ge(m.x_turned, g - nx + 1)
                    pool.tensor_copy(m.idx[:, :], idx_all[:, tile(g)]).then_inc(m.idx_ready, 1)
                    pool.wait_ge(m.idx_ready, nth)
                    pool.sem_inc(m.lists_taken, 1)
                    pool.indirect_dma_start(out=m.rows[b][:, :], out_offset=None, in_=src,
                                            in_offset=bass.IndirectOffsetOnAxis(ap=m.idx[:, 0:1], axis=0)).then_inc(m.rows_loaded[b], 16)

                if not shared_x:
                    def step(i):
                        for c in range(PER_STEP):
                            g = PER_STEP * i + c
                            if not (first(i) and c == 0):
                                pool.wait_ge(m.rows_loaded[(c - 1) % 2], 16 * (2 * i + (c + 1) // 2))
                            gather(g, c % 2, g + 1)
                    repeat(pool, n_steps, step)
                    return

                def scatter(g, b, nth, n_same):
                    pool.wait_ge(m.y_read, g + 1)
                    pool.tensor_copy(m.idx[:, :], idx_all[:, tile(g)]).then_inc(m.idx_ready, 1)
                    pool.wait_ge(m.idx_ready, nth)
                    pool.sem_inc(m.lists_taken, 1)
                    pool.indirect_dma_start(out=add_to, out_offset=bass.IndirectOffsetOnAxis(ap=m.idx[:, 0:1], axis=0),
                                            in_=m.y[b][:, :], in_offset=None, compute_op=ALU.add).then_inc(m.y_stored[b], 16)
                    pool.wait_ge(m.y_stored[b], 16 * n_same)

                gather(0, 0, 1)
                pool.wait_ge(m.rows_loaded[0], 16)
                gather(1, 0, 2)
                pool.wait_ge(m.rows_loaded[0], 32)

                with pool.Fori(0, n_steps // 2 - 1) as i:
                    for b in range(2):
                        scatter(2 * i + b, b, 4 * i + 2 * b + 3, i + 1)
                        gather(2 * i + b + 2, 0, 4 * i + 2 * b + 4)
                        pool.wait_ge(m.rows_loaded[0], 16 * (2 * i + b + 3))
                for b in range(2):
                    scatter(n_steps - 2 + b, b, 2 * n_steps - 1 + b, n_steps // 2)

            @block.tensor
            def _(pe):
                def turn_x(g, b, nth):
                    pe.wait_ge(m.rows_loaded[b], 16 * nth)
                    if not (isinstance(g, int) and g == 0):
                        pe.wait_ge(m.xT_ready, g)
                    turn_rows(nc, m.rows[b], m.xT_ps, ident).then_inc(m.x_turned, 1)

                def turn_hid(q):
                    pe.wait_ge(m.hid_ready, q + 1)
                    turn_hidden(nc, m, ident).then_inc(m.hid_turned, 1)

                def down(q, i, c):
                    pe.wait_ge(m.w2_loaded[c % 2], 16 * (2 * i + c // 2 + 1))
                    pe.wait_ge(m.hidT_ready, q + 1)
                    start, stop = not shared_x or c == 0, not shared_x or c == PER_STEP - 1
                    if start:
                        g = i if shared_x else q
                        if not (isinstance(g, int) and g == 0):
                            pe.wait_ge(m.y_read, g)
                    down_product(nc, m.w2[c % 2], m, start, stop).then_inc(m.y_ready, 1)

                def step(i):
                    for c in range(PER_STEP):
                        q, b = PER_STEP * i + c, c % 2
                        x_T = m.x_T[b % nx]
                        before = None if first(i) and c == 0 else (q - 1, i if c else i - 1, (c - 1) % PER_STEP)
                        pe.wait_ge(m.xT_ready, group(i, c) + 1)
                        pe.wait_ge(m.w1_loaded[b], 16 * (2 * i + c // 2 + 1))
                        if before:
                            pe.wait_ge(m.silu_ready, q)
                        up_product(nc, m.w1[b], x_T, m.gate_ps).then_inc(m.gate_ready, 1)
                        if before:
                            turn_hid(before[0])
                        pe.wait_ge(m.w3_loaded[b], 16 * (2 * i + c // 2 + 1))
                        up_product(nc, m.w3[b], x_T, m.up_ps).then_inc(m.up_ready, 1)
                        if not shared_x:
                            if c < PER_STEP - 1 or not (isinstance(i, int) and i == n_steps - 1):
                                turn_x(q + 1, (c + 1) % 2, 2 * i + (c + 1) // 2 + 1)
                        elif c == PER_STEP - 1 and not (isinstance(i, int) and i == n_steps - 1):
                            turn_x(i + 1, 0, i + 2)
                        if before:
                            down(*before)

                turn_x(0, 0, 1)
                step(0)
                with pe.Fori(1, n_steps - 1) as i:
                    step(i)
                step(n_steps - 1)
                turn_hid(n_chunks - 1)
                down(n_chunks - 1, n_steps - 1, PER_STEP - 1)

            @block.scalar
            def _(act):
                def copy_x(g, b):
                    act.wait_ge(m.x_turned, g + 1)
                    act.activation(m.x_T[b][:, :, :], m.xT_ps[:, :, :].rearrange("p a (k s) -> p (a k) s", s=SLOTS), ACT.Copy).then_inc(m.xT_ready, 1)

                def copy_hid(q):
                    act.wait_ge(m.hid_turned, q + 1)
                    act.activation(m.hid_T[:, :, :], m.hT_ps[:, :].rearrange("p (k s) -> p k s", s=SLOTS), ACT.Copy).then_inc(m.hidT_ready, 1)

                def step(i):
                    for c in range(PER_STEP):
                        q = PER_STEP * i + c
                        last = isinstance(i, int) and i == n_steps - 1
                        act.wait_ge(m.gate_ready, q + 1)
                        if not (first(i) and c == 0):
                            act.wait_ge(m.hid_ready, q)
                        act.activation(m.silu[:, :], m.gate_ps[:, :], ACT.Silu).then_inc(m.silu_ready, 1)
                        if not (first(i) and c == 0):
                            copy_hid(q - 1)
                        if not shared_x and not (last and c == PER_STEP - 1):
                            copy_x(q + 1, (c + 1) % 2)
                        if shared_x and c == PER_STEP - 1 and not last:
                            copy_x(i + 1, 0)

                copy_x(0, 0)
                step(0)
                with act.Fori(1, n_steps - 1) as i:
                    step(i)
                step(n_steps - 1)
                copy_hid(n_chunks - 1)

            @block.vector
            def _(dve):
                def hidden(q):
                    dve.wait_ge(m.silu_ready, q + 1)
                    dve.wait_ge(m.up_ready, q + 1)
                    if not (isinstance(q, int) and q == 0):
                        dve.wait_ge(m.hid_turned, q)
                    dve.tensor_tensor(m.hid[:, :], m.up_ps[:, :], m.silu[:, :], ALU.mult).then_inc(m.hid_ready, 1)

                def results(g, q, b, nth):
                    dve.wait_ge(m.y_ready, q + 1)
                    if not (isinstance(nth, int) and nth == 1):
                        dve.wait_ge(m.y_stored[b], 16 * (nth - 1))
                    y = m.y_ps[:, :, :].rearrange("p a n -> p (a n)")
                    if scale is None:
                        dve.tensor_copy(m.y[b][:, :], y).then_inc(m.y_read, 1)
                    else:
                        dve.tensor_scalar(m.y[b][:, :], y, scale[:, tile(g)], None, ALU.mult).then_inc(m.y_read, 1)

                if shared_x:
                    def two_steps(i):
                        for b in range(2):
                            for c in range(PER_STEP):
                                hidden(PER_STEP * (2 * i + b) + c)
                                if c == 0 and not (first(i) and b == 0):
                                    g = 2 * i + b - 1
                                    results(g, PER_STEP * g + PER_STEP - 1, 1 - b, i + b)
                    two_steps(0)
                    two_steps(1)
                    with dve.Fori(2, n_steps // 2) as i:
                        two_steps(i)
                    results(n_steps - 1, n_chunks - 1, 1, n_steps // 2)
                else:
                    def step(i):
                        for c in range(PER_STEP):
                            q = PER_STEP * i + c
                            hidden(q)
                            if not (first(i) and c == 0):
                                results(q - 1, q - 1, (c - 1) % 2, 2 * i + (c + 1) // 2)
                    repeat(dve, n_steps, step)
                    results(n_chunks - 1, n_chunks - 1, 1, n_chunks // 2)


def overflow_phase(nc, w1, w3, w2, tables, src, y_rows, ident):
    idx_all, over_exp, n_over = tables["idx_all"], tables["over_exp"], tables["n_over"]
    with ExpertStore(nc, "over", 1) as m:
        w1_v, w3_v = (w.rearrange("e (k p) f -> e p k f", p=P) for w in (w1, w3))
        w2_v = w2.rearrange("e (k p) d -> e p k d", p=P)

        def where_needed(engine, body, after=None):
            n = engine.value_load(n_over[0:1, 0:1], min_val=0, max_val=N_OVER)
            with engine.If(n > 0):
                repeat(engine, N_OVER, body)
                if after:
                    after()

        with nc.Block() as block:
            @block.sync
            def _(sp):
                def load(j):
                    e = sp.value_load(over_exp[0:1, tile(j)], min_val=0, max_val=N_EXP - 1)
                    if not first(j):
                        sp.wait_ge(m.y_ready, j)
                        sp.wait_ge(m.w1_loaded[0], 16)
                    sp.dma_start(m.w1[0][:, :, :], w1_v[tile(e), :, :, :].rearrange("o p k f -> (o p) k f")).then_inc(m.w1_loaded[0], 16)
                    sp.dma_start(m.w3[0][:, :, :], w3_v[tile(e), :, :, :].rearrange("o p k f -> (o p) k f")).then_inc(m.w3_loaded[0], 16)
                    sp.dma_start(m.w2[0][:, :, :], w2_v[tile(e), :, :, :].rearrange("o p k f -> (o p) k f")).then_inc(m.w2_loaded[0], 16)
                    sp.wait_ge(m.y_read, j + 1)
                    sp.dma_start(y_rows[bass.ds((j + N_EXP) * SLOTS, SLOTS), :], m.y[0][:, :]).then_inc(m.y_stored[0], 16)
                where_needed(sp, load, lambda: sp.wait_ge(m.y_stored[0], 16 * N_OVER))

            @block.gpsimd
            def _(pool):

                def gather(j):
                    if not first(j):
                        pool.wait_ge(m.x_turned, j)
                    pool.tensor_copy(m.idx[:, :], idx_all[:, tile(j + N_EXP)]).then_inc(m.idx_ready, 1)
                    pool.wait_ge(m.idx_ready, j + 1)
                    pool.sem_inc(m.lists_taken, 1)
                    pool.indirect_dma_start(out=m.rows[0][:, :], out_offset=None, in_=src,
                                            in_offset=bass.IndirectOffsetOnAxis(ap=m.idx[:, 0:1], axis=0)).then_inc(m.rows_loaded[0], 16)
                    pool.wait_ge(m.rows_loaded[0], 16 * (j + 1))
                where_needed(pool, gather)

            @block.tensor
            def _(pe):
                def products(j):
                    pe.wait_ge(m.rows_loaded[0], 16 * (j + 1))
                    turn_rows(nc, m.rows[0], m.xT_ps, ident).then_inc(m.x_turned, 1)
                    pe.wait_ge(m.xT_ready, j + 1)
                    pe.wait_ge(m.w1_loaded[0], 16 * (j + 1))
                    up_product(nc, m.w1[0], m.x_T[0], m.gate_ps).then_inc(m.gate_ready, 1)
                    pe.wait_ge(m.w3_loaded[0], 16 * (j + 1))
                    up_product(nc, m.w3[0], m.x_T[0], m.up_ps).then_inc(m.up_ready, 1)
                    pe.wait_ge(m.hid_ready, j + 1)
                    turn_hidden(nc, m, ident).then_inc(m.hid_turned, 1)
                    pe.wait_ge(m.hidT_ready, j + 1)
                    pe.wait_ge(m.w2_loaded[0], 16 * (j + 1))
                    if not first(j):
                        pe.wait_ge(m.y_read, j)
                    down_product(nc, m.w2[0], m, True, True).then_inc(m.y_ready, 1)
                where_needed(pe, products)

            @block.scalar
            def _(act):
                def middle(j):
                    act.wait_ge(m.x_turned, j + 1)
                    act.activation(m.x_T[0][:, :, :], m.xT_ps[:, :, :].rearrange("p a (k s) -> p (a k) s", s=SLOTS), ACT.Copy).then_inc(m.xT_ready, 1)
                    act.wait_ge(m.gate_ready, j + 1)
                    act.activation(m.silu[:, :], m.gate_ps[:, :], ACT.Silu).then_inc(m.silu_ready, 1)
                    act.wait_ge(m.hid_turned, j + 1)
                    act.activation(m.hid_T[:, :, :], m.hT_ps[:, :].rearrange("p (k s) -> p k s", s=SLOTS), ACT.Copy).then_inc(m.hidT_ready, 1)
                where_needed(act, middle)

            @block.vector
            def _(dve):
                def products(j):
                    dve.wait_ge(m.silu_ready, j + 1)
                    dve.wait_ge(m.up_ready, j + 1)
                    dve.tensor_tensor(m.hid[:, :], m.up_ps[:, :], m.silu[:, :], ALU.mult).then_inc(m.hid_ready, 1)
                    dve.wait_ge(m.y_ready, j + 1)
                    if not first(j):
                        dve.wait_ge(m.y_stored[0], 16 * j)
                    dve.tensor_copy(m.y[0][:, :], m.y_ps[:, :, :].rearrange("p a n -> p (a n)")).then_inc(m.y_read, 1)
                where_needed(dve, products)


def combine_phase(nc, x1, y_rows, tables, gain1, gain2, ident, x2, h_T):
    gates, dest = tables["gates"], tables["dest"]
    with Store(nc, "combine") as m:
        x = [m.sb(f"x{b}", [P, D]) for b in range(2)]
        y = [[m.sb(f"y{j}_{b}", [P, D]) for b in range(2)] for j in range(2)]
        n1 = [m.sb(f"n1_{b}", [P, D]) for b in range(2)]
        n2 = [m.sb(f"n2_{b}", [P, D]) for b in range(2)]
        sq = m.sb("sq", [P, D])
        g = [m.sb(f"g{j}", [P, D]) for j in range(2)]
        ssum = m.sb("ssum", [P, 2 * NT])
        rms = m.sb("rms", [P, 2 * NT])
        rstd = m.sb("rstd", [P, 2 * NT])
        eps = m.sb("eps", [P, 1])
        turned = [m.ps(f"turned{b}", [P, 2, BANK]) for b in range(2)]
        g_loaded = m.sem("g_loaded")
        x_loaded = [m.sem(f"x_loaded{b}") for b in range(2)]
        y_loaded = [m.sem(f"y_loaded{b}") for b in range(2)]
        step = m.sem("step")
        sum_ready = m.sem("sum_ready")
        rms_ready = m.sem("rms_ready")
        n1_ready = m.sem("n1_ready")
        n2_ready = m.sem("n2_ready")
        n2_turned = m.sem("n2_turned")
        copied = m.sem("copied")
        stored = [m.sem(f"stored{b}") for b in range(2)]
        with nc.Block() as block:
            @block.sync
            def _(sp):
                for j, gain in enumerate((gain1, gain2)):
                    sp.dma_start(g[j][:, :], row(gain).partition_broadcast(P)).then_inc(g_loaded, 16)
                for t in range(NT):
                    b = t % 2
                    if t >= 2:
                        sp.wait_ge(n1_ready, t - 1)
                    sp.dma_start(x[b][:, :], x1[bass.ts(t, P), :]).then_inc(x_loaded[b], 16)

            @block.gpsimd
            def _(pool):
                for t in range(NT):
                    b = t % 2
                    if t >= 2:
                        pool.wait_ge(n1_ready, t - 1)
                    for j in range(2):
                        pool.indirect_dma_start(out=y[j][b][:, :], out_offset=None, in_=y_rows,
                                                in_offset=bass.IndirectOffsetOnAxis(ap=dest[:, 2 * t + j:2 * t + j + 1], axis=0)).then_inc(y_loaded[b], 16)

            @block.vector
            def _(dve):
                c = Chain(dve, step)
                c.then(dve.memset(eps[:, :], EPS))
                dve.wait_ge(g_loaded, 32)

                def norm(src, j, t, out, ready):
                    n = 2 * t + j
                    dve.tensor_tensor_reduce(out=sq[:, :], in0=src[:, :], in1=src[:, :], scale=1.0, scalar=0.0, op0=ALU.mult, op1=ALU.add,
                                             accum_out=ssum[:, n:n + 1]).then_inc(sum_ready, 1)
                    dve.wait_ge(rms_ready, n + 1)
                    c.then(dve.reciprocal(rstd[:, n:n + 1], rms[:, n:n + 1]))
                    if t >= 2:
                        dve.wait_ge(stored[t % 2], 16 * (t // 2)) if j == 0 else dve.wait_ge(n2_turned, t - 1)
                    dve.scalar_tensor_tensor(out[:, :], src[:, :], rstd[:, n:n + 1], g[j][:, :], ALU.mult, ALU.mult).then_inc(ready, 1)
                    dve.wait_ge(ready, t + 1)

                for t in range(NT):
                    b = t % 2
                    dve.wait_ge(x_loaded[b], 16 * (t // 2 + 1))
                    dve.wait_ge(y_loaded[b], 32 * (t // 2 + 1))
                    for j in range(2):
                        c.then(dve.scalar_tensor_tensor(x[b][:, :], y[j][b][:, :], gates[:, j, t:t + 1], x[b][:, :], ALU.mult, ALU.add))
                    norm(x[b], 0, t, n1[b], n1_ready)
                    norm(n1[b], 1, t, n2[b], n2_ready)

            @block.scalar
            def _(act):
                act.wait_ge(step, 1)
                for t in range(NT):
                    b = t % 2
                    for j in range(2):
                        n = 2 * t + j
                        act.wait_ge(sum_ready, n + 1)
                        act.activation(rms[:, n:n + 1], ssum[:, n:n + 1], ACT.Sqrt, scale=1.0 / D, bias=eps[:, :]).then_inc(rms_ready, 1)
                        if j == 0:
                            act.wait_ge(n1_ready, t + 1)
                            act.dma_start(x2[bass.ts(t, P), :], n1[b][:, :]).then_inc(stored[b], 16)
                    act.wait_ge(n2_turned, t + 1)
                    act.activation(h_T[:, :, bass.ts(t, P)], turned[b][:, :, :].rearrange("p a (k q) -> p (a k) q", q=P), ACT.Copy).then_inc(copied, 1)
                for b in range(2):
                    act.wait_ge(stored[b], 16 * (NT // 2))

            @block.tensor
            def _(pe):
                for t in range(NT):
                    b = t % 2
                    pe.wait_ge(n2_ready, t + 1)
                    if t >= 2:
                        pe.wait_ge(copied, t - 1)
                    turn_rows(nc, n2[b], turned[b], ident).then_inc(n2_turned, 1)


LRU_W, LRU_H, LRU_D, LRU_TAPS, LRU_C = 1024, 16, 64, 4, 8.0
HY_W, HY_ORDER, HY_TAPS = 1024, 2, 3
N_LRU = LRU_W // P
COL_AX, COL_AGATE = 0, LRU_W
COL_HY = 2 * LRU_W
COL_GA = COL_HY + (HY_ORDER + 1) * HY_W
COL_GB = COL_GA + D
LOG1P_TERMS = 9


def wide_product(nc, out, w, rhs_T):
    for h in range(2):
        for k in range(ND):
            last = nc.tensor.matmul(out[:, h, :], w[:, k, :], rhs_T[:, k, bass.ts(h, BANK)], start=(k == 0), stop=(k == ND - 1))
    return last


def lru_phase(nc, h_T, w_in, conv_w, conv_b, w_r, b_r, w_i, b_i, lam, ident, ya_T):
    R_CONVB, R_BR, R_BI, R_LAM = (LRU_TAPS * N_LRU, (LRU_TAPS + 1) * N_LRU, (LRU_TAPS + 3) * N_LRU, (LRU_TAPS + 5) * N_LRU)
    N_ROWS = (LRU_TAPS + 7) * N_LRU
    PAD_L, PAD = LRU_TAPS // 2, LRU_TAPS - 1
    NB = range(2)
    with Store(nc, "lru") as m:
        wx = [m.sb(f"wx{b}", [P, ND, P]) for b in NB]
        wg = [m.sb(f"wg{b}", [P, ND, P]) for b in NB]
        w_gate = [m.sb(f"w_gate{b}", [P, 2, 2, P]) for b in NB]
        vec_rows = m.sb("vec_rows", [N_ROWS, P])
        vec = m.sb("vec", [P, N_ROWS])
        rate = m.sb("rate", [P, 2 * N_LRU])
        rate_neg = m.sb("rate_neg", [P, 2 * N_LRU])
        u = m.sb("u", [P, 2 * N_LRU])
        s = m.sb("s", [P, 2 * N_LRU])
        s2 = m.sb("s2", [P, 2 * N_LRU])
        poly = m.sb("poly", [P, 2 * N_LRU])
        a_x = [m.sb(f"a_x{b}", [P, T + PAD]) for b in NB]
        xa = [m.sb(f"xa{b}", [P, T]) for b in NB]
        a_gate = [m.sb(f"a_gate{b}", [P, T]) for b in NB]
        r = [[m.sb(f"r{b}{d}", [P, T]) for d in NB] for b in NB]
        x_in = [[m.sb(f"x_in{b}{d}", [P, T]) for d in NB] for b in NB]
        a = [[m.sb(f"a{b}{d}", [P, T]) for d in NB] for b in NB]
        a_sq = [m.sb(f"a_sq{d}", [P, T]) for d in NB]
        h = [m.sb(f"h{d}", [P, T]) for d in NB]
        ax_ps = m.ps("ax_ps", [P, 2, BANK])
        ag_ps = m.ps("ag_ps", [P, 2, BANK])
        gate_ps = m.ps("gate_ps", [P, 2, 2, BANK])
        cleared = m.sem("cleared")
        vec_loaded = m.sem("vec_loaded")
        vec_turned = m.sem("vec_turned")
        vec_ready = m.sem("vec_ready")
        u_ready = m.sem("u_ready")
        rate_ready = m.sem("rate_ready")
        step = m.sem("step")
        w_loaded = [m.sem(f"w_loaded{b}") for b in NB]
        gate_loaded = [m.sem(f"gate_loaded{b}") for b in NB]
        proj_made = m.sem("proj_made")
        ax_copied = m.sem("ax_copied")
        gelu_done = m.sem("gelu_done")
        conv_step = m.sem("conv_step")
        xa_ready = m.sem("xa_ready")
        gates_made = m.sem("gates_made")
        sig_ready = m.sem("sig_ready")
        tanh_ready = m.sem("tanh_ready")
        x_in_ready = m.sem("x_in_ready")
        sq_ready = m.sem("sq_ready")
        rest_ready = m.sem("rest_ready")
        factor_ready = m.sem("factor_ready")
        scan_step = m.sem("scan_step")
        sum_ready = m.sem("sum_ready")
        ya_ready = m.sem("ya_ready")
        w_k = w_in.rearrange("(k p) n -> p k n", p=P)

        def col(j, n=0):
            return vec[:, bass.ds(j + n, 1)]

        with nc.Block() as block:
            @block.gpsimd
            def _(pool):
                for b in NB:
                    pool.memset(a_x[b][:, :], 0.0).then_inc(cleared, 1)
                    pool.memset(w_gate[b][:, :, :, :], 0.0).then_inc(cleared, 1)

            @block.sync
            def _(sp):
                for n, src in ((0, conv_w.rearrange("k (t p) -> (k t) p", p=P)), (R_CONVB, conv_b.rearrange("(t p) -> t p", p=P)),
                               (R_BR, b_r.rearrange("d (t p) -> (d t) p", p=P)), (R_BI, b_i.rearrange("d (t p) -> (d t) p", p=P)),
                               (R_LAM, lam.rearrange("d (t p) -> (d t) p", p=P))):
                    sp.dma_start(vec_rows[n:n + src.shape[0], :], src).then_inc(vec_loaded, 16)
                sp.wait_ge(cleared, 4)

                def load(i):
                    for b in NB:
                        j = 2 * i + b
                        if not first(i):
                            sp.wait_ge(proj_made, 4 * i + 2 * b - 2)
                        sp.dma_start(wx[b][:, :, :], w_k[:, :, bass.ds(j * P + COL_AX, P)]).then_inc(w_loaded[b], 16)
                        sp.dma_start(wg[b][:, :, :], w_k[:, :, bass.ds(j * P + COL_AGATE, P)]).then_inc(w_loaded[b], 16)
                        if not first(i):
                            sp.wait_ge(gates_made, 4 * i + 2 * b - 2)
                        for g, src in enumerate((w_r, w_i)):
                            for e in range(2):
                                half = slice(e * LRU_D, (e + 1) * LRU_D)
                                sp.dma_start(w_gate[b][half, g, :, half],
                                             src[:, bass.ds(2 * j + e, 1), :, :].rearrange("d o p n -> (o p) d n")).then_inc(gate_loaded[b], 16)
                repeat(sp, N_LRU // 2, load)

            @block.tensor
            def _(pe):
                pe.wait_ge(vec_loaded, 16 * 5)
                nc.tensor.transpose(ax_ps[:, 0, 0:N_ROWS], vec_rows[:, :], ident[0:N_ROWS, 0:N_ROWS]).then_inc(vec_turned, 1)
                pe.wait_ge(vec_ready, 1)

                def project(j, i, b):
                    pe.wait_ge(w_loaded[b], 32 * (i + 1))
                    for nth, (out, w, read) in enumerate(((ax_ps, wx, ax_copied), (ag_ps, wg, gelu_done))):
                        if not first(j):
                            pe.wait_ge(read, j)
                        wide_product(nc, out, w[b], h_T).then_inc(proj_made, 1)

                def gates(j, i, b):
                    pe.wait_ge(xa_ready, j + 1)
                    pe.wait_ge(gate_loaded[b], 64 * (i + 1))
                    for d in NB:
                        if d or not first(j):
                            pe.wait_ge(sig_ready, 2 * (2 * j + d))
                        for g in range(2):
                            for t in range(2):
                                last = nc.tensor.matmul(gate_ps[:, g, t, :], w_gate[b][:, g, d, :], xa[b][:, bass.ts(t, BANK)], start=True, stop=True)
                        last.then_inc(gates_made, 1)

                def two_tiles(i):
                    project(2 * i, i, 0)
                    if not first(i):
                        gates(2 * i - 1, i - 1, 1)
                    project(2 * i + 1, i, 1)
                    gates(2 * i, i, 0)
                repeat(pe, N_LRU // 2, two_tiles)
                gates(N_LRU - 1, N_LRU // 2 - 1, 1)

            @block.scalar
            def _(act):
                act.wait_ge(u_ready, 1)
                act.activation(u[:, :], u[:, :], ACT.Exp).then_inc(u_ready, 1)
                act.wait_ge(rate_ready, 1)
                act.wait_ge(cleared, 4)

                def inputs(j, i, b):
                    act.wait_ge(proj_made, 2 * j + 1)
                    if not first(i):
                        act.wait_ge(xa_ready, j - 1)
                    act.activation(a_x[b][:, PAD_L:PAD_L + T], ax_ps[:, :, :].rearrange("p a n -> p (a n)"), ACT.Copy).then_inc(ax_copied, 1)
                    act.wait_ge(proj_made, 2 * j + 2)
                    if not first(i):
                        act.wait_ge(ya_ready, j - 1)
                    act.activation(a_gate[b][:, :], ag_ps[:, :, :].rearrange("p a n -> p (a n)"), ACT.Gelu_apprx_tanh).then_inc(gelu_done, 1)

                def gates(j, i, b):
                    for d in NB:
                        act.wait_ge(gates_made, 2 * j + d + 1)
                        for g, (out, n) in enumerate(((r, R_BR), (x_in, R_BI))):
                            act.activation(out[b][d][:, :], gate_ps[:, g, :, :].rearrange("p a n -> p (a n)"), ACT.Sigmoid,
                                           bias=col(j, n + d * N_LRU)).then_inc(sig_ready, 1)
                    act.wait_ge(sig_ready, 4 * j + 4)
                    for d in NB:
                        act.activation(a[b][d][:, :], r[b][d][:, :], ACT.Exp, scale=rate_neg[:, bass.ds(j + d * N_LRU, 1)])
                    for d in NB:
                        act.activation(r[b][d][:, :], r[b][d][:, :], ACT.Tanh, scale=rate[:, bass.ds(j + d * N_LRU, 1)]).then_inc(tanh_ready, 1)
                    for d in NB:
                        act.wait_ge(rest_ready, 2 * j + d + 1)
                        act.activation(r[b][d][:, :], r[b][d][:, :], ACT.Sqrt).then_inc(factor_ready, 1)

                def two_tiles(i):
                    inputs(2 * i, i, 0)
                    if not first(i):
                        gates(2 * i - 1, i - 1, 1)
                    inputs(2 * i + 1, i, 1)
                    gates(2 * i, i, 0)
                repeat(act, N_LRU // 2, two_tiles)
                gates(N_LRU - 1, N_LRU // 2 - 1, 1)

            @block.vector
            def _(dve):
                c = Chain(dve, step)
                dve.wait_ge(vec_turned, 1)
                dve.tensor_copy(vec[:, :], ax_ps[:, 0, 0:N_ROWS]).then_inc(vec_ready, 1)
                dve.wait_ge(vec_ready, 1)
                lam_v = vec[:, R_LAM:R_LAM + 2 * N_LRU]
                c.then(dve.tensor_scalar(rate_neg[:, :], lam_v, -1.0, None, ALU.mult))
                dve.tensor_tensor(u[:, :], lam_v, rate_neg[:, :], ALU.min).then_inc(u_ready, 1)
                c.then(dve.tensor_scalar(rate[:, :], rate_neg[:, :], 0.0, None, ALU.max))
                dve.wait_ge(u_ready, 2)
                c.then(dve.tensor_scalar(s[:, :], u[:, :], 2.0, None, ALU.add))
                c.then(dve.reciprocal(s[:, :], s[:, :]))
                c.then(dve.tensor_tensor(s[:, :], s[:, :], u[:, :], ALU.mult))
                c.then(dve.tensor_tensor(s2[:, :], s[:, :], s[:, :], ALU.mult))
                for n in reversed(range(LOG1P_TERMS)):
                    term = 2.0 / (2 * n + 1)
                    if n == LOG1P_TERMS - 1:
                        c.then(dve.tensor_scalar(poly[:, :], s2[:, :], 0.0, term, ALU.mult, ALU.add))
                    else:
                        c.then(dve.tensor_tensor(poly[:, :], poly[:, :], s2[:, :], ALU.mult))
                        c.then(dve.tensor_scalar(poly[:, :], poly[:, :], term, None, ALU.add))
                c.then(dve.tensor_tensor(poly[:, :], poly[:, :], s[:, :], ALU.mult))
                c.then(dve.tensor_tensor(rate[:, :], rate[:, :], poly[:, :], ALU.add))
                c.then(dve.tensor_scalar(rate[:, :], rate[:, :], LRU_C, None, ALU.mult))
                dve.tensor_scalar(rate_neg[:, :], rate[:, :], -1.0, None, ALU.mult).then_inc(rate_ready, 1)

                def conv(j, i, b):
                    dve.wait_ge(ax_copied, j + 1)
                    if not first(i):
                        dve.wait_ge(gates_made, 2 * j - 2)
                    dve.tensor_scalar(xa[b][:, :], a_x[b][:, 0:T], col(j), col(j, R_CONVB), ALU.mult, ALU.add).then_inc(conv_step, 1)
                    for k in range(1, LRU_TAPS):
                        dve.wait_ge(conv_step, (LRU_TAPS - 1) * j + k)
                        dve.scalar_tensor_tensor(xa[b][:, :], a_x[b][:, k:k + T], col(j, k * N_LRU), xa[b][:, :],
                                                 ALU.mult, ALU.add).then_inc(xa_ready if k == LRU_TAPS - 1 else conv_step, 1)

                def scan(j, i, b):
                    dve.wait_ge(xa_ready, j + 1)
                    for d in NB:
                        dve.wait_ge(sig_ready, 4 * j + 2 * d + 2)
                        dve.tensor_tensor(x_in[b][d][:, :], x_in[b][d][:, :], xa[b][:, :], ALU.mult).then_inc(x_in_ready, 1)
                    for d in NB:
                        dve.wait_ge(tanh_ready, 2 * j + d + 1)
                        dve.tensor_tensor(a_sq[d][:, :], a[b][d][:, :], a[b][d][:, :], ALU.mult).then_inc(sq_ready, 1)
                    for d in NB:
                        dve.wait_ge(sq_ready, 2 * j + d + 1)
                        dve.scalar_tensor_tensor(r[b][d][:, :], a_sq[d][:, :], 1.0, r[b][d][:, :], ALU.add, ALU.mult).then_inc(rest_ready, 1)
                    for d in NB:
                        rest = slice(1 - d, T - d)
                        dve.wait_ge(factor_ready, 2 * j + d + 1)
                        dve.wait_ge(x_in_ready, 2 * j + d + 1)
                        dve.tensor_tensor(x_in[b][d][:, rest], x_in[b][d][:, rest], r[b][d][:, rest], ALU.mult).then_inc(scan_step, 1)
                    for d in NB:
                        dve.wait_ge(scan_step, 4 * j + d + 1)
                        order = slice(None, None, -1 if d else 1)
                        dve.tensor_tensor_scan(h[d][:, order], a[b][d][:, order], x_in[b][d][:, order], 0.0, ALU.mult, ALU.add).then_inc(scan_step, 1)
                    dve.wait_ge(scan_step, 4 * j + 4)
                    dve.tensor_tensor(h[0][:, :], h[0][:, :], h[1][:, :], ALU.add).then_inc(sum_ready, 1)
                    dve.wait_ge(gelu_done, j + 1)
                    dve.wait_ge(sum_ready, j + 1)
                    dve.tensor_tensor(ya_T[:, tile(j), :].rearrange("p o t -> p (o t)"), h[0][:, :], a_gate[b][:, :], ALU.mult).then_inc(ya_ready, 1)

                def two_tiles(i):
                    conv(2 * i, i, 0)
                    if not first(i):
                        scan(2 * i - 1, i - 1, 1)
                    conv(2 * i + 1, i, 1)
                    scan(2 * i, i, 0)
                repeat(dve, N_LRU // 2, two_tiles)
                scan(N_LRU - 1, N_LRU // 2 - 1, 1)


def hyena_inputs_phase(nc, h_T, w_in, conv_w, conv_b, ident, v_x1, x2_T):
    N_NAT, N_ALL = 2 * HY_W // P, 3 * HY_W // P
    R_BIAS = HY_TAPS * N_ALL
    N_ROWS = (HY_TAPS + 1) * N_ALL
    PAD_L, PAD = HY_TAPS // 2, HY_TAPS - 1
    NB = range(2)
    with Store(nc, "hyin") as m:
        w = [m.sb(f"w{b}", [P, ND, P]) for b in NB]
        vec_rows = m.sb("vec_rows", [N_ROWS, P])
        vec = m.sb("vec", [P, N_ROWS])
        raw = [m.sb(f"raw{b}", [P, T + PAD]) for b in NB]
        conv = [m.sb(f"conv{b}", [P, T]) for b in NB]
        rows = [m.sb(f"rows{b}", [P, NT, P]) for b in NB]
        proj_ps = [m.ps(f"proj{b}", [P, 2, BANK]) for b in NB]
        turned_ps = [m.ps(f"turned{b}", [P, 2, BANK]) for b in NB]
        cleared = m.sem("cleared")
        vec_loaded = m.sem("vec_loaded")
        vec_turned = m.sem("vec_turned")
        vec_ready = m.sem("vec_ready")
        w_loaded = [m.sem(f"w_loaded{b}") for b in NB]
        proj_made = m.sem("proj_made")
        raw_ready = m.sem("raw_ready")
        tap_done = m.sem("tap_done")
        conv_ready = m.sem("conv_ready")
        turned = m.sem("turned")
        rows_ready = m.sem("rows_ready")
        taken = m.sem("taken")
        stored = [m.sem(f"stored{b}") for b in NB]
        w_k = w_in.rearrange("(k p) n -> p k n", p=P)
        nat = v_x1.rearrange("(t p) c -> p t c", p=P)

        def loops(engine, body):
            body(0, True)
            with engine.Fori(1, N_NAT // 2) as i:
                body(i, True)
            with engine.Fori(N_NAT // 2, N_ALL // 2) as i:
                body(i, False)

        with nc.Block() as block:
            @block.gpsimd
            def _(pool):
                for b in NB:
                    pool.memset(raw[b][:, :], 0.0).then_inc(cleared, 1)

                def store(i, turn):
                    for b in NB:
                        j = 2 * i + b
                        if turn:
                            pool.wait_ge(rows_ready, j + 1)
                            pool.sem_inc(taken, 1)
                            pool.dma_start(nat[:, :, bass.ds(j * P, P)], rows[b][:, :, :]).then_inc(stored[b], 16)
                        else:
                            pool.wait_ge(conv_ready, j + 1)
                            pool.sem_inc(taken, 1)
                            pool.dma_start(x2_T[bass.ds((j - N_NAT) * P, P), :], conv[b][:, :]).then_inc(stored[b], 16)
                loops(pool, store)
                for b in NB:
                    pool.wait_ge(stored[b], 16 * (N_ALL // 2))

            @block.sync
            def _(sp):
                sp.dma_start(vec_rows[0:R_BIAS, :], conv_w.rearrange("k (t p) -> (k t) p", p=P)).then_inc(vec_loaded, 16)
                sp.dma_start(vec_rows[R_BIAS:, :], conv_b.rearrange("(t p) -> t p", p=P)).then_inc(vec_loaded, 16)

                def load(i):
                    for b in NB:
                        j = 2 * i + b
                        if not first(i):
                            sp.wait_ge(proj_made, j - 1)
                        sp.dma_start(w[b][:, :, :], w_k[:, :, bass.ds(j * P + COL_HY, P)]).then_inc(w_loaded[b], 16)
                repeat(sp, N_ALL // 2, load)

            @block.tensor
            def _(pe):
                pe.wait_ge(vec_loaded, 32)
                nc.tensor.transpose(turned_ps[0][:, 0, 0:N_ROWS], vec_rows[:, :], ident[0:N_ROWS, 0:N_ROWS]).then_inc(vec_turned, 1)
                pe.wait_ge(vec_ready, 1)

                def turn(j, b):
                    pe.wait_ge(conv_ready, j + 1)
                    if not (isinstance(j, int) and j < 2):
                        pe.wait_ge(rows_ready, j - 1)
                    turn_rows(nc, conv[b], turned_ps[b], ident).then_inc(turned, 1)

                def two_tiles(i, turning):
                    for b in NB:
                        j = 2 * i + b
                        pe.wait_ge(w_loaded[b], 16 * (i + 1))
                        if not first(i):
                            pe.wait_ge(raw_ready, j - 1)
                        wide_product(nc, proj_ps[b], w[b], h_T).then_inc(proj_made, 1)
                        if turning and not (first(i) and b == 0):
                            turn(j - 1, 1 - b)

                two_tiles(0, True)
                with pe.Fori(1, N_NAT // 2) as i:
                    two_tiles(i, True)
                turn(N_NAT - 1, 1)
                with pe.Fori(N_NAT // 2, N_ALL // 2) as i:
                    two_tiles(i, False)

            @block.scalar
            def _(act):
                act.wait_ge(cleared, 2)

                def copy_rows(j, i, b):
                    act.wait_ge(turned, j + 1)
                    if not first(i):
                        act.wait_ge(stored[b], 16 * i)
                    act.activation(rows[b][:, :, :], turned_ps[b][:, :, :].rearrange("p a (k c) -> p (a k) c", c=P), ACT.Copy).then_inc(rows_ready, 1)

                def two_tiles(i, turning):
                    for b in NB:
                        j = 2 * i + b
                        act.wait_ge(proj_made, j + 1)
                        if not first(i):
                            act.wait_ge(conv_ready, j - 1)
                        act.activation(raw[b][:, PAD_L:PAD_L + T], proj_ps[b][:, :, :].rearrange("p a n -> p (a n)"), ACT.Copy).then_inc(raw_ready, 1)
                        if turning and not (first(i) and b == 0):
                            copy_rows(j - 1, i if b else i - 1, 1 - b)

                two_tiles(0, True)
                two_tiles(1, True)
                with act.Fori(2, N_NAT // 2) as i:
                    two_tiles(i, True)
                copy_rows(N_NAT - 1, N_NAT // 2 - 1, 1)
                with act.Fori(N_NAT // 2, N_ALL // 2) as i:
                    two_tiles(i, False)

            @block.vector
            def _(dve):
                dve.wait_ge(vec_turned, 1)
                dve.tensor_copy(vec[:, :], turned_ps[0][:, 0, 0:N_ROWS]).then_inc(vec_ready, 1)
                dve.wait_ge(vec_ready, 1)

                def two_tiles(i, turning):
                    for b in NB:
                        j = 2 * i + b
                        dve.wait_ge(raw_ready, j + 1)
                        if not first(i):
                            if turning:
                                dve.wait_ge(turned, j - 1)
                            else:
                                dve.wait_ge(stored[b], 16 * i)
                        dve.tensor_scalar(conv[b][:, :], raw[b][:, 0:T], vec[:, bass.ds(j, 1)], vec[:, bass.ds(j + R_BIAS, 1)],
                                          ALU.mult, ALU.add).then_inc(tap_done, 1)
                        for k in range(1, HY_TAPS):
                            dve.wait_ge(tap_done, (HY_TAPS - 1) * j + k)
                            dve.scalar_tensor_tensor(conv[b][:, :], raw[b][:, k:k + T], vec[:, bass.ds(j + k * N_ALL, 1)], conv[b][:, :],
                                                     ALU.mult, ALU.add).then_inc(conv_ready if k == HY_TAPS - 1 else tap_done, 1)
                loops(dve, two_tiles)


def gates_phase(nc, h_T, ya_T, w_in, w_a_out, part_T, gate_T):
    NB = range(2)
    with Store(nc, "gates") as m:
        w = [[m.sb(f"w{n}{b}", [P, ND, P]) for n in ("ga", "gb", "a")] for b in NB]
        sig_a = [m.sb(f"sig_a{b}", [P, T]) for b in NB]
        sig_b = [m.sb(f"sig_b{b}", [P, T]) for b in NB]
        part = [m.sb(f"part{b}", [P, T]) for b in NB]
        ga_ps = m.ps("ga_ps", [P, 2, BANK])
        gb_ps = m.ps("gb_ps", [P, 2, BANK])
        a_ps = m.ps("a_ps", [P, 2, BANK])
        w_loaded = [m.sem(f"w_loaded{b}") for b in NB]
        made = m.sem("made")
        sig_ready = m.sem("sig_ready")
        part_ready = m.sem("part_ready")
        taken = m.sem("taken")
        sig_stored = [m.sem(f"sig_stored{b}") for b in NB]
        part_stored = [m.sem(f"part_stored{b}") for b in NB]
        srcs = [(w_in.rearrange("(k p) n -> p k n", p=P), COL_GA), (w_in.rearrange("(k p) n -> p k n", p=P), COL_GB),
                (w_a_out.rearrange("(k p) n -> p k n", p=P), 0)]
        with nc.Block() as block:
            @block.sync
            def _(sp):
                def load(i):
                    for b in NB:
                        j = 2 * i + b
                        if not first(i):
                            sp.wait_ge(made, 6 * i + 3 * b - 3)
                        for n, (src, at) in enumerate(srcs):
                            sp.dma_start(w[b][n][:, :, :], src[:, :, bass.ds(j * P + at, P)]).then_inc(w_loaded[b], 16)
                repeat(sp, ND // 2, load)

            @block.gpsimd
            def _(pool):
                with pool.Fori(0, ND // 2) as i:
                    for b in NB:
                        j = 2 * i + b
                        pool.wait_ge(sig_ready, 2 * j + 2)
                        pool.sem_inc(taken, 1)
                        pool.dma_start(gate_T[bass.ds(j * P, P), :], sig_b[b][:, :]).then_inc(sig_stored[b], 16)
                        pool.wait_ge(part_ready, j + 1)
                        pool.sem_inc(taken, 1)
                        pool.dma_start(part_T[bass.ds(j * P, P), :], part[b][:, :]).then_inc(part_stored[b], 16)
                for b in NB:
                    pool.wait_ge(sig_stored[b], 16 * (ND // 2))
                    pool.wait_ge(part_stored[b], 16 * (ND // 2))

            @block.tensor
            def _(pe):
                def two_tiles(i):
                    for b in NB:
                        j = 2 * i + b
                        pe.wait_ge(w_loaded[b], 48 * (i + 1))
                        for n, (out, rhs) in enumerate(((ga_ps, h_T), (gb_ps, h_T), (a_ps, ya_T))):
                            if not first(j):
                                pe.wait_ge(*((sig_ready, 2 * j + n - 1), (sig_ready, 2 * j + n - 1), (part_ready, j))[n])
                            wide_product(nc, out, w[b][n], rhs).then_inc(made, 1)
                repeat(pe, ND // 2, two_tiles)

            @block.scalar
            def _(act):
                def two_tiles(i):
                    for b in NB:
                        j = 2 * i + b
                        act.wait_ge(made, 3 * j + 1)
                        if not first(i):
                            act.wait_ge(part_ready, j - 1)
                        act.activation(sig_a[b][:, :], ga_ps[:, :, :].rearrange("p a n -> p (a n)"), ACT.Sigmoid).then_inc(sig_ready, 1)
                        act.wait_ge(made, 3 * j + 2)
                        if not first(i):
                            act.wait_ge(sig_stored[b], 16 * i)
                        act.activation(sig_b[b][:, :], gb_ps[:, :, :].rearrange("p a n -> p (a n)"), ACT.Sigmoid).then_inc(sig_ready, 1)
                repeat(act, ND // 2, two_tiles)

            @block.vector
            def _(dve):
                def two_tiles(i):
                    for b in NB:
                        j = 2 * i + b
                        dve.wait_ge(sig_ready, 2 * j + 1)
                        dve.wait_ge(made, 3 * j + 3)
                        if not first(i):
                            dve.wait_ge(part_stored[b], 16 * i)
                        dve.tensor_tensor(part[b][:, :], a_ps[:, :, :].rearrange("p a n -> p (a n)"), sig_a[b][:, :], ALU.mult).then_inc(part_ready, 1)
                repeat(dve, ND // 2, two_tiles)


def merge_phase(nc, z_T, w_b_out, part_T, gate_T, merged_T):
    NB = range(2)
    with Store(nc, "merge") as m:
        z = m.sb("z", [P, ND, T])
        w = [m.sb(f"w{b}", [P, ND, P]) for b in NB]
        part = [m.sb(f"part{b}", [P, T]) for b in NB]
        gate = [m.sb(f"gate{b}", [P, T]) for b in NB]
        prod = [m.sb(f"prod{b}", [P, T]) for b in NB]
        b_ps = [m.ps(f"b_ps{b}", [P, 2, BANK]) for b in NB]
        z_loaded = m.sem("z_loaded")
        w_loaded = [m.sem(f"w_loaded{b}") for b in NB]
        parts_loaded = [m.sem(f"parts_loaded{b}") for b in NB]
        made = m.sem("made")
        prod_ready = m.sem("prod_ready")
        merged_ready = m.sem("merged_ready")
        w_k = w_b_out.rearrange("(k p) n -> p k n", p=P)
        with nc.Block() as block:
            @block.sync
            def _(sp):
                def load(i):
                    for b in NB:
                        j = 2 * i + b
                        if not first(i):
                            sp.wait_ge(made, j - 1)
                        sp.dma_start(w[b][:, :, :], w_k[:, :, bass.ds(j * P, P)]).then_inc(w_loaded[b], 16)
                        if first(i) and b == 0:
                            sp.dma_start(z[:, :, :], z_T.rearrange("(k p) t -> p k t", p=P)).then_inc(z_loaded, 16)
                        if not first(i):
                            sp.wait_ge(merged_ready, j - 1)
                        sp.dma_start(gate[b][:, :], gate_T[bass.ds(j * P, P), :]).then_inc(parts_loaded[b], 16)
                        sp.dma_start(part[b][:, :], part_T[bass.ds(j * P, P), :]).then_inc(parts_loaded[b], 16)
                repeat(sp, ND // 2, load)

            @block.tensor
            def _(pe):
                pe.wait_ge(z_loaded, 16)

                def two_tiles(i):
                    for b in NB:
                        j = 2 * i + b
                        pe.wait_ge(w_loaded[b], 16 * (i + 1))
                        if not first(i):
                            pe.wait_ge(prod_ready, j - 1)
                        wide_product(nc, b_ps[b], w[b], z).then_inc(made, 1)
                repeat(pe, ND // 2, two_tiles)

            @block.vector
            def _(dve):
                def two_tiles(i):
                    for b in NB:
                        j = 2 * i + b
                        dve.wait_ge(parts_loaded[b], 32 * (i + 1))
                        dve.wait_ge(made, j + 1)
                        dve.tensor_tensor(prod[b][:, :], b_ps[b][:, :, :].rearrange("p a n -> p (a n)"), gate[b][:, :], ALU.mult).then_inc(prod_ready, 1)
                        dve.wait_ge(prod_ready, j + 1)
                        dve.tensor_tensor(merged_T[:, tile(j), :].rearrange("p o t -> p (o t)"), prod[b][:, :], part[b][:, :], ALU.add).then_inc(merged_ready, 1)
                repeat(dve, ND // 2, two_tiles)


FILT_EMB, FILT_HID = 33, 64
FILT_BANDS = (FILT_EMB - 1) // 2
DECAY_FAST, DECAY_SLOW, DECAY_TARGET = 0.3, 1.5, 1e-2
TWO_PI = (6.28125, 0.0019350051879882812, 3.01991598196781e-07)
SIN_MAX = 3.1415925
TO_WHOLE = 1.5 * 2 ** 23
HB = 256
NHB = T // HB
HJ = HB // P
HF = HB // P
HC = BANK
COS, SIN, COS_NEG, SIN_NEG = range(4)


def filter_positions():
    f4 = np.float32
    lag = np.linspace(0.0, 1.0, T, dtype=f4)[:, None]
    w = f4(2.0 * np.pi / T) * np.arange(T, dtype=f4)[:, None]
    f = np.linspace(1e-4, FILT_BANDS - 1, FILT_BANDS, dtype=f4)[None, :]
    return np.ascontiguousarray(np.concatenate([lag, np.cos(w * f), -np.sin(w * f)], axis=-1).T.astype(f4))


def filter_decay():
    f4 = np.float32
    lag = np.linspace(0.0, 1.0, T, dtype=f4)[:, None]
    rates = np.abs(np.linspace(np.log(DECAY_TARGET) / DECAY_SLOW, np.log(DECAY_TARGET) / DECAY_FAST, HY_W, dtype=f4))
    return np.ascontiguousarray(np.exp(-lag * rates[None, :]).astype(f4))


def block_angles():
    f = np.stack([np.arange(P) * HF + n for n in range(HF)])
    return np.pi * np.arange(HB)[:, None, None] * (2 * f[None] + 1) / (2 * HB)


def block_transform():
    angle = block_angles()
    kinds = np.stack([np.cos(angle), np.sin(angle), -np.cos(angle), -np.sin(angle)], axis=1)
    return np.ascontiguousarray(kinds.reshape(HJ, P, 4, HF, P).transpose(1, 0, 2, 3, 4).astype(np.float32))


def block_inverse():
    angle = block_angles().transpose(2, 1, 0)
    return np.ascontiguousarray((np.stack([np.cos(angle), -np.sin(angle)], axis=2) / HB).astype(np.float32))


def filter_phase(nc, positions, w1, b1, w2, b2, freq, hid_T):
    H = FILT_HID
    with Store(nc, "filter") as m:
        pos = m.sb("pos", [FILT_EMB, T])
        w = [m.sb("w1", [FILT_EMB, H]), m.sb("w2", [H, H])]
        b = [m.sb(f"b{n}", [H, 1]) for n in range(2)]
        fr = [m.sb(f"freq{n}", [H, 1]) for n in range(2)]
        arg = m.sb("arg", [H, T])
        turns = m.sb("turns", [H, T])
        hid1 = m.sb("hid1", [H, T])
        ps = m.ps("ps", [P, 2, BANK])
        loaded = m.sem("loaded")
        made = m.sem("made")
        step = m.sem("step")
        arg_ready = m.sem("arg_ready")
        hid_ready = m.sem("hid_ready")
        with nc.Block() as block:
            @block.sync
            def _(sp):
                sp.dma_start(pos[:, :], positions).then_inc(loaded, 16)
                for n, (wn, bn) in enumerate(((w1, b1), (w2, b2))):
                    sp.dma_start(w[n][:, :], wn).then_inc(loaded, 16)
                    with nc.allow_non_contiguous_dma(reason="a number per partition"):
                        sp.dma_start(b[n][:, :], bn.rearrange("(p o) -> p o", o=1)).then_inc(loaded, 16)
                        sp.dma_start(fr[n][:, :], freq[n:n + 1, :].rearrange("o p -> p o")).then_inc(loaded, 16)

            @block.tensor
            def _(pe):
                pe.wait_ge(loaded, 16 * 7)
                for n, src in enumerate((pos, hid1)):
                    if n:
                        pe.wait_ge(hid_ready, 1)
                    for t in range(2):
                        last = nc.tensor.matmul(ps[0:H, t, :], w[n][:, :], src[:, bass.ts(t, BANK)], start=True, stop=True)
                    last.then_inc(made, 1)

            @block.vector
            def _(dve):
                c = Chain(dve, step)
                dve.wait_ge(loaded, 16 * 7)
                for n in range(2):
                    dve.wait_ge(made, n + 1)
                    c.then(dve.tensor_scalar(arg[:, :], ps[0:H, :, :].rearrange("p a n -> p (a n)"), b[n][:, :], fr[n][:, :], ALU.add, ALU.mult))
                    c.then(dve.tensor_scalar(turns[:, :], arg[:, :], 1.0 / (2.0 * np.pi), TO_WHOLE, ALU.mult, ALU.add))
                    c.then(dve.tensor_scalar(turns[:, :], turns[:, :], -TO_WHOLE, None, ALU.add))
                    for part in TWO_PI:
                        c.then(dve.scalar_tensor_tensor(arg[:, :], turns[:, :], -part, arg[:, :], ALU.mult, ALU.add))
                    dve.tensor_scalar(arg[:, :], arg[:, :], -SIN_MAX, SIN_MAX, ALU.max, ALU.min).then_inc(arg_ready, 1)
                    dve.wait_ge(hid_ready, n + 1)

            @block.scalar
            def _(act):
                for n, out in enumerate((hid1, hid_T)):
                    act.wait_ge(arg_ready, n + 1)
                    act.activation(out[:, :], arg[:, :], ACT.Sin).then_inc(hid_ready, 1)


def hyena_phase(nc, v_x1, x2_T, hid_T, w3, bias, decay, transform, inverse, z1, z_T):
    PASSES = [(o, h) for o in range(HY_ORDER) for h in range(HY_W // HC)]
    NP = len(PASSES)
    SHIFTS = range(1 - NHB, NHB)
    FWD, BWD = range(2)

    def sources(d):
        if d > 0:
            return [((COS, COS), (SIN_NEG, SIN_NEG), FWD, d), ((SIN, SIN_NEG), (COS, COS_NEG), FWD, d - 1)]
        if d == 0:
            return [((COS, COS), (SIN_NEG, SIN_NEG), FWD, 0), ((COS, COS), (SIN, SIN), BWD, 0)]
        return [((COS, COS), (SIN, SIN), BWD, -d), ((SIN, SIN_NEG), (COS_NEG, COS), BWD, -d - 1)]

    program = [("F", 0, 0)] + [("K", 0, d) for d in (-3, -2, -1, 0)]
    for n in range(NP):
        more = n + 1 < NP
        program += [("U", n, i) for i in reversed(range(NHB))]
        program += [("Y", n - 1, NHB - 1)] if n else []
        program += [("K", n, d) for d in range(1, NHB)]
        program += [("Y", n, 0)] + ([("F", n + 1, 0)] if more else [])
        for m_ in range(1, NHB):
            program += [("K", n + 1, m_ - NHB)] if more else []
            program += [("Y", n, m_)] if m_ < NHB - 1 else []
        program += [("K", n + 1, 0)] if more else [("Y", n, NHB - 1)]
    moved = {what: n for n, what in enumerate(w for w in program if w[0] in "UK")}
    turned_back = {what: n for n, what in enumerate(w for w in program if w[0] == "Y")}
    def pair(n, m_, i):
        return NHB * NHB * n + NHB * m_ + NHB - i

    with Store(nc, "hyena") as m:
        tr = m.sb("tr", [P, HJ, 4, HF, P])
        inv = m.sb("inv", [P, HF, 2, HB])
        w3_sb = m.sb("w3", [FILT_HID, 2, HC])
        bias_sb = m.sb("bias", [1, HC])
        decay_sb = [m.sb(f"decay{b}", [P, HC]) for b in range(2)]
        filt = m.sb("filt", [P, 2, NT, HC])
        u = [m.sb(f"u{b}", [P, HJ, HC]) for b in range(2)]
        U = [m.sb(f"U{i}", [P, 2, HF * HC]) for i in range(NHB)]
        K = {d: m.sb(f"K{d + NHB}", [P, 2, HF * HC]) for d in SHIFTS}
        Y = [m.sb(f"Y{b}", [P, 2, HF * HC]) for b in range(2)]
        by_re = m.sb("by_re", [P, 2, HF * HC])
        by_im = m.sb("by_im", [P, 2, HF * HC])
        gate = [m.sb(f"gate{b}", [P, HJ * HC]) for b in range(2)]
        z = [m.sb(f"z{b}", [P, HJ * HC]) for b in range(2)]
        tr_ps = [m.ps(f"tr_ps{c}", [P, HF * HC]) for c in range(2)]
        inv_ps = m.ps("inv_ps", [P, HJ * HC])
        filt_ps = [m.ps(f"filt_ps{b}", [P, HC]) for b in range(2)]
        tables_loaded = m.sem("tables_loaded")
        w3_loaded = m.sem("w3_loaded")
        decay_loaded = [m.sem(f"decay_loaded{b}") for b in range(2)]
        u_loaded = [m.sem(f"u_loaded{b}") for b in range(2)]
        gate_loaded = [m.sem(f"gate_loaded{b}") for b in range(2)]
        filt_made = m.sem("filt_made")
        filt_ready = m.sem("filt_ready")
        ends_set = m.sem("ends_set")
        tr_made = m.sem("tr_made")
        tr_copied = m.sem("tr_copied")
        re_made = m.sem("re_made")
        pair_made = m.sem("pair_made")
        sum_step = m.sem("sum_step")
        y_ready = m.sem("y_ready")
        inv_made = m.sem("inv_made")
        z_ready = m.sem("z_ready")
        z_stored = [m.sem(f"z_stored{b}") for b in range(2)]
        N_F = 2 * NT
        ENDS = 2

        def u_src(n, i):
            o, h = PASSES[n]
            rows = (z1 if o else v_x1)[bass.ts(i, HB), bass.ts(h, HC)]
            return rows.rearrange("(j p) c -> p j c", p=P)

        def z_place(n, m_):
            o, h = PASSES[n]
            if o == 0:
                return z1[bass.ts(m_, HB), bass.ts(h, HC)].rearrange("(j p) c -> p j c", p=P), dict(j=HJ)
            return z_T[bass.ts(h, HC), bass.ts(m_, HB)].rearrange("(j p) t -> p j t", p=P), dict(j=HC // P)

        def gate_src(n, m_):
            o, h = PASSES[n]
            if o == 0:
                return v_x1[bass.ts(m_, HB), bass.ds(HY_W + h * HC, HC)].rearrange("(j p) c -> p j c", p=P)
            return x2_T[bass.ts(h, HC), bass.ts(m_, HB)].rearrange("(j p) t -> p j t", p=P)

        with nc.Block() as block:
            @block.sync
            def _(sp):
                sp.dma_start(tr[:, :, :, :, :], transform).then_inc(tables_loaded, 16)
                sp.dma_start(inv[:, :, :, :], inverse).then_inc(tables_loaded, 16)
                n_u = 0
                for what, n, at in program:
                    o, h = PASSES[n]
                    if what == "F":
                        if n:
                            sp.wait_ge(filt_made, N_F * n)
                            sp.wait_ge(ends_set, ENDS * n)
                        cols = w3[:, bass.ds(o * 2 * HY_W, 2 * HY_W)].rearrange("k (d c) -> k d c", d=2)
                        sp.dma_start(w3_sb[:, :, :], cols[:, :, bass.ts(h, HC)]).then_inc(w3_loaded, 16)
                        sp.dma_start(bias_sb[:, :], bias[o:o + 1, bass.ts(h, HC)]).then_inc(w3_loaded, 16)
                        for t in range(NT):
                            if NT * n + t >= 2:
                                sp.wait_ge(filt_ready, N_F * n + 2 * t - 2)
                            sp.dma_start(decay_sb[t % 2][:, :], decay[bass.ts(t, P), bass.ts(h, HC)]).then_inc(decay_loaded[t % 2], 16)
                    elif what == "U":
                        if n_u >= 2:
                            before = [w for w in program if w[0] == "U"][n_u - 2]
                            sp.wait_ge(tr_made, 2 * moved[before] + 2)
                        if o:
                            done = turned_back["Y", n - 2, at] // 2 + 1
                            sp.wait_ge(z_stored[turned_back["Y", n - 2, at] % 2], 16 * done)
                        sp.dma_start(u[n_u % 2][:, :, :], u_src(n, at)).then_inc(u_loaded[n_u % 2], 16)
                        n_u += 1
                    elif what == "Y":
                        e = turned_back[what, n, at]
                        if e >= 2:
                            sp.wait_ge(z_ready, e - 1)
                        src = gate_src(n, at)
                        sp.dma_start(gate[e % 2][:, :].rearrange("p (j x) -> p j x", j=src.shape[1]), src).then_inc(gate_loaded[e % 2], 16)

            @block.gpsimd
            def _(pool):
                for (what, n, at), e in turned_back.items():
                    dst, split = z_place(n, at)
                    pool.wait_ge(z_ready, e + 1)
                    pool.dma_start(dst, z[e % 2][:, :].rearrange("p (j x) -> p j x", **split)).then_inc(z_stored[e % 2], 16)
                for b in range(2):
                    pool.wait_ge(z_stored[b], 16 * len(turned_back) // 2)

            @block.tensor
            def _(pe):
                pe.wait_ge(tables_loaded, 32)
                n_u = 0
                for what, n, at in program:
                    o, h = PASSES[n]
                    if what == "F":
                        pe.wait_ge(w3_loaded, 32 * (n + 1))
                        for t in range(NT):
                            for d in range(2):
                                f = N_F * n + 2 * t + d
                                if f >= 2:
                                    pe.wait_ge(filt_ready, f - 1)
                                nc.tensor.matmul(filt_ps[d][:, :], hid_T[:, bass.ts(t, P)], w3_sb[:, d, :], start=True, stop=True).then_inc(filt_made, 1)
                        continue
                    if what == "Y":
                        e = turned_back[what, n, at]
                        y = Y[at % 2]
                        pe.wait_ge(y_ready, NHB * n + at + 1)
                        if e:
                            pe.wait_ge(z_ready, e)
                        terms = [(c, f) for c in range(2) for f in range(HF)]
                        for j in range(HJ if o == 0 else HC // P):
                            for c, f in terms:
                                if o == 0:
                                    out, lhsT, rhs = inv_ps[:, bass.ts(j, HC)], inv[:, f, c, bass.ts(j, P)], y[:, c, bass.ts(f, HC)]
                                else:
                                    out, lhsT, rhs = inv_ps[:, bass.ts(j, HB)], y[:, c, bass.ds(f * HC + j * P, P)], inv[:, f, c, :]
                                last = nc.tensor.matmul(out, lhsT, rhs, start=((c, f) == terms[0]), stop=((c, f) == terms[-1]))
                        last.then_inc(inv_made, 1)
                        continue
                    q = moved[what, n, at]
                    if what == "U":
                        pe.wait_ge(u_loaded[n_u % 2], 16 * (n_u // 2 + 1))
                        parts = [((COS, COS), (SIN_NEG, SIN_NEG), u[n_u % 2][:, :, :])]
                        n_u += 1
                    else:
                        pe.wait_ge(filt_ready, N_F * (n + 1))
                        pe.wait_ge(ends_set, ENDS * (n + 1))
                        parts = [(re, im, filt[:, d, bass.ts(blk, HJ), :]) for re, im, d, blk in sources(at)]
                    for c in range(2):
                        if q:
                            pe.wait_ge(tr_copied, 2 * q + c - 1)
                        for f in range(HF):
                            terms = [(part[c][f], part[2], j) for part in parts for j in range(HJ)]
                            for x, (kind, src, j) in enumerate(terms):
                                last = nc.tensor.matmul(tr_ps[c][:, bass.ts(f, HC)], tr[:, j, kind, f, :], src[:, j, :],
                                                        start=(x == 0), stop=(x == len(terms) - 1))
                        last.then_inc(tr_made, 1)

            @block.scalar
            def _(act):
                for (what, n, at), q in moved.items():
                    for c in range(2):
                        act.wait_ge(tr_made, 2 * q + c + 1)
                        if n and c == 0:
                            act.wait_ge(pair_made, pair(n - 1, NHB - 1, at) if what == "U" else
                                        pair(n - 1, min(NHB - 1, NHB - 1 + at), NHB - 1 - max(at, 0)))
                        dst = U[at] if what == "U" else K[at]
                        act.activation(dst[:, c, :], tr_ps[c][:, :], ACT.Copy).then_inc(tr_copied, 1)

            @block.vector
            def _(dve):
                n_sum = 0

                def filters(n):
                    if n:
                        dve.wait_ge(tr_made, 2 * moved["K", n - 1, NHB - 1] + 2)
                    for t in range(NT):
                        dve.wait_ge(decay_loaded[t % 2], 16 * (NT // 2 * n + t // 2 + 1))
                        for d in range(2):
                            f = N_F * n + 2 * t + d
                            dve.wait_ge(filt_made, f + 1)
                            dve.tensor_tensor(filt[:, d, t, :], filt_ps[d][:, :], decay_sb[t % 2][:, :], ALU.mult).then_inc(filt_ready, 1)
                    dve.wait_ge(filt_ready, N_F * (n + 1))
                    dve.wait_ge(w3_loaded, 32 * (n + 1))
                    dve.tensor_tensor(filt[0:1, FWD, 0, :], filt[0:1, FWD, 0, :], bias_sb[:, :], ALU.add).then_inc(ends_set, 1)
                    dve.memset(filt[0:1, BWD, 0, :], 0.0).then_inc(ends_set, 1)

                def results(n, m_):
                    e = turned_back["Y", n, m_]
                    dve.wait_ge(inv_made, e + 1)
                    dve.wait_ge(gate_loaded[e % 2], 16 * (e // 2 + 1))
                    if e >= 2:
                        dve.wait_ge(z_stored[e % 2], 16 * (e // 2))
                    dve.tensor_tensor(z[e % 2][:, :], inv_ps[:, :], gate[e % 2][:, :], ALU.mult).then_inc(z_ready, 1)

                filters(0)
                for n in range(NP):
                    for m_ in range(NHB):
                        y = Y[m_ % 2]
                        if NHB * n + m_ >= 2:
                            before = ("Y", n, m_ - 2) if m_ >= 2 else ("Y", n - 1, m_ + NHB - 2)
                            dve.wait_ge(inv_made, turned_back[before] + 1)
                        for i in reversed(range(NHB)):
                            d = m_ - i
                            start = i == NHB - 1
                            dve.wait_ge(tr_copied, 2 * max(moved["U", n, i], moved["K", n, d]) + 2)
                            both = lambda c: U[i][:, c, :].unsqueeze(1).to_broadcast([P, 2, HF * HC])
                            dve.tensor_tensor((y if start else by_re)[:, :, :], K[d][:, :, :], both(0), ALU.mult).then_inc(re_made, 1)
                            dve.tensor_tensor(by_im[:, :, :], K[d][:, ::-1, :], both(1), ALU.mult).then_inc(pair_made, 1)
                            dve.wait_ge(re_made, pair(n, m_, i))
                            if not start:
                                dve.tensor_tensor(y[:, :, :], y[:, :, :], by_re[:, :, :], ALU.add).then_inc(sum_step, 1)
                                n_sum += 1
                                dve.wait_ge(sum_step, n_sum)
                            dve.wait_ge(pair_made, pair(n, m_, i))
                            dve.tensor_tensor(y[:, 0, :], y[:, 0, :], by_im[:, 0, :], ALU.subtract).then_inc(sum_step, 1)
                            dve.tensor_tensor(y[:, 1, :], y[:, 1, :], by_im[:, 1, :], ALU.add).then_inc(y_ready if i == 0 else sum_step, 1)
                            n_sum += 1 if i == 0 else 2
                            dve.wait_ge(sum_step, n_sum) if i else dve.wait_ge(y_ready, NHB * n + m_ + 1)
                        if m_ == 0 and n:
                            results(n - 1, NHB - 1)
                        if m_:
                            results(n, m_ - 1)
                        if m_ == 1 and n + 1 < NP:
                            filters(n + 1)
                results(NP - 1, NHB - 1)


N_EXP2, F_EXP2 = 16, 2 * D
CAP = 2 * T // N_EXP2
MAX_AT_ONCE = 8
TAKEN = -1.0


def expert_choice_phase(nc, h_T, w_router, ident, idx, scale):
    NE = N_EXP2
    with Store(nc, "choice") as m:
        w = m.sb("w", [P, ND, NE])
        aff = m.sb("aff", [P, NT, NE])
        best = m.sb("best", [P, NT])
        total = m.sb("total", [P, NT])
        aff_T = m.sb("aff_T", [NE, T])
        left = m.sb("left", [NE, T])
        top = m.sb("top", [NE, MAX_AT_ONCE])
        chosen = m.sb("chosen", [NE, T])
        ones_T = m.sb("ones_T", [NE, T])
        place = m.sb("place", [NE, T])
        place_t = m.sb("place_t", [P, NT, NE])
        slot = m.sb("slot", [P, CAP])
        what = m.sb("what", [P, NT, NE, 2])
        RING = 4
        hot = [m.sb(f"hot{r}", [P, CAP]) for r in range(RING)]
        logit_ps = m.ps("logit_ps", [P, NT, NE])
        aff_ps = m.ps("aff_ps", [NE, T])
        place_ps = m.ps("place_ps", [P, NT, NE])
        list_ps = m.ps("list_ps", [P, NE, 2])
        loaded = m.sem("loaded")
        made = m.sem("made")
        logits_ready = m.sem("logits_ready")
        diff_ready = m.sem("diff_ready")
        exp_ready = m.sem("exp_ready")
        aff_ready = m.sem("aff_ready")
        aff_turned = m.sem("aff_turned")
        place_ready = m.sem("place_ready")
        place_turned = m.sem("place_turned")
        hot_ready = m.sem("hot_ready")
        hot_used = m.sem("hot_used")
        step = m.sem("step")

        def over_e(x):
            return x.unsqueeze(2).to_broadcast([P, NT, NE])

        with nc.Block() as block:
            @block.sync
            def _(sp):
                sp.dma_start(w[:, :, :], w_router.rearrange("(k p) n -> p k n", p=P)).then_inc(loaded, 16)

            @block.gpsimd
            def _(pool):
                pool.iota(slot[:, :], pattern=[[1, CAP]], base=0, channel_multiplier=0, allow_small_or_imprecise_dtypes=True).then_inc(made, 1)
                pool.iota(what[:, :, :, 0], pattern=[[P, NT], [0, NE]], base=0, channel_multiplier=1, allow_small_or_imprecise_dtypes=True).then_inc(made, 1)
                pool.memset(ones_T[:, :], 1.0).then_inc(made, 1)

            @block.tensor
            def _(pe):
                pe.wait_ge(loaded, 16)
                for t in range(NT):
                    for k in range(ND):
                        last = nc.tensor.matmul(logit_ps[:, t, :], h_T[:, k, bass.ts(t, P)], w[:, k, :], start=(k == 0), stop=(k == ND - 1))
                last.then_inc(logits_ready, 1)
                pe.wait_ge(aff_ready, 1)
                for t in range(NT):
                    last = nc.tensor.transpose(aff_ps[:, bass.ts(t, P)], aff[:, t, :], ident[:, :])
                last.then_inc(aff_turned, 1)
                pe.wait_ge(place_ready, 1)
                for t in range(NT):
                    last = nc.tensor.transpose(place_ps[:, t, :], place[:, bass.ts(t, P)], ident[0:NE, 0:NE])
                last.then_inc(place_turned, 1)
                for e in range(NE):
                    for t in range(NT):
                        g = NT * e + t
                        pe.wait_ge(hot_ready, g + 1)
                        nc.tensor.matmul(list_ps[:, e, :], hot[g % RING][:, :], what[:, t, e, :], start=(t == 0), stop=(t == NT - 1)).then_inc(hot_used, 1)

            @block.scalar
            def _(act):
                act.wait_ge(diff_ready, 1)
                act.activation(aff[:, :, :], aff[:, :, :], ACT.Exp).then_inc(exp_ready, 1)

            @block.vector
            def _(dve):
                c = Chain(dve, step)
                dve.wait_ge(made, 3)
                dve.wait_ge(logits_ready, 1)
                c.then(dve.reduce_max(best[:, :], logit_ps[:, :, :], axis=AXX))
                dve.tensor_tensor(aff[:, :, :], logit_ps[:, :, :], over_e(best[:, :]), ALU.subtract).then_inc(diff_ready, 1)
                dve.wait_ge(exp_ready, 1)
                c.then(dve.reduce_sum(total[:, :], aff[:, :, :], axis=AXX))
                c.then(dve.reciprocal(total[:, :], total[:, :]))
                dve.tensor_tensor(aff[:, :, :], aff[:, :, :], over_e(total[:, :]), ALU.mult).then_inc(aff_ready, 1)
                dve.wait_ge(aff_ready, 1)
                c.then(dve.tensor_copy(what[:, :, :, 1], aff[:, :, :]))
                dve.wait_ge(aff_turned, 1)
                c.then(dve.tensor_copy(left[:, :], aff_ps[:, :]))
                for n in range(CAP // MAX_AT_ONCE):
                    c.then(dve.max(top[:, :], left[:, :]))
                    c.then(dve.match_replace(left[:, :], top[:, :], left[:, :], TAKEN))
                c.then(dve.tensor_scalar(chosen[:, :], left[:, :], TAKEN, None, ALU.is_equal))
                c.then(dve.tensor_tensor_scan(place[:, :], ones_T[:, :], chosen[:, :], 0.0, ALU.mult, ALU.add))
                c.then(dve.tensor_tensor(place[:, :], place[:, :], chosen[:, :], ALU.mult))
                dve.tensor_scalar(place[:, :], place[:, :], 1.0, None, ALU.subtract).then_inc(place_ready, 1)
                dve.wait_ge(place_turned, 1)
                c.then(dve.tensor_copy(place_t[:, :, :], place_ps[:, :, :]))
                for e in range(NE):
                    for t in range(NT):
                        g = NT * e + t
                        if g >= RING:
                            dve.wait_ge(hot_used, g - RING + 1)
                        dve.tensor_scalar(hot[g % RING][:, :], slot[:, :], place_t[:, t, e:e + 1], None, ALU.is_equal).then_inc(hot_ready, 1)
                dve.wait_ge(hot_used, NE * NT)
                c.then(dve.tensor_copy(idx[:, :], list_ps[:, :, 0]))
                c.then(dve.tensor_copy(scale[:, :], list_ps[:, :, 1]))


INPUTS = ("x", "norm1_g", "w_in", "gla_gate_w2", "gla_gate_b", "gla_norm_g", "w_out", "norm2_g", "router_group_w", "router_group_b",
          "router_expert_w", "router_expert_b", "expert_w1", "expert_w3", "expert_w2", "final_norm_g", "g_mix_2", "w_in_2", "conv_a_w_2",
          "conv_a_b_2", "lru_w_r_2", "lru_b_r_2", "lru_w_i_2", "lru_b_i_2", "lru_lambda_2", "w_a_out_2", "conv_b_w_2", "conv_b_b_2",
          "filt_w1_2", "filt_b1_2", "filt_w2_2", "filt_b2_2", "filt_w3_2", "filt_freq_2", "filt_bias_2", "w_b_out_2", "w_o_2", "g_ffn_2",
          "w_router_2", "w_gate_2", "w_up_2", "w_down_2", "g_final_2")


def constants():
    return {"gla_masks": gla_level_masks(), "att_bias": attention_bias(), "filt_positions": filter_positions(), "filt_decay": filter_decay(),
            "block_transform": block_transform(), "block_inverse": block_inverse()}


def build_program(nc, a, out):
    def dram(name, shape, dt=F32):
        return nc.dram_tensor(f"tmp_{name}", shape, dt, kind="Internal").ap()

    x1, h2, x2, x3, h3, total = (dram(n, [T, D]) for n in ("x1", "h2", "x2", "x3", "h3", "total"))
    row_tok = dram("row_tok", [N_BLK * SLOTS, 1], I32)
    y_rows = dram("y_rows", [N_BLK * SLOTS, D])
    v_x1, x2_T, z1, z_T = dram("v_x1", [T, 2 * HY_W]), dram("x2_T", [HY_W, T]), dram("z1", [T, HY_W]), dram("z_T", [HY_W, T])
    part_T, gate_T = dram("part_T", [D, T]), dram("gate_T", [D, T])

    ident = nc.alloc_sbuf_tensor("ident", [P, P], F32)
    ones_col = nc.alloc_sbuf_tensor("ones_col", [P, 1], F32)
    tables = {"gates": nc.alloc_sbuf_tensor("gates", [P, 2, NT], F32), "dest": nc.alloc_sbuf_tensor("dest", [P, 2 * NT], I32),
              "idx_all": nc.alloc_sbuf_tensor("idx_all", [P, N_BLK], I32), "over_exp": nc.alloc_sbuf_tensor("over_exp", [1, N_OVER], I32),
              "n_over": nc.alloc_sbuf_tensor("n_over", [1, 1], I32)}
    idx2 = nc.alloc_sbuf_tensor("idx2", [P, N_EXP2], I32)
    scale2 = nc.alloc_sbuf_tensor("scale2", [P, N_EXP2], F32)
    Store.used = []
    setup_constants(nc, ident, ones_col)

    with Store(nc, "mixer") as s:
        o_T = s.sb("o_T", [P, ND, T])
        with Store(nc, "mixer_in") as s_in:
            n_T = s_in.sb("n_T", [P, ND, T])
            norm_phase(nc, "norm1", a["x"], a["norm1_g"], ident, transposed=n_T)
            gla_phase(nc, n_T, a["w_in"], a["gla_gate_w2"], a["gla_gate_b"], a["gla_norm_g"], a["gla_masks"], ident, o_T)
            attention_phase(nc, n_T, a["w_in"], a["att_bias"], ident, o_T)
        residual_phase(nc, "out1", o_T, a["w_out"], a["x"], [x1])

    Store.give_back_semaphores(nc)

    with Store(nc, "routed") as s:
        h2_T = s.sb("h2_T", [P, ND, T])
        norm_phase(nc, "norm2", x1, a["norm2_g"], ident, natural=h2, transposed=h2_T)
        router_phase(nc, h2_T, a["router_group_w"], a["router_group_b"], a["router_expert_w"], a["router_expert_b"], tables, row_tok, y_rows)
    up_v, gate_v = (a[n].rearrange("e (k p) f -> e p k f", p=P) for n in ("expert_w1", "expert_w3"))
    down_v = a["expert_w2"].rearrange("e (k p) d -> e p k d", p=P)

    def expert(view):
        return lambda i, c: view[bass.ds(i * PER_STEP + c, 1), :, :, :].rearrange("o p k f -> (o p) k f")
    expert_phase(nc, "moe1", N_EXP // PER_STEP, expert(up_v), expert(gate_v), expert(down_v), tables["idx_all"], h2, ident, False, y_rows=y_rows)
    overflow_phase(nc, a["expert_w1"], a["expert_w3"], a["expert_w2"], tables, h2, y_rows, ident)

    Store.give_back_semaphores(nc)

    with Store(nc, "block2") as s:
        h_T = s.sb("h_T", [P, ND, T])
        ya_T = s.sb("ya_T", [P, N_LRU, T])
        combine_phase(nc, x1, y_rows, tables, a["final_norm_g"], a["g_mix_2"], ident, x2, h_T)
        lru_phase(nc, h_T, a["w_in_2"], a["conv_a_w_2"], a["conv_a_b_2"], a["lru_w_r_2"], a["lru_b_r_2"], a["lru_w_i_2"], a["lru_b_i_2"],
                  a["lru_lambda_2"], ident, ya_T)
        hyena_inputs_phase(nc, h_T, a["w_in_2"], a["conv_b_w_2"], a["conv_b_b_2"], ident, v_x1, x2_T)
        gates_phase(nc, h_T, ya_T, a["w_in_2"], a["w_a_out_2"], part_T, gate_T)
    with Store(nc, "long") as s:
        hid_T = s.sb("hid_T", [FILT_HID, T])
        filter_phase(nc, a["filt_positions"], a["filt_w1_2"], a["filt_b1_2"], a["filt_w2_2"], a["filt_b2_2"], a["filt_freq_2"], hid_T)
        hyena_phase(nc, v_x1, x2_T, hid_T, a["filt_w3_2"], a["filt_bias_2"], a["filt_decay"], a["block_transform"], a["block_inverse"], z1, z_T)
    with Store(nc, "merged") as s:
        merged_T = s.sb("merged_T", [P, ND, T])
        merge_phase(nc, z_T, a["w_b_out_2"], part_T, gate_T, merged_T)
        residual_phase(nc, "out2", merged_T, a["w_o_2"], x2, [x3, total])

    Store.give_back_semaphores(nc)

    with Store(nc, "chosen") as s:
        h3_T = s.sb("h3_T", [P, ND, T])
        norm_phase(nc, "norm3", x3, a["g_ffn_2"], ident, natural=h3, transposed=h3_T)
        expert_choice_phase(nc, h3_T, a["w_router_2"], ident, idx2, scale2)
    gate2_v, up2_v = (a[n].rearrange("e (k p) f -> e p k f", p=P) for n in ("w_gate_2", "w_up_2"))
    down2_v = a["w_down_2"].rearrange("e (k p) d -> e p k d", p=P)

    def columns(view):
        return lambda i, c: view[bass.ds(i, 1), :, :, bass.ts(c, CHUNK)].rearrange("o p k f -> (o p) k f")

    def rows(view):
        return lambda i, c: view[bass.ds(i, 1), :, bass.ts(c, CHUNK // P), :].rearrange("o p k d -> (o p) k d")
    expert_phase(nc, "moe2", N_EXP2, columns(gate2_v), columns(up2_v), rows(down2_v), idx2, h3, ident, True, scale=scale2, add_to=total)
    norm_phase(nc, "norm4", total, a["g_final_2"], ident, natural=out)


def kernel(**inputs):
    import concourse.bacc as bacc
    from concourse.bass_utils import run_bass_kernel_spmd

    nc = bacc.Bacc("TRN2", target_bir_lowering=False, num_devices=1)
    arrays, views = {}, {}
    for name, array in [(n, inputs[n]) for n in INPUTS] + list(constants().items()):
        array = np.ascontiguousarray(array)
        if array.ndim > 1 and array.shape[0] == 1:
            array = array.reshape(array.shape[1:])
        arrays[f"in_{name}_dram"] = array
        views[name] = nc.dram_tensor(f"in_{name}_dram", array.shape, mybir.dt.from_np(array.dtype), kind="ExternalInput").ap()
    out = nc.dram_tensor("out_0_dram", (1, T, D), F32, kind="ExternalOutput").ap()
    build_program(nc, views, out.rearrange("o t d -> (o t) d"))
    results = run_bass_kernel_spmd(nc, [arrays], core_ids=[0])
    return results.results[0]["out_0_dram"]
```

```python
from contextlib import ExitStack

import numpy as np

import concourse.bass as bass
from concourse import mybir

F32 = mybir.dt.float32
I32 = mybir.dt.int32
U32 = mybir.dt.uint32
F32R = mybir.dt.float32r
ACT = mybir.ActivationFunctionType
ALU = mybir.AluOpType
AXX = mybir.AxisListType.X

P = 128
T = 1024
D = 1024
NT = T // P
ND = D // P
EPS = 1e-6
BANK = 512


class Store:

    used = []

    def __init__(self, nc, name, side="left"):
        self.nc, self.name, self.side, self.stack = nc, name, side, ExitStack()

    def __enter__(self):
        self.stack.__enter__()
        return self

    def __exit__(self, *a):
        return self.stack.__exit__(*a)

    def open(self):
        return self.__enter__()

    def close(self):
        self.stack.close()

    def sb(self, name, shape, dt=F32):
        return self.stack.enter_context(self.nc.sbuf_tensor(f"{self.name}_{name}", shape, dt, side=self.side))

    def parts(self, name, shape):
        return Parts(self, name, self.sb(name, shape))

    def ps(self, name, shape, dt=F32):
        return self.stack.enter_context(self.nc.psum_tensor(f"{self.name}_{name}", shape, dt))

    def sem(self, name):
        Store.used.append(self.nc.alloc_semaphore(f"{self.name}_{name}"))
        return Store.used[-1]

    @staticmethod
    def give_back_semaphores(nc):
        nc.clear_and_free_semaphores(Store.used)
        nc.all_engine_barrier()
        Store.used = []


def first(i):
    return isinstance(i, int) and i == 0


def repeat(engine, n, body):
    body(0)
    with engine.Fori(1, n) as i:
        body(i)


def tile(t):
    return bass.ds(t, 1)


def row(vec):
    return vec.rearrange("(o n) -> o n", o=1)


class Parts:

    def __init__(self, store, name, whole):
        nc = store.nc
        self.whole = whole
        self.upper = store.sb(f"{name}_upper", whole.shape, F32R)
        self.rest = nc.alloc_sbuf_tensor_at(f"{store.name}_{name}_rest", whole.shape, F32R,
                                            offset=nc.lookup_mls(whole).memorylocations[0].addr)


WHOLE = (slice(None), slice(None), slice(None))


def split(dve, x, at, rounded, n, ready):
    dve.tensor_copy(x.upper[at], x.whole[at]).then_inc(rounded, 1)
    dve.wait_ge(rounded, n)
    dve.tensor_tensor(x.rest[at], x.whole[at], x.upper[at].bitcast(F32), ALU.subtract).then_inc(ready, 1)


def three_passes(lhs, rhs):
    return ((lhs.upper, rhs.upper), (lhs.upper, rhs.rest), (lhs.rest, rhs.upper))


def setup_constants(nc, ident, ones_col):
    cleared = nc.alloc_semaphore("ident_cleared")
    with nc.Block() as block:
        @block.gpsimd
        def _(pool):
            pool.memset(ident[:, :], 0.0).then_inc(cleared, 1)
            pool.memset(ones_col[:, :], 1.0)
            pool.wait_ge(cleared, 1)
            pool.affine_select(out=ident[:, :], in_=ident[:, :], compare_op=ALU.not_equal, fill=1.0,
                               base=0, pattern=[[-1, P]], channel_multiplier=1)


def norm_phase(nc, name, src, gain, ident, natural=None, transposed=None):
    with Store(nc, name) as m:
        xt = [m.sb(f"x{b}", [P, D]) for b in range(2)]
        xn = [m.sb(f"xn{b}", [P, D]) for b in range(2)]
        squares = m.sb("squares", [P, D])
        gain_b = m.sb("gain", [P, D])
        ssum = m.sb("ssum", [P, 2])
        rms = m.sb("rms", [P, 2])
        rstd = m.sb("rstd", [P, 2])
        eps = m.sb("eps", [P, 1])
        turned = [m.ps(f"turned{b}", [P, 2, BANK]) for b in range(2)]
        eps_set = m.sem("eps_set")
        x_loaded = [m.sem(f"x_loaded{b}") for b in range(2)]
        gain_loaded = m.sem("gain_loaded")
        ssum_ready = m.sem("ssum_ready")
        rms_ready = m.sem("rms_ready")
        rstd_ready = m.sem("rstd_ready")
        xn_ready = m.sem("xn_ready")
        xn_turned = m.sem("xn_turned")
        turned_copied = m.sem("turned_copied")
        stored = [m.sem(f"stored{b}") for b in range(2)]
        src_t = src.rearrange("(t p) d -> t p d", p=P)
        nat_t = natural.rearrange("(t p) d -> t p d", p=P) if natural is not None else None
        with nc.Block() as block:
            @block.sync
            def _(sp):
                sp.dma_start(gain_b[:, :], row(gain).partition_broadcast(P)).then_inc(gain_loaded, 16)

                def load(i):
                    for b in range(2):
                        if not first(i):
                            sp.wait_ge(xn_ready, 2 * i + b - 1)
                        sp.dma_start(xt[b][:, :], src_t[tile(2 * i + b), :, :]).then_inc(x_loaded[b], 16)
                repeat(sp, NT // 2, load)

            @block.gpsimd
            def _(pool):
                if natural is None:
                    return
                with pool.Fori(0, NT // 2) as i:
                    for b in range(2):
                        pool.wait_ge(xn_ready, 2 * i + b + 1)
                        pool.dma_start(nat_t[tile(2 * i + b), :, :], xn[b][:, :]).then_inc(stored[b], 16)
                for b in range(2):
                    pool.wait_ge(stored[b], 16 * (NT // 2))

            @block.scalar
            def _(act):
                act.wait_ge(eps_set, 1)
                with act.Fori(0, NT // 2) as i:
                    for b in range(2):
                        act.wait_ge(x_loaded[b], 16 * (i + 1))
                        act.activation(squares[:, :], xt[b][:, :], ACT.Square, accum_out=ssum[:, b:b + 1]).then_inc(ssum_ready, 1)
                        act.wait_ge(ssum_ready, 2 * i + b + 1)
                        act.activation(rms[:, b:b + 1], ssum[:, b:b + 1], ACT.Sqrt, scale=1.0 / D, bias=eps[:, :]).then_inc(rms_ready, 1)
                    for b in range(2 if transposed is not None else 0):
                        act.wait_ge(xn_turned, 2 * i + b + 1)
                        act.activation(transposed[:, :, bass.ds((2 * i + b) * P, P)],
                                       turned[b][:, :, :].rearrange("p a (k t) -> p (a k) t", t=P), ACT.Copy).then_inc(turned_copied, 1)

            @block.vector
            def _(dve):
                dve.memset(eps[:, :], EPS).then_inc(eps_set, 1)
                dve.wait_ge(gain_loaded, 16)

                def norm(i):
                    for b in range(2):
                        dve.wait_ge(rms_ready, 2 * i + b + 1)
                        dve.reciprocal(rstd[:, b:b + 1], rms[:, b:b + 1]).then_inc(rstd_ready, 1)
                        dve.wait_ge(rstd_ready, 2 * i + b + 1)
                        if not first(i):
                            if transposed is not None:
                                dve.wait_ge(xn_turned, 2 * i + b - 1)
                            if natural is not None:
                                dve.wait_ge(stored[b], 16 * i)
                        dve.scalar_tensor_tensor(xn[b][:, :], xt[b][:, :], rstd[:, b:b + 1], gain_b[:, :],
                                                 ALU.mult, ALU.mult).then_inc(xn_ready, 1)
                repeat(dve, NT // 2, norm)

            @block.tensor
            def _(pe):
                if transposed is None:
                    return

                def turn(i):
                    for b in range(2):
                        pe.wait_ge(xn_ready, 2 * i + b + 1)
                        if not first(i):
                            pe.wait_ge(turned_copied, 2 * i + b - 1)
                        for k in range(ND):
                            last = nc.tensor.transpose(turned[b][:, k // 4, bass.ts(k % 4, P)], xn[b][:, bass.ts(k, P)], ident[:, :])
                        last.then_inc(xn_turned, 1)
                repeat(pe, NT // 2, turn)


def residual_norm_phase(nc, name, act_T, w, res, outs, gain, ident, normed, normed_T):
    with Store(nc, name) as m:
        w_p = m.parts("w", [P, ND, D])
        act_p = Parts(m, "act", act_T)
        res_sb = [m.sb(f"res{b}", [P, D]) for b in range(2)]
        x = [m.sb(f"x{b}", [P, D]) for b in range(2)]
        xn = [m.sb(f"xn{b}", [P, D]) for b in range(2)]
        squares = m.sb("squares", [P, D])
        gain_b = m.sb("gain", [P, D])
        ssum = m.sb("ssum", [P, NT])
        rms = m.sb("rms", [P, NT])
        rstd = m.sb("rstd", [P, NT])
        eps = m.sb("eps", [P, 1])
        prod = [m.ps(f"prod{b}", [P, 2, BANK]) for b in range(2)]
        turned = [m.ps(f"turned{b}", [P, 2, BANK]) for b in range(2)]
        w_loaded = [m.sem(f"w_loaded{k}") for k in range(ND)]
        res_loaded = [m.sem(f"res_loaded{b}") for b in range(2)]
        gain_loaded = m.sem("gain_loaded")
        rounded = m.sem("rounded")
        w_split = m.sem("w_split")
        act_split = m.sem("act_split")
        prod_ready = m.sem("prod_ready")
        x_ready = m.sem("x_ready")
        eps_set = m.sem("eps_set")
        ssum_ready = m.sem("ssum_ready")
        rms_ready = m.sem("rms_ready")
        rstd_ready = m.sem("rstd_ready")
        xn_ready = m.sem("xn_ready")
        xn_turned = m.sem("xn_turned")
        copied = m.sem("copied")
        x_stored = [m.sem(f"x_stored{b}") for b in range(2)]
        xn_stored = [m.sem(f"xn_stored{b}") for b in range(2)]
        with nc.Block() as block:
            @block.sync
            def _(sp):
                for k in range(ND):
                    sp.dma_start(w_p.whole[:, k, :], w[bass.ts(k, P), :]).then_inc(w_loaded[k], 16)
                sp.dma_start(gain_b[:, :], row(gain).partition_broadcast(P)).then_inc(gain_loaded, 16)
                for t in range(NT):
                    if t >= 2:
                        sp.wait_ge(x_ready, t - 1)
                    sp.dma_start(res_sb[t % 2][:, :], res[bass.ts(t, P), :]).then_inc(res_loaded[t % 2], 16)

            @block.gpsimd
            def _(pool):
                for t in range(NT):
                    b = t % 2
                    pool.wait_ge(x_ready, t + 1)
                    for out in outs:
                        pool.dma_start(out[bass.ts(t, P), :], x[b][:, :]).then_inc(x_stored[b], 16)
                    pool.wait_ge(xn_ready, t + 1)
                    pool.dma_start(normed[bass.ts(t, P), :], xn[b][:, :]).then_inc(xn_stored[b], 16)
                for b in range(2):
                    pool.wait_ge(x_stored[b], 16 * len(outs) * (NT // 2))
                    pool.wait_ge(xn_stored[b], 16 * (NT // 2))

            @block.tensor
            def _(pe):
                def turn(t):
                    pe.wait_ge(xn_ready, t + 1)
                    if t >= 2:
                        pe.wait_ge(copied, t - 1)
                    turn_rows(nc, xn[t % 2], turned[t % 2], ident).then_inc(xn_turned, 1)

                for t in range(NT):
                    pe.wait_ge(act_split, t + 1)
                    if t >= 2:
                        pe.wait_ge(x_ready, t - 1)
                    for k in range(ND):
                        if t == 0:
                            pe.wait_ge(w_split, k + 1)
                        for h in range(2):
                            for n, (lhs, rhs) in enumerate(three_passes(act_p, w_p)):
                                last = nc.tensor.matmul(prod[t % 2][:, h, :], lhs[:, k, bass.ts(t, P)], rhs[:, k, bass.ts(h, BANK)],
                                                        start=(k == 0 and n == 0), stop=(k == ND - 1 and n == 2))
                    last.then_inc(prod_ready, 1)
                    if t:
                        turn(t - 1)
                turn(NT - 1)

            @block.scalar
            def _(act):
                act.wait_ge(eps_set, 1)
                for t in range(NT):
                    act.wait_ge(ssum_ready, t + 1)
                    act.activation(rms[:, t:t + 1], ssum[:, t:t + 1], ACT.Sqrt, scale=1.0 / D, bias=eps[:, :]).then_inc(rms_ready, 1)
                    act.wait_ge(xn_turned, t + 1)
                    act.activation(normed_T[:, :, bass.ts(t, P)], turned[t % 2][:, :, :].rearrange("p a (k q) -> p (a k) q", q=P), ACT.Copy).then_inc(copied, 1)

            @block.vector
            def _(dve):
                dve.memset(eps[:, :], EPS).then_inc(eps_set, 1)

                def split_act(t):
                    split(dve, act_p, (slice(None), slice(None), bass.ts(t, P)), rounded, 1 if t == 0 else ND + 1 + t, act_split)

                split_act(0)
                for k in range(ND):
                    dve.wait_ge(w_loaded[k], 16)
                    split(dve, w_p, (slice(None), k, slice(None)), rounded, k + 2, w_split)
                dve.wait_ge(gain_loaded, 16)
                for t in range(NT):
                    b = t % 2
                    if t + 1 < NT:
                        split_act(t + 1)
                    dve.wait_ge(prod_ready, t + 1)
                    dve.wait_ge(res_loaded[b], 16 * (t // 2 + 1))
                    if t >= 2:
                        dve.wait_ge(x_stored[b], 16 * len(outs) * (t // 2))
                        dve.wait_ge(xn_stored[b], 16 * (t // 2))
                        dve.wait_ge(xn_turned, t - 1)
                    dve.tensor_tensor(x[b][:, :], prod[b][:, :, :].rearrange("p a n -> p (a n)"), res_sb[b][:, :], ALU.add).then_inc(x_ready, 1)
                    dve.wait_ge(x_ready, t + 1)
                    dve.tensor_tensor_reduce(out=squares[:, :], in0=x[b][:, :], in1=x[b][:, :], scale=1.0, scalar=0.0, op0=ALU.mult, op1=ALU.add,
                                             accum_out=ssum[:, t:t + 1]).then_inc(ssum_ready, 1)
                    dve.wait_ge(rms_ready, t + 1)
                    dve.reciprocal(rstd[:, t:t + 1], rms[:, t:t + 1]).then_inc(rstd_ready, 1)
                    dve.wait_ge(rstd_ready, t + 1)
                    dve.scalar_tensor_tensor(xn[b][:, :], x[b][:, :], rstd[:, t:t + 1], gain_b[:, :], ALU.mult, ALU.mult).then_inc(xn_ready, 1)
                    dve.wait_ge(xn_ready, t + 1)


GLA_H, GLA_K, GLA_V, GLA_LOW = 4, 64, 128, 16
GLA_QK = GLA_H * GLA_K
GLA_VW = GLA_H * GLA_V
GLA_TAU = 16.0
ATT_H, ATT_D = 8, 64
ATT_W = ATT_H * ATT_D
COL_GQ, COL_GK, COL_GV, COL_GR = 0, GLA_QK, 2 * GLA_QK, 2 * GLA_QK + GLA_VW
COL_LOW = COL_GR + GLA_VW
COL_AQ = COL_LOW + GLA_LOW
COL_AK, COL_AV = COL_AQ + ATT_W, COL_AQ + 2 * ATT_W
LEVELS = [1 << s for s in range(7)]


def gla_level_masks():
    key, query = np.arange(P)[:, None], np.arange(P)[None, :]
    masks = [(key // (2 * s) == query // (2 * s)) & (key // s % 2 == 0) & (query // s % 2 == 1) for s in LEVELS]
    masks.append(key == query)
    return np.ascontiguousarray(np.stack(masks, axis=1).astype(np.uint32))


def gla_phase(nc, n_T, w_in, gate_w2, gate_b, norm_g, masks, ident, o_T):
    NQ = GLA_QK // P
    RING = 4
    with Store(nc, "gla") as m:
        wqk = m.sb("wqk", [P, ND, 2 * GLA_QK])
        wv = m.sb("wv", [P, ND, GLA_VW])
        wr = m.sb("wr", [P, ND, GLA_VW])
        wlow = m.sb("wlow", [P, ND, GLA_LOW])
        w2 = m.sb("w2", [GLA_LOW, GLA_QK])
        bias = m.sb("bias", [P, NQ])
        ng_b = m.sb("ng", [P, GLA_V])
        mask = m.sb("mask", [P, len(LEVELS) + 1, P], U32)
        q_T = m.sb("q", [P, NQ, T])
        k_T = m.sb("k", [P, NQ, T])
        cum = m.sb("cum", [P, NQ, T])
        t1 = m.sb("t1", [P, NQ, T])
        mix = [m.sb(f"mix{b}", [P, NQ, T]) for b in range(2)]
        v = m.sb("v", [P, NT, GLA_VW])
        gate = m.sb("gate", [P, NT, GLA_VW])
        low_T = mix[1][0:GLA_LOW, 0, :]
        t2 = mix[0]
        score_T = wqk[:, :, :].rearrange("p t (h q) -> p t h q", q=P)
        kd = wv[:, 0:NT // 2, :].rearrange("p a (b c) -> p (a b) c", c=GLA_QK)
        state = wr[:, :, :].rearrange("p a (t v) -> p (a t) v", v=2 * GLA_V).rearrange("p (j t) v -> p j t v", j=NQ)
        a_tile = m.sb("a_tile", [P, NQ, NT])
        o_n = [m.sb(f"o_n{b}", [P, GLA_VW]) for b in range(2)]
        osq = m.sb("osq", [P, GLA_VW])
        ssum = m.sb("ssum", [P, NT, GLA_H])
        rms = m.sb("rms", [P, NT, GLA_H])
        rstd = m.sb("rstd", [P, NT, GLA_H])
        eps = m.sb("eps", [P, 1])
        one = m.sb("one", [P, P])
        two_banks = [m.ps(f"banks{r}", [P, 2, BANK]) for r in range(4)]
        bank = [two_banks[r // 2][:, r % 2, :] for r in range(8)]
        w_loaded = {n: m.sem(n + "_loaded") for n in ("low", "small", "qk", "v", "r", "mask")}
        proj_ready = m.sem("proj_ready")
        proj_read = m.sem("proj_read")
        low_ready = m.sem("low_ready")
        la_step = m.sem("la_step")
        ln_ready = m.sem("ln_ready")
        dve_step = m.sem("dve_step")
        diff_ready = m.sem("diff_ready")
        decay_ready = m.sem("decay_ready")
        mix_ready = m.sem("mix_ready")
        scored = m.sem("scored")
        picked = m.sem("picked")
        kd_turned = m.sem("kd_turned")
        kd_ready = m.sem("kd_ready")
        update_ready = m.sem("update_ready")
        state_ready = m.sem("state_ready")
        o_ready = m.sem("o_ready")
        osq_ready = m.sem("osq_ready")
        osum_ready = m.sem("osum_ready")
        rms_ready = m.sem("rms_ready")
        on_ready = m.sem("on_ready")
        on_turned = m.sem("on_turned")
        o_stored = m.sem("o_stored")
        w_k = w_in.rearrange("(k p) n -> p k n", p=P)
        PROJ = [("low", 0, h) for h in range(2)] + [("z", j, h) for j in range(NQ) for h in range(2)]
        PROJ += [(n, j, h) for n in ("q", "k") for j in range(NQ) for h in range(2)]
        PROJ += [("v", t, 0) for t in range(NT)] + [("r", t, 0) for t in range(NT)]
        N_LOW, N_Z, N_QK = 2, 2 + 2 * NQ, 2 + 6 * NQ
        N_V, N_PROJ = N_QK + NT, N_QK + 2 * NT
        NL = len(LEVELS)
        with nc.Block() as block:
            @block.sync
            def _(sp):
                sp.dma_start(wlow[:, :, :], w_k[:, :, COL_LOW:COL_LOW + GLA_LOW]).then_inc(w_loaded["low"], 16)
                sp.dma_start(w2[:, :], gate_w2).then_inc(w_loaded["small"], 16)
                with nc.allow_non_contiguous_dma(reason="a bias per partition"):
                    sp.dma_start(bias[:, :], gate_b.rearrange("(j p) -> p j", p=P)).then_inc(w_loaded["small"], 16)
                sp.dma_start(ng_b[:, :], row(norm_g).partition_broadcast(P)).then_inc(w_loaded["small"], 16)
                sp.dma_start(wqk[:, :, :], w_k[:, :, COL_GQ:COL_GQ + 2 * GLA_QK]).then_inc(w_loaded["qk"], 16)
                sp.dma_start(wv[:, :, :], w_k[:, :, COL_GV:COL_GV + GLA_VW]).then_inc(w_loaded["v"], 16)
                sp.dma_start(wr[:, :, :], w_k[:, :, COL_GR:COL_GR + GLA_VW]).then_inc(w_loaded["r"], 16)
                sp.dma_start(mask[:, :, :], masks).then_inc(w_loaded["mask"], 16)

            @block.tensor
            def _(pe):
                pe.wait_ge(w_loaded["low"], 16)
                for g, (what, j, h) in enumerate(PROJ):
                    out = bank[g % RING]
                    if g >= RING + N_LOW:
                        pe.wait_ge(proj_read, g - RING - N_LOW + 1)
                    elif g >= RING:
                        pe.wait_ge(low_ready, g - RING + 1)
                    if what == "z":
                        if g == N_LOW:
                            pe.wait_ge(w_loaded["small"], 48)
                            pe.wait_ge(low_ready, 2)
                        last = nc.tensor.matmul(out[:, :], w2[:, bass.ts(j, P)], low_T[:, bass.ts(h, BANK)], start=True, stop=True)
                    else:
                        if g == N_Z:
                            pe.wait_ge(w_loaded["qk"], 16)
                        if g == N_QK:
                            pe.wait_ge(w_loaded["v"], 16)
                        if g == N_V:
                            pe.wait_ge(w_loaded["r"], 16)
                        for k in range(ND):
                            if what == "low":
                                o, lhsT, rhs = out[0:GLA_LOW, :], wlow[:, k, :], n_T[:, k, bass.ts(h, BANK)]
                            elif what in "qk":
                                o, lhsT, rhs = out[:, :], wqk[:, k, bass.ds((what == "k") * GLA_QK + j * P, P)], n_T[:, k, bass.ts(h, BANK)]
                            else:
                                o, lhsT, rhs = out[:, :], n_T[:, k, bass.ts(j, P)], (wv if what == "v" else wr)[:, k, :]
                            last = nc.tensor.matmul(o, lhsT, rhs, start=(k == 0), stop=(k == ND - 1))
                    last.then_inc(proj_ready, 1)

                s = 0
                for level in range(NL + 1):
                    if level < NL:
                        pe.wait_ge(mix_ready, 2 * (level + 1))
                    if level == 0:
                        pe.wait_ge(proj_read, N_PROJ - N_LOW)
                    for t in range(NT):
                        if s >= 2:
                            pe.wait_ge(picked, s - 1)
                        for odd in range(2):
                            part = slice(odd * GLA_K, (odd + 1) * GLA_K)
                            for j in range(NQ):
                                lhsT = (k_T if level == NL else mix[level % 2])[part, j, bass.ts(t, P)]
                                rhs = (q_T if level == NL else mix[level % 2])[part, j, bass.ts(t, P)]
                                last = nc.tensor.matmul(two_banks[s % 2][:, odd, bass.ts(j, P)], lhsT, rhs, start=True, stop=True)
                        last.then_inc(scored, 1)
                        s += 1

                pe.wait_ge(mix_ready, 2 * NL + 1)
                for t in range(NT):
                    if t >= 2:
                        pe.wait_ge(kd_ready, t - 1)
                    for j in range(NQ):
                        last = nc.tensor.transpose(bank[4 + t % 2][:, bass.ts(j, P)], mix[NL % 2][:, j, bass.ts(t, P)], ident[:, :])
                    last.then_inc(kd_turned, 1)

                pe.wait_ge(picked, NT * (NL + 1))
                pe.wait_ge(mix_ready, 2 * NL + 2)
                for t in range(NT):
                    b = t % 2
                    pe.wait_ge(kd_ready, t + 1)
                    if t >= 1:
                        pe.wait_ge(state_ready, GLA_H * t)
                    for j in range(NQ):
                        last = nc.tensor.matmul(bank[6][:, bass.ts(j, 2 * GLA_V)], kd[:, t, bass.ts(j, P)], v[:, t, bass.ts(j, 2 * GLA_V)],
                                                start=True, stop=True)
                    last.then_inc(update_ready, 1)
                    if t >= 2:
                        pe.wait_ge(on_ready, t - 1)
                    for j in range(NQ):
                        if t > 0:
                            nc.tensor.matmul(bank[b][:, bass.ts(j, 2 * GLA_V)], mix[(NL + 1) % 2][:, j, bass.ts(t, P)], state[:, j, t, :],
                                             start=True, stop=False)
                        for odd in range(2):
                            hd = 2 * j + odd
                            last = nc.tensor.matmul(bank[b][:, bass.ts(hd, GLA_V)], score_T[:, t, odd * NQ + j, :], v[:, t, bass.ts(hd, GLA_V)],
                                                    start=(t == 0), stop=(t == 0 or odd == 1))
                    last.then_inc(o_ready, 1)
                    for u in ([t - 1] if t else []) + ([t] if t == NT - 1 else []):
                        pe.wait_ge(on_ready, u + 1)
                        if u >= 2:
                            pe.wait_ge(o_stored, u - 1)
                        for hd in range(GLA_H):
                            last = nc.tensor.transpose(bank[2 + u % 2][:, bass.ts(hd, P)], o_n[u % 2][:, bass.ts(hd, P)], ident[:, :])
                        last.then_inc(on_turned, 1)

            @block.scalar
            def _(act):
                act.wait_ge(w_loaded["small"], 48)
                for g in range(N_LOW, N_Z):
                    j, h = PROJ[g][1:]
                    act.wait_ge(proj_ready, g + 1)
                    act.activation(t1[:, j, bass.ts(h, BANK)], bank[g % RING][:, :], ACT.Identity, bias=bias[:, j:j + 1]).then_inc(proj_read, 1)
                act.wait_ge(proj_read, N_Z - N_LOW)
                act.activation(t2[:, :, :], t1[:, :, :], ACT.Abs).then_inc(la_step, 1)
                act.wait_ge(la_step, 1)
                act.activation(t2[:, :, :], t2[:, :, :], ACT.Exp, scale=-1.0).then_inc(la_step, 1)
                act.wait_ge(la_step, 2)
                act.activation(t2[:, :, :], t2[:, :, :], ACT.Ln, bias=one[:, 0:1]).then_inc(ln_ready, 1)
                for g in range(N_Z, N_PROJ):
                    what, j, h = PROJ[g]
                    act.wait_ge(proj_ready, g + 1)
                    if what in "qk":
                        act.activation((q_T if what == "q" else k_T)[:, j, bass.ts(h, BANK)], bank[g % RING][:, :], ACT.Copy,
                                       scale=GLA_K ** -0.5 if what == "q" else 1.0).then_inc(proj_read, 1)
                    elif what == "v":
                        act.activation(v[:, j, :], bank[g % RING][:, :], ACT.Copy).then_inc(proj_read, 1)
                    else:
                        act.activation(gate[:, j, :], bank[g % RING][:, :], ACT.Silu).then_inc(proj_read, 1)
                for level, s in enumerate(LEVELS):
                    act.wait_ge(diff_ready, level + 1)
                    halves = t1[:, :, :].rearrange("p j (n two s) -> p (j n) two s", two=2, s=s)
                    act.activation(halves[:, :, 0, :], halves[:, :, 0, :], ACT.Exp, scale=-1.0).then_inc(decay_ready, 1)
                    act.activation(halves[:, :, 1, :], halves[:, :, 1, :], ACT.Exp).then_inc(decay_ready, 1)
                act.wait_ge(diff_ready, NL + 1)
                act.activation(t1[:, :, :], t1[:, :, :], ACT.Exp, scale=-1.0).then_inc(decay_ready, 1)
                ends = cum[:, :, :].rearrange("p j (t c) -> p j t c", c=P)[:, :, :, P - 1]
                act.activation(a_tile[:, :, :], ends, ACT.Exp).then_inc(decay_ready, 1)
                act.wait_ge(decay_ready, 2 * NL + 2)
                act.activation(cum[:, :, :], cum[:, :, :], ACT.Exp).then_inc(decay_ready, 1)
                for t in range(NT):
                    act.wait_ge(kd_turned, t + 1)
                    act.activation(kd[:, t, :], bank[4 + t % 2][:, 0:GLA_QK], ACT.Copy).then_inc(kd_ready, 1)
                for t in range(NT):
                    act.wait_ge(osum_ready, t + 1)
                    act.activation(rms[:, t, :], ssum[:, t, :], ACT.Sqrt, scale=1.0 / GLA_V, bias=eps[:, :]).then_inc(rms_ready, 1)
                    for u in ([t - 1] if t else []) + ([t] if t == NT - 1 else []):
                        act.wait_ge(on_turned, u + 1)
                        act.activation(o_T[:, 0:GLA_H, bass.ts(u, P)], bank[2 + u % 2][:, :].rearrange("p (h t) -> p h t", t=P),
                                       ACT.Copy).then_inc(o_stored, 1)

            @block.vector
            def _(dve):
                dve.memset(eps[:, :], EPS).then_inc(dve_step, 1)
                dve.memset(one[:, :], 1.0).then_inc(dve_step, 1)
                n = 2
                for h in range(N_LOW):
                    dve.wait_ge(proj_ready, h + 1)
                    dve.tensor_copy(low_T[:, bass.ts(h, BANK)], bank[h][0:GLA_LOW, :]).then_inc(low_ready, 1)
                dve.wait_ge(proj_ready, N_QK)
                dve.memset(wqk[:, :, :], 0.0).then_inc(dve_step, 1)
                n += 1
                dve.wait_ge(ln_ready, 1)
                dve.tensor_scalar(t1[:, :, :], t1[:, :, :], 0.0, None, ALU.min).then_inc(dve_step, 1)
                n += 1
                dve.wait_ge(dve_step, n)
                dve.tensor_tensor(t1[:, :, :], t1[:, :, :], t2[:, :, :], ALU.subtract).then_inc(dve_step, 1)
                n += 1
                dve.wait_ge(dve_step, n)
                dve.tensor_scalar(t2[:, :, :], t1[:, :, :], 1.0 / GLA_TAU, None, ALU.mult).then_inc(dve_step, 1)
                n += 1
                dve.wait_ge(dve_step, n)
                for j in range(NQ):
                    for t in range(NT):
                        dve.tensor_tensor_scan(cum[:, j, bass.ts(t, P)], one[:, :], t2[:, j, bass.ts(t, P)], 0.0, ALU.mult, ALU.add).then_inc(dve_step, 1)
                        n += 1
                dve.wait_ge(dve_step, n)
                dve.wait_ge(w_loaded["mask"], 16)
                dve.wait_ge(proj_read, N_PROJ - N_LOW)
                dve.memset(wr[:, :, :], 0.0).then_inc(dve_step, 1)
                n += 1
                dve.wait_ge(dve_step, n)

                def level_diff(s):
                    blocks = cum[:, :, :].rearrange("p j (n b) -> p (j n) b", b=2 * s)
                    middle = blocks[:, :, s - 1:s].to_broadcast([P, NQ * T // (2 * s), 2 * s])
                    dve.tensor_tensor(t1[:, :, :].rearrange("p j (n b) -> p (j n) b", b=2 * s), blocks, middle, ALU.subtract).then_inc(diff_ready, 1)

                def pick(level):
                    for t in range(NT):
                        g = level * NT + t
                        dve.wait_ge(scored, g + 1)
                        dve.copy_predicated(score_T[:, t, :, :].rearrange("p (o j) q -> p o j q", o=2),
                            mask[:, level:level + 1, :].unsqueeze(1).to_broadcast([P, 2, NQ, P]),
                                            two_banks[g % 2][:, :, 0:NQ * P].rearrange("p o (j q) -> p o j q", q=P)).then_inc(picked, 1)

                for level, s in enumerate(LEVELS):
                    if level:
                        dve.wait_ge(mix_ready, 2 * level)
                    level_diff(s)
                    if level:
                        pick(level - 1)
                    dve.wait_ge(decay_ready, 2 * (level + 1))
                    out = mix[level % 2][:, :, :].rearrange("p j (n two s) -> p (j n) two s", two=2, s=s)
                    dec = t1[:, :, :].rearrange("p j (n two s) -> p (j n) two s", two=2, s=s)
                    if level >= 2:
                        dve.wait_ge(scored, NT * (level - 1))
                    for half, src in enumerate((k_T, q_T)):
                        dve.tensor_tensor(out[:, :, half, :], src[:, :, :].rearrange("p j (n two s) -> p (j n) two s", two=2, s=s)[:, :, half, :],
                                          dec[:, :, half, :], ALU.mult).then_inc(mix_ready, 1)
                dve.wait_ge(mix_ready, 2 * NL)
                tiles = cum[:, :, :].rearrange("p j (t c) -> p (j t) c", c=P)
                dve.tensor_tensor(t1[:, :, :].rearrange("p j (t c) -> p (j t) c", c=P), tiles,
                                  tiles[:, :, P - 1:P].to_broadcast([P, NQ * NT, P]), ALU.subtract).then_inc(diff_ready, 1)
                pick(NL - 1)
                pick(NL)
                dve.wait_ge(decay_ready, 2 * NL + 3)
                dve.tensor_tensor(mix[NL % 2][:, :, :], k_T[:, :, :], t1[:, :, :], ALU.mult).then_inc(mix_ready, 1)
                dve.tensor_tensor(mix[(NL + 1) % 2][:, :, :], q_T[:, :, :], cum[:, :, :], ALU.mult).then_inc(mix_ready, 1)
                dve.tensor_tensor(gate[:, :, :].rearrange("p t (h v) -> p (t h) v", v=GLA_V), gate[:, :, :].rearrange("p t (h v) -> p (t h) v", v=GLA_V),
                                  ng_b[:, :].rearrange("p (o v) -> p o v", o=1).to_broadcast([P, NT * GLA_H, GLA_V]), ALU.mult).then_inc(dve_step, 1)
                n += 1
                for t in range(NT):
                    dve.wait_ge(update_ready, t + 1)
                    if t:
                        dve.wait_ge(state_ready, GLA_H * t)
                    for hd in range(GLA_H):
                        j, part, cols = hd // 2, slice((hd % 2) * GLA_K, (hd % 2 + 1) * GLA_K), slice((hd % 2) * GLA_V, (hd % 2 + 1) * GLA_V)
                        new = bank[6][part, bass.ts(hd, GLA_V)]
                        if t == 0:
                            dve.tensor_copy(state[part, j, 1, cols], new).then_inc(state_ready, 1)
                        elif t + 1 < NT:
                            dve.scalar_tensor_tensor(state[part, j, t + 1, cols], state[part, j, t, cols], a_tile[part, j, t:t + 1], new,
                                                     ALU.mult, ALU.add).then_inc(state_ready, 1)
                    dve.wait_ge(o_ready, t + 1)
                    o = bank[t % 2][:, :]
                    if t >= 2:
                        dve.wait_ge(on_turned, t - 1)
                    dve.tensor_copy(o_n[t % 2][:, :], o).then_inc(dve_step, 1)
                    n += 1
                    dve.wait_ge(dve_step, n)
                    dve.tensor_tensor(osq[:, :], o_n[t % 2][:, :], o_n[t % 2][:, :], ALU.mult).then_inc(dve_step, 1)
                    n += 1
                    dve.wait_ge(dve_step, n)
                    dve.reduce_sum(ssum[:, t, :], osq[:, :].rearrange("p (h v) -> p h v", v=GLA_V), axis=AXX).then_inc(osum_ready, 1)
                    dve.wait_ge(rms_ready, t + 1)
                    dve.reciprocal(rstd[:, t, :], rms[:, t, :]).then_inc(dve_step, 1)
                    n += 1
                    dve.tensor_tensor(o_n[t % 2][:, :], o_n[t % 2][:, :], gate[:, t, :], ALU.mult).then_inc(dve_step, 1)
                    n += 1
                    dve.wait_ge(dve_step, n)
                    dve.tensor_tensor(o_n[t % 2][:, :].rearrange("p (h v) -> p h v", v=GLA_V), o_n[t % 2][:, :].rearrange("p (h v) -> p h v", v=GLA_V),
                                      rstd[:, t, :].unsqueeze(2).to_broadcast([P, GLA_H, GLA_V]), ALU.mult).then_inc(on_ready, 1)


DILATIONS = ((128, 1), (512, 4), (2048, 16))
MASKED = -1e30


def attention_bias():
    q = np.arange(P)[:, None, None]
    back = (np.arange(NT - 1, -1, -1)[None, :, None] * P + q - np.arange(P)[None, None, :])
    count = sum(((back >= 0) & (back <= w) & (back % d == 0)).astype(np.int64) for w, d in DILATIONS)
    return np.where(count > 0, np.log(np.maximum(count, 1)), MASKED).astype(np.float32).reshape(P, T)


def attention_phase(nc, n_T, w_in, bias, ident, o_T):
    PAIRS = ATT_H // 2
    NSTEP = 2 * NT
    NEED = [n % NT + 1 for n in range(NSTEP)]
    with Store(nc, "att") as m:
        w = {n: m.sb("w" + n, [P, ND, P]) for n in "qkv"}
        proj = {n: m.sb(n + "T", [P, T]) for n in "qkv"}
        v = m.sb("v", [P, NT, P])
        bias_sb = m.sb("bias", [P, T])
        logit = [m.sb(f"logit{b}", [P, T]) for b in range(2)]
        prob = [m.sb(f"prob{b}", [P, T]) for b in range(2)]
        prob_T = [m.sb(f"probT{b}", [P, NT, P]) for b in range(2)]
        top = m.sb("top", [P, NSTEP])
        neg_top = m.sb("neg_top", [P, NSTEP])
        den = m.sb("den", [P, NSTEP])
        rden = m.sb("rden", [P, NSTEP])
        o_rows = m.sb("o_rows", [P, NT, P])
        score = [m.ps(f"score{b}", [P, 2, BANK]) for b in range(2)]
        turned = m.ps("turned", [P, 2, BANK])
        o_ps = [m.ps(f"o{b}", [P, BANK]) for b in range(2)]
        w_loaded = m.sem("w_loaded")
        bias_loaded = m.sem("bias_loaded")
        proj_ready = m.sem("proj_ready")
        proj_read = m.sem("proj_read")
        v_turned = m.sem("v_turned")
        v_ready = m.sem("v_ready")
        score_ready = m.sem("score_ready")
        top_found = m.sem("top_found")
        top_ready = m.sem("top_ready")
        prob_ready = m.sem("prob_ready")
        prob_turned = m.sem("prob_turned")
        probT_ready = m.sem("probT_ready")
        o_ready = m.sem("o_ready")
        rden_ready = m.sem("rden_ready")
        o_normed = m.sem("o_normed")
        o_turned = m.sem("o_turned")
        o_stored = m.sem("o_stored")
        w_k = w_in.rearrange("(k p) n -> p k n", p=P)
        PROJ = [(n, h) for n in "qkv" for h in range(2)]
        proj_bank = [score[g // 2 % 2][:, g % 2, :] for g in range(len(PROJ))]
        NP = len(PROJ)
        with nc.Block() as block:
            @block.sync
            def _(sp):
                sp.dma_start(bias_sb[:, :], bias).then_inc(bias_loaded, 16)

                def load(i):
                    if not first(i):
                        sp.wait_ge(proj_ready, NP * i)
                    for n, col in (("q", COL_AQ), ("k", COL_AK), ("v", COL_AV)):
                        sp.dma_start(w[n][:, :, :], w_k[:, :, bass.ds(i * P + col, P)]).then_inc(w_loaded, 16)
                repeat(sp, PAIRS, load)

            @block.tensor
            def _(pe):
                def pair(i):
                    base = NSTEP * i
                    pe.wait_ge(w_loaded, 48 * (i + 1))
                    if not first(i):
                        pe.wait_ge(top_found, base)
                    for g, (n, h) in enumerate(PROJ):
                        if g >= 4:
                            pe.wait_ge(proj_read, NP * i + g - 3)
                        for k in range(ND):
                            last = nc.tensor.matmul(proj_bank[g], w[n][:, k, :], n_T[:, k, bass.ts(h, BANK)], start=(k == 0), stop=(k == ND - 1))
                        last.then_inc(proj_ready, 1)
                    pe.wait_ge(proj_read, NP * (i + 1))
                    if not first(i):
                        pe.wait_ge(o_stored, 2 * i)
                    for c in range(2):
                        for j in range(4):
                            last = nc.tensor.transpose(turned[:, c, bass.ts(j, P)], proj["v"][:, bass.ts(4 * c + j, P)], ident[:, :])
                        last.then_inc(v_turned, 1)

                    def scores(n):
                        hd, t = n // NT, n % NT
                        part = slice(hd * ATT_D, (hd + 1) * ATT_D)
                        if n >= 2:
                            pe.wait_ge(top_found, base + n - 1)
                        for c in range(2):
                            width = min(max(NEED[n] * P - c * BANK, 0), BANK)
                            if width:
                                last = nc.tensor.matmul(score[n % 2][:, c, 0:width], proj["q"][part, bass.ts(t, P)],
                                                        proj["k"][part, c * BANK:c * BANK + width], start=True, stop=True)
                        last.then_inc(score_ready, 1)

                    def turn(n):
                        pe.wait_ge(prob_ready, base + n + 1)
                        if n == 0:
                            pe.wait_ge(v_ready, 2 * (i + 1))
                        else:
                            pe.wait_ge(probT_ready, base + n)
                        for j in range(NEED[n]):
                            last = nc.tensor.transpose(turned[:, j // 4, bass.ts(j % 4, P)], prob[n % 2][:, bass.ts(j, P)], ident[:, :])
                        last.then_inc(prob_turned, 1)

                    def weigh(n):
                        hd = n // NT
                        pe.wait_ge(probT_ready, base + n + 1)
                        if not (first(i) and n < 2):
                            pe.wait_ge(o_normed, base + n - 1)
                        for j in range(NEED[n]):
                            last = nc.tensor.matmul(o_ps[n % 2][:, 0:ATT_D], prob_T[n % 2][:, j, :], v[:, j, bass.ts(hd, ATT_D)],
                                                    start=(j == 0), stop=(j == NEED[n] - 1))
                        last.then_inc(o_ready, 1)

                    for n in range(NSTEP + 2):
                        if n < NSTEP:
                            scores(n)
                        if 1 <= n <= NSTEP:
                            turn(n - 1)
                        if n >= 2:
                            weigh(n - 2)
                    pe.wait_ge(o_normed, base + NSTEP)
                    for c in range(2):
                        for j in range(4):
                            last = nc.tensor.transpose(turned[:, c, bass.ts(j, P)], o_rows[:, 4 * c + j, :], ident[:, :])
                        last.then_inc(o_turned, 1)
                repeat(pe, PAIRS, pair)

            @block.scalar
            def _(act):
                def pair(i):
                    base = NSTEP * i
                    for g, (n, h) in enumerate(PROJ):
                        act.wait_ge(proj_ready, NP * i + g + 1)
                        act.activation(proj[n][:, bass.ts(h, BANK)], proj_bank[g], ACT.Copy,
                                       scale=ATT_D ** -0.5 if n == "q" else 1.0).then_inc(proj_read, 1)
                    for c in range(2):
                        act.wait_ge(v_turned, 2 * i + c + 1)
                        act.activation(v[:, bass.ts(c, 4), :], turned[:, c, :].rearrange("p (j d) -> p j d", d=P), ACT.Copy).then_inc(v_ready, 1)

                    def copy_probs(n):
                        act.wait_ge(prob_turned, base + n + 1)
                        if not (first(i) and n < 2):
                            act.wait_ge(o_ready, base + n - 1)
                        act.activation(prob_T[n % 2][:, 0:NEED[n], :], turned[:, :, :].rearrange("p c (j q) -> p (c j) q", q=P)[:, 0:NEED[n], :],
                                       ACT.Copy).then_inc(probT_ready, 1)

                    for n in range(NSTEP):
                        act.wait_ge(top_ready, base + n + 1)
                        if not (first(i) and n < 2):
                            act.wait_ge(prob_turned, base + n - 1)
                        act.activation(prob[n % 2][:, 0:NEED[n] * P], logit[n % 2][:, 0:NEED[n] * P], ACT.Exp, bias=neg_top[:, n:n + 1],
                                       accum_out=den[:, n:n + 1]).then_inc(prob_ready, 1)
                        if n >= 1:
                            copy_probs(n - 1)
                    copy_probs(NSTEP - 1)
                    for c in range(2):
                        act.wait_ge(o_turned, 2 * i + c + 1)
                        act.activation(o_T[:, tile(i + GLA_VW // P), bass.ts(c, BANK)], turned[:, c, :], ACT.Copy).then_inc(o_stored, 1)
                repeat(act, PAIRS, pair)

            @block.vector
            def _(dve):
                dve.wait_ge(bias_loaded, 16)

                def pair(i):
                    base = NSTEP * i

                    def normed(n):
                        hd, t = n // NT, n % NT
                        dve.wait_ge(prob_ready, base + n + 1)
                        dve.reciprocal(rden[:, n:n + 1], den[:, n:n + 1]).then_inc(rden_ready, 1)
                        dve.wait_ge(rden_ready, base + n + 1)
                        dve.wait_ge(o_ready, base + n + 1)
                        if n == 0 and not first(i):
                            dve.wait_ge(o_turned, 2 * i)
                        dve.tensor_scalar(o_rows[:, t, bass.ts(hd, ATT_D)], o_ps[n % 2][:, 0:ATT_D], rden[:, n:n + 1], None, ALU.mult).then_inc(o_normed, 1)

                    for n in range(NSTEP):
                        cols = NEED[n] * P
                        dve.wait_ge(score_ready, base + n + 1)
                        if not (first(i) and n < 2):
                            dve.wait_ge(prob_ready, base + n - 1)
                        dve.memset(neg_top[:, n:n + 1], 0.0)
                        dve.tensor_tensor_reduce(out=logit[n % 2][:, 0:cols], in0=score[n % 2][:, :, :].rearrange("p c k -> p (c k)")[:, 0:cols],
                                                 in1=bias_sb[:, T - cols:T], scale=1.0, scalar=MASKED, op0=ALU.add, op1=ALU.max,
                                                 accum_out=top[:, n:n + 1]).then_inc(top_found, 1)
                        dve.wait_ge(top_found, base + n + 1)
                        dve.tensor_scalar(neg_top[:, n:n + 1], top[:, n:n + 1], -1.0, None, ALU.mult).then_inc(top_ready, 1)
                        if n >= 2:
                            normed(n - 2)
                    normed(NSTEP - 2)
                    normed(NSTEP - 1)
                repeat(dve, PAIRS, pair)


N_EXP, N_GRP, F_EXP = 32, 4, 512
PER_GRP = N_EXP // N_GRP
SLOTS = P
N_OVER = 2 * T // SLOTS - 1
N_BLK = N_EXP + N_OVER
BIG = 1e30


class Chain:

    def __init__(self, engine, sem):
        self.engine, self.sem, self.n = engine, sem, 0

    def then(self, instruction):
        instruction.then_inc(self.sem, 1)
        self.n += 1
        self.engine.wait_ge(self.sem, self.n)


def router_phase(nc, h_T, w_grp, b_grp, w_exp, b_exp, tables, row_tok, y_rows, next_weights):
    gates, dest, idx_all, over_exp, n_over = (tables[n] for n in ("gates", "dest", "idx_all", "over_exp", "n_over"))
    NG4, NE = N_GRP, N_EXP
    with Store(nc, "router") as m:
        w = m.sb("w", [P, ND, NG4 + NE])
        bias = m.sb("bias", [P, NG4 + NE])
        g = m.sb("g", [P, NT, NG4])
        e = m.sb("e", [P, NT, NE])
        g_hot = m.sb("g_hot", [P, NT, NG4])
        gt = m.sb("gt", [P, NT, NG4])
        best = m.sb("best", [P, NT])
        where = m.sb("where", [P, NT])
        g_sum = m.sb("g_sum", [P, NT])
        hot = [m.sb(f"hot{j}", [P, NT, NE]) for j in range(2)]
        value = [m.sb(f"value{j}", [P, NT]) for j in range(2)]
        te = m.sb("te", [P, NT, NE])
        ratio = m.sb("ratio", [P, NT])
        both = m.sb("both", [P, NT, NE])
        pos = m.sb("pos", [P, NT, NE])
        total = m.sb("total", [P, NE])
        over = m.sb("over", [P, NE])
        over_end = m.sb("over_end", [P, NE])
        jump = m.sb("jump", [P, NE])
        ones_e = m.sb("ones_e", [P, NE])
        ones_sq = m.sb("ones_sq", [P, P])
        before = m.sb("before", [P, P])
        down4 = m.sb("down4", [P, NG4])
        down32 = m.sb("down32", [P, NE])
        first_row = m.sb("first_row", [P, NE])
        blk = m.sb("blk", [1, N_OVER])
        cmp = m.sb("cmp", [1, N_OVER, NE])
        cnt = m.sb("cnt", [1, N_OVER])
        dest_f = m.sb("dest_f", [P, NT, 2])
        tok = m.sb("tok", [P, NT], I32)
        zero = m.sb("zero", [P, N_BLK], I32)
        zero_rows = m.sb("zero_rows", [P, D])
        rows_cleared = m.sem("rows_cleared")
        y_cleared = m.sem("y_cleared")
        logit_ps = m.ps("logit", [P, BANK])
        pos_ps = m.ps("pos_ps", [P, BANK])
        tot_ps = m.ps("tot_ps", [P, BANK])
        loaded = m.sem("loaded")
        made = m.sem("made")
        zeroed = m.sem("zeroed")
        logits_ready = m.sem("logits_ready")
        diff_ready = m.sem("diff_ready")
        exp_ready = m.sem("exp_ready")
        both_ready = m.sem("both_ready")
        pos_ready = m.sem("pos_ready")
        step = m.sem("step")
        dest_ready = m.sem("dest_ready")
        listed = m.sem("listed")
        idx_loaded = m.sem("idx_loaded")

        def over_e(x):
            return x.unsqueeze(2).to_broadcast([P, NT, NE])

        def over_t(x, n):
            return x.unsqueeze(1).to_broadcast([P, NT, n])

        with nc.Block() as block:
            @block.sync
            def _(sp):
                for cols, src in ((slice(0, NG4), w_grp), (slice(NG4, NG4 + NE), w_exp)):
                    sp.dma_start(w[:, :, cols], src.rearrange("(k p) n -> p k n", p=P)).then_inc(loaded, 16)
                for cols, src in ((slice(0, NG4), b_grp), (slice(NG4, NG4 + NE), b_exp)):
                    sp.dma_start(bias[:, cols], row(src).partition_broadcast(P)).then_inc(loaded, 16)
                next_weights.load_first(sp)
                sp.wait_ge(rows_cleared, 1)
                sp.dma_start(y_rows[N_EXP * SLOTS:, :].rearrange("(b p) d -> p b d", p=P),
                             zero_rows[:, :].unsqueeze(1).to_broadcast([P, N_OVER, D])).then_inc(y_cleared, 16)
                sp.wait_ge(y_cleared, 16)

            @block.gpsimd
            def _(pool):
                pool.memset(zero_rows[:, :], 0.0).then_inc(rows_cleared, 1)
                pool.iota(down4[:, :], pattern=[[-1, NG4]], base=NG4, channel_multiplier=0, allow_small_or_imprecise_dtypes=True).then_inc(made, 1)
                pool.iota(down32[:, :], pattern=[[-1, NE]], base=NE, channel_multiplier=0, allow_small_or_imprecise_dtypes=True).then_inc(made, 1)
                pool.iota(first_row[:, :], pattern=[[SLOTS, NE]], base=0, channel_multiplier=0, allow_small_or_imprecise_dtypes=True).then_inc(made, 1)
                pool.iota(blk[:, :], pattern=[[1, N_OVER]], base=0, channel_multiplier=0, allow_small_or_imprecise_dtypes=True).then_inc(made, 1)
                pool.iota(tok[:, :], pattern=[[P, NT]], base=0, channel_multiplier=1).then_inc(made, 1)
                pool.memset(ones_e[:, :], 1.0).then_inc(made, 1)
                pool.memset(ones_sq[:, :], 1.0).then_inc(made, 1)
                pool.memset(zero[:, :], 0).then_inc(made, 1)
                pool.wait_ge(made, 8)
                pool.affine_select(out=before[:, :], in_=ones_sq[:, :], compare_op=ALU.is_gt, fill=0.0, base=0, pattern=[[1, P]],
                                   channel_multiplier=-1).then_inc(made, 1)
                pool.dma_start(row_tok.rearrange("(p b) o -> p (b o)", p=P), zero[:, :]).then_inc(zeroed, 16)
                pool.wait_ge(zeroed, 16)
                pool.wait_ge(dest_ready, 1)
                for t in range(NT):
                    for j in range(2):
                        pool.indirect_dma_start(out=row_tok, out_offset=bass.IndirectOffsetOnAxis(ap=dest[:, 2 * t + j:2 * t + j + 1], axis=0),
                                                in_=tok[:, t:t + 1], in_offset=None).then_inc(listed, 16)
                pool.wait_ge(listed, 16 * 2 * NT)
                with nc.allow_non_contiguous_dma(reason="a row number per partition"):
                    pool.dma_start(idx_all[:, :], row_tok.rearrange("(b p) o -> p (b o)", p=P)).then_inc(idx_loaded, 16)
                pool.wait_ge(idx_loaded, 16)

            @block.tensor
            def _(pe):
                pe.wait_ge(loaded, 64)
                for t in range(NT):
                    for k in range(ND):
                        last = nc.tensor.matmul(logit_ps[:, bass.ts(t, NG4 + NE)], h_T[:, k, bass.ts(t, P)], w[:, k, :], start=(k == 0), stop=(k == ND - 1))
                last.then_inc(logits_ready, 1)
                pe.wait_ge(both_ready, 1)
                pe.wait_ge(made, 9)
                for t in range(NT):
                    for u in range(t):
                        nc.tensor.matmul(pos_ps[:, bass.ts(t, NE)], ones_sq[:, :], both[:, u, :], start=(u == 0), stop=False)
                    nc.tensor.matmul(pos_ps[:, bass.ts(t, NE)], before[:, :], both[:, t, :], start=(t == 0), stop=True)
                for u in range(NT):
                    last = nc.tensor.matmul(tot_ps[:, 0:NE], ones_sq[:, :], both[:, u, :], start=(u == 0), stop=(u == NT - 1))
                last.then_inc(pos_ready, 1)

            @block.scalar
            def _(act):
                act.wait_ge(diff_ready, 1)
                act.activation(gt[:, :, :], gt[:, :, :], ACT.Exp).then_inc(exp_ready, 1)
                act.wait_ge(diff_ready, 2)
                act.activation(ratio[:, :], ratio[:, :], ACT.Exp).then_inc(exp_ready, 1)

            @block.vector
            def _(dve):
                c = Chain(dve, step)
                dve.wait_ge(loaded, 64)
                dve.wait_ge(made, 9)
                dve.wait_ge(logits_ready, 1)
                logits = logit_ps[:, 0:NT * (NG4 + NE)].rearrange("p (t n) -> p t n", n=NG4 + NE)
                c.then(dve.tensor_tensor(g[:, :, :], logits[:, :, 0:NG4], over_t(bias[:, 0:NG4], NG4), ALU.add))
                c.then(dve.tensor_tensor(e[:, :, :], logits[:, :, NG4:], over_t(bias[:, NG4:], NE), ALU.add))
                c.then(dve.reduce_max(best[:, :], g[:, :, :], axis=AXX))
                b4 = best[:, :].unsqueeze(2).to_broadcast([P, NT, NG4])
                dve.tensor_tensor(gt[:, :, :], g[:, :, :], b4, ALU.subtract).then_inc(diff_ready, 1)
                c.then(dve.tensor_tensor(g_hot[:, :, :], g[:, :, :], b4, ALU.is_ge))
                c.then(dve.tensor_tensor(g_hot[:, :, :], g_hot[:, :, :], over_t(down4[:, :], NG4), ALU.mult))
                c.then(dve.reduce_max(where[:, :], g_hot[:, :, :], axis=AXX))
                c.then(dve.tensor_tensor(g_hot[:, :, :], over_t(down4[:, :], NG4), where[:, :].unsqueeze(2).to_broadcast([P, NT, NG4]), ALU.is_equal))
                dve.wait_ge(exp_ready, 1)
                c.then(dve.reduce_sum(g_sum[:, :], gt[:, :, :], axis=AXX))
                hot8 = g_hot[:, :, :].rearrange("p t g -> p (t g)").unsqueeze(2).to_broadcast([P, NT * NG4, PER_GRP])
                e8 = e[:, :, :].rearrange("p t (g n) -> p (t g) n", n=PER_GRP)
                c.then(dve.tensor_tensor(e8, e8, hot8, ALU.mult))
                c.then(dve.tensor_scalar(g_hot[:, :, :], g_hot[:, :, :], 1.0, BIG, ALU.subtract, ALU.mult))
                c.then(dve.tensor_tensor(e8, e8, hot8, ALU.add))
                for j in range(2):
                    c.then(dve.reduce_max(value[j][:, :], e[:, :, :], axis=AXX))
                    c.then(dve.tensor_tensor(te[:, :, :], e[:, :, :], over_e(value[j][:, :]), ALU.is_ge))
                    c.then(dve.tensor_tensor(te[:, :, :], te[:, :, :], over_t(down32[:, :], NE), ALU.mult))
                    c.then(dve.reduce_max(where[:, :], te[:, :, :], axis=AXX))
                    c.then(dve.tensor_tensor(hot[j][:, :, :], over_t(down32[:, :], NE), over_e(where[:, :]), ALU.is_equal))
                    if j == 0:
                        c.then(dve.scalar_tensor_tensor(e[:, :, :], hot[0][:, :, :], -BIG, e[:, :, :], ALU.mult, ALU.add))
                dve.tensor_tensor(both[:, :, :], hot[0][:, :, :], hot[1][:, :, :], ALU.add).then_inc(both_ready, 1)
                dve.tensor_tensor(ratio[:, :], value[1][:, :], value[0][:, :], ALU.subtract).then_inc(diff_ready, 1)
                dve.wait_ge(exp_ready, 2)
                c.then(dve.tensor_scalar(best[:, :], ratio[:, :], 1.0, None, ALU.add))
                c.then(dve.tensor_tensor(best[:, :], best[:, :], g_sum[:, :], ALU.mult))
                c.then(dve.reciprocal(gates[:, 0, :], best[:, :]))
                c.then(dve.tensor_tensor(gates[:, 1, :], gates[:, 0, :], ratio[:, :], ALU.mult))
                dve.wait_ge(pos_ready, 1)
                c.then(dve.tensor_copy(pos[:, :, :], pos_ps[:, 0:NT * NE].rearrange("p (t n) -> p t n", n=NE)))
                c.then(dve.tensor_copy(total[:, :], tot_ps[:, 0:NE]))
                c.then(dve.tensor_scalar(over[:, :], total[:, :], float(SLOTS), None, ALU.is_gt))
                for n in range(2, T // SLOTS):
                    c.then(dve.scalar_tensor_tensor(over[:, :], total[:, :], float(n * SLOTS), over[:, :], ALU.is_gt, ALU.add))
                c.then(dve.tensor_tensor_scan(over_end[:, :], ones_e[:, :], over[:, :], 0.0, ALU.mult, ALU.add))
                c.then(dve.tensor_tensor(jump[:, :], over_end[:, :], over[:, :], ALU.subtract))
                c.then(dve.tensor_scalar(jump[:, :], jump[:, :], float(SLOTS), float((N_EXP - 1) * SLOTS), ALU.mult, ALU.add))
                c.then(dve.tensor_tensor(jump[:, :], jump[:, :], first_row[:, :], ALU.subtract))
                c.then(dve.tensor_scalar(te[:, :, :], pos[:, :, :], float(SLOTS), None, ALU.is_ge))
                c.then(dve.tensor_tensor(te[:, :, :], te[:, :, :], over_t(jump[:, :], NE), ALU.mult))
                c.then(dve.tensor_tensor(te[:, :, :], te[:, :, :], pos[:, :, :], ALU.add))
                c.then(dve.tensor_tensor(te[:, :, :], te[:, :, :], over_t(first_row[:, :], NE), ALU.add))
                for j in range(2):
                    c.then(dve.tensor_tensor(hot[j][:, :, :], hot[j][:, :, :], te[:, :, :], ALU.mult))
                    c.then(dve.reduce_sum(dest_f[:, :, j], hot[j][:, :, :], axis=AXX))
                dve.tensor_copy(dest[:, :], dest_f[:, :, :].rearrange("p t j -> p (t j)")).then_inc(dest_ready, 1)
                c.then(dve.tensor_tensor(cmp[:, :, :], over_end[0:1, :].unsqueeze(1).to_broadcast([1, N_OVER, NE]),
                                         blk[:, :].unsqueeze(2).to_broadcast([1, N_OVER, NE]), ALU.is_le))
                c.then(dve.reduce_sum(cnt[:, :], cmp[:, :, :], axis=AXX))
                c.then(dve.tensor_scalar(over_exp[:, :], cnt[:, :], float(N_EXP - 1), None, ALU.min))
                c.then(dve.tensor_copy(n_over[:, :], over_end[0:1, NE - 1:NE]))


CHUNK = F_EXP
PER_STEP = 4


class ExpertWeights(Store):

    def __init__(self, nc, name, n_buffers, w1_of, w3_of, w2_of):
        super().__init__(nc, name, side="right")
        self.n_buffers, self.w1_of, self.w3_of, self.w2_of = n_buffers, w1_of, w3_of, w2_of

    def __enter__(m):
        super().__enter__()
        m.w1 = [m.sb(f"w1_{b}", [P, ND, CHUNK]) for b in range(m.n_buffers)]
        m.w3 = [m.sb(f"w3_{b}", [P, ND, CHUNK]) for b in range(m.n_buffers)]
        m.w2 = [m.sb(f"w2_{b}", [P, CHUNK // P, D]) for b in range(m.n_buffers)]
        m.w1_loaded = [m.sem(f"w1_loaded{b}") for b in range(m.n_buffers)]
        m.w3_loaded = [m.sem(f"w3_loaded{b}") for b in range(m.n_buffers)]
        m.w2_loaded = [m.sem(f"w2_loaded{b}") for b in range(m.n_buffers)]
        return m

    def load_first(m, sp):
        for b in range(m.n_buffers):
            sp.dma_start(m.w1[b][:, :, :], m.w1_of(0, b)).then_inc(m.w1_loaded[b], 16)
            sp.dma_start(m.w3[b][:, :, :], m.w3_of(0, b)).then_inc(m.w3_loaded[b], 16)
            sp.dma_start(m.w2[b][:, :, :], m.w2_of(0, b)).then_inc(m.w2_loaded[b], 16)


class ExpertStore(Store):

    def __init__(self, nc, name, n_x, weights=None):
        super().__init__(nc, name)
        self.n_x, self.weights = n_x, weights

    def __enter__(m):
        super().__enter__()
        m.idx = m.sb("idx", [P, 1], I32)
        m.rows = [m.sb(f"rows{b}", [P, D]) for b in range(m.n_x)]
        m.x_T = [m.sb(f"xT{b}", [P, ND, SLOTS]) for b in range(m.n_x)]
        if m.weights:
            m.w1 = [Parts(m, f"w1_{b}", m.weights.w1[b]) for b in range(2)]
            m.w3 = [Parts(m, f"w3_{b}", m.weights.w3[b]) for b in range(2)]
            m.x = [Parts(m, f"x{b}", m.x_T[b]) for b in range(m.n_x)]
            m.w_rounded = m.sem("w_rounded")
            m.w_split = m.sem("w_split")
            m.x_rounded = m.sem("x_rounded")
            m.x_split = m.sem("x_split")
        m.silu = m.sb("silu", [P, CHUNK])
        m.hid = m.sb("hid", [P, CHUNK])
        m.hid_T = m.sb("hidT", [P, CHUNK // P, SLOTS])
        m.y = [m.sb(f"y{b}", [P, D]) for b in range(2)]
        m.gate_ps = m.ps("gate_ps", [P, CHUNK])
        m.up_ps = m.ps("up_ps", [P, CHUNK])
        m.hT_ps = m.ps("hT_ps", [P, BANK])
        m.xT_ps = m.ps("xT_ps", [P, 2, BANK])
        m.y_ps = m.ps("y_ps", [P, 2, BANK])
        m.idx_ready = m.sem("idx_ready")
        m.lists_taken = m.sem("lists_taken")
        m.x_turned = m.sem("x_turned")
        m.xT_ready = m.sem("xT_ready")
        m.gate_ready = m.sem("gate_ready")
        m.up_ready = m.sem("up_ready")
        m.silu_ready = m.sem("silu_ready")
        m.hid_ready = m.sem("hid_ready")
        m.hid_turned = m.sem("hid_turned")
        m.hidT_ready = m.sem("hidT_ready")
        m.y_ready = m.sem("y_ready")
        m.y_read = m.sem("y_read")
        m.rows_loaded = [m.sem(f"rows_loaded{b}") for b in range(m.n_x)]
        m.y_stored = [m.sem(f"y_stored{b}") for b in range(2)]
        return m


def up_product(nc, passes, out):
    for k in range(ND):
        for n, (x_T, w) in enumerate(passes):
            last = nc.tensor.matmul(out[:, :], x_T[:, k, :], w[:, k, :], start=(k == 0 and n == 0), stop=(k == ND - 1 and n == len(passes) - 1))
    return last


def turn_rows(nc, rows, out, ident):
    for k in range(ND):
        last = nc.tensor.transpose(out[:, k // 4, bass.ts(k % 4, P)], rows[:, bass.ts(k, P)], ident[:, :])
    return last


def turn_hidden(nc, m, ident):
    for k in range(CHUNK // P):
        last = nc.tensor.transpose(m.hT_ps[:, bass.ts(k, P)], m.hid[:, bass.ts(k, P)], ident[:, :])
    return last


def down_product(nc, w2, m, start, stop):
    for h in range(2):
        for k in range(CHUNK // P):
            last = nc.tensor.matmul(m.y_ps[:, h, :], m.hid_T[:, k, :], w2[:, k, bass.ts(h, BANK)],
                                    start=(start and k == 0), stop=(stop and k == CHUNK // P - 1))
    return last


def expert_phase(nc, name, n_steps, weights, idx_all, src, ident, shared_x, y_rows=None, scale=None, add_to=None):
    n_chunks = n_steps * PER_STEP
    n_groups = n_steps if shared_x else n_chunks
    with ExpertStore(nc, name, 1 if shared_x else 2, weights) as m:
        nx = m.n_x

        def group(i, c):
            return i if shared_x else PER_STEP * i + c

        with nc.Block() as block:
            @block.sync
            def _(sp):
                def load_w2(i, c):
                    b = c % 2
                    sp.wait_ge(m.y_ready, PER_STEP * i + c - 1)
                    sp.dma_start(weights.w2[b][:, :, :], weights.w2_of(i, c)).then_inc(weights.w2_loaded[b], 16)

                def step(i):
                    for c in range(PER_STEP):
                        q, b = PER_STEP * i + c, c % 2
                        if not (first(i) and c < 2):
                            sp.wait_ge(m.gate_ready, q - 1)
                            sp.dma_start(weights.w1[b][:, :, :], weights.w1_of(i, c)).then_inc(weights.w1_loaded[b], 16)
                            sp.wait_ge(m.up_ready, q - 1)
                            sp.dma_start(weights.w3[b][:, :, :], weights.w3_of(i, c)).then_inc(weights.w3_loaded[b], 16)
                        if not (first(i) and c < 3):
                            load_w2(*((i, c - 1) if c else (i - 1, PER_STEP - 1)))

                repeat(sp, n_steps, step)
                load_w2(n_steps - 1, PER_STEP - 1)

            @block.gpsimd
            def _(pool):
                def gather(g, b, nth):
                    if not (isinstance(g, int) and g < nx):
                        pool.wait_ge(m.x_turned, g - nx + 1)
                    pool.tensor_copy(m.idx[:, :], idx_all[:, tile(g)]).then_inc(m.idx_ready, 1)
                    pool.wait_ge(m.idx_ready, nth)
                    pool.sem_inc(m.lists_taken, 1)
                    pool.indirect_dma_start(out=m.rows[b][:, :], out_offset=None, in_=src,
                                            in_offset=bass.IndirectOffsetOnAxis(ap=m.idx[:, 0:1], axis=0)).then_inc(m.rows_loaded[b], 16)

                if not shared_x:
                    def step(i):
                        for c in range(PER_STEP):
                            g = PER_STEP * i + c
                            if not (first(i) and c == 0):
                                pool.wait_ge(m.rows_loaded[(c - 1) % 2], 16 * (2 * i + (c + 1) // 2))
                            gather(g, c % 2, g + 1)
                    repeat(pool, n_steps, step)
                    return

                def scatter(g, b, nth, n_same):
                    pool.wait_ge(m.y_read, g + 1)
                    pool.tensor_copy(m.idx[:, :], idx_all[:, tile(g)]).then_inc(m.idx_ready, 1)
                    pool.wait_ge(m.idx_ready, nth)
                    pool.sem_inc(m.lists_taken, 1)
                    pool.indirect_dma_start(out=add_to, out_offset=bass.IndirectOffsetOnAxis(ap=m.idx[:, 0:1], axis=0),
                                            in_=m.y[b][:, :], in_offset=None, compute_op=ALU.add).then_inc(m.y_stored[b], 16)
                    pool.wait_ge(m.y_stored[b], 16 * n_same)

                gather(0, 0, 1)
                pool.wait_ge(m.rows_loaded[0], 16)
                gather(1, 0, 2)
                pool.wait_ge(m.rows_loaded[0], 32)

                with pool.Fori(0, n_steps // 2 - 1) as i:
                    for b in range(2):
                        scatter(2 * i + b, b, 4 * i + 2 * b + 3, i + 1)
                        gather(2 * i + b + 2, 0, 4 * i + 2 * b + 4)
                        pool.wait_ge(m.rows_loaded[0], 16 * (2 * i + b + 3))
                for b in range(2):
                    scatter(n_steps - 2 + b, b, 2 * n_steps - 1 + b, n_steps // 2)

            @block.tensor
            def _(pe):
                def turn_x(g, b, nth):
                    pe.wait_ge(m.rows_loaded[b], 16 * nth)
                    if not (isinstance(g, int) and g == 0):
                        pe.wait_ge(m.xT_ready, g)
                    turn_rows(nc, m.rows[b], m.xT_ps, ident).then_inc(m.x_turned, 1)

                def turn_hid(q):
                    pe.wait_ge(m.hid_ready, q + 1)
                    turn_hidden(nc, m, ident).then_inc(m.hid_turned, 1)

                def down(q, i, c):
                    pe.wait_ge(weights.w2_loaded[c % 2], 16 * (2 * i + c // 2 + 1))
                    pe.wait_ge(m.hidT_ready, q + 1)
                    start, stop = not shared_x or c == 0, not shared_x or c == PER_STEP - 1
                    if start:
                        g = i if shared_x else q
                        if not (isinstance(g, int) and g == 0):
                            pe.wait_ge(m.y_read, g)
                    down_product(nc, weights.w2[c % 2], m, start, stop).then_inc(m.y_ready, 1)

                def step(i):
                    for c in range(PER_STEP):
                        q, b = PER_STEP * i + c, c % 2
                        x = m.x[b % nx]
                        before = None if first(i) and c == 0 else (q - 1, i if c else i - 1, (c - 1) % PER_STEP)
                        pe.wait_ge(m.x_split, group(i, c) + 1)
                        pe.wait_ge(m.w_split, 2 * q + 1)
                        if before:
                            pe.wait_ge(m.silu_ready, q)
                        up_product(nc, three_passes(x, m.w1[b]), m.gate_ps).then_inc(m.gate_ready, 1)
                        if before:
                            turn_hid(before[0])
                        pe.wait_ge(m.w_split, 2 * q + 2)
                        up_product(nc, three_passes(x, m.w3[b]), m.up_ps).then_inc(m.up_ready, 1)
                        if not shared_x:
                            if c < PER_STEP - 1 or not (isinstance(i, int) and i == n_steps - 1):
                                turn_x(q + 1, (c + 1) % 2, 2 * i + (c + 1) // 2 + 1)
                        elif c == PER_STEP - 1 and not (isinstance(i, int) and i == n_steps - 1):
                            turn_x(i + 1, 0, i + 2)
                        if before:
                            down(*before)

                turn_x(0, 0, 1)
                step(0)
                with pe.Fori(1, n_steps - 1) as i:
                    step(i)
                step(n_steps - 1)
                turn_hid(n_chunks - 1)
                down(n_chunks - 1, n_steps - 1, PER_STEP - 1)

            @block.scalar
            def _(act):
                def copy_x(g, b):
                    act.wait_ge(m.x_turned, g + 1)
                    act.activation(m.x_T[b][:, :, :], m.xT_ps[:, :, :].rearrange("p a (k s) -> p (a k) s", s=SLOTS), ACT.Copy).then_inc(m.xT_ready, 1)

                def store_y(q, b):
                    act.wait_ge(m.y_read, q + 1)
                    act.dma_start(y_rows[bass.ds(q * SLOTS, SLOTS), :], m.y[b][:, :]).then_inc(m.y_stored[b], 16)

                def copy_hid(q):
                    act.wait_ge(m.hid_turned, q + 1)
                    act.activation(m.hid_T[:, :, :], m.hT_ps[:, :].rearrange("p (k s) -> p k s", s=SLOTS), ACT.Copy).then_inc(m.hidT_ready, 1)

                def step(i):
                    for c in range(PER_STEP):
                        q = PER_STEP * i + c
                        last = isinstance(i, int) and i == n_steps - 1
                        act.wait_ge(m.gate_ready, q + 1)
                        if not (first(i) and c == 0):
                            act.wait_ge(m.hid_ready, q)
                        act.activation(m.silu[:, :], m.gate_ps[:, :], ACT.Silu).then_inc(m.silu_ready, 1)
                        if not (first(i) and c == 0):
                            copy_hid(q - 1)
                        if not shared_x and not (last and c == PER_STEP - 1):
                            copy_x(q + 1, (c + 1) % 2)
                        if not shared_x and not (first(i) and c < 2):
                            store_y(q - 2, c % 2)
                        if shared_x and c == PER_STEP - 1 and not last:
                            copy_x(i + 1, 0)

                copy_x(0, 0)
                step(0)
                with act.Fori(1, n_steps - 1) as i:
                    step(i)
                step(n_steps - 1)
                copy_hid(n_chunks - 1)
                if not shared_x:
                    for q in range(n_chunks - 2, n_chunks):
                        store_y(q, q % 2)
                    for b in range(2):
                        act.wait_ge(m.y_stored[b], 16 * n_chunks // 2)

            @block.vector
            def _(dve):
                def split_w(i, c):
                    q, b = PER_STEP * i + c, c % 2
                    for n, (w, loaded, used) in enumerate(((m.w1, weights.w1_loaded, m.gate_ready), (m.w3, weights.w3_loaded, m.up_ready))):
                        dve.wait_ge(loaded[b], 16 * (2 * i + c // 2 + 1))
                        if not (first(i) and c < 2):
                            dve.wait_ge(used, q - 1)
                        split(dve, w[b], WHOLE, m.w_rounded, 2 * q + n + 1, m.w_split)

                def split_x(g, b):
                    dve.wait_ge(m.xT_ready, g + 1)
                    split(dve, m.x[b], WHOLE, m.x_rounded, g + 1, m.x_split)

                def split_next_w(i, c):
                    if c < PER_STEP - 1:
                        split_w(i, c + 1)
                    elif not (isinstance(i, int) and i == n_steps - 1):
                        split_w(i + 1, 0)

                split_w(0, 0)
                split_x(0, 0)

                def hidden(q):
                    dve.wait_ge(m.silu_ready, q + 1)
                    dve.wait_ge(m.up_ready, q + 1)
                    if not (isinstance(q, int) and q == 0):
                        dve.wait_ge(m.hid_turned, q)
                    dve.tensor_tensor(m.hid[:, :], m.up_ps[:, :], m.silu[:, :], ALU.mult).then_inc(m.hid_ready, 1)

                def results(g, q, b, nth):
                    dve.wait_ge(m.y_ready, q + 1)
                    if not (isinstance(nth, int) and nth == 1):
                        dve.wait_ge(m.y_stored[b], 16 * (nth - 1))
                    y = m.y_ps[:, :, :].rearrange("p a n -> p (a n)")
                    if scale is None:
                        dve.tensor_copy(m.y[b][:, :], y).then_inc(m.y_read, 1)
                    else:
                        dve.tensor_scalar(m.y[b][:, :], y, scale[:, tile(g)], None, ALU.mult).then_inc(m.y_read, 1)

                if shared_x:
                    def two_steps(i):
                        for b in range(2):
                            g = 2 * i + b
                            for c in range(PER_STEP):
                                split_next_w(g, c)
                                hidden(PER_STEP * g + c)
                                if c == PER_STEP - 1 and not (isinstance(g, int) and g == n_steps - 1):
                                    split_x(g + 1, 0)
                                if c == 0 and not (first(i) and b == 0):
                                    results(g - 1, PER_STEP * g - 1, 1 - b, i + b)
                    two_steps(0)
                    two_steps(1)
                    with dve.Fori(2, n_steps // 2 - 1) as i:
                        two_steps(i)
                    two_steps(n_steps // 2 - 1)
                    results(n_steps - 1, n_chunks - 1, 1, n_steps // 2)
                else:
                    def step(i):
                        for c in range(PER_STEP):
                            q = PER_STEP * i + c
                            split_next_w(i, c)
                            hidden(q)
                            if not (isinstance(q, int) and q == n_chunks - 1):
                                split_x(q + 1, (c + 1) % 2)
                            if not (first(i) and c == 0):
                                results(q - 1, q - 1, (c - 1) % 2, 2 * i + (c + 1) // 2)
                    step(0)
                    with dve.Fori(1, n_steps - 1) as i:
                        step(i)
                    step(n_steps - 1)
                    results(n_chunks - 1, n_chunks - 1, 1, n_chunks // 2)


def overflow_phase(nc, w1, w3, w2, tables, src, y_rows, ident):
    idx_all, over_exp, n_over = tables["idx_all"], tables["over_exp"], tables["n_over"]
    with ExpertWeights(nc, "over_w", 1, None, None, None) as w, ExpertStore(nc, "over", 1) as m:
        w1_v, w3_v = (x.rearrange("e (k p) f -> e p k f", p=P) for x in (w1, w3))
        w2_v = w2.rearrange("e (k p) d -> e p k d", p=P)

        def where_needed(engine, body, after=None):
            n = engine.value_load(n_over[0:1, 0:1], min_val=0, max_val=N_OVER)
            with engine.If(n > 0):
                repeat(engine, N_OVER, body)
                if after:
                    after()

        with nc.Block() as block:
            @block.sync
            def _(sp):
                def load(j):
                    e = sp.value_load(over_exp[0:1, tile(j)], min_val=0, max_val=N_EXP - 1)
                    if not first(j):
                        sp.wait_ge(m.y_ready, j)
                        sp.wait_ge(w.w1_loaded[0], 16)
                    sp.dma_start(w.w1[0][:, :, :], w1_v[tile(e), :, :, :].rearrange("o p k f -> (o p) k f")).then_inc(w.w1_loaded[0], 16)
                    sp.dma_start(w.w3[0][:, :, :], w3_v[tile(e), :, :, :].rearrange("o p k f -> (o p) k f")).then_inc(w.w3_loaded[0], 16)
                    sp.dma_start(w.w2[0][:, :, :], w2_v[tile(e), :, :, :].rearrange("o p k f -> (o p) k f")).then_inc(w.w2_loaded[0], 16)
                    sp.wait_ge(m.y_read, j + 1)
                    sp.dma_start(y_rows[bass.ds((j + N_EXP) * SLOTS, SLOTS), :], m.y[0][:, :]).then_inc(m.y_stored[0], 16)
                where_needed(sp, load, lambda: sp.wait_ge(m.y_stored[0], 16 * N_OVER))

            @block.gpsimd
            def _(pool):

                def gather(j):
                    if not first(j):
                        pool.wait_ge(m.x_turned, j)
                    pool.tensor_copy(m.idx[:, :], idx_all[:, tile(j + N_EXP)]).then_inc(m.idx_ready, 1)
                    pool.wait_ge(m.idx_ready, j + 1)
                    pool.sem_inc(m.lists_taken, 1)
                    pool.indirect_dma_start(out=m.rows[0][:, :], out_offset=None, in_=src,
                                            in_offset=bass.IndirectOffsetOnAxis(ap=m.idx[:, 0:1], axis=0)).then_inc(m.rows_loaded[0], 16)
                    pool.wait_ge(m.rows_loaded[0], 16 * (j + 1))
                where_needed(pool, gather)

            @block.tensor
            def _(pe):
                def products(j):
                    pe.wait_ge(m.rows_loaded[0], 16 * (j + 1))
                    turn_rows(nc, m.rows[0], m.xT_ps, ident).then_inc(m.x_turned, 1)
                    pe.wait_ge(m.xT_ready, j + 1)
                    pe.wait_ge(w.w1_loaded[0], 16 * (j + 1))
                    up_product(nc, [(m.x_T[0], w.w1[0])], m.gate_ps).then_inc(m.gate_ready, 1)
                    pe.wait_ge(w.w3_loaded[0], 16 * (j + 1))
                    up_product(nc, [(m.x_T[0], w.w3[0])], m.up_ps).then_inc(m.up_ready, 1)
                    pe.wait_ge(m.hid_ready, j + 1)
                    turn_hidden(nc, m, ident).then_inc(m.hid_turned, 1)
                    pe.wait_ge(m.hidT_ready, j + 1)
                    pe.wait_ge(w.w2_loaded[0], 16 * (j + 1))
                    if not first(j):
                        pe.wait_ge(m.y_read, j)
                    down_product(nc, w.w2[0], m, True, True).then_inc(m.y_ready, 1)
                where_needed(pe, products)

            @block.scalar
            def _(act):
                def middle(j):
                    act.wait_ge(m.x_turned, j + 1)
                    act.activation(m.x_T[0][:, :, :], m.xT_ps[:, :, :].rearrange("p a (k s) -> p (a k) s", s=SLOTS), ACT.Copy).then_inc(m.xT_ready, 1)
                    act.wait_ge(m.gate_ready, j + 1)
                    act.activation(m.silu[:, :], m.gate_ps[:, :], ACT.Silu).then_inc(m.silu_ready, 1)
                    act.wait_ge(m.hid_turned, j + 1)
                    act.activation(m.hid_T[:, :, :], m.hT_ps[:, :].rearrange("p (k s) -> p k s", s=SLOTS), ACT.Copy).then_inc(m.hidT_ready, 1)
                where_needed(act, middle)

            @block.vector
            def _(dve):
                def products(j):
                    dve.wait_ge(m.silu_ready, j + 1)
                    dve.wait_ge(m.up_ready, j + 1)
                    dve.tensor_tensor(m.hid[:, :], m.up_ps[:, :], m.silu[:, :], ALU.mult).then_inc(m.hid_ready, 1)
                    dve.wait_ge(m.y_ready, j + 1)
                    if not first(j):
                        dve.wait_ge(m.y_stored[0], 16 * j)
                    dve.tensor_copy(m.y[0][:, :], m.y_ps[:, :, :].rearrange("p a n -> p (a n)")).then_inc(m.y_read, 1)
                where_needed(dve, products)


def combine_phase(nc, x1, y_rows, tables, gain1, gain2, ident, x2, h_T):
    gates, dest = tables["gates"], tables["dest"]
    with Store(nc, "combine") as m:
        x = [m.sb(f"x{b}", [P, D]) for b in range(2)]
        y = [[m.sb(f"y{j}_{b}", [P, D]) for b in range(2)] for j in range(2)]
        n1 = [m.sb(f"n1_{b}", [P, D]) for b in range(2)]
        n2 = [m.sb(f"n2_{b}", [P, D]) for b in range(2)]
        sq = m.sb("sq", [P, D])
        g = [m.sb(f"g{j}", [P, D]) for j in range(2)]
        ssum = m.sb("ssum", [P, 2 * NT])
        rms = m.sb("rms", [P, 2 * NT])
        rstd = m.sb("rstd", [P, 2 * NT])
        eps = m.sb("eps", [P, 1])
        turned = [m.ps(f"turned{b}", [P, 2, BANK]) for b in range(2)]
        g_loaded = m.sem("g_loaded")
        x_loaded = [m.sem(f"x_loaded{b}") for b in range(2)]
        y_loaded = [m.sem(f"y_loaded{b}") for b in range(2)]
        step = m.sem("step")
        sum_ready = m.sem("sum_ready")
        rms_ready = m.sem("rms_ready")
        n1_ready = m.sem("n1_ready")
        n2_ready = m.sem("n2_ready")
        n2_turned = m.sem("n2_turned")
        copied = m.sem("copied")
        rounded = m.sem("rounded")
        h_split = m.sem("h_split")
        stored = [m.sem(f"stored{b}") for b in range(2)]
        with nc.Block() as block:
            @block.sync
            def _(sp):
                for j, gain in enumerate((gain1, gain2)):
                    sp.dma_start(g[j][:, :], row(gain).partition_broadcast(P)).then_inc(g_loaded, 16)
                for t in range(NT):
                    b = t % 2
                    if t >= 2:
                        sp.wait_ge(n1_ready, t - 1)
                    sp.dma_start(x[b][:, :], x1[bass.ts(t, P), :]).then_inc(x_loaded[b], 16)

            @block.gpsimd
            def _(pool):
                for t in range(NT):
                    b = t % 2
                    if t >= 2:
                        pool.wait_ge(n1_ready, t - 1)
                    for j in range(2):
                        pool.indirect_dma_start(out=y[j][b][:, :], out_offset=None, in_=y_rows,
                                                in_offset=bass.IndirectOffsetOnAxis(ap=dest[:, 2 * t + j:2 * t + j + 1], axis=0)).then_inc(y_loaded[b], 16)

            @block.vector
            def _(dve):
                c = Chain(dve, step)
                c.then(dve.memset(eps[:, :], EPS))
                dve.wait_ge(g_loaded, 32)

                def norm(src, j, t, out, ready):
                    n = 2 * t + j
                    dve.tensor_tensor_reduce(out=sq[:, :], in0=src[:, :], in1=src[:, :], scale=1.0, scalar=0.0, op0=ALU.mult, op1=ALU.add,
                                             accum_out=ssum[:, n:n + 1]).then_inc(sum_ready, 1)
                    dve.wait_ge(rms_ready, n + 1)
                    c.then(dve.reciprocal(rstd[:, n:n + 1], rms[:, n:n + 1]))
                    if t >= 2:
                        dve.wait_ge(stored[t % 2], 16 * (t // 2)) if j == 0 else dve.wait_ge(n2_turned, t - 1)
                    dve.scalar_tensor_tensor(out[:, :], src[:, :], rstd[:, n:n + 1], g[j][:, :], ALU.mult, ALU.mult).then_inc(ready, 1)
                    dve.wait_ge(ready, t + 1)

                def split_turned(t):
                    dve.wait_ge(copied, t + 1)
                    split(dve, h_T, (slice(None), slice(None), bass.ts(t, P)), rounded, t + 1, h_split)

                for t in range(NT):
                    b = t % 2
                    dve.wait_ge(x_loaded[b], 16 * (t // 2 + 1))
                    dve.wait_ge(y_loaded[b], 32 * (t // 2 + 1))
                    for j in range(2):
                        c.then(dve.scalar_tensor_tensor(x[b][:, :], y[j][b][:, :], gates[:, j, t:t + 1], x[b][:, :], ALU.mult, ALU.add))
                    norm(x[b], 0, t, n1[b], n1_ready)
                    norm(n1[b], 1, t, n2[b], n2_ready)
                    if t:
                        split_turned(t - 1)
                split_turned(NT - 1)

            @block.scalar
            def _(act):
                act.wait_ge(step, 1)
                for t in range(NT):
                    b = t % 2
                    for j in range(2):
                        n = 2 * t + j
                        act.wait_ge(sum_ready, n + 1)
                        act.activation(rms[:, n:n + 1], ssum[:, n:n + 1], ACT.Sqrt, scale=1.0 / D, bias=eps[:, :]).then_inc(rms_ready, 1)
                        if j == 0:
                            act.wait_ge(n1_ready, t + 1)
                            act.dma_start(x2[bass.ts(t, P), :], n1[b][:, :]).then_inc(stored[b], 16)
                    act.wait_ge(n2_turned, t + 1)
                    act.activation(h_T.whole[:, :, bass.ts(t, P)], turned[b][:, :, :].rearrange("p a (k q) -> p (a k) q", q=P), ACT.Copy).then_inc(copied, 1)
                for b in range(2):
                    act.wait_ge(stored[b], 16 * (NT // 2))

            @block.tensor
            def _(pe):
                for t in range(NT):
                    b = t % 2
                    pe.wait_ge(n2_ready, t + 1)
                    if t >= 2:
                        pe.wait_ge(copied, t - 1)
                    turn_rows(nc, n2[b], turned[b], ident).then_inc(n2_turned, 1)


LRU_W, LRU_H, LRU_D, LRU_TAPS, LRU_C = 1024, 16, 64, 4, 8.0
HY_W, HY_ORDER, HY_TAPS = 1024, 2, 3
N_LRU = LRU_W // P
COL_AX, COL_AGATE = 0, LRU_W
COL_HY = 2 * LRU_W
COL_GA = COL_HY + (HY_ORDER + 1) * HY_W
COL_GB = COL_GA + D
LOG1P_TERMS = 9


def wide_product(nc, out, w, rhs_T):
    for h in range(2):
        for k in range(ND):
            for n, (lhs, rhs) in enumerate(three_passes(w, rhs_T)):
                last = nc.tensor.matmul(out[:, h, :], lhs[:, k, :], rhs[:, k, bass.ts(h, BANK)],
                                        start=(k == 0 and n == 0), stop=(k == ND - 1 and n == 2))
    return last


def lru_phase(nc, h_T, w_in, conv_w, conv_b, w_r, b_r, w_i, b_i, lam, ident, ya_T):
    R_CONVB, R_BR, R_BI, R_LAM = (LRU_TAPS * N_LRU, (LRU_TAPS + 1) * N_LRU, (LRU_TAPS + 3) * N_LRU, (LRU_TAPS + 5) * N_LRU)
    N_ROWS = (LRU_TAPS + 7) * N_LRU
    PAD_L, PAD = LRU_TAPS // 2, LRU_TAPS - 1
    NB = range(2)
    with Store(nc, "lru") as m:
        w = [[m.parts(f"w{n}{b}", [P, ND, P]) for b in NB] for n in "xg"]
        w_gate = [m.sb(f"w_gate{b}", [P, 2, 2, P]) for b in NB]
        vec_rows = m.sb("vec_rows", [N_ROWS, P])
        vec = m.sb("vec", [P, N_ROWS])
        rate = m.sb("rate", [P, 2 * N_LRU])
        rate_neg = m.sb("rate_neg", [P, 2 * N_LRU])
        u = m.sb("u", [P, 2 * N_LRU])
        s = m.sb("s", [P, 2 * N_LRU])
        s2 = m.sb("s2", [P, 2 * N_LRU])
        poly = m.sb("poly", [P, 2 * N_LRU])
        a_x = [m.sb(f"a_x{b}", [P, T + PAD]) for b in NB]
        xa = [m.sb(f"xa{b}", [P, T]) for b in NB]
        a_gate = [m.sb(f"a_gate{b}", [P, T]) for b in NB]
        r = [[m.sb(f"r{b}{d}", [P, T]) for d in NB] for b in NB]
        x_in = [[m.sb(f"x_in{b}{d}", [P, T]) for d in NB] for b in NB]
        a = [[m.sb(f"a{b}{d}", [P, T]) for d in NB] for b in NB]
        h = [m.sb(f"h{d}", [P, T]) for d in NB]
        a_sq = h
        ya = [m.sb(f"ya{b}", [P, T]) for b in NB]
        ax_ps = m.ps("ax_ps", [P, 2, BANK])
        ag_ps = m.ps("ag_ps", [P, 2, BANK])
        gate_ps = m.ps("gate_ps", [P, 2, 2, BANK])
        cleared = m.sem("cleared")
        vec_loaded = m.sem("vec_loaded")
        vec_turned = m.sem("vec_turned")
        vec_ready = m.sem("vec_ready")
        u_ready = m.sem("u_ready")
        u_made = m.sem("u_made")
        rate_ready = m.sem("rate_ready")
        step = m.sem("step")
        w_loaded = [m.sem(f"w_loaded{b}") for b in NB]
        gate_loaded = [m.sem(f"gate_loaded{b}") for b in NB]
        proj_made = m.sem("proj_made")
        ax_copied = m.sem("ax_copied")
        gelu_done = m.sem("gelu_done")
        conv_step = m.sem("conv_step")
        xa_ready = m.sem("xa_ready")
        gates_made = m.sem("gates_made")
        sig_ready = m.sem("sig_ready")
        tanh_ready = m.sem("tanh_ready")
        x_in_ready = m.sem("x_in_ready")
        sq_ready = m.sem("sq_ready")
        rest_ready = m.sem("rest_ready")
        factor_ready = m.sem("factor_ready")
        scan_step = m.sem("scan_step")
        sum_ready = m.sem("sum_ready")
        ya_ready = m.sem("ya_ready")
        rounded = m.sem("rounded")
        w_split = m.sem("w_split")
        taken = m.sem("taken")
        ya_stored = [m.sem(f"ya_stored{b}") for b in NB]
        w_k = w_in.rearrange("(k p) n -> p k n", p=P)

        def col(j, n=0):
            return vec[:, bass.ds(j + n, 1)]

        with nc.Block() as block:
            @block.gpsimd
            def _(pool):
                for b in NB:
                    pool.memset(a_x[b][:, :], 0.0).then_inc(cleared, 1)
                    pool.memset(w_gate[b][:, :, :, :], 0.0).then_inc(cleared, 1)
                with pool.Fori(0, N_LRU // 2) as i:
                    for b in NB:
                        j = 2 * i + b
                        pool.wait_ge(ya_ready, j + 1)
                        pool.sem_inc(taken, 1)
                        pool.dma_start(ya_T[bass.ds(j * P, P), :], ya[b][:, :]).then_inc(ya_stored[b], 16)
                for b in NB:
                    pool.wait_ge(ya_stored[b], 16 * (N_LRU // 2))

            @block.sync
            def _(sp):
                def load_vectors():
                    for n, src in ((0, conv_w.rearrange("k (t p) -> (k t) p", p=P)), (R_CONVB, conv_b.rearrange("(t p) -> t p", p=P)),
                                   (R_BR, b_r.rearrange("d (t p) -> (d t) p", p=P)), (R_BI, b_i.rearrange("d (t p) -> (d t) p", p=P)),
                                   (R_LAM, lam.rearrange("d (t p) -> (d t) p", p=P))):
                        sp.dma_start(vec_rows[n:n + src.shape[0], :], src).then_inc(vec_loaded, 16)
                    sp.wait_ge(cleared, 4)

                def load(i):
                    for b in NB:
                        j = 2 * i + b
                        if not first(i):
                            sp.wait_ge(proj_made, 4 * i + 2 * b - 2)
                        for n, at in enumerate((COL_AX, COL_AGATE)):
                            sp.dma_start(w[n][b].whole[:, :, :], w_k[:, :, bass.ds(j * P + at, P)]).then_inc(w_loaded[b], 16)
                        if first(i) and b == 0:
                            load_vectors()
                        if not first(i):
                            sp.wait_ge(gates_made, 4 * i + 2 * b - 2)
                        for g, src in enumerate((w_r, w_i)):
                            for e in range(2):
                                half = slice(e * LRU_D, (e + 1) * LRU_D)
                                sp.dma_start(w_gate[b][half, g, :, half],
                                             src[:, bass.ds(2 * j + e, 1), :, :].rearrange("d o p n -> (o p) d n")).then_inc(gate_loaded[b], 16)
                repeat(sp, N_LRU // 2, load)

            @block.tensor
            def _(pe):
                def project(j, i, b):
                    for n, (out, read) in enumerate(((ax_ps, ax_copied), (ag_ps, gelu_done))):
                        pe.wait_ge(w_split, 2 * j + n + 1)
                        if not first(j):
                            pe.wait_ge(read, j)
                        wide_product(nc, out, w[n][b], h_T).then_inc(proj_made, 1)
                    if first(j):
                        pe.wait_ge(vec_loaded, 16 * 5)
                        nc.tensor.transpose(gate_ps[:, 0, 0, 0:N_ROWS], vec_rows[:, :], ident[0:N_ROWS, 0:N_ROWS]).then_inc(vec_turned, 1)

                def gates(j, i, b):
                    pe.wait_ge(xa_ready, j + 1)
                    pe.wait_ge(gate_loaded[b], 64 * (i + 1))
                    for d in NB:
                        if d or not first(j):
                            pe.wait_ge(sig_ready, 2 * (2 * j + d))
                        for g in range(2):
                            for t in range(2):
                                last = nc.tensor.matmul(gate_ps[:, g, t, :], w_gate[b][:, g, d, :], xa[b][:, bass.ts(t, BANK)], start=True, stop=True)
                        last.then_inc(gates_made, 1)

                def two_tiles(i):
                    project(2 * i, i, 0)
                    if not first(i):
                        gates(2 * i - 1, i - 1, 1)
                    project(2 * i + 1, i, 1)
                    gates(2 * i, i, 0)
                repeat(pe, N_LRU // 2, two_tiles)
                gates(N_LRU - 1, N_LRU // 2 - 1, 1)

            @block.scalar
            def _(act):
                act.wait_ge(cleared, 4)

                def inputs(j, i, b):
                    act.wait_ge(proj_made, 2 * j + 1)
                    if not first(i):
                        act.wait_ge(xa_ready, j - 1)
                    act.activation(a_x[b][:, PAD_L:PAD_L + T], ax_ps[:, :, :].rearrange("p a n -> p (a n)"), ACT.Copy).then_inc(ax_copied, 1)
                    act.wait_ge(proj_made, 2 * j + 2)
                    if not first(i):
                        act.wait_ge(ya_ready, j - 1)
                    act.activation(a_gate[b][:, :], ag_ps[:, :, :].rearrange("p a n -> p (a n)"), ACT.Gelu_apprx_tanh).then_inc(gelu_done, 1)
                    if first(j):
                        act.wait_ge(u_ready, 1)
                        act.activation(u[:, :], u[:, :], ACT.Exp).then_inc(u_made, 1)
                        act.wait_ge(rate_ready, 1)

                def gates(j, i, b):
                    for d in NB:
                        act.wait_ge(gates_made, 2 * j + d + 1)
                        for g, (out, n) in enumerate(((r, R_BR), (x_in, R_BI))):
                            act.activation(out[b][d][:, :], gate_ps[:, g, :, :].rearrange("p a n -> p (a n)"), ACT.Sigmoid,
                                           bias=col(j, n + d * N_LRU)).then_inc(sig_ready, 1)
                    act.wait_ge(sig_ready, 4 * j + 4)
                    for d in NB:
                        act.activation(a[b][d][:, :], r[b][d][:, :], ACT.Exp, scale=rate_neg[:, bass.ds(j + d * N_LRU, 1)])
                    for d in NB:
                        act.activation(r[b][d][:, :], r[b][d][:, :], ACT.Tanh, scale=rate[:, bass.ds(j + d * N_LRU, 1)]).then_inc(tanh_ready, 1)
                    for d in NB:
                        act.wait_ge(rest_ready, 2 * j + d + 1)
                        act.activation(r[b][d][:, :], r[b][d][:, :], ACT.Sqrt).then_inc(factor_ready, 1)

                def two_tiles(i):
                    inputs(2 * i, i, 0)
                    if not first(i):
                        gates(2 * i - 1, i - 1, 1)
                    inputs(2 * i + 1, i, 1)
                    gates(2 * i, i, 0)
                repeat(act, N_LRU // 2, two_tiles)
                gates(N_LRU - 1, N_LRU // 2 - 1, 1)

            @block.vector
            def _(dve):
                def split_w(j, i, b):
                    dve.wait_ge(w_loaded[b], 32 * (i + 1))
                    for n in range(2):
                        split(dve, w[n][b], WHOLE, rounded, 2 * j + n + 1, w_split)

                split_w(0, 0, 0)
                split_w(1, 0, 1)
                c = Chain(dve, step)
                dve.wait_ge(vec_turned, 1)
                dve.tensor_copy(vec[:, :], gate_ps[:, 0, 0, 0:N_ROWS]).then_inc(vec_ready, 1)
                dve.wait_ge(vec_ready, 1)
                lam_v = vec[:, R_LAM:R_LAM + 2 * N_LRU]
                c.then(dve.tensor_scalar(rate_neg[:, :], lam_v, -1.0, None, ALU.mult))
                dve.tensor_tensor(u[:, :], lam_v, rate_neg[:, :], ALU.min).then_inc(u_ready, 1)
                c.then(dve.tensor_scalar(rate[:, :], rate_neg[:, :], 0.0, None, ALU.max))
                dve.wait_ge(u_made, 1)
                c.then(dve.tensor_scalar(s[:, :], u[:, :], 2.0, None, ALU.add))
                c.then(dve.reciprocal(s[:, :], s[:, :]))
                c.then(dve.tensor_tensor(s[:, :], s[:, :], u[:, :], ALU.mult))
                c.then(dve.tensor_tensor(s2[:, :], s[:, :], s[:, :], ALU.mult))
                for n in reversed(range(LOG1P_TERMS)):
                    term = 2.0 / (2 * n + 1)
                    if n == LOG1P_TERMS - 1:
                        c.then(dve.tensor_scalar(poly[:, :], s2[:, :], 0.0, term, ALU.mult, ALU.add))
                    else:
                        c.then(dve.tensor_tensor(poly[:, :], poly[:, :], s2[:, :], ALU.mult))
                        c.then(dve.tensor_scalar(poly[:, :], poly[:, :], term, None, ALU.add))
                c.then(dve.tensor_tensor(poly[:, :], poly[:, :], s[:, :], ALU.mult))
                c.then(dve.tensor_tensor(rate[:, :], rate[:, :], poly[:, :], ALU.add))
                c.then(dve.tensor_scalar(rate[:, :], rate[:, :], LRU_C, None, ALU.mult))
                dve.tensor_scalar(rate_neg[:, :], rate[:, :], -1.0, None, ALU.mult).then_inc(rate_ready, 1)

                def conv(j, i, b):
                    dve.wait_ge(ax_copied, j + 1)
                    if not first(i):
                        dve.wait_ge(gates_made, 2 * j - 2)
                    dve.tensor_scalar(xa[b][:, :], a_x[b][:, 0:T], col(j), col(j, R_CONVB), ALU.mult, ALU.add).then_inc(conv_step, 1)
                    for k in range(1, LRU_TAPS):
                        dve.wait_ge(conv_step, (LRU_TAPS - 1) * j + k)
                        dve.scalar_tensor_tensor(xa[b][:, :], a_x[b][:, k:k + T], col(j, k * N_LRU), xa[b][:, :],
                                                 ALU.mult, ALU.add).then_inc(xa_ready if k == LRU_TAPS - 1 else conv_step, 1)

                def scan(j, i, b):
                    dve.wait_ge(xa_ready, j + 1)
                    for d in NB:
                        dve.wait_ge(sig_ready, 4 * j + 2 * d + 2)
                        dve.tensor_tensor(x_in[b][d][:, :], x_in[b][d][:, :], xa[b][:, :], ALU.mult).then_inc(x_in_ready, 1)
                    if not first(j):
                        dve.wait_ge(ya_ready, j)
                    for d in NB:
                        dve.wait_ge(tanh_ready, 2 * j + d + 1)
                        dve.tensor_tensor(a_sq[d][:, :], a[b][d][:, :], a[b][d][:, :], ALU.mult).then_inc(sq_ready, 1)
                    for d in NB:
                        dve.wait_ge(sq_ready, 2 * j + d + 1)
                        dve.scalar_tensor_tensor(r[b][d][:, :], a_sq[d][:, :], 1.0, r[b][d][:, :], ALU.add, ALU.mult).then_inc(rest_ready, 1)
                    for d in NB:
                        rest = slice(1 - d, T - d)
                        dve.wait_ge(factor_ready, 2 * j + d + 1)
                        dve.wait_ge(x_in_ready, 2 * j + d + 1)
                        dve.tensor_tensor(x_in[b][d][:, rest], x_in[b][d][:, rest], r[b][d][:, rest], ALU.mult).then_inc(scan_step, 1)
                    for d in NB:
                        dve.wait_ge(scan_step, 4 * j + d + 1)
                        order = slice(None, None, -1 if d else 1)
                        dve.tensor_tensor_scan(h[d][:, order], a[b][d][:, order], x_in[b][d][:, order], 0.0, ALU.mult, ALU.add).then_inc(scan_step, 1)
                    dve.wait_ge(scan_step, 4 * j + 4)
                    dve.tensor_tensor(h[0][:, :], h[0][:, :], h[1][:, :], ALU.add).then_inc(sum_ready, 1)
                    dve.wait_ge(gelu_done, j + 1)
                    dve.wait_ge(sum_ready, j + 1)
                    if not (isinstance(i, int) and i == 0):
                        dve.wait_ge(ya_stored[b], 16 * i)
                    dve.tensor_tensor(ya[b][:, :], h[0][:, :], a_gate[b][:, :], ALU.mult).then_inc(ya_ready, 1)

                def split_next(j, i, b):
                    dve.wait_ge(proj_made, 2 * j - 2)
                    split_w(j, i, b)

                def two_tiles(i):
                    last = isinstance(i, int) and i == N_LRU // 2 - 1
                    conv(2 * i, i, 0)
                    if not first(i):
                        split_next(2 * i + 1, i, 1)
                        scan(2 * i - 1, i - 1, 1)
                    conv(2 * i + 1, i, 1)
                    if not last:
                        split_next(2 * i + 2, i + 1, 0)
                    scan(2 * i, i, 0)
                two_tiles(0)
                two_tiles(1)
                with dve.Fori(2, N_LRU // 2 - 1) as i:
                    two_tiles(i)
                two_tiles(N_LRU // 2 - 1)
                scan(N_LRU - 1, N_LRU // 2 - 1, 1)


def hyena_inputs_phase(nc, h_T, w_in, conv_w, conv_b, ident, v_x1, x2_T):
    N_NAT, N_ALL = 2 * HY_W // P, 3 * HY_W // P
    R_BIAS = HY_TAPS * N_ALL
    N_ROWS = (HY_TAPS + 1) * N_ALL
    PAD_L, PAD = HY_TAPS // 2, HY_TAPS - 1
    NB = range(2)
    with Store(nc, "hyin") as m:
        w = [m.parts(f"w{b}", [P, ND, P]) for b in NB]
        vec_rows = m.sb("vec_rows", [N_ROWS, P])
        vec = m.sb("vec", [P, N_ROWS])
        raw = [m.sb(f"raw{b}", [P, T + PAD]) for b in NB]
        conv = [m.sb(f"conv{b}", [P, T]) for b in NB]
        rows = [m.sb(f"rows{b}", [P, NT, P]) for b in NB]
        proj_ps = [m.ps(f"proj{b}", [P, 2, BANK]) for b in NB]
        turned_ps = [m.ps(f"turned{b}", [P, 2, BANK]) for b in NB]
        cleared = m.sem("cleared")
        vec_loaded = m.sem("vec_loaded")
        vec_turned = m.sem("vec_turned")
        vec_ready = m.sem("vec_ready")
        w_loaded = [m.sem(f"w_loaded{b}") for b in NB]
        rounded = m.sem("rounded")
        w_split = m.sem("w_split")
        proj_made = m.sem("proj_made")
        raw_ready = m.sem("raw_ready")
        tap_done = m.sem("tap_done")
        conv_ready = m.sem("conv_ready")
        turned = m.sem("turned")
        rows_ready = m.sem("rows_ready")
        taken = m.sem("taken")
        stored = [m.sem(f"stored{b}") for b in NB]
        w_k = w_in.rearrange("(k p) n -> p k n", p=P)
        nat = v_x1.rearrange("(t p) c -> p t c", p=P)

        def loops(engine, body):
            body(0, True)
            with engine.Fori(1, N_NAT // 2) as i:
                body(i, True)
            with engine.Fori(N_NAT // 2, N_ALL // 2) as i:
                body(i, False)

        with nc.Block() as block:
            @block.gpsimd
            def _(pool):
                for b in NB:
                    pool.memset(raw[b][:, :], 0.0).then_inc(cleared, 1)

                def store(i, turn):
                    for b in NB:
                        j = 2 * i + b
                        if turn:
                            pool.wait_ge(rows_ready, j + 1)
                            pool.sem_inc(taken, 1)
                            pool.dma_start(nat[:, :, bass.ds(j * P, P)], rows[b][:, :, :]).then_inc(stored[b], 16)
                        else:
                            pool.wait_ge(conv_ready, j + 1)
                            pool.sem_inc(taken, 1)
                            pool.dma_start(x2_T[bass.ds((j - N_NAT) * P, P), :], conv[b][:, :]).then_inc(stored[b], 16)
                loops(pool, store)
                for b in NB:
                    pool.wait_ge(stored[b], 16 * (N_ALL // 2))

            @block.sync
            def _(sp):
                def load(i):
                    for b in NB:
                        j = 2 * i + b
                        if not first(i):
                            sp.wait_ge(proj_made, j - 1)
                        sp.dma_start(w[b].whole[:, :, :], w_k[:, :, bass.ds(j * P + COL_HY, P)]).then_inc(w_loaded[b], 16)
                        if first(i) and b == 0:
                            sp.dma_start(vec_rows[0:R_BIAS, :], conv_w.rearrange("k (t p) -> (k t) p", p=P)).then_inc(vec_loaded, 16)
                            sp.dma_start(vec_rows[R_BIAS:, :], conv_b.rearrange("(t p) -> t p", p=P)).then_inc(vec_loaded, 16)
                repeat(sp, N_ALL // 2, load)

            @block.tensor
            def _(pe):
                def turn(j, b):
                    pe.wait_ge(conv_ready, j + 1)
                    if not (isinstance(j, int) and j < 2):
                        pe.wait_ge(rows_ready, j - 1)
                    turn_rows(nc, conv[b], turned_ps[b], ident).then_inc(turned, 1)

                def two_tiles(i, turning):
                    for b in NB:
                        j = 2 * i + b
                        pe.wait_ge(w_split, j + 1)
                        if not first(i):
                            pe.wait_ge(raw_ready, j - 1)
                        wide_product(nc, proj_ps[b], w[b], h_T).then_inc(proj_made, 1)
                        if first(j):
                            pe.wait_ge(vec_loaded, 32)
                            nc.tensor.transpose(turned_ps[1][:, 0, 0:N_ROWS], vec_rows[:, :], ident[0:N_ROWS, 0:N_ROWS]).then_inc(vec_turned, 1)
                        if turning and not (first(i) and b == 0):
                            turn(j - 1, 1 - b)

                two_tiles(0, True)
                with pe.Fori(1, N_NAT // 2) as i:
                    two_tiles(i, True)
                turn(N_NAT - 1, 1)
                with pe.Fori(N_NAT // 2, N_ALL // 2) as i:
                    two_tiles(i, False)

            @block.scalar
            def _(act):
                act.wait_ge(cleared, 2)

                def copy_rows(j, i, b):
                    act.wait_ge(turned, j + 1)
                    if not first(i):
                        act.wait_ge(stored[b], 16 * i)
                    act.activation(rows[b][:, :, :], turned_ps[b][:, :, :].rearrange("p a (k c) -> p (a k) c", c=P), ACT.Copy).then_inc(rows_ready, 1)

                def two_tiles(i, turning):
                    for b in NB:
                        j = 2 * i + b
                        act.wait_ge(proj_made, j + 1)
                        if not first(i):
                            act.wait_ge(conv_ready, j - 1)
                        act.activation(raw[b][:, PAD_L:PAD_L + T], proj_ps[b][:, :, :].rearrange("p a n -> p (a n)"), ACT.Copy).then_inc(raw_ready, 1)
                        if turning and not (first(i) and b == 0):
                            copy_rows(j - 1, i if b else i - 1, 1 - b)

                two_tiles(0, True)
                two_tiles(1, True)
                with act.Fori(2, N_NAT // 2) as i:
                    two_tiles(i, True)
                copy_rows(N_NAT - 1, N_NAT // 2 - 1, 1)
                with act.Fori(N_NAT // 2, N_ALL // 2) as i:
                    two_tiles(i, False)

            @block.vector
            def _(dve):
                def split_w(j, i, b):
                    dve.wait_ge(w_loaded[b], 16 * (i + 1))
                    if not (isinstance(j, int) and j < 2):
                        dve.wait_ge(proj_made, j - 1)
                    split(dve, w[b], WHOLE, rounded, j + 1, w_split)

                split_w(0, 0, 0)

                def two_tiles(i, turning):
                    for b in NB:
                        j = 2 * i + b
                        if not (isinstance(j, int) and j == N_ALL - 1):
                            split_w(j + 1, i + b, 1 - b)
                        if first(j):
                            dve.wait_ge(vec_turned, 1)
                            dve.tensor_copy(vec[:, :], turned_ps[1][:, 0, 0:N_ROWS]).then_inc(vec_ready, 1)
                            dve.wait_ge(vec_ready, 1)
                        dve.wait_ge(raw_ready, j + 1)
                        if not first(i):
                            if turning:
                                dve.wait_ge(turned, j - 1)
                            else:
                                dve.wait_ge(stored[b], 16 * i)
                        dve.tensor_scalar(conv[b][:, :], raw[b][:, 0:T], vec[:, bass.ds(j, 1)], vec[:, bass.ds(j + R_BIAS, 1)],
                                          ALU.mult, ALU.add).then_inc(tap_done, 1)
                        for k in range(1, HY_TAPS):
                            dve.wait_ge(tap_done, (HY_TAPS - 1) * j + k)
                            dve.scalar_tensor_tensor(conv[b][:, :], raw[b][:, k:k + T], vec[:, bass.ds(j + k * N_ALL, 1)], conv[b][:, :],
                                                     ALU.mult, ALU.add).then_inc(conv_ready if k == HY_TAPS - 1 else tap_done, 1)
                two_tiles(0, True)
                with dve.Fori(1, N_NAT // 2) as i:
                    two_tiles(i, True)
                with dve.Fori(N_NAT // 2, N_ALL // 2 - 1) as i:
                    two_tiles(i, False)
                two_tiles(N_ALL // 2 - 1, False)


def gates_phase(nc, h_T, ya_T, w_in, w_a_out, part_T, gate_T):
    NB = range(2)
    with Store(nc, "gates") as m:
        w = [[m.parts(f"w{n}{b}", [P, ND, P]) for n in ("ga", "gb", "a")] for b in NB]
        ya = m.parts("ya", [P, N_LRU, T])
        sig_a = [m.sb(f"sig_a{b}", [P, T]) for b in NB]
        sig_b = [m.sb(f"sig_b{b}", [P, T]) for b in NB]
        part = [m.sb(f"part{b}", [P, T]) for b in NB]
        ga_ps = m.ps("ga_ps", [P, 2, BANK])
        gb_ps = m.ps("gb_ps", [P, 2, BANK])
        a_ps = m.ps("a_ps", [P, 2, BANK])
        w_loaded = [m.sem(f"w_loaded{b}") for b in NB]
        ya_loaded = [m.sem(f"ya_loaded{h}") for h in range(2)]
        rounded = m.sem("rounded")
        w_split = m.sem("w_split")
        ya_split = m.sem("ya_split")
        made = m.sem("made")
        sig_ready = m.sem("sig_ready")
        part_ready = m.sem("part_ready")
        taken = m.sem("taken")
        sig_stored = [m.sem(f"sig_stored{b}") for b in NB]
        part_stored = [m.sem(f"part_stored{b}") for b in NB]
        srcs = [(w_in.rearrange("(k p) n -> p k n", p=P), COL_GA), (w_in.rearrange("(k p) n -> p k n", p=P), COL_GB),
                (w_a_out.rearrange("(k p) n -> p k n", p=P), 0)]
        with nc.Block() as block:
            @block.sync
            def _(sp):
                def load(i):
                    for b in NB:
                        j = 2 * i + b
                        if not first(i):
                            sp.wait_ge(made, 6 * i + 3 * b - 3)
                        for n, (src, at) in enumerate(srcs):
                            sp.dma_start(w[b][n].whole[:, :, :], src[:, :, bass.ds(j * P + at, P)]).then_inc(w_loaded[b], 16)
                        if first(i) and b == 0:
                            for h in range(2):
                                sp.dma_start(ya.whole[:, :, bass.ts(h, BANK)],
                                             ya_T.rearrange("(k p) t -> p k t", p=P)[:, :, bass.ts(h, BANK)]).then_inc(ya_loaded[h], 16)
                repeat(sp, ND // 2, load)

            @block.gpsimd
            def _(pool):
                with pool.Fori(0, ND // 2) as i:
                    for b in NB:
                        j = 2 * i + b
                        pool.wait_ge(sig_ready, 2 * j + 2)
                        pool.sem_inc(taken, 1)
                        pool.dma_start(gate_T[bass.ds(j * P, P), :], sig_b[b][:, :]).then_inc(sig_stored[b], 16)
                        pool.wait_ge(part_ready, j + 1)
                        pool.sem_inc(taken, 1)
                        pool.dma_start(part_T[bass.ds(j * P, P), :], part[b][:, :]).then_inc(part_stored[b], 16)
                for b in NB:
                    pool.wait_ge(sig_stored[b], 16 * (ND // 2))
                    pool.wait_ge(part_stored[b], 16 * (ND // 2))

            @block.tensor
            def _(pe):
                def two_tiles(i):
                    for b in NB:
                        j = 2 * i + b
                        for n, (out, rhs) in enumerate(((ga_ps, h_T), (gb_ps, h_T), (a_ps, ya))):
                            pe.wait_ge(w_split, 3 * j + n + 1)
                            if n == 2:
                                pe.wait_ge(ya_split, 2)
                            if not first(j):
                                pe.wait_ge(*((sig_ready, 2 * j + n - 1), (sig_ready, 2 * j + n - 1), (part_ready, j))[n])
                            wide_product(nc, out, w[b][n], rhs).then_inc(made, 1)
                repeat(pe, ND // 2, two_tiles)

            @block.scalar
            def _(act):
                def two_tiles(i):
                    for b in NB:
                        j = 2 * i + b
                        act.wait_ge(made, 3 * j + 1)
                        if not first(i):
                            act.wait_ge(part_ready, j - 1)
                        act.activation(sig_a[b][:, :], ga_ps[:, :, :].rearrange("p a n -> p (a n)"), ACT.Sigmoid).then_inc(sig_ready, 1)
                        act.wait_ge(made, 3 * j + 2)
                        if not first(i):
                            act.wait_ge(sig_stored[b], 16 * i)
                        act.activation(sig_b[b][:, :], gb_ps[:, :, :].rearrange("p a n -> p (a n)"), ACT.Sigmoid).then_inc(sig_ready, 1)
                repeat(act, ND // 2, two_tiles)

            @block.vector
            def _(dve):
                def split_w(j, i, b):
                    dve.wait_ge(w_loaded[b], 48 * (i + 1))
                    for n in range(3):
                        if not (isinstance(j, int) and j < 2):
                            dve.wait_ge(made, 3 * j + n - 5)
                        split(dve, w[b][n], WHOLE, rounded, 3 * j + n + (1 if first(j) else 3), w_split)

                split_w(0, 0, 0)
                for h in range(2):
                    dve.wait_ge(ya_loaded[h], 16)
                    split(dve, ya, (slice(None), slice(None), bass.ts(h, BANK)), rounded, 4 + h, ya_split)

                def two_tiles(i):
                    for b in NB:
                        j = 2 * i + b
                        if not (isinstance(j, int) and j == ND - 1):
                            split_w(j + 1, i + b, 1 - b)
                        dve.wait_ge(sig_ready, 2 * j + 1)
                        dve.wait_ge(made, 3 * j + 3)
                        if not first(i):
                            dve.wait_ge(part_stored[b], 16 * i)
                        dve.tensor_tensor(part[b][:, :], a_ps[:, :, :].rearrange("p a n -> p (a n)"), sig_a[b][:, :], ALU.mult).then_inc(part_ready, 1)
                two_tiles(0)
                with dve.Fori(1, ND // 2 - 1) as i:
                    two_tiles(i)
                two_tiles(ND // 2 - 1)


def merge_phase(nc, z_T, w_b_out, part_T, gate_T, merged_T):
    NB = range(2)
    with Store(nc, "merge") as m:
        z = m.parts("z", [P, ND, T])
        w = [m.parts(f"w{b}", [P, ND, P]) for b in NB]
        part = [m.sb(f"part{b}", [P, T]) for b in NB]
        gate = [m.sb(f"gate{b}", [P, T]) for b in NB]
        prod = [m.sb(f"prod{b}", [P, T]) for b in NB]
        b_ps = [m.ps(f"b_ps{b}", [P, 2, BANK]) for b in NB]
        z_loaded = [m.sem(f"z_loaded{h}") for h in range(2)]
        rounded = m.sem("rounded")
        z_split = m.sem("z_split")
        w_split = m.sem("w_split")
        w_loaded = [m.sem(f"w_loaded{b}") for b in NB]
        parts_loaded = [m.sem(f"parts_loaded{b}") for b in NB]
        made = m.sem("made")
        prod_ready = m.sem("prod_ready")
        merged_ready = m.sem("merged_ready")
        w_k = w_b_out.rearrange("(k p) n -> p k n", p=P)
        with nc.Block() as block:
            @block.sync
            def _(sp):
                def load(i):
                    for b in NB:
                        j = 2 * i + b
                        if not first(i):
                            sp.wait_ge(made, j - 1)
                        sp.dma_start(w[b].whole[:, :, :], w_k[:, :, bass.ds(j * P, P)]).then_inc(w_loaded[b], 16)
                        if first(i) and b == 0:
                            for h in range(2):
                                sp.dma_start(z.whole[:, :, bass.ts(h, BANK)],
                                             z_T.rearrange("(k p) t -> p k t", p=P)[:, :, bass.ts(h, BANK)]).then_inc(z_loaded[h], 16)
                        if not first(i):
                            sp.wait_ge(merged_ready, j - 1)
                        sp.dma_start(gate[b][:, :], gate_T[bass.ds(j * P, P), :]).then_inc(parts_loaded[b], 16)
                        sp.dma_start(part[b][:, :], part_T[bass.ds(j * P, P), :]).then_inc(parts_loaded[b], 16)
                repeat(sp, ND // 2, load)

            @block.tensor
            def _(pe):
                pe.wait_ge(z_split, 2)

                def two_tiles(i):
                    for b in NB:
                        j = 2 * i + b
                        pe.wait_ge(w_split, j + 1)
                        if not first(i):
                            pe.wait_ge(prod_ready, j - 1)
                        wide_product(nc, b_ps[b], w[b], z).then_inc(made, 1)
                repeat(pe, ND // 2, two_tiles)

            @block.vector
            def _(dve):
                def split_w(j, i, b):
                    dve.wait_ge(w_loaded[b], 16 * (i + 1))
                    if not (isinstance(j, int) and j < 2):
                        dve.wait_ge(made, j - 1)
                    split(dve, w[b], WHOLE, rounded, j + (1 if first(j) else 3), w_split)

                split_w(0, 0, 0)
                for h in range(2):
                    dve.wait_ge(z_loaded[h], 16)
                    split(dve, z, (slice(None), slice(None), bass.ts(h, BANK)), rounded, 2 + h, z_split)

                def two_tiles(i):
                    for b in NB:
                        j = 2 * i + b
                        if not (isinstance(j, int) and j == ND - 1):
                            split_w(j + 1, i + b, 1 - b)
                        dve.wait_ge(parts_loaded[b], 32 * (i + 1))
                        dve.wait_ge(made, j + 1)
                        dve.tensor_tensor(prod[b][:, :], b_ps[b][:, :, :].rearrange("p a n -> p (a n)"), gate[b][:, :], ALU.mult).then_inc(prod_ready, 1)
                        dve.wait_ge(prod_ready, j + 1)
                        dve.tensor_tensor(merged_T[:, tile(j), :].rearrange("p o t -> p (o t)"), prod[b][:, :], part[b][:, :], ALU.add).then_inc(merged_ready, 1)
                two_tiles(0)
                with dve.Fori(1, ND // 2 - 1) as i:
                    two_tiles(i)
                two_tiles(ND // 2 - 1)


FILT_EMB, FILT_HID = 33, 64
FILT_BANDS = (FILT_EMB - 1) // 2
DECAY_FAST, DECAY_SLOW, DECAY_TARGET = 0.3, 1.5, 1e-2
TWO_PI = (6.28125, 0.0019350051879882812, 3.01991598196781e-07)
SIN_MAX = 3.1415925
TO_WHOLE = 1.5 * 2 ** 23
HB = 256
NHB = T // HB
HJ = HB // P
HF = HB // P
HC = BANK
COS, SIN, COS_NEG, SIN_NEG = range(4)


def filter_positions():
    f4 = np.float32
    lag = np.linspace(0.0, 1.0, T, dtype=f4)[:, None]
    w = f4(2.0 * np.pi / T) * np.arange(T, dtype=f4)[:, None]
    f = np.linspace(1e-4, FILT_BANDS - 1, FILT_BANDS, dtype=f4)[None, :]
    return np.ascontiguousarray(np.concatenate([lag, np.cos(w * f), -np.sin(w * f)], axis=-1).T.astype(f4))


def filter_decay():
    f4 = np.float32
    lag = np.linspace(0.0, 1.0, T, dtype=f4)[:, None]
    rates = np.abs(np.linspace(np.log(DECAY_TARGET) / DECAY_SLOW, np.log(DECAY_TARGET) / DECAY_FAST, HY_W, dtype=f4))
    return np.ascontiguousarray(np.exp(-lag * rates[None, :]).astype(f4))


def block_angles():
    f = np.stack([np.arange(P) * HF + n for n in range(HF)])
    return np.pi * np.arange(HB)[:, None, None] * (2 * f[None] + 1) / (2 * HB)


def block_transform():
    angle = block_angles()
    kinds = np.stack([np.cos(angle), np.sin(angle), -np.cos(angle), -np.sin(angle)], axis=1)
    return np.ascontiguousarray(kinds.reshape(HJ, P, 4, HF, P).transpose(1, 0, 2, 3, 4).astype(np.float32))


def block_inverse():
    angle = block_angles().transpose(2, 1, 0)
    return np.ascontiguousarray((np.stack([np.cos(angle), -np.sin(angle)], axis=2) / HB).astype(np.float32))


def filter_phase(nc, positions, w1, b1, w2, b2, freq, hid_T):
    H = FILT_HID
    with Store(nc, "filter") as m:
        pos = m.sb("pos", [FILT_EMB, T])
        w = [m.sb("w1", [FILT_EMB, H]), m.sb("w2", [H, H])]
        b = [m.sb(f"b{n}", [H, 1]) for n in range(2)]
        fr = [m.sb(f"freq{n}", [H, 1]) for n in range(2)]
        arg = m.sb("arg", [H, T])
        turns = m.sb("turns", [H, T])
        hid1 = m.sb("hid1", [H, T])
        ps = m.ps("ps", [P, 2, BANK])
        loaded = m.sem("loaded")
        made = m.sem("made")
        step = m.sem("step")
        arg_ready = m.sem("arg_ready")
        hid_ready = m.sem("hid_ready")
        with nc.Block() as block:
            @block.sync
            def _(sp):
                sp.dma_start(pos[:, :], positions).then_inc(loaded, 16)
                for n, (wn, bn) in enumerate(((w1, b1), (w2, b2))):
                    sp.dma_start(w[n][:, :], wn).then_inc(loaded, 16)
                    with nc.allow_non_contiguous_dma(reason="a number per partition"):
                        sp.dma_start(b[n][:, :], bn.rearrange("(p o) -> p o", o=1)).then_inc(loaded, 16)
                        sp.dma_start(fr[n][:, :], freq[n:n + 1, :].rearrange("o p -> p o")).then_inc(loaded, 16)

            @block.tensor
            def _(pe):
                pe.wait_ge(loaded, 16 * 7)
                for n, src in enumerate((pos, hid1)):
                    if n:
                        pe.wait_ge(hid_ready, 1)
                    for t in range(2):
                        last = nc.tensor.matmul(ps[0:H, t, :], w[n][:, :], src[:, bass.ts(t, BANK)], start=True, stop=True)
                    last.then_inc(made, 1)

            @block.vector
            def _(dve):
                c = Chain(dve, step)
                dve.wait_ge(loaded, 16 * 7)
                for n in range(2):
                    dve.wait_ge(made, n + 1)
                    c.then(dve.tensor_scalar(arg[:, :], ps[0:H, :, :].rearrange("p a n -> p (a n)"), b[n][:, :], fr[n][:, :], ALU.add, ALU.mult))
                    c.then(dve.tensor_scalar(turns[:, :], arg[:, :], 1.0 / (2.0 * np.pi), TO_WHOLE, ALU.mult, ALU.add))
                    c.then(dve.tensor_scalar(turns[:, :], turns[:, :], -TO_WHOLE, None, ALU.add))
                    for part in TWO_PI:
                        c.then(dve.scalar_tensor_tensor(arg[:, :], turns[:, :], -part, arg[:, :], ALU.mult, ALU.add))
                    dve.tensor_scalar(arg[:, :], arg[:, :], -SIN_MAX, SIN_MAX, ALU.max, ALU.min).then_inc(arg_ready, 1)
                    dve.wait_ge(hid_ready, n + 1)

            @block.scalar
            def _(act):
                for n, out in enumerate((hid1, hid_T)):
                    act.wait_ge(arg_ready, n + 1)
                    act.activation(out[:, :], arg[:, :], ACT.Sin).then_inc(hid_ready, 1)


def hyena_phase(nc, v_x1, x2_T, hid_T, w3, bias, decay, transform, inverse, z1, z_T):
    PASSES = [(o, h) for o in range(HY_ORDER) for h in range(HY_W // HC)]
    NP = len(PASSES)
    SHIFTS = range(1 - NHB, NHB)
    FWD, BWD = range(2)

    def sources(d):
        if d > 0:
            return [((COS, COS), (SIN_NEG, SIN_NEG), FWD, d), ((SIN, SIN_NEG), (COS, COS_NEG), FWD, d - 1)]
        if d == 0:
            return [((COS, COS), (SIN_NEG, SIN_NEG), FWD, 0), ((COS, COS), (SIN, SIN), BWD, 0)]
        return [((COS, COS), (SIN, SIN), BWD, -d), ((SIN, SIN_NEG), (COS_NEG, COS), BWD, -d - 1)]

    program = [("F", 0, 0)] + [("K", 0, d) for d in (-3, -2, -1, 0)]
    for n in range(NP):
        more = n + 1 < NP
        program += [("U", n, i) for i in reversed(range(NHB))]
        program += [("Y", n - 1, NHB - 1)] if n else []
        program += [("K", n, d) for d in range(1, NHB)]
        program += [("Y", n, 0)] + ([("F", n + 1, 0)] if more else [])
        for m_ in range(1, NHB):
            program += [("K", n + 1, m_ - NHB)] if more else []
            program += [("Y", n, m_)] if m_ < NHB - 1 else []
        program += [("K", n + 1, 0)] if more else [("Y", n, NHB - 1)]
    moved = {what: n for n, what in enumerate(w for w in program if w[0] in "UK")}
    turned_back = {what: n for n, what in enumerate(w for w in program if w[0] == "Y")}
    def pair(n, m_, i):
        return NHB * NHB * n + NHB * m_ + NHB - i

    with Store(nc, "hyena") as m:
        tr = m.sb("tr", [P, HJ, 4, HF, P])
        inv = m.sb("inv", [P, HF, 2, HB])
        w3_sb = m.sb("w3", [FILT_HID, 2, HC])
        bias_sb = m.sb("bias", [1, HC])
        decay_sb = [m.sb(f"decay{b}", [P, HC]) for b in range(2)]
        filt = m.sb("filt", [P, 2, NT, HC])
        u = [m.sb(f"u{b}", [P, HJ, HC]) for b in range(2)]
        U = [m.sb(f"U{i}", [P, 2, HF * HC]) for i in range(NHB)]
        K = {d: m.sb(f"K{d + NHB}", [P, 2, HF * HC]) for d in SHIFTS}
        Y = [m.sb(f"Y{b}", [P, 2, HF * HC]) for b in range(2)]
        by_re = m.sb("by_re", [P, 2, HF * HC])
        by_im = m.sb("by_im", [P, 2, HF * HC])
        gate = [m.sb(f"gate{b}", [P, HJ * HC]) for b in range(2)]
        z = [m.sb(f"z{b}", [P, HJ * HC]) for b in range(2)]
        tr_ps = [m.ps(f"tr_ps{c}", [P, HF * HC]) for c in range(2)]
        inv_ps = m.ps("inv_ps", [P, HJ * HC])
        filt_ps = [m.ps(f"filt_ps{b}", [P, HC]) for b in range(2)]
        tables_loaded = m.sem("tables_loaded")
        w3_loaded = m.sem("w3_loaded")
        decay_loaded = [m.sem(f"decay_loaded{b}") for b in range(2)]
        u_loaded = [m.sem(f"u_loaded{b}") for b in range(2)]
        gate_loaded = [m.sem(f"gate_loaded{b}") for b in range(2)]
        filt_made = m.sem("filt_made")
        filt_ready = m.sem("filt_ready")
        ends_set = m.sem("ends_set")
        tr_made = m.sem("tr_made")
        tr_copied = m.sem("tr_copied")
        re_made = m.sem("re_made")
        pair_made = m.sem("pair_made")
        sum_step = m.sem("sum_step")
        y_ready = m.sem("y_ready")
        inv_made = m.sem("inv_made")
        z_ready = m.sem("z_ready")
        z_stored = [m.sem(f"z_stored{b}") for b in range(2)]
        N_F = 2 * NT
        ENDS = 2

        def u_src(n, i):
            o, h = PASSES[n]
            rows = (z1 if o else v_x1)[bass.ts(i, HB), bass.ts(h, HC)]
            return rows.rearrange("(j p) c -> p j c", p=P)

        def z_place(n, m_):
            o, h = PASSES[n]
            if o == 0:
                return z1[bass.ts(m_, HB), bass.ts(h, HC)].rearrange("(j p) c -> p j c", p=P), dict(j=HJ)
            return z_T[bass.ts(h, HC), bass.ts(m_, HB)].rearrange("(j p) t -> p j t", p=P), dict(j=HC // P)

        def gate_src(n, m_):
            o, h = PASSES[n]
            if o == 0:
                return v_x1[bass.ts(m_, HB), bass.ds(HY_W + h * HC, HC)].rearrange("(j p) c -> p j c", p=P)
            return x2_T[bass.ts(h, HC), bass.ts(m_, HB)].rearrange("(j p) t -> p j t", p=P)

        with nc.Block() as block:
            @block.sync
            def _(sp):
                sp.dma_start(tr[:, :, :, :, :], transform).then_inc(tables_loaded, 16)
                sp.dma_start(inv[:, :, :, :], inverse).then_inc(tables_loaded, 16)
                n_u = 0
                for what, n, at in program:
                    o, h = PASSES[n]
                    if what == "F":
                        if n:
                            sp.wait_ge(filt_made, N_F * n)
                            sp.wait_ge(ends_set, ENDS * n)
                        cols = w3[:, bass.ds(o * 2 * HY_W, 2 * HY_W)].rearrange("k (d c) -> k d c", d=2)
                        sp.dma_start(w3_sb[:, :, :], cols[:, :, bass.ts(h, HC)]).then_inc(w3_loaded, 16)
                        sp.dma_start(bias_sb[:, :], bias[o:o + 1, bass.ts(h, HC)]).then_inc(w3_loaded, 16)
                        for t in range(NT):
                            if NT * n + t >= 2:
                                sp.wait_ge(filt_ready, N_F * n + 2 * t - 2)
                            sp.dma_start(decay_sb[t % 2][:, :], decay[bass.ts(t, P), bass.ts(h, HC)]).then_inc(decay_loaded[t % 2], 16)
                    elif what == "U":
                        if n_u >= 2:
                            before = [w for w in program if w[0] == "U"][n_u - 2]
                            sp.wait_ge(tr_made, 2 * moved[before] + 2)
                        if o:
                            done = turned_back["Y", n - 2, at] // 2 + 1
                            sp.wait_ge(z_stored[turned_back["Y", n - 2, at] % 2], 16 * done)
                        sp.dma_start(u[n_u % 2][:, :, :], u_src(n, at)).then_inc(u_loaded[n_u % 2], 16)
                        n_u += 1
                    elif what == "Y":
                        e = turned_back[what, n, at]
                        if e >= 2:
                            sp.wait_ge(z_ready, e - 1)
                        src = gate_src(n, at)
                        sp.dma_start(gate[e % 2][:, :].rearrange("p (j x) -> p j x", j=src.shape[1]), src).then_inc(gate_loaded[e % 2], 16)

            @block.gpsimd
            def _(pool):
                for (what, n, at), e in turned_back.items():
                    dst, split = z_place(n, at)
                    pool.wait_ge(z_ready, e + 1)
                    pool.dma_start(dst, z[e % 2][:, :].rearrange("p (j x) -> p j x", **split)).then_inc(z_stored[e % 2], 16)
                for b in range(2):
                    pool.wait_ge(z_stored[b], 16 * len(turned_back) // 2)

            @block.tensor
            def _(pe):
                pe.wait_ge(tables_loaded, 32)
                n_u = 0
                for what, n, at in program:
                    o, h = PASSES[n]
                    if what == "F":
                        pe.wait_ge(w3_loaded, 32 * (n + 1))
                        for t in range(NT):
                            for d in range(2):
                                f = N_F * n + 2 * t + d
                                if f >= 2:
                                    pe.wait_ge(filt_ready, f - 1)
                                nc.tensor.matmul(filt_ps[d][:, :], hid_T[:, bass.ts(t, P)], w3_sb[:, d, :], start=True, stop=True).then_inc(filt_made, 1)
                        continue
                    if what == "Y":
                        e = turned_back[what, n, at]
                        y = Y[at % 2]
                        pe.wait_ge(y_ready, NHB * n + at + 1)
                        if e:
                            pe.wait_ge(z_ready, e)
                        terms = [(c, f) for c in range(2) for f in range(HF)]
                        for j in range(HJ if o == 0 else HC // P):
                            for c, f in terms:
                                if o == 0:
                                    out, lhsT, rhs = inv_ps[:, bass.ts(j, HC)], inv[:, f, c, bass.ts(j, P)], y[:, c, bass.ts(f, HC)]
                                else:
                                    out, lhsT, rhs = inv_ps[:, bass.ts(j, HB)], y[:, c, bass.ds(f * HC + j * P, P)], inv[:, f, c, :]
                                last = nc.tensor.matmul(out, lhsT, rhs, start=((c, f) == terms[0]), stop=((c, f) == terms[-1]))
                        last.then_inc(inv_made, 1)
                        continue
                    q = moved[what, n, at]
                    if what == "U":
                        pe.wait_ge(u_loaded[n_u % 2], 16 * (n_u // 2 + 1))
                        parts = [((COS, COS), (SIN_NEG, SIN_NEG), u[n_u % 2][:, :, :])]
                        n_u += 1
                    else:
                        pe.wait_ge(filt_ready, N_F * (n + 1))
                        pe.wait_ge(ends_set, ENDS * (n + 1))
                        parts = [(re, im, filt[:, d, bass.ts(blk, HJ), :]) for re, im, d, blk in sources(at)]
                    for c in range(2):
                        if q:
                            pe.wait_ge(tr_copied, 2 * q + c - 1)
                        for f in range(HF):
                            terms = [(part[c][f], part[2], j) for part in parts for j in range(HJ)]
                            for x, (kind, src, j) in enumerate(terms):
                                last = nc.tensor.matmul(tr_ps[c][:, bass.ts(f, HC)], tr[:, j, kind, f, :], src[:, j, :],
                                                        start=(x == 0), stop=(x == len(terms) - 1))
                        last.then_inc(tr_made, 1)

            @block.scalar
            def _(act):
                for (what, n, at), q in moved.items():
                    for c in range(2):
                        act.wait_ge(tr_made, 2 * q + c + 1)
                        if n and c == 0:
                            act.wait_ge(pair_made, pair(n - 1, NHB - 1, at) if what == "U" else
                                        pair(n - 1, min(NHB - 1, NHB - 1 + at), NHB - 1 - max(at, 0)))
                        dst = U[at] if what == "U" else K[at]
                        act.activation(dst[:, c, :], tr_ps[c][:, :], ACT.Copy).then_inc(tr_copied, 1)

            @block.vector
            def _(dve):
                n_sum = 0

                def filters(n):
                    if n:
                        dve.wait_ge(tr_made, 2 * moved["K", n - 1, NHB - 1] + 2)
                    for t in range(NT):
                        dve.wait_ge(decay_loaded[t % 2], 16 * (NT // 2 * n + t // 2 + 1))
                        for d in range(2):
                            f = N_F * n + 2 * t + d
                            dve.wait_ge(filt_made, f + 1)
                            dve.tensor_tensor(filt[:, d, t, :], filt_ps[d][:, :], decay_sb[t % 2][:, :], ALU.mult).then_inc(filt_ready, 1)
                    dve.wait_ge(filt_ready, N_F * (n + 1))
                    dve.wait_ge(w3_loaded, 32 * (n + 1))
                    dve.tensor_tensor(filt[0:1, FWD, 0, :], filt[0:1, FWD, 0, :], bias_sb[:, :], ALU.add).then_inc(ends_set, 1)
                    dve.memset(filt[0:1, BWD, 0, :], 0.0).then_inc(ends_set, 1)

                def results(n, m_):
                    e = turned_back["Y", n, m_]
                    dve.wait_ge(inv_made, e + 1)
                    dve.wait_ge(gate_loaded[e % 2], 16 * (e // 2 + 1))
                    if e >= 2:
                        dve.wait_ge(z_stored[e % 2], 16 * (e // 2))
                    dve.tensor_tensor(z[e % 2][:, :], inv_ps[:, :], gate[e % 2][:, :], ALU.mult).then_inc(z_ready, 1)

                filters(0)
                for n in range(NP):
                    for m_ in range(NHB):
                        y = Y[m_ % 2]
                        if NHB * n + m_ >= 2:
                            before = ("Y", n, m_ - 2) if m_ >= 2 else ("Y", n - 1, m_ + NHB - 2)
                            dve.wait_ge(inv_made, turned_back[before] + 1)
                        for i in reversed(range(NHB)):
                            d = m_ - i
                            start = i == NHB - 1
                            dve.wait_ge(tr_copied, 2 * max(moved["U", n, i], moved["K", n, d]) + 2)
                            both = lambda c: U[i][:, c, :].unsqueeze(1).to_broadcast([P, 2, HF * HC])
                            dve.tensor_tensor((y if start else by_re)[:, :, :], K[d][:, :, :], both(0), ALU.mult).then_inc(re_made, 1)
                            dve.tensor_tensor(by_im[:, :, :], K[d][:, ::-1, :], both(1), ALU.mult).then_inc(pair_made, 1)
                            dve.wait_ge(re_made, pair(n, m_, i))
                            if not start:
                                dve.tensor_tensor(y[:, :, :], y[:, :, :], by_re[:, :, :], ALU.add).then_inc(sum_step, 1)
                                n_sum += 1
                                dve.wait_ge(sum_step, n_sum)
                            dve.wait_ge(pair_made, pair(n, m_, i))
                            dve.tensor_tensor(y[:, 0, :], y[:, 0, :], by_im[:, 0, :], ALU.subtract).then_inc(sum_step, 1)
                            dve.tensor_tensor(y[:, 1, :], y[:, 1, :], by_im[:, 1, :], ALU.add).then_inc(y_ready if i == 0 else sum_step, 1)
                            n_sum += 1 if i == 0 else 2
                            dve.wait_ge(sum_step, n_sum) if i else dve.wait_ge(y_ready, NHB * n + m_ + 1)
                        if m_ == 0 and n:
                            results(n - 1, NHB - 1)
                        if m_:
                            results(n, m_ - 1)
                        if m_ == 1 and n + 1 < NP:
                            filters(n + 1)
                results(NP - 1, NHB - 1)


N_EXP2, F_EXP2 = 16, 2 * D
CAP = 2 * T // N_EXP2
MAX_AT_ONCE = 8
TAKEN = -1.0


def expert_choice_phase(nc, h_T, w_router, ident, idx, scale, next_weights):
    NE = N_EXP2
    with Store(nc, "choice") as m:
        w = m.sb("w", [P, ND, NE])
        aff = m.sb("aff", [P, NT, NE])
        best = m.sb("best", [P, NT])
        total = m.sb("total", [P, NT])
        left = m.sb("left", [NE, T])
        top = m.sb("top", [NE, MAX_AT_ONCE])
        chosen = m.sb("chosen", [NE, T])
        ones_T = m.sb("ones_T", [NE, T])
        place = m.sb("place", [NE, T])
        place_t = m.sb("place_t", [P, NT, NE])
        slot = m.sb("slot", [P, CAP])
        what = m.sb("what", [P, NT, NE, 2])
        RING = 4
        hot = [m.sb(f"hot{r}", [P, CAP]) for r in range(RING)]
        logit_ps = m.ps("logit_ps", [P, NT, NE])
        aff_ps = m.ps("aff_ps", [NE, T])
        place_ps = m.ps("place_ps", [P, NT, NE])
        list_ps = m.ps("list_ps", [P, NE, 2])
        loaded = m.sem("loaded")
        made = m.sem("made")
        logits_ready = m.sem("logits_ready")
        diff_ready = m.sem("diff_ready")
        exp_ready = m.sem("exp_ready")
        aff_ready = m.sem("aff_ready")
        aff_turned = m.sem("aff_turned")
        place_ready = m.sem("place_ready")
        place_turned = m.sem("place_turned")
        hot_ready = m.sem("hot_ready")
        hot_used = m.sem("hot_used")
        step = m.sem("step")

        def over_e(x):
            return x.unsqueeze(2).to_broadcast([P, NT, NE])

        with nc.Block() as block:
            @block.sync
            def _(sp):
                sp.dma_start(w[:, :, :], w_router.rearrange("(k p) n -> p k n", p=P)).then_inc(loaded, 16)
                next_weights.load_first(sp)

            @block.gpsimd
            def _(pool):
                pool.iota(slot[:, :], pattern=[[1, CAP]], base=0, channel_multiplier=0, allow_small_or_imprecise_dtypes=True).then_inc(made, 1)
                pool.iota(what[:, :, :, 0], pattern=[[P, NT], [0, NE]], base=0, channel_multiplier=1, allow_small_or_imprecise_dtypes=True).then_inc(made, 1)
                pool.memset(ones_T[:, :], 1.0).then_inc(made, 1)

            @block.tensor
            def _(pe):
                pe.wait_ge(loaded, 16)
                for t in range(NT):
                    for k in range(ND):
                        last = nc.tensor.matmul(logit_ps[:, t, :], h_T[:, k, bass.ts(t, P)], w[:, k, :], start=(k == 0), stop=(k == ND - 1))
                last.then_inc(logits_ready, 1)
                pe.wait_ge(aff_ready, 1)
                for t in range(NT):
                    last = nc.tensor.transpose(aff_ps[:, bass.ts(t, P)], aff[:, t, :], ident[:, :])
                last.then_inc(aff_turned, 1)
                pe.wait_ge(place_ready, 1)
                for t in range(NT):
                    last = nc.tensor.transpose(place_ps[:, t, :], place[:, bass.ts(t, P)], ident[0:NE, 0:NE])
                last.then_inc(place_turned, 1)
                for e in range(NE):
                    for t in range(NT):
                        g = NT * e + t
                        pe.wait_ge(hot_ready, g + 1)
                        nc.tensor.matmul(list_ps[:, e, :], hot[g % RING][:, :], what[:, t, e, :], start=(t == 0), stop=(t == NT - 1)).then_inc(hot_used, 1)

            @block.scalar
            def _(act):
                act.wait_ge(diff_ready, 1)
                act.activation(aff[:, :, :], aff[:, :, :], ACT.Exp).then_inc(exp_ready, 1)

            @block.vector
            def _(dve):
                c = Chain(dve, step)
                dve.wait_ge(made, 3)
                dve.wait_ge(logits_ready, 1)
                c.then(dve.reduce_max(best[:, :], logit_ps[:, :, :], axis=AXX))
                dve.tensor_tensor(aff[:, :, :], logit_ps[:, :, :], over_e(best[:, :]), ALU.subtract).then_inc(diff_ready, 1)
                dve.wait_ge(exp_ready, 1)
                c.then(dve.reduce_sum(total[:, :], aff[:, :, :], axis=AXX))
                c.then(dve.reciprocal(total[:, :], total[:, :]))
                dve.tensor_tensor(aff[:, :, :], aff[:, :, :], over_e(total[:, :]), ALU.mult).then_inc(aff_ready, 1)
                dve.wait_ge(aff_ready, 1)
                c.then(dve.tensor_copy(what[:, :, :, 1], aff[:, :, :]))
                dve.wait_ge(aff_turned, 1)
                c.then(dve.tensor_copy(left[:, :], aff_ps[:, :]))
                for n in range(CAP // MAX_AT_ONCE):
                    c.then(dve.max(top[:, :], left[:, :]))
                    c.then(dve.match_replace(left[:, :], top[:, :], left[:, :], TAKEN))
                c.then(dve.tensor_scalar(chosen[:, :], left[:, :], TAKEN, None, ALU.is_equal))
                c.then(dve.tensor_tensor_scan(place[:, :], ones_T[:, :], chosen[:, :], 0.0, ALU.mult, ALU.add))
                c.then(dve.tensor_tensor(place[:, :], place[:, :], chosen[:, :], ALU.mult))
                dve.tensor_scalar(place[:, :], place[:, :], 1.0, None, ALU.subtract).then_inc(place_ready, 1)
                dve.wait_ge(place_turned, 1)
                c.then(dve.tensor_copy(place_t[:, :, :], place_ps[:, :, :]))
                for e in range(NE):
                    for t in range(NT):
                        g = NT * e + t
                        if g >= RING:
                            dve.wait_ge(hot_used, g - RING + 1)
                        dve.tensor_scalar(hot[g % RING][:, :], slot[:, :], place_t[:, t, e:e + 1], None, ALU.is_equal).then_inc(hot_ready, 1)
                dve.wait_ge(hot_used, NE * NT)
                c.then(dve.tensor_copy(idx[:, :], list_ps[:, :, 0]))
                c.then(dve.tensor_copy(scale[:, :], list_ps[:, :, 1]))


INPUTS = ("x", "norm1_g", "w_in", "gla_gate_w2", "gla_gate_b", "gla_norm_g", "w_out", "norm2_g", "router_group_w", "router_group_b",
          "router_expert_w", "router_expert_b", "expert_w1", "expert_w3", "expert_w2", "final_norm_g", "g_mix_2", "w_in_2", "conv_a_w_2",
          "conv_a_b_2", "lru_w_r_2", "lru_b_r_2", "lru_w_i_2", "lru_b_i_2", "lru_lambda_2", "w_a_out_2", "conv_b_w_2", "conv_b_b_2",
          "filt_w1_2", "filt_b1_2", "filt_w2_2", "filt_b2_2", "filt_w3_2", "filt_freq_2", "filt_bias_2", "w_b_out_2", "w_o_2", "g_ffn_2",
          "w_router_2", "w_gate_2", "w_up_2", "w_down_2", "g_final_2")


def constants():
    return {"gla_masks": gla_level_masks(), "att_bias": attention_bias(), "filt_positions": filter_positions(), "filt_decay": filter_decay(),
            "block_transform": block_transform(), "block_inverse": block_inverse()}


def build_program(nc, a, out):
    def dram(name, shape, dt=F32):
        return nc.dram_tensor(f"tmp_{name}", shape, dt, kind="Internal").ap()

    x1, h2, x2, h3, total = (dram(n, [T, D]) for n in ("x1", "h2", "x2", "h3", "total"))
    row_tok = dram("row_tok", [N_BLK * SLOTS, 1], I32)
    y_rows = dram("y_rows", [N_BLK * SLOTS, D])
    ya_T = dram("ya_T", [LRU_W, T])
    v_x1, x2_T, z1, z_T = dram("v_x1", [T, 2 * HY_W]), dram("x2_T", [HY_W, T]), dram("z1", [T, HY_W]), dram("z_T", [HY_W, T])
    part_T, gate_T = dram("part_T", [D, T]), dram("gate_T", [D, T])

    ident = nc.alloc_sbuf_tensor("ident", [P, P], F32)
    ones_col = nc.alloc_sbuf_tensor("ones_col", [P, 1], F32)
    tables = {"gates": nc.alloc_sbuf_tensor("gates", [P, 2, NT], F32), "dest": nc.alloc_sbuf_tensor("dest", [P, 2 * NT], I32),
              "idx_all": nc.alloc_sbuf_tensor("idx_all", [P, N_BLK], I32), "over_exp": nc.alloc_sbuf_tensor("over_exp", [1, N_OVER], I32),
              "n_over": nc.alloc_sbuf_tensor("n_over", [1, 1], I32)}
    idx2 = nc.alloc_sbuf_tensor("idx2", [P, N_EXP2], I32)
    scale2 = nc.alloc_sbuf_tensor("scale2", [P, N_EXP2], F32)
    Store.used = []
    setup_constants(nc, ident, ones_col)

    with Store(nc, "mixer") as s:
        o_T = s.sb("o_T", [P, ND, T])
        with Store(nc, "mixer_in") as s_in:
            n_T = s_in.sb("n_T", [P, ND, T])
            norm_phase(nc, "norm1", a["x"], a["norm1_g"], ident, transposed=n_T)
            gla_phase(nc, n_T, a["w_in"], a["gla_gate_w2"], a["gla_gate_b"], a["gla_norm_g"], a["gla_masks"], ident, o_T)
            attention_phase(nc, n_T, a["w_in"], a["att_bias"], ident, o_T)
        h2_T = s.sb("h2_T", [P, ND, T])
        residual_norm_phase(nc, "out1", o_T, a["w_out"], a["x"], [x1], a["norm2_g"], ident, h2, h2_T)

        def expert(name):
            view = a[name].rearrange("e (k p) n -> e p k n", p=P)
            return lambda i, c: view[bass.ds(i * PER_STEP + c, 1), :, :, :].rearrange("o p k n -> (o p) k n")
        weights1 = ExpertWeights(nc, "moe1_w", 2, expert("expert_w1"), expert("expert_w3"), expert("expert_w2")).open()
        router_phase(nc, h2_T, a["router_group_w"], a["router_group_b"], a["router_expert_w"], a["router_expert_b"], tables, row_tok, y_rows, weights1)
    expert_phase(nc, "moe1", N_EXP // PER_STEP, weights1, tables["idx_all"], h2, ident, False, y_rows=y_rows)
    weights1.close()
    overflow_phase(nc, a["expert_w1"], a["expert_w3"], a["expert_w2"], tables, h2, y_rows, ident)

    Store.give_back_semaphores(nc)

    with Store(nc, "block2") as s:
        h_T = s.parts("h_T", [P, ND, T])
        combine_phase(nc, x1, y_rows, tables, a["final_norm_g"], a["g_mix_2"], ident, x2, h_T)
        lru_phase(nc, h_T, a["w_in_2"], a["conv_a_w_2"], a["conv_a_b_2"], a["lru_w_r_2"], a["lru_b_r_2"], a["lru_w_i_2"], a["lru_b_i_2"],
                  a["lru_lambda_2"], ident, ya_T)
        hyena_inputs_phase(nc, h_T, a["w_in_2"], a["conv_b_w_2"], a["conv_b_b_2"], ident, v_x1, x2_T)
        gates_phase(nc, h_T, ya_T, a["w_in_2"], a["w_a_out_2"], part_T, gate_T)
    with Store(nc, "long") as s:
        hid_T = s.sb("hid_T", [FILT_HID, T])
        filter_phase(nc, a["filt_positions"], a["filt_w1_2"], a["filt_b1_2"], a["filt_w2_2"], a["filt_b2_2"], a["filt_freq_2"], hid_T)
        hyena_phase(nc, v_x1, x2_T, hid_T, a["filt_w3_2"], a["filt_bias_2"], a["filt_decay"], a["block_transform"], a["block_inverse"], z1, z_T)
    with Store(nc, "merged") as s:
        merged_T = s.sb("merged_T", [P, ND, T])
        merge_phase(nc, z_T, a["w_b_out_2"], part_T, gate_T, merged_T)
        Store.give_back_semaphores(nc)
        h3_T = s.sb("h3_T", [P, ND, T])
        residual_norm_phase(nc, "out2", merged_T, a["w_o_2"], x2, [total], a["g_ffn_2"], ident, h3, h3_T)

        def columns(name):
            view = a[name].rearrange("e (k p) f -> e p k f", p=P)
            return lambda i, c: view[bass.ds(i, 1), :, :, bass.ts(c, CHUNK)].rearrange("o p k f -> (o p) k f")

        def rows(name):
            view = a[name].rearrange("e (k p) d -> e p k d", p=P)
            return lambda i, c: view[bass.ds(i, 1), :, bass.ts(c, CHUNK // P), :].rearrange("o p k d -> (o p) k d")
        weights2 = ExpertWeights(nc, "moe2_w", 2, columns("w_gate_2"), columns("w_up_2"), rows("w_down_2")).open()
        expert_choice_phase(nc, h3_T, a["w_router_2"], ident, idx2, scale2, weights2)
    expert_phase(nc, "moe2", N_EXP2, weights2, idx2, h3, ident, True, scale=scale2, add_to=total)
    weights2.close()
    norm_phase(nc, "norm4", total, a["g_final_2"], ident, natural=out)


def kernel(**inputs):
    import concourse.bacc as bacc
    from concourse.bass_utils import run_bass_kernel_spmd

    nc = bacc.Bacc("TRN2", target_bir_lowering=False, num_devices=1)
    arrays, views = {}, {}
    for name, array in [(n, inputs[n]) for n in INPUTS] + list(constants().items()):
        array = np.ascontiguousarray(array)
        if array.ndim > 1 and array.shape[0] == 1:
            array = array.reshape(array.shape[1:])
        arrays[f"in_{name}_dram"] = array
        views[name] = nc.dram_tensor(f"in_{name}_dram", array.shape, mybir.dt.from_np(array.dtype), kind="ExternalInput").ap()
    out = nc.dram_tensor("out_0_dram", (1, T, D), F32, kind="ExternalOutput").ap()
    build_program(nc, views, out.rearrange("o t d -> (o t) d"))
    results = run_bass_kernel_spmd(nc, [arrays], core_ids=[0])
    return results.results[0]["out_0_dram"]
```

```python
from collections import namedtuple
from contextlib import ExitStack

import numpy as np

import concourse.bass as bass
from concourse import mybir

F32 = mybir.dt.float32
I32 = mybir.dt.int32
U32 = mybir.dt.uint32
F32R = mybir.dt.float32r
ACT = mybir.ActivationFunctionType
ALU = mybir.AluOpType
AXX = mybir.AxisListType.X

P = 128
T = 1024
D = 1024
NT = T // P
ND = D // P
EPS = 1e-6
BANK = 512


class Store:

    used = []

    def __init__(self, nc, name, side="left"):
        self.nc, self.name, self.side, self.stack = nc, name, side, ExitStack()

    def __enter__(self):
        self.stack.__enter__()
        return self

    def __exit__(self, *a):
        return self.stack.__exit__(*a)

    def open(self):
        return self.__enter__()

    def close(self):
        self.stack.close()

    def sb(self, name, shape, dt=F32):
        return self.stack.enter_context(self.nc.sbuf_tensor(f"{self.name}_{name}", shape, dt, side=self.side))

    def parts(self, name, shape):
        return Parts(self, name, self.sb(name, shape))

    def ps(self, name, shape, dt=F32):
        return self.stack.enter_context(self.nc.psum_tensor(f"{self.name}_{name}", shape, dt))

    def sem(self, name):
        Store.used.append(self.nc.alloc_semaphore(f"{self.name}_{name}"))
        return Store.used[-1]

    @staticmethod
    def give_back_semaphores(nc):
        nc.clear_and_free_semaphores(Store.used)
        nc.all_engine_barrier()
        Store.used = []


def first(i):
    return isinstance(i, int) and i == 0


def repeat(engine, n, body):
    body(0)
    with engine.Fori(1, n) as i:
        body(i)


def tile(t):
    return bass.ds(t, 1)


def row(vec):
    return vec.rearrange("(o n) -> o n", o=1)


class Parts:

    def __init__(self, store, name, whole):
        nc = store.nc
        self.whole = whole
        self.upper = store.sb(f"{name}_upper", whole.shape, F32R)
        self.rest = nc.alloc_sbuf_tensor_at(f"{store.name}_{name}_rest", whole.shape, F32R,
                                            offset=nc.lookup_mls(whole).memorylocations[0].addr)


Split = namedtuple("Split", "upper rest")

WHOLE = (slice(None), slice(None), slice(None))


def split(dve, x, at, rounded, n, ready):
    dve.tensor_copy(x.upper[at], x.whole[at]).then_inc(rounded, 1)
    dve.wait_ge(rounded, n)
    dve.tensor_tensor(x.rest[at], x.whole[at], x.upper[at].bitcast(F32), ALU.subtract).then_inc(ready, 1)


def three_passes(lhs, rhs):
    return ((lhs.upper, rhs.upper), (lhs.upper, rhs.rest), (lhs.rest, rhs.upper))


def setup_constants(nc, ident, ones_col):
    cleared = nc.alloc_semaphore("ident_cleared")
    with nc.Block() as block:
        @block.gpsimd
        def _(pool):
            pool.memset(ident[:, :], 0.0).then_inc(cleared, 1)
            pool.memset(ones_col[:, :], 1.0)
            pool.wait_ge(cleared, 1)
            pool.affine_select(out=ident[:, :], in_=ident[:, :], compare_op=ALU.not_equal, fill=1.0,
                               base=0, pattern=[[-1, P]], channel_multiplier=1)


def norm_phase(nc, name, src, gain, ident, natural=None, transposed=None):
    with Store(nc, name) as m:
        xt = [m.sb(f"x{b}", [P, D]) for b in range(2)]
        xn = [m.sb(f"xn{b}", [P, D]) for b in range(2)]
        squares = [m.sb(f"squares{b}", [P, D]) for b in range(2)]
        gain_b = m.sb("gain", [P, D])
        ssum = m.sb("ssum", [P, 2])
        rms = m.sb("rms", [P, 2])
        rstd = m.sb("rstd", [P, 2])
        eps = m.sb("eps", [P, 1])
        turned = [m.ps(f"turned{b}", [P, 2, BANK]) for b in range(2)]
        eps_set = m.sem("eps_set")
        x_loaded = [m.sem(f"x_loaded{b}") for b in range(2)]
        gain_loaded = m.sem("gain_loaded")
        ssum_ready = m.sem("ssum_ready")
        rms_ready = m.sem("rms_ready")
        rstd_ready = m.sem("rstd_ready")
        xn_ready = m.sem("xn_ready")
        xn_turned = m.sem("xn_turned")
        turned_copied = m.sem("turned_copied")
        stored = [m.sem(f"stored{b}") for b in range(2)]
        src_t = src.rearrange("(t p) d -> t p d", p=P)
        nat_t = natural.rearrange("(t p) d -> t p d", p=P) if natural is not None else None
        with nc.Block() as block:
            @block.sync
            def _(sp):
                sp.dma_start(gain_b[:, :], row(gain).partition_broadcast(P)).then_inc(gain_loaded, 16)

                def load(i):
                    for b in range(2):
                        if not first(i):
                            sp.wait_ge(xn_ready, 2 * i + b - 1)
                        sp.dma_start(xt[b][:, :], src_t[tile(2 * i + b), :, :]).then_inc(x_loaded[b], 16)
                repeat(sp, NT // 2, load)

            @block.gpsimd
            def _(pool):
                if natural is None:
                    return
                with pool.Fori(0, NT // 2) as i:
                    for b in range(2):
                        pool.wait_ge(xn_ready, 2 * i + b + 1)
                        pool.dma_start(nat_t[tile(2 * i + b), :, :], xn[b][:, :]).then_inc(stored[b], 16)
                for b in range(2):
                    pool.wait_ge(stored[b], 16 * (NT // 2))

            @block.scalar
            def _(act):
                act.wait_ge(eps_set, 1)
                with act.Fori(0, NT // 2) as i:
                    for b in range(2):
                        act.wait_ge(ssum_ready, 2 * i + b + 1)
                        act.activation(rms[:, b:b + 1], ssum[:, b:b + 1], ACT.Sqrt, scale=1.0 / D, bias=eps[:, :]).then_inc(rms_ready, 1)
                    for b in range(2 if transposed is not None else 0):
                        act.wait_ge(xn_turned, 2 * i + b + 1)
                        act.activation(transposed[:, :, bass.ds((2 * i + b) * P, P)],
                                       turned[b][:, :, :].rearrange("p a (k t) -> p (a k) t", t=P), ACT.Copy).then_inc(turned_copied, 1)

            @block.vector
            def _(dve):
                dve.memset(eps[:, :], EPS).then_inc(eps_set, 1)
                dve.wait_ge(gain_loaded, 16)

                def norm(i):
                    for b in range(2):
                        dve.wait_ge(x_loaded[b], 16 * (i + 1))
                        dve.tensor_tensor_reduce(out=squares[b][:, :], in0=xt[b][:, :], in1=xt[b][:, :], scale=1.0, scalar=0.0, op0=ALU.mult, op1=ALU.add,
                                                 accum_out=ssum[:, b:b + 1]).then_inc(ssum_ready, 1)
                    for b in range(2):
                        dve.wait_ge(rms_ready, 2 * i + b + 1)
                        dve.reciprocal(rstd[:, b:b + 1], rms[:, b:b + 1]).then_inc(rstd_ready, 1)
                        dve.wait_ge(rstd_ready, 2 * i + b + 1)
                        if not first(i):
                            if transposed is not None:
                                dve.wait_ge(xn_turned, 2 * i + b - 1)
                            if natural is not None:
                                dve.wait_ge(stored[b], 16 * i)
                        dve.scalar_tensor_tensor(xn[b][:, :], xt[b][:, :], rstd[:, b:b + 1], gain_b[:, :],
                                                 ALU.mult, ALU.mult).then_inc(xn_ready, 1)
                repeat(dve, NT // 2, norm)

            @block.tensor
            def _(pe):
                if transposed is None:
                    return

                def turn(i):
                    for b in range(2):
                        pe.wait_ge(xn_ready, 2 * i + b + 1)
                        if not first(i):
                            pe.wait_ge(turned_copied, 2 * i + b - 1)
                        for k in range(ND):
                            last = nc.tensor.transpose(turned[b][:, k // 4, bass.ts(k % 4, P)], xn[b][:, bass.ts(k, P)], ident[:, :])
                        last.then_inc(xn_turned, 1)
                repeat(pe, NT // 2, turn)


def residual_norm_phase(nc, name, act_T, w, res, outs, gain, ident, normed, normed_T, next_inputs):
    with Store(nc, name) as m:
        w_p = m.parts("w", [P, ND, D])
        act_p = Parts(m, "act", act_T)
        res_sb = [m.sb(f"res{b}", [P, D]) for b in range(2)]
        x = [m.sb(f"x{b}", [P, D]) for b in range(2)]
        xn = [m.sb(f"xn{b}", [P, D]) for b in range(2)]
        squares = m.sb("squares", [P, D])
        gain_b = m.sb("gain", [P, D])
        ssum = m.sb("ssum", [P, NT])
        rms = m.sb("rms", [P, NT])
        rstd = m.sb("rstd", [P, NT])
        eps = m.sb("eps", [P, 1])
        prod = [m.ps(f"prod{b}", [P, 2, BANK]) for b in range(2)]
        turned = [m.ps(f"turned{b}", [P, 2, BANK]) for b in range(2)]
        w_loaded = [m.sem(f"w_loaded{k}") for k in range(ND)]
        res_loaded = [m.sem(f"res_loaded{b}") for b in range(2)]
        gain_loaded = m.sem("gain_loaded")
        rounded = m.sem("rounded")
        w_split = m.sem("w_split")
        act_split = m.sem("act_split")
        prod_ready = m.sem("prod_ready")
        x_ready = m.sem("x_ready")
        eps_set = m.sem("eps_set")
        ssum_ready = m.sem("ssum_ready")
        rms_ready = m.sem("rms_ready")
        rstd_ready = m.sem("rstd_ready")
        xn_ready = m.sem("xn_ready")
        xn_turned = m.sem("xn_turned")
        copied = m.sem("copied")
        x_stored = [m.sem(f"x_stored{b}") for b in range(2)]
        xn_stored = [m.sem(f"xn_stored{b}") for b in range(2)]
        with nc.Block() as block:
            @block.sync
            def _(sp):
                for k in range(ND):
                    sp.dma_start(w_p.whole[:, k, :], w[bass.ts(k, P), :]).then_inc(w_loaded[k], 16)
                sp.dma_start(gain_b[:, :], row(gain).partition_broadcast(P)).then_inc(gain_loaded, 16)
                for t in range(NT):
                    if t == 2:
                        next_inputs.load(sp)
                    if t >= 2:
                        sp.wait_ge(x_ready, t - 1)
                    sp.dma_start(res_sb[t % 2][:, :], res[bass.ts(t, P), :]).then_inc(res_loaded[t % 2], 16)

            @block.gpsimd
            def _(pool):
                for t in range(NT):
                    b = t % 2
                    pool.wait_ge(x_ready, t + 1)
                    for out in outs:
                        pool.dma_start(out[bass.ts(t, P), :], x[b][:, :]).then_inc(x_stored[b], 16)
                    pool.wait_ge(xn_ready, t + 1)
                    pool.dma_start(normed[bass.ts(t, P), :], xn[b][:, :]).then_inc(xn_stored[b], 16)
                for b in range(2):
                    pool.wait_ge(x_stored[b], 16 * len(outs) * (NT // 2))
                    pool.wait_ge(xn_stored[b], 16 * (NT // 2))

            @block.tensor
            def _(pe):
                def turn(t):
                    pe.wait_ge(xn_ready, t + 1)
                    if t >= 2:
                        pe.wait_ge(copied, t - 1)
                    turn_rows(nc, xn[t % 2], turned[t % 2], ident).then_inc(xn_turned, 1)

                for t in range(NT):
                    pe.wait_ge(act_split, t + 1)
                    if t >= 2:
                        pe.wait_ge(x_ready, t - 1)
                    for k in range(ND):
                        if t == 0:
                            pe.wait_ge(w_split, k + 1)
                        for h in range(2):
                            for n, (lhs, rhs) in enumerate(three_passes(act_p, w_p)):
                                last = nc.tensor.matmul(prod[t % 2][:, h, :], lhs[:, k, bass.ts(t, P)], rhs[:, k, bass.ts(h, BANK)],
                                                        start=(k == 0 and n == 0), stop=(k == ND - 1 and n == 2))
                    last.then_inc(prod_ready, 1)
                    if t:
                        turn(t - 1)
                turn(NT - 1)

            @block.scalar
            def _(act):
                act.wait_ge(eps_set, 1)
                for t in range(NT):
                    act.wait_ge(ssum_ready, t + 1)
                    act.activation(rms[:, t:t + 1], ssum[:, t:t + 1], ACT.Sqrt, scale=1.0 / D, bias=eps[:, :]).then_inc(rms_ready, 1)
                    act.wait_ge(xn_turned, t + 1)
                    act.activation(normed_T[:, :, bass.ts(t, P)], turned[t % 2][:, :, :].rearrange("p a (k q) -> p (a k) q", q=P), ACT.Copy).then_inc(copied, 1)

            @block.vector
            def _(dve):
                dve.memset(eps[:, :], EPS).then_inc(eps_set, 1)

                def split_act(t):
                    split(dve, act_p, (slice(None), slice(None), bass.ts(t, P)), rounded, 1 if t == 0 else ND + 1 + t, act_split)

                split_act(0)
                for k in range(ND):
                    dve.wait_ge(w_loaded[k], 16)
                    split(dve, w_p, (slice(None), k, slice(None)), rounded, k + 2, w_split)
                dve.wait_ge(gain_loaded, 16)
                for t in range(NT):
                    b = t % 2
                    if t + 1 < NT:
                        split_act(t + 1)
                    dve.wait_ge(prod_ready, t + 1)
                    dve.wait_ge(res_loaded[b], 16 * (t // 2 + 1))
                    if t >= 2:
                        dve.wait_ge(x_stored[b], 16 * len(outs) * (t // 2))
                        dve.wait_ge(xn_stored[b], 16 * (t // 2))
                        dve.wait_ge(xn_turned, t - 1)
                    dve.tensor_tensor(x[b][:, :], prod[b][:, :, :].rearrange("p a n -> p (a n)"), res_sb[b][:, :], ALU.add).then_inc(x_ready, 1)
                    dve.wait_ge(x_ready, t + 1)
                    dve.tensor_tensor_reduce(out=squares[:, :], in0=x[b][:, :], in1=x[b][:, :], scale=1.0, scalar=0.0, op0=ALU.mult, op1=ALU.add,
                                             accum_out=ssum[:, t:t + 1]).then_inc(ssum_ready, 1)
                    dve.wait_ge(rms_ready, t + 1)
                    dve.reciprocal(rstd[:, t:t + 1], rms[:, t:t + 1]).then_inc(rstd_ready, 1)
                    dve.wait_ge(rstd_ready, t + 1)
                    dve.scalar_tensor_tensor(xn[b][:, :], x[b][:, :], rstd[:, t:t + 1], gain_b[:, :], ALU.mult, ALU.mult).then_inc(xn_ready, 1)
                    dve.wait_ge(xn_ready, t + 1)


GLA_H, GLA_K, GLA_V, GLA_LOW = 4, 64, 128, 16
GLA_QK = GLA_H * GLA_K
GLA_VW = GLA_H * GLA_V
GLA_TAU = 16.0
ATT_H, ATT_D = 8, 64
ATT_W = ATT_H * ATT_D
COL_GQ, COL_GK, COL_GV, COL_GR = 0, GLA_QK, 2 * GLA_QK, 2 * GLA_QK + GLA_VW
COL_LOW = COL_GR + GLA_VW
COL_AQ = COL_LOW + GLA_LOW
COL_AK, COL_AV = COL_AQ + ATT_W, COL_AQ + 2 * ATT_W
LEVELS = [1 << s for s in range(7)]


def gla_level_masks():
    key, query = np.arange(P)[:, None], np.arange(P)[None, :]
    masks = [(key // (2 * s) == query // (2 * s)) & (key // s % 2 == 0) & (query // s % 2 == 1) for s in LEVELS]
    masks.append(key == query)
    return np.ascontiguousarray(np.stack(masks, axis=1).astype(np.uint32))


def gla_phase(nc, n_T, w_in, gate_w2, gate_b, norm_g, masks, ident, o_T):
    NQ = GLA_QK // P
    RING = 4
    with Store(nc, "gla") as m:
        wqk = m.sb("wqk", [P, ND, 2 * GLA_QK])
        wv = m.sb("wv", [P, ND, GLA_VW])
        wr = m.sb("wr", [P, ND, GLA_VW])
        wlow = m.sb("wlow", [P, ND, GLA_LOW])
        w2 = m.sb("w2", [GLA_LOW, GLA_QK])
        bias = m.sb("bias", [P, NQ])
        ng_b = m.sb("ng", [P, GLA_V])
        mask = m.sb("mask", [P, len(LEVELS) + 1, P], U32)
        q_T = m.sb("q", [P, NQ, T])
        k_T = m.sb("k", [P, NQ, T])
        cum = m.sb("cum", [P, NQ, T])
        t1 = m.sb("t1", [P, NQ, T])
        mix = [m.sb(f"mix{b}", [P, NQ, T]) for b in range(2)]
        v = m.sb("v", [P, NT, GLA_VW])
        gate = m.sb("gate", [P, NT, GLA_VW])
        apart = [o_T[:, GLA_H + 2 * b:GLA_H + 2 * b + 2, :].rearrange("p odd (j q) -> p odd j q", j=NQ) for b in range(2)]
        low_T = mix[1][0:GLA_LOW, 0, :]
        t2 = mix[0]
        score_T = wqk[:, :, :].rearrange("p t (h q) -> p t h q", q=P)
        kd = wv[:, 0:NT // 2, :].rearrange("p a (b c) -> p (a b) c", c=GLA_QK)
        state = wr[:, :, :].rearrange("p a (t v) -> p (a t) v", v=2 * GLA_V).rearrange("p (j t) v -> p j t v", j=NQ)
        a_tile = m.sb("a_tile", [P, NQ, NT])
        o_n = [m.sb(f"o_n{b}", [P, GLA_VW]) for b in range(2)]
        osq = m.sb("osq", [P, GLA_VW])
        ssum = m.sb("ssum", [P, NT, GLA_H])
        rms = m.sb("rms", [P, NT, GLA_H])
        rstd = m.sb("rstd", [P, NT, GLA_H])
        eps = m.sb("eps", [P, 1])
        one = m.sb("one", [P, P])
        two_banks = [m.ps(f"banks{r}", [P, 2, BANK]) for r in range(4)]
        bank = [two_banks[r // 2][:, r % 2, :] for r in range(8)]
        w_loaded = {n: m.sem(n + "_loaded") for n in ("low", "small", "qk", "v", "r", "mask")}
        proj_ready = m.sem("proj_ready")
        proj_read = m.sem("proj_read")
        low_ready = m.sem("low_ready")
        la_step = m.sem("la_step")
        ln_ready = m.sem("ln_ready")
        dve_step = m.sem("dve_step")
        diff_ready = m.sem("diff_ready")
        decay_ready = m.sem("decay_ready")
        mix_ready = m.sem("mix_ready")
        apart_cleared = m.sem("apart_cleared")
        mix_cleared = m.sem("mix_cleared")
        state_cleared = m.sem("state_cleared")
        scored = m.sem("scored")
        picked = m.sem("picked")
        kd_turned = m.sem("kd_turned")
        kd_ready = m.sem("kd_ready")
        update_ready = m.sem("update_ready")
        state_ready = m.sem("state_ready")
        o_ready = m.sem("o_ready")
        osum_ready = m.sem("osum_ready")
        rms_ready = m.sem("rms_ready")
        on_ready = m.sem("on_ready")
        on_turned = m.sem("on_turned")
        o_stored = m.sem("o_stored")
        w_k = w_in.rearrange("(k p) n -> p k n", p=P)
        PROJ = [("low", 0, h) for h in range(2)] + [("z", j, h) for j in range(NQ) for h in range(2)]
        PROJ += [(n, j, h) for n in ("q", "k") for j in range(NQ) for h in range(2)]
        PROJ += [("v", t, 0) for t in range(NT)] + [("r", t, 0) for t in range(NT)]
        N_LOW, N_Z, N_QK = 2, 2 + 2 * NQ, 2 + 6 * NQ
        N_V, N_PROJ = N_QK + NT, N_QK + 2 * NT
        NL = len(LEVELS)
        NG = NT // 2
        AFTER_LEVEL = [N_QK + 2 + 3 * level // 2 for level in range(NL)]
        with nc.Block() as block:
            @block.gpsimd
            def _(pool):
                pool.memset(o_T[:, GLA_H:ND, :], 0.0).then_inc(apart_cleared, 1)
                pool.wait_ge(proj_ready, N_PROJ)
                pool.memset(wr[:, :, :], 0.0).then_inc(state_cleared, 1)

            @block.sync
            def _(sp):
                sp.dma_start(wlow[:, :, :], w_k[:, :, COL_LOW:COL_LOW + GLA_LOW]).then_inc(w_loaded["low"], 16)
                sp.dma_start(w2[:, :], gate_w2).then_inc(w_loaded["small"], 16)
                with nc.allow_non_contiguous_dma(reason="a bias per partition"):
                    sp.dma_start(bias[:, :], gate_b.rearrange("(j p) -> p j", p=P)).then_inc(w_loaded["small"], 16)
                sp.dma_start(ng_b[:, :], row(norm_g).partition_broadcast(P)).then_inc(w_loaded["small"], 16)
                sp.dma_start(wqk[:, :, :], w_k[:, :, COL_GQ:COL_GQ + 2 * GLA_QK]).then_inc(w_loaded["qk"], 16)
                sp.dma_start(wv[:, :, :], w_k[:, :, COL_GV:COL_GV + GLA_VW]).then_inc(w_loaded["v"], 16)
                sp.dma_start(wr[:, :, :], w_k[:, :, COL_GR:COL_GR + GLA_VW]).then_inc(w_loaded["r"], 16)
                sp.dma_start(mask[:, :, :], masks).then_inc(w_loaded["mask"], 16)

            @block.tensor
            def _(pe):
                def level_scores(level):
                    pe.wait_ge(mix_ready, 3 * (level + 1))
                    if level == 0:
                        pe.wait_ge(picked, NT)
                    for u in range(NG):
                        s = NG * level + u
                        if level:
                            pe.wait_ge(picked, NT + s - NG + 1)
                        scores = bank[RING + u].rearrange("p (t odd j q) -> p t odd j q", t=2, odd=2, j=NQ)
                        for t in range(2):
                            for j in range(NQ):
                                last = nc.tensor.matmul(scores[:, t, :, j, :], mix[level % 2][:, j, bass.ts(2 * u + t, P)],
                                                        apart[level % 2][:, :, j, bass.ts(2 * u + t, P // 2)], start=True, stop=True)
                        last.then_inc(scored, 1)

                pe.wait_ge(w_loaded["low"], 16)
                for g, (what, j, h) in enumerate(PROJ):
                    out = bank[g % RING]
                    if g >= RING + N_LOW:
                        pe.wait_ge(proj_read, g - RING - N_LOW + 1)
                    elif g >= RING:
                        pe.wait_ge(low_ready, g - RING + 1)
                    if what == "z":
                        if g == N_LOW:
                            pe.wait_ge(w_loaded["small"], 48)
                            pe.wait_ge(low_ready, 2)
                        last = nc.tensor.matmul(out[:, :], w2[:, bass.ts(j, P)], low_T[:, bass.ts(h, BANK)], start=True, stop=True)
                    else:
                        if g == N_Z:
                            pe.wait_ge(w_loaded["qk"], 16)
                        if g == N_QK:
                            pe.wait_ge(w_loaded["v"], 16)
                        if g == N_QK + 1:
                            pe.wait_ge(proj_read, N_QK - N_LOW)
                            for t in range(NT):
                                if t >= 2:
                                    pe.wait_ge(picked, t - 1)
                                for odd in range(2):
                                    part = slice(odd * GLA_K, (odd + 1) * GLA_K)
                                    for j in range(NQ):
                                        last = nc.tensor.matmul(two_banks[2 + t % 2][:, odd, bass.ts(j, P)], k_T[part, j, bass.ts(t, P)],
                                                                q_T[part, j, bass.ts(t, P)], start=True, stop=True)
                                last.then_inc(scored, 1)
                        if g in AFTER_LEVEL:
                            level_scores(AFTER_LEVEL.index(g))
                        if g == N_V:
                            pe.wait_ge(w_loaded["r"], 16)
                        for k in range(ND):
                            if what == "low":
                                o, lhsT, rhs = out[0:GLA_LOW, :], wlow[:, k, :], n_T[:, k, bass.ts(h, BANK)]
                            elif what in "qk":
                                o, lhsT, rhs = out[:, :], wqk[:, k, bass.ds((what == "k") * GLA_QK + j * P, P)], n_T[:, k, bass.ts(h, BANK)]
                            else:
                                o, lhsT, rhs = out[:, :], n_T[:, k, bass.ts(j, P)], (wv if what == "v" else wr)[:, k, :]
                            last = nc.tensor.matmul(o, lhsT, rhs, start=(k == 0), stop=(k == ND - 1))
                    last.then_inc(proj_ready, 1)

                pe.wait_ge(mix_ready, 3 * NL + 1)
                for t in range(NT):
                    if t >= 2:
                        pe.wait_ge(kd_ready, t - 1)
                    for j in range(NQ):
                        last = nc.tensor.transpose(bank[4 + t % 2][:, bass.ts(j, P)], mix[NL % 2][:, j, bass.ts(t, P)], ident[:, :])
                    last.then_inc(kd_turned, 1)

                pe.wait_ge(proj_read, N_PROJ - N_LOW)
                pe.wait_ge(picked, NT + NG * NL)
                pe.wait_ge(mix_ready, 3 * NL + 2)
                for t in range(NT):
                    b = t % 2
                    pe.wait_ge(kd_ready, t + 1)
                    if t >= 1:
                        pe.wait_ge(state_ready, GLA_H * t)
                    for j in range(NQ):
                        last = nc.tensor.matmul(bank[6][:, bass.ts(j, 2 * GLA_V)], kd[:, t, bass.ts(j, P)], v[:, t, bass.ts(j, 2 * GLA_V)],
                                                start=True, stop=True)
                    last.then_inc(update_ready, 1)
                    if t >= 2:
                        pe.wait_ge(on_ready, t - 1)
                    for j in range(NQ):
                        if t > 0:
                            nc.tensor.matmul(bank[b][:, bass.ts(j, 2 * GLA_V)], mix[(NL + 1) % 2][:, j, bass.ts(t, P)], state[:, j, t, :],
                                             start=True, stop=False)
                        for odd in range(2):
                            hd = 2 * j + odd
                            last = nc.tensor.matmul(bank[b][:, bass.ts(hd, GLA_V)], score_T[:, t, odd * NQ + j, :], v[:, t, bass.ts(hd, GLA_V)],
                                                    start=(t == 0), stop=(t == 0 or odd == 1))
                    last.then_inc(o_ready, 1)
                    for u in ([t - 1] if t else []) + ([t] if t == NT - 1 else []):
                        pe.wait_ge(on_ready, u + 1)
                        if u >= 2:
                            pe.wait_ge(o_stored, u - 1)
                        for hd in range(GLA_H):
                            last = nc.tensor.transpose(bank[2 + u % 2][:, bass.ts(hd, P)], o_n[u % 2][:, bass.ts(hd, P)], ident[:, :])
                        last.then_inc(on_turned, 1)

            @block.scalar
            def _(act):
                act.wait_ge(w_loaded["small"], 48)
                for g in range(N_LOW, N_Z):
                    j, h = PROJ[g][1:]
                    act.wait_ge(proj_ready, g + 1)
                    act.activation(t1[:, j, bass.ts(h, BANK)], bank[g % RING][:, :], ACT.Identity, bias=bias[:, j:j + 1]).then_inc(proj_read, 1)
                act.wait_ge(proj_read, N_Z - N_LOW)
                act.activation(t2[:, :, :], t1[:, :, :], ACT.Abs).then_inc(la_step, 1)
                act.wait_ge(la_step, 1)
                act.activation(t2[:, :, :], t2[:, :, :], ACT.Exp, scale=-1.0).then_inc(la_step, 1)
                act.wait_ge(la_step, 2)
                act.activation(t2[:, :, :], t2[:, :, :], ACT.Ln, bias=one[:, 0:1]).then_inc(ln_ready, 1)

                def decays(level):
                    act.wait_ge(diff_ready, level + 1)
                    halves = t1[:, :, :].rearrange("p j (n two s) -> p (j n) two s", two=2, s=LEVELS[level])
                    act.activation(halves[:, :, 0, :], halves[:, :, 0, :], ACT.Exp, scale=-1.0).then_inc(decay_ready, 1)
                    act.activation(halves[:, :, 1, :], halves[:, :, 1, :], ACT.Exp).then_inc(decay_ready, 1)

                for g in range(N_Z, N_PROJ):
                    what, j, h = PROJ[g]
                    act.wait_ge(proj_ready, g + 1)
                    if what in "qk":
                        act.activation((q_T if what == "q" else k_T)[:, j, bass.ts(h, BANK)], bank[g % RING][:, :], ACT.Copy,
                                       scale=GLA_K ** -0.5 if what == "q" else 1.0).then_inc(proj_read, 1)
                    elif what == "v":
                        act.activation(v[:, j, :], bank[g % RING][:, :], ACT.Copy).then_inc(proj_read, 1)
                    else:
                        act.activation(gate[:, j, :], bank[g % RING][:, :], ACT.Silu).then_inc(proj_read, 1)
                    if g + 2 in AFTER_LEVEL:
                        decays(AFTER_LEVEL.index(g + 2))
                act.wait_ge(diff_ready, NL + 1)
                act.activation(t1[:, :, :], t1[:, :, :], ACT.Exp, scale=-1.0).then_inc(decay_ready, 1)
                ends = cum[:, :, :].rearrange("p j (t c) -> p j t c", c=P)[:, :, :, P - 1]
                act.activation(a_tile[:, :, :], ends, ACT.Exp).then_inc(decay_ready, 1)
                act.wait_ge(decay_ready, 2 * NL + 2)
                act.activation(cum[:, :, :], cum[:, :, :], ACT.Exp).then_inc(decay_ready, 1)
                for t in range(NT):
                    act.wait_ge(kd_turned, t + 1)
                    act.activation(kd[:, t, :], bank[4 + t % 2][:, 0:GLA_QK], ACT.Copy).then_inc(kd_ready, 1)
                for t in range(NT):
                    act.wait_ge(o_ready, t + 1)
                    for hd in range(GLA_H):
                        last = act.activation(osq[:, bass.ts(hd, GLA_V)], bank[t % 2][:, bass.ts(hd, GLA_V)], ACT.Square, accum_out=ssum[:, t, hd:hd + 1])
                    last.then_inc(osum_ready, 1)
                    act.wait_ge(osum_ready, t + 1)
                    act.activation(rms[:, t, :], ssum[:, t, :], ACT.Sqrt, scale=1.0 / GLA_V, bias=eps[:, :]).then_inc(rms_ready, 1)
                    for u in ([t - 1] if t else []) + ([t] if t == NT - 1 else []):
                        act.wait_ge(on_turned, u + 1)
                        act.activation(o_T[:, 0:GLA_H, bass.ts(u, P)], bank[2 + u % 2][:, :].rearrange("p (h t) -> p h t", t=P),
                                       ACT.Copy).then_inc(o_stored, 1)

            @block.vector
            def _(dve):
                dve.memset(eps[:, :], EPS).then_inc(dve_step, 1)
                dve.memset(one[:, :], 1.0).then_inc(dve_step, 1)
                n = 2
                for h in range(N_LOW):
                    dve.wait_ge(proj_ready, h + 1)
                    dve.tensor_copy(low_T[:, bass.ts(h, BANK)], bank[h][0:GLA_LOW, :]).then_inc(low_ready, 1)
                dve.wait_ge(proj_ready, N_Z)
                dve.memset(mix[1][:, :, :], 0.0).then_inc(mix_cleared, 1)
                dve.wait_ge(ln_ready, 1)
                dve.tensor_scalar(t1[:, :, :], t1[:, :, :], 0.0, None, ALU.min).then_inc(dve_step, 1)
                n += 1
                dve.wait_ge(dve_step, n)
                dve.tensor_tensor(t1[:, :, :], t1[:, :, :], t2[:, :, :], ALU.subtract).then_inc(dve_step, 1)
                n += 1
                dve.wait_ge(dve_step, n)
                dve.tensor_scalar(t2[:, :, :], t1[:, :, :], 1.0 / GLA_TAU, None, ALU.mult).then_inc(dve_step, 1)
                n += 1
                dve.wait_ge(dve_step, n)
                for j in range(NQ):
                    for t in range(NT):
                        dve.tensor_tensor_scan(cum[:, j, bass.ts(t, P)], one[:, :], t2[:, j, bass.ts(t, P)], 0.0, ALU.mult, ALU.add).then_inc(dve_step, 1)
                        n += 1
                dve.wait_ge(proj_ready, N_QK)
                dve.memset(wqk[:, :, :], 0.0).then_inc(dve_step, 1)
                n += 1
                dve.wait_ge(dve_step, n)
                dve.wait_ge(w_loaded["mask"], 16)
                for t in range(NT):
                    dve.wait_ge(scored, t + 1)
                    dve.copy_predicated(score_T[:, t, :, :].rearrange("p (o j) q -> p o j q", o=2),
                                        mask[:, NL:NL + 1, :].unsqueeze(1).to_broadcast([P, 2, NQ, P]),
                                        two_banks[2 + t % 2][:, :, 0:NQ * P].rearrange("p o (j q) -> p o j q", q=P)).then_inc(picked, 1)

                def level_diff(s):
                    blocks = cum[:, :, :].rearrange("p j (n b) -> p (j n) b", b=2 * s)
                    middle = blocks[:, :, s - 1:s].to_broadcast([P, NQ * T // (2 * s), 2 * s])
                    dve.tensor_tensor(t1[:, :, :].rearrange("p j (n b) -> p (j n) b", b=2 * s), blocks, middle, ALU.subtract).then_inc(diff_ready, 1)

                def pick(level):
                    s = LEVELS[level]
                    for u in range(NG):
                        g = NG * level + u
                        dve.wait_ge(scored, NT + g + 1)
                        later = score_T[:, 2 * u:2 * u + 2, :, :].rearrange("p t h (n two s) -> p (t h) n two s", two=2, s=s)[:, :, :, 1, :]
                        pairs = mask[:, level, :].rearrange("p (n two s) -> p n two s", two=2, s=s)[:, :, 1, :]
                        dve.copy_predicated(later, pairs.unsqueeze(1).to_broadcast([P, 2 * GLA_H, P // (2 * s), s]),
                                            bank[RING + u].rearrange("p (h n s) -> p h n s", h=2 * GLA_H, s=s)).then_inc(picked, 1)

                dve.wait_ge(apart_cleared, 1)
                dve.wait_ge(mix_cleared, 1)
                for level, s in enumerate(LEVELS):
                    if level:
                        dve.wait_ge(mix_ready, 3 * level)
                    level_diff(s)
                    if level:
                        pick(level - 1)
                    dve.wait_ge(decay_ready, 2 * (level + 1))

                    def half(array, h):
                        return array.rearrange("p j (n two s) -> p (j n) two s", two=2, s=s)[:, :, h, :]
                    if level >= 2:
                        dve.wait_ge(scored, NT + NG * (level - 1))
                    dve.tensor_tensor(half(mix[level % 2][:, :, :], 0), half(k_T[:, :, :], 0), half(t1[:, :, :], 0), ALU.mult).then_inc(mix_ready, 1)
                    for odd in range(2):
                        part = slice(odd * GLA_K, (odd + 1) * GLA_K)
                        dve.tensor_tensor(apart[level % 2][part, odd, :, :].rearrange("p j (n s) -> p (j n) s", s=s),
                                          half(q_T[part, :, :], 1), half(t1[part, :, :], 1), ALU.mult).then_inc(mix_ready, 1)
                dve.wait_ge(mix_ready, 3 * NL)
                tiles = cum[:, :, :].rearrange("p j (t c) -> p (j t) c", c=P)
                dve.tensor_tensor(t1[:, :, :].rearrange("p j (t c) -> p (j t) c", c=P), tiles,
                                  tiles[:, :, P - 1:P].to_broadcast([P, NQ * NT, P]), ALU.subtract).then_inc(diff_ready, 1)
                pick(NL - 1)
                dve.wait_ge(decay_ready, 2 * NL + 3)
                dve.tensor_tensor(mix[NL % 2][:, :, :], k_T[:, :, :], t1[:, :, :], ALU.mult).then_inc(mix_ready, 1)
                dve.tensor_tensor(mix[(NL + 1) % 2][:, :, :], q_T[:, :, :], cum[:, :, :], ALU.mult).then_inc(mix_ready, 1)
                dve.wait_ge(proj_read, N_PROJ - N_LOW)
                dve.tensor_tensor(gate[:, :, :].rearrange("p t (h v) -> p (t h) v", v=GLA_V), gate[:, :, :].rearrange("p t (h v) -> p (t h) v", v=GLA_V),
                                  ng_b[:, :].rearrange("p (o v) -> p o v", o=1).to_broadcast([P, NT * GLA_H, GLA_V]), ALU.mult).then_inc(dve_step, 1)
                n += 1
                dve.wait_ge(state_cleared, 1)
                for t in range(NT):
                    dve.wait_ge(update_ready, t + 1)
                    if t:
                        dve.wait_ge(state_ready, GLA_H * t)
                    for hd in range(GLA_H):
                        j, part, cols = hd // 2, slice((hd % 2) * GLA_K, (hd % 2 + 1) * GLA_K), slice((hd % 2) * GLA_V, (hd % 2 + 1) * GLA_V)
                        new = bank[6][part, bass.ts(hd, GLA_V)]
                        if t == 0:
                            dve.tensor_copy(state[part, j, 1, cols], new).then_inc(state_ready, 1)
                        elif t + 1 < NT:
                            dve.scalar_tensor_tensor(state[part, j, t + 1, cols], state[part, j, t, cols], a_tile[part, j, t:t + 1], new,
                                                     ALU.mult, ALU.add).then_inc(state_ready, 1)
                    dve.wait_ge(rms_ready, t + 1)
                    dve.reciprocal(rstd[:, t, :], rms[:, t, :]).then_inc(dve_step, 1)
                    n += 1
                    if t >= 2:
                        dve.wait_ge(on_turned, t - 1)
                    dve.wait_ge(dve_step, n)
                    for hd in range(GLA_H):
                        cols = bass.ts(hd, GLA_V)
                        last = dve.scalar_tensor_tensor(o_n[t % 2][:, cols], bank[t % 2][:, cols], rstd[:, t, hd:hd + 1], gate[:, t, cols], ALU.mult, ALU.mult)
                    last.then_inc(on_ready, 1)


DILATIONS = ((128, 1), (512, 4), (2048, 16))
MASKED = -1e30


def attention_bias():
    q = np.arange(P)[:, None, None]
    back = (np.arange(NT - 1, -1, -1)[None, :, None] * P + q - np.arange(P)[None, None, :])
    count = sum(((back >= 0) & (back <= w) & (back % d == 0)).astype(np.int64) for w, d in DILATIONS)
    return np.where(count > 0, np.log(np.maximum(count, 1)), MASKED).astype(np.float32).reshape(P, T)


def attention_phase(nc, n_T, w_in, bias, ident, o_T):
    PAIRS = ATT_H // 2
    NSTEP = 2 * NT
    NEED = [n % NT + 1 for n in range(NSTEP)]
    with Store(nc, "att") as m:
        n_parts = Parts(m, "n_T", n_T)
        w = {n: m.parts("w" + n, [P, ND, P]) for n in "qkv"}
        q_T = Split(m.sb("q_upper", [P, T], F32R), m.sb("q_rest", [P, T], F32R))
        keys = Split(m.sb("k_upper", [P, 2, T], F32R), m.sb("k_rest", [P, 2, T], F32R))
        zeros = m.sb("zeros", [P, T])
        v_T = m.sb("vT", [P, T])
        v = m.sb("v", [P, NT, P])
        bias_sb = m.sb("bias", [P, T])
        logit = [m.sb(f"logit{b}", [P, T]) for b in range(2)]
        prob = [m.sb(f"prob{b}", [P, T]) for b in range(2)]
        prob_T = [m.sb(f"probT{b}", [P, NT, P]) for b in range(2)]
        top = m.sb("top", [P, NSTEP])
        neg_top = m.sb("neg_top", [P, NSTEP])
        den = m.sb("den", [P, NSTEP])
        rden = m.sb("rden", [P, NSTEP])
        o_rows = m.sb("o_rows", [P, NT, P])
        score = [m.ps(f"score{b}", [P, 2, BANK]) for b in range(2)]
        turned = m.ps("turned", [P, 2, BANK])
        o_ps = [m.ps(f"o{b}", [P, BANK]) for b in range(2)]
        w_loaded = {n: m.sem(f"w{n}_loaded") for n in "qkv"}
        w_rounded = m.sem("w_rounded")
        w_split = m.sem("w_split")
        n_rounded = m.sem("n_rounded")
        n_split = m.sem("n_split")
        bias_loaded = m.sem("bias_loaded")
        proj_ready = m.sem("proj_ready")
        qk_rounded = m.sem("qk_rounded")
        qk_read = m.sem("qk_read")
        v_copied = m.sem("v_copied")
        zeros_ready = m.sem("zeros_ready")
        keys_cleared = m.sem("keys_cleared")
        v_turned = m.sem("v_turned")
        v_ready = m.sem("v_ready")
        score_ready = m.sem("score_ready")
        top_found = m.sem("top_found")
        top_ready = m.sem("top_ready")
        prob_ready = m.sem("prob_ready")
        prob_turned = m.sem("prob_turned")
        probT_ready = m.sem("probT_ready")
        o_ready = m.sem("o_ready")
        rden_ready = m.sem("rden_ready")
        o_normed = m.sem("o_normed")
        o_turned = m.sem("o_turned")
        o_stored = m.sem("o_stored")
        w_k = w_in.rearrange("(k p) n -> p k n", p=P)
        PROJ = [(n, h) for n in "qkv" for h in range(2)]
        proj_bank = [score[g // 2 % 2][:, g % 2, :] for g in range(len(PROJ))]
        NP = len(PROJ)
        with nc.Block() as block:
            HEAD_ROWS = [slice(hd * ATT_D, (hd + 1) * ATT_D) for hd in range(2)]

            @block.gpsimd
            def _(pool):
                pool.memset(zeros[:, :], 0.0).then_inc(zeros_ready, 1)

            @block.sync
            def _(sp):
                def load(i):
                    if not first(i):
                        sp.wait_ge(proj_ready, NP * i)
                    for n, col in (("q", COL_AQ), ("k", COL_AK), ("v", COL_AV)):
                        sp.dma_start(w[n].whole[:, :, :], w_k[:, :, bass.ds(i * P + col, P)]).then_inc(w_loaded[n], 16)
                    if first(i):
                        sp.dma_start(bias_sb[:, :], bias).then_inc(bias_loaded, 16)
                repeat(sp, PAIRS, load)

            @block.tensor
            def _(pe):
                def pair(i):
                    base = NSTEP * i
                    if not first(i):
                        pe.wait_ge(top_found, base)
                    for g, (n, h) in enumerate(PROJ):
                        if h == 0:
                            pe.wait_ge(w_split, 3 * i + g // 2 + 1)
                        if g >= 4:
                            pe.wait_ge(qk_read, 4 * i + g - 3)
                        for k in range(ND):
                            if first(i) and g == 0:
                                pe.wait_ge(n_split, k + 1)
                            for x, (w_part, n_part) in enumerate(three_passes(w[n], n_parts)):
                                last = nc.tensor.matmul(proj_bank[g], w_part[:, k, :], n_part[:, k, bass.ts(h, BANK)],
                                                        start=(k == 0 and x == 0), stop=(k == ND - 1 and x == 2))
                        last.then_inc(proj_ready, 1)
                    pe.wait_ge(qk_read, 4 * (i + 1))
                    pe.wait_ge(v_copied, 2 * (i + 1))
                    if first(i):
                        pe.wait_ge(keys_cleared, 4)
                    if not first(i):
                        pe.wait_ge(o_stored, 2 * i)
                    for c in range(2):
                        for j in range(4):
                            last = nc.tensor.transpose(turned[:, c, bass.ts(j, P)], v_T[:, bass.ts(4 * c + j, P)], ident[:, :])
                        last.then_inc(v_turned, 1)

                    def scores(n):
                        hd, t = n // NT, n % NT
                        if n >= 2:
                            pe.wait_ge(top_found, base + n - 1)
                        for c in range(2):
                            width = min(max(NEED[n] * P - c * BANK, 0), BANK)
                            if width:
                                for x, (q_part, k_part) in enumerate(three_passes(q_T, keys)):
                                    last = nc.tensor.matmul(score[n % 2][:, c, 0:width], q_part[:, bass.ts(t, P)],
                                                            k_part[:, hd, c * BANK:c * BANK + width], start=(x == 0), stop=(x == 2))
                        last.then_inc(score_ready, 1)

                    def turn(n):
                        pe.wait_ge(prob_ready, base + n + 1)
                        if n == 0:
                            pe.wait_ge(v_ready, 2 * (i + 1))
                        else:
                            pe.wait_ge(probT_ready, base + n)
                        for j in range(NEED[n]):
                            last = nc.tensor.transpose(turned[:, j // 4, bass.ts(j % 4, P)], prob[n % 2][:, bass.ts(j, P)], ident[:, :])
                        last.then_inc(prob_turned, 1)

                    def weigh(n):
                        hd = n // NT
                        pe.wait_ge(probT_ready, base + n + 1)
                        if not (first(i) and n < 2):
                            pe.wait_ge(o_normed, base + n - 1)
                        for j in range(NEED[n]):
                            last = nc.tensor.matmul(o_ps[n % 2][:, 0:ATT_D], prob_T[n % 2][:, j, :], v[:, j, bass.ts(hd, ATT_D)],
                                                    start=(j == 0), stop=(j == NEED[n] - 1))
                        last.then_inc(o_ready, 1)

                    for n in range(NSTEP + 2):
                        if n < NSTEP:
                            scores(n)
                        if 1 <= n <= NSTEP:
                            turn(n - 1)
                        if n >= 2:
                            weigh(n - 2)
                    pe.wait_ge(o_normed, base + NSTEP)
                    for c in range(2):
                        for j in range(4):
                            last = nc.tensor.transpose(turned[:, c, bass.ts(j, P)], o_rows[:, 4 * c + j, :], ident[:, :])
                        last.then_inc(o_turned, 1)
                repeat(pe, PAIRS, pair)

            @block.scalar
            def _(act):
                for k in range(ND):
                    act.activation(n_parts.upper[:, k, :], n_parts.whole[:, k, :], ACT.Copy).then_inc(n_rounded, 1)

                def pair(i):
                    base = NSTEP * i
                    for g, (n, h) in enumerate(PROJ):
                        act.wait_ge(proj_ready, NP * i + g + 1)
                        cols = bass.ts(h, BANK)
                        if n == "q":
                            act.activation(q_T.upper[:, cols], proj_bank[g], ACT.Copy, scale=ATT_D ** -0.5).then_inc(qk_rounded, 1)
                        elif n == "k":
                            for hd, rows in enumerate(HEAD_ROWS):
                                last = act.activation(keys.upper[rows, hd, cols], proj_bank[g][rows, :], ACT.Copy)
                            last.then_inc(qk_rounded, 1)
                        else:
                            act.activation(v_T[:, cols], proj_bank[g], ACT.Copy).then_inc(v_copied, 1)
                    for c in range(2):
                        act.wait_ge(v_turned, 2 * i + c + 1)
                        act.activation(v[:, bass.ts(c, 4), :], turned[:, c, :].rearrange("p (j d) -> p j d", d=P), ACT.Copy).then_inc(v_ready, 1)

                    def copy_probs(n):
                        act.wait_ge(prob_turned, base + n + 1)
                        if not (first(i) and n < 2):
                            act.wait_ge(o_ready, base + n - 1)
                        act.activation(prob_T[n % 2][:, 0:NEED[n], :], turned[:, :, :].rearrange("p c (j q) -> p (c j) q", q=P)[:, 0:NEED[n], :],
                                       ACT.Copy).then_inc(probT_ready, 1)

                    for n in range(NSTEP):
                        if n >= 1:
                            copy_probs(n - 1)
                        act.wait_ge(top_ready, base + n + 1)
                        if not (first(i) and n < 2):
                            act.wait_ge(prob_turned, base + n - 1)
                        act.activation(prob[n % 2][:, 0:NEED[n] * P], logit[n % 2][:, 0:NEED[n] * P], ACT.Exp, bias=neg_top[:, n:n + 1],
                                       accum_out=den[:, n:n + 1]).then_inc(prob_ready, 1)
                    copy_probs(NSTEP - 1)
                    for c in range(2):
                        act.wait_ge(o_turned, 2 * i + c + 1)
                        act.activation(o_T[:, tile(i + GLA_VW // P), bass.ts(c, BANK)], turned[:, c, :], ACT.Copy).then_inc(o_stored, 1)
                repeat(act, PAIRS, pair)

            @block.vector
            def _(dve):
                def split_w(x, i):
                    n = "qkv"[x]
                    dve.wait_ge(w_loaded[n], 16 * (i + 1))
                    split(dve, w[n], WHOLE, w_rounded, 3 * i + x + 1, w_split)

                for k in range(ND):
                    dve.wait_ge(n_rounded, k + 1)
                    dve.tensor_tensor(n_parts.rest[:, k, :], n_parts.whole[:, k, :], n_parts.upper[:, k, :].bitcast(F32), ALU.subtract).then_inc(n_split, 1)
                    if k == 1:
                        split_w(0, 0)
                dve.wait_ge(zeros_ready, 1)
                for part in keys:
                    for hd, rows in enumerate(HEAD_ROWS):
                        dve.tensor_copy(part[rows, 1 - hd, :], zeros[rows, :]).then_inc(keys_cleared, 1)
                dve.wait_ge(bias_loaded, 16)

                def pair(i):
                    base = NSTEP * i
                    for x in range(1 if first(i) else 0, 3):
                        split_w(x, i)
                    for g in range(4):
                        n, h = PROJ[g]
                        cols = bass.ts(h, BANK)
                        dve.wait_ge(qk_rounded, 4 * i + g + 1)
                        if n == "q":
                            dve.scalar_tensor_tensor(q_T.rest[:, cols], proj_bank[g], ATT_D ** -0.5, q_T.upper[:, cols].bitcast(F32),
                                                     ALU.mult, ALU.subtract).then_inc(qk_read, 1)
                        else:
                            for hd, rows in enumerate(HEAD_ROWS):
                                last = dve.tensor_tensor(keys.rest[rows, hd, cols], proj_bank[g][rows, :], keys.upper[rows, hd, cols].bitcast(F32), ALU.subtract)
                            last.then_inc(qk_read, 1)

                    def normed(n):
                        hd, t = n // NT, n % NT
                        dve.wait_ge(prob_ready, base + n + 1)
                        dve.reciprocal(rden[:, n:n + 1], den[:, n:n + 1]).then_inc(rden_ready, 1)
                        dve.wait_ge(rden_ready, base + n + 1)
                        dve.wait_ge(o_ready, base + n + 1)
                        if n == 0 and not first(i):
                            dve.wait_ge(o_turned, 2 * i)
                        dve.tensor_scalar(o_rows[:, t, bass.ts(hd, ATT_D)], o_ps[n % 2][:, 0:ATT_D], rden[:, n:n + 1], None, ALU.mult).then_inc(o_normed, 1)

                    for n in range(NSTEP):
                        cols = NEED[n] * P
                        dve.wait_ge(score_ready, base + n + 1)
                        if not (first(i) and n < 2):
                            dve.wait_ge(prob_ready, base + n - 1)
                        dve.memset(neg_top[:, n:n + 1], 0.0)
                        dve.tensor_tensor_reduce(out=logit[n % 2][:, 0:cols], in0=score[n % 2][:, :, :].rearrange("p c k -> p (c k)")[:, 0:cols],
                                                 in1=bias_sb[:, T - cols:T], scale=1.0, scalar=MASKED, op0=ALU.add, op1=ALU.max,
                                                 accum_out=top[:, n:n + 1]).then_inc(top_found, 1)
                        dve.wait_ge(top_found, base + n + 1)
                        dve.tensor_scalar(neg_top[:, n:n + 1], top[:, n:n + 1], -1.0, None, ALU.mult).then_inc(top_ready, 1)
                        if n >= 2:
                            normed(n - 2)
                    normed(NSTEP - 2)
                    normed(NSTEP - 1)
                repeat(dve, PAIRS, pair)


N_EXP, N_GRP, F_EXP = 32, 4, 512
PER_GRP = N_EXP // N_GRP
SLOTS = P
N_OVER = 2 * T // SLOTS - 1
N_BLK = N_EXP + N_OVER
BIG = 1e30


class Chain:

    def __init__(self, engine, sem):
        self.engine, self.sem, self.n = engine, sem, 0

    def then(self, instruction):
        instruction.then_inc(self.sem, 1)
        self.n += 1
        self.engine.wait_ge(self.sem, self.n)


class RouterInputs(Store):

    def __init__(self, nc, name, ws, bs):
        super().__init__(nc, name, side="right")
        self.ws, self.bs = ws, bs

    def open(m):
        super().open()
        m.w = m.sb("w", [P, ND, sum(w.shape[1] for w in m.ws)])
        m.bias = m.sb("bias", [P, max(1, sum(b.shape[0] for b in m.bs))])
        m.loaded = m.sem("loaded")
        m.all_loaded = 16 * (len(m.ws) + len(m.bs))
        return m

    def load(m, sp):
        at = 0
        for w in m.ws:
            sp.dma_start(m.w[:, :, at:at + w.shape[1]], w.rearrange("(k p) n -> p k n", p=P)).then_inc(m.loaded, 16)
            at += w.shape[1]
        at = 0
        for b in m.bs:
            sp.dma_start(m.bias[:, at:at + b.shape[0]], row(b).partition_broadcast(P)).then_inc(m.loaded, 16)
            at += b.shape[0]


def add_logits(m, n):
    m.logit_T = m.sb("logit_T", [n, T])
    m.logit_T_ps = m.ps("logit_T_ps", [n, T])
    m.logit_T_made = m.sem("logit_T_made")
    m.logit_T_copied = m.sem("logit_T_copied")


def router_logits(nc, pe, m, h_T, w, out, ident, ready):
    n = w.shape[2]
    for h in range(2):
        for k in range(ND):
            last = nc.tensor.matmul(m.logit_T_ps[:, bass.ts(h, BANK)], w[:, k, :], h_T[:, k, bass.ts(h, BANK)], start=(k == 0), stop=(k == ND - 1))
        last.then_inc(m.logit_T_made, 1)
    for t in range(NT):
        if t % (NT // 2) == 0:
            pe.wait_ge(m.logit_T_copied, t // (NT // 2) + 1)
        last = nc.tensor.transpose(out[:, t, :], m.logit_T[:, bass.ts(t, P)], ident[0:n, 0:n])
    last.then_inc(ready, 1)


def copy_logits(act, m):
    for h in range(2):
        act.wait_ge(m.logit_T_made, h + 1)
        act.activation(m.logit_T[:, bass.ts(h, BANK)], m.logit_T_ps[:, bass.ts(h, BANK)], ACT.Copy).then_inc(m.logit_T_copied, 1)


def router_phase(nc, h_T, inputs, ident, tables, row_tok, y_rows, next_weights):
    gates, dest, idx_all, over_exp, n_over = (tables[n] for n in ("gates", "dest", "idx_all", "over_exp", "n_over"))
    NG4, NE = N_GRP, N_EXP
    with Store(nc, "router") as m:
        w, bias, loaded = inputs.w, inputs.bias, inputs.loaded
        g = m.sb("g", [P, NT, NG4])
        e = m.sb("e", [P, NT, NE])
        g_hot = m.sb("g_hot", [P, NT, NG4])
        gt = m.sb("gt", [P, NT, NG4])
        best = m.sb("best", [P, NT])
        where = m.sb("where", [P, NT])
        g_sum = m.sb("g_sum", [P, NT])
        hot = [m.sb(f"hot{j}", [P, NT, NE]) for j in range(2)]
        value = [m.sb(f"value{j}", [P, NT]) for j in range(2)]
        te = m.sb("te", [P, NT, NE])
        ratio = m.sb("ratio", [P, NT])
        both = m.sb("both", [P, NT, NE])
        pos = m.sb("pos", [P, NT, NE])
        earlier = m.sb("earlier", [P, NT + 1, NE])
        over = m.sb("over", [P, NE])
        over_end = m.sb("over_end", [P, NE])
        jump = m.sb("jump", [P, NE])
        ones_e = m.sb("ones_e", [P, NE])
        ones_sq = m.sb("ones_sq", [P, P])
        before = m.sb("before", [P, P])
        down4 = m.sb("down4", [P, NG4])
        down32 = m.sb("down32", [P, NE])
        first_row = m.sb("first_row", [P, NE])
        blk = m.sb("blk", [1, N_OVER])
        cmp = m.sb("cmp", [1, N_OVER, NE])
        cnt = m.sb("cnt", [1, N_OVER])
        dest_f = m.sb("dest_f", [P, NT, 2])
        tok = m.sb("tok", [P, NT], I32)
        zero = m.sb("zero", [P, N_BLK], I32)
        zero_rows = m.sb("zero_rows", [P, D])
        rows_cleared = m.sem("rows_cleared")
        y_cleared = m.sem("y_cleared")
        logit_ps = m.ps("logit", [P, NT, NG4 + NE])
        pos_ps = m.ps("pos_ps", [P, BANK])
        tot_ps = m.ps("tot_ps", [P, BANK])
        made = m.sem("made")
        zeroed = m.sem("zeroed")
        logits_ready = m.sem("logits_ready")
        diff_ready = m.sem("diff_ready")
        exp_ready = m.sem("exp_ready")
        both_ready = m.sem("both_ready")
        pos_ready = m.sem("pos_ready")
        step = m.sem("step")
        dest_ready = m.sem("dest_ready")
        listed = m.sem("listed")
        idx_loaded = m.sem("idx_loaded")

        def over_e(x):
            return x.unsqueeze(2).to_broadcast([P, NT, NE])

        def over_t(x, n):
            return x.unsqueeze(1).to_broadcast([P, NT, n])

        add_logits(m, NG4 + NE)
        with nc.Block() as block:
            @block.sync
            def _(sp):
                next_weights.load_first(sp)
                sp.wait_ge(rows_cleared, 1)
                sp.dma_start(y_rows[N_EXP * SLOTS:, :].rearrange("(b p) d -> p b d", p=P),
                             zero_rows[:, :].unsqueeze(1).to_broadcast([P, N_OVER, D])).then_inc(y_cleared, 16)
                sp.wait_ge(y_cleared, 16)

            @block.gpsimd
            def _(pool):
                pool.memset(zero_rows[:, :], 0.0).then_inc(rows_cleared, 1)
                pool.iota(down4[:, :], pattern=[[-1, NG4]], base=NG4, channel_multiplier=0, allow_small_or_imprecise_dtypes=True).then_inc(made, 1)
                pool.iota(down32[:, :], pattern=[[-1, NE]], base=NE, channel_multiplier=0, allow_small_or_imprecise_dtypes=True).then_inc(made, 1)
                pool.iota(first_row[:, :], pattern=[[SLOTS, NE]], base=0, channel_multiplier=0, allow_small_or_imprecise_dtypes=True).then_inc(made, 1)
                pool.iota(blk[:, :], pattern=[[1, N_OVER]], base=0, channel_multiplier=0, allow_small_or_imprecise_dtypes=True).then_inc(made, 1)
                pool.iota(tok[:, :], pattern=[[P, NT]], base=0, channel_multiplier=1).then_inc(made, 1)
                pool.memset(ones_e[:, :], 1.0).then_inc(made, 1)
                pool.memset(ones_sq[:, :], 1.0).then_inc(made, 1)
                pool.memset(zero[:, :], 0).then_inc(made, 1)
                pool.wait_ge(made, 8)
                pool.affine_select(out=before[:, :], in_=ones_sq[:, :], compare_op=ALU.is_gt, fill=0.0, base=0, pattern=[[1, P]],
                                   channel_multiplier=-1).then_inc(made, 1)
                pool.dma_start(row_tok.rearrange("(p b) o -> p (b o)", p=P), zero[:, :]).then_inc(zeroed, 16)
                pool.wait_ge(zeroed, 16)
                pool.wait_ge(dest_ready, 1)
                for t in range(NT):
                    for j in range(2):
                        pool.indirect_dma_start(out=row_tok, out_offset=bass.IndirectOffsetOnAxis(ap=dest[:, 2 * t + j:2 * t + j + 1], axis=0),
                                                in_=tok[:, t:t + 1], in_offset=None).then_inc(listed, 16)
                pool.wait_ge(listed, 16 * 2 * NT)
                with nc.allow_non_contiguous_dma(reason="a row number per partition"):
                    pool.dma_start(idx_all[:, :], row_tok.rearrange("(b p) o -> p (b o)", p=P)).then_inc(idx_loaded, 16)
                pool.wait_ge(idx_loaded, 16)

            @block.tensor
            def _(pe):
                pe.wait_ge(loaded, inputs.all_loaded)
                router_logits(nc, pe, m, h_T, w, logit_ps, ident, logits_ready)
                pe.wait_ge(both_ready, 1)
                pe.wait_ge(made, 9)
                every = both[:, :, :].rearrange("p t n -> p (t n)")
                nc.tensor.matmul(pos_ps[:, 0:NT * NE], before[:, :], every, start=True, stop=True)
                nc.tensor.matmul(tot_ps[:, 0:NT * NE], ones_sq[:, :], every, start=True, stop=True).then_inc(pos_ready, 1)

            @block.scalar
            def _(act):
                copy_logits(act, m)
                act.wait_ge(diff_ready, 1)
                act.activation(gt[:, :, :], gt[:, :, :], ACT.Exp).then_inc(exp_ready, 1)
                act.wait_ge(diff_ready, 2)
                act.activation(ratio[:, :], ratio[:, :], ACT.Exp).then_inc(exp_ready, 1)

            @block.vector
            def _(dve):
                c = Chain(dve, step)
                dve.wait_ge(loaded, inputs.all_loaded)
                dve.wait_ge(made, 9)
                dve.wait_ge(logits_ready, 1)
                logits = logit_ps
                c.then(dve.tensor_tensor(g[:, :, :], logits[:, :, 0:NG4], over_t(bias[:, 0:NG4], NG4), ALU.add))
                c.then(dve.tensor_tensor(e[:, :, :], logits[:, :, NG4:], over_t(bias[:, NG4:], NE), ALU.add))
                c.then(dve.reduce_max(best[:, :], g[:, :, :], axis=AXX))
                b4 = best[:, :].unsqueeze(2).to_broadcast([P, NT, NG4])
                dve.tensor_tensor(gt[:, :, :], g[:, :, :], b4, ALU.subtract).then_inc(diff_ready, 1)
                c.then(dve.tensor_tensor(g_hot[:, :, :], g[:, :, :], b4, ALU.is_ge))
                c.then(dve.tensor_tensor(g_hot[:, :, :], g_hot[:, :, :], over_t(down4[:, :], NG4), ALU.mult))
                c.then(dve.reduce_max(where[:, :], g_hot[:, :, :], axis=AXX))
                c.then(dve.tensor_tensor(g_hot[:, :, :], over_t(down4[:, :], NG4), where[:, :].unsqueeze(2).to_broadcast([P, NT, NG4]), ALU.is_equal))
                dve.wait_ge(exp_ready, 1)
                c.then(dve.reduce_sum(g_sum[:, :], gt[:, :, :], axis=AXX))
                hot8 = g_hot[:, :, :].rearrange("p t g -> p (t g)").unsqueeze(2).to_broadcast([P, NT * NG4, PER_GRP])
                e8 = e[:, :, :].rearrange("p t (g n) -> p (t g) n", n=PER_GRP)
                c.then(dve.tensor_tensor(e8, e8, hot8, ALU.mult))
                c.then(dve.tensor_scalar(g_hot[:, :, :], g_hot[:, :, :], 1.0, BIG, ALU.subtract, ALU.mult))
                c.then(dve.tensor_tensor(e8, e8, hot8, ALU.add))
                for j in range(2):
                    c.then(dve.reduce_max(value[j][:, :], e[:, :, :], axis=AXX))
                    c.then(dve.tensor_tensor(te[:, :, :], e[:, :, :], over_e(value[j][:, :]), ALU.is_ge))
                    c.then(dve.tensor_tensor(te[:, :, :], te[:, :, :], over_t(down32[:, :], NE), ALU.mult))
                    c.then(dve.reduce_max(where[:, :], te[:, :, :], axis=AXX))
                    c.then(dve.tensor_tensor(hot[j][:, :, :], over_t(down32[:, :], NE), over_e(where[:, :]), ALU.is_equal))
                    if j == 0:
                        c.then(dve.scalar_tensor_tensor(e[:, :, :], hot[0][:, :, :], -BIG, e[:, :, :], ALU.mult, ALU.add))
                dve.tensor_tensor(both[:, :, :], hot[0][:, :, :], hot[1][:, :, :], ALU.add).then_inc(both_ready, 1)
                dve.tensor_tensor(ratio[:, :], value[1][:, :], value[0][:, :], ALU.subtract).then_inc(diff_ready, 1)
                dve.wait_ge(exp_ready, 2)
                c.then(dve.tensor_scalar(best[:, :], ratio[:, :], 1.0, None, ALU.add))
                c.then(dve.tensor_tensor(best[:, :], best[:, :], g_sum[:, :], ALU.mult))
                c.then(dve.reciprocal(gates[:, 0, :], best[:, :]))
                c.then(dve.tensor_tensor(gates[:, 1, :], gates[:, 0, :], ratio[:, :], ALU.mult))
                dve.wait_ge(pos_ready, 1)
                tots = tot_ps[:, 0:NT * NE].rearrange("p (t n) -> p t n", n=NE)
                c.then(dve.memset(earlier[:, 0, :], 0.0))
                for t in range(NT):
                    c.then(dve.tensor_tensor(earlier[:, t + 1, :], earlier[:, t, :], tots[:, t, :], ALU.add))
                total = earlier[:, NT, :]
                c.then(dve.tensor_tensor(pos[:, :, :], pos_ps[:, 0:NT * NE].rearrange("p (t n) -> p t n", n=NE), earlier[:, 0:NT, :], ALU.add))
                c.then(dve.tensor_scalar(over[:, :], total, float(SLOTS), None, ALU.is_gt))
                for n in range(2, T // SLOTS):
                    c.then(dve.scalar_tensor_tensor(over[:, :], total, float(n * SLOTS), over[:, :], ALU.is_gt, ALU.add))
                c.then(dve.tensor_tensor_scan(over_end[:, :], ones_e[:, :], over[:, :], 0.0, ALU.mult, ALU.add))
                c.then(dve.tensor_tensor(jump[:, :], over_end[:, :], over[:, :], ALU.subtract))
                c.then(dve.tensor_scalar(jump[:, :], jump[:, :], float(SLOTS), float((N_EXP - 1) * SLOTS), ALU.mult, ALU.add))
                c.then(dve.tensor_tensor(jump[:, :], jump[:, :], first_row[:, :], ALU.subtract))
                c.then(dve.tensor_scalar(te[:, :, :], pos[:, :, :], float(SLOTS), None, ALU.is_ge))
                c.then(dve.tensor_tensor(te[:, :, :], te[:, :, :], over_t(jump[:, :], NE), ALU.mult))
                c.then(dve.tensor_tensor(te[:, :, :], te[:, :, :], pos[:, :, :], ALU.add))
                c.then(dve.tensor_tensor(te[:, :, :], te[:, :, :], over_t(first_row[:, :], NE), ALU.add))
                for j in range(2):
                    c.then(dve.tensor_tensor(hot[j][:, :, :], hot[j][:, :, :], te[:, :, :], ALU.mult))
                    c.then(dve.reduce_sum(dest_f[:, :, j], hot[j][:, :, :], axis=AXX))
                dve.tensor_copy(dest[:, :], dest_f[:, :, :].rearrange("p t j -> p (t j)")).then_inc(dest_ready, 1)
                c.then(dve.tensor_tensor(cmp[:, :, :], over_end[0:1, :].unsqueeze(1).to_broadcast([1, N_OVER, NE]),
                                         blk[:, :].unsqueeze(2).to_broadcast([1, N_OVER, NE]), ALU.is_le))
                c.then(dve.reduce_sum(cnt[:, :], cmp[:, :, :], axis=AXX))
                c.then(dve.tensor_scalar(over_exp[:, :], cnt[:, :], float(N_EXP - 1), None, ALU.min))
                c.then(dve.tensor_copy(n_over[:, :], over_end[0:1, NE - 1:NE]))


CHUNK = F_EXP
PER_STEP = 4


class ExpertWeights(Store):

    def __init__(self, nc, name, n_buffers, w1_of, w3_of, w2_of):
        super().__init__(nc, name, side="right")
        self.n_buffers, self.w1_of, self.w3_of, self.w2_of = n_buffers, w1_of, w3_of, w2_of

    def __enter__(m):
        super().__enter__()
        m.w1 = [m.sb(f"w1_{b}", [P, ND, CHUNK]) for b in range(m.n_buffers)]
        m.w3 = [m.sb(f"w3_{b}", [P, ND, CHUNK]) for b in range(m.n_buffers)]
        m.w2 = [m.sb(f"w2_{b}", [P, CHUNK // P, D]) for b in range(m.n_buffers)]
        m.w1_loaded = [m.sem(f"w1_loaded{b}") for b in range(m.n_buffers)]
        m.w3_loaded = [m.sem(f"w3_loaded{b}") for b in range(m.n_buffers)]
        m.w2_loaded = [m.sem(f"w2_loaded{b}") for b in range(m.n_buffers)]
        return m

    def load_first(m, sp):
        for b in range(m.n_buffers):
            sp.dma_start(m.w1[b][:, :, :], m.w1_of(0, b)).then_inc(m.w1_loaded[b], 16)
            sp.dma_start(m.w3[b][:, :, :], m.w3_of(0, b)).then_inc(m.w3_loaded[b], 16)
            sp.dma_start(m.w2[b][:, :, :], m.w2_of(0, b)).then_inc(m.w2_loaded[b], 16)


class ExpertStore(Store):

    def __init__(self, nc, name, n_x, weights=None):
        super().__init__(nc, name)
        self.n_x, self.weights = n_x, weights

    def __enter__(m):
        super().__enter__()
        m.idx = m.sb("idx", [P, 1], I32)
        m.rows = [m.sb(f"rows{b}", [P, D]) for b in range(m.n_x)]
        m.x_T = [m.sb(f"xT{b}", [P, ND, SLOTS]) for b in range(m.n_x)]
        if m.weights:
            m.w1 = [Parts(m, f"w1_{b}", m.weights.w1[b]) for b in range(2)]
            m.w3 = [Parts(m, f"w3_{b}", m.weights.w3[b]) for b in range(2)]
            m.x = [Parts(m, f"x{b}", m.x_T[b]) for b in range(m.n_x)]
            m.w_rounded = m.sem("w_rounded")
            m.w_split = m.sem("w_split")
            m.x_rounded = m.sem("x_rounded")
            m.x_split = m.sem("x_split")
        m.silu = m.sb("silu", [P, CHUNK])
        m.hid = m.sb("hid", [P, CHUNK])
        m.hid_T = m.sb("hidT", [P, CHUNK // P, SLOTS])
        m.y = [m.sb(f"y{b}", [P, D]) for b in range(2)]
        m.gate_ps = m.ps("gate_ps", [P, CHUNK])
        m.up_ps = m.ps("up_ps", [P, CHUNK])
        m.hT_ps = m.ps("hT_ps", [P, BANK])
        m.xT_ps = m.ps("xT_ps", [P, 2, BANK])
        m.y_ps = m.ps("y_ps", [P, 2, BANK])
        m.idx_ready = m.sem("idx_ready")
        m.lists_taken = m.sem("lists_taken")
        m.x_turned = m.sem("x_turned")
        m.xT_ready = m.sem("xT_ready")
        m.gate_ready = m.sem("gate_ready")
        m.up_ready = m.sem("up_ready")
        m.silu_ready = m.sem("silu_ready")
        m.hid_ready = m.sem("hid_ready")
        m.hid_turned = m.sem("hid_turned")
        m.hidT_ready = m.sem("hidT_ready")
        m.y_ready = m.sem("y_ready")
        m.y_read = m.sem("y_read")
        m.rows_loaded = [m.sem(f"rows_loaded{b}") for b in range(m.n_x)]
        m.y_stored = [m.sem(f"y_stored{b}") for b in range(2)]
        return m


def up_product(nc, passes, out):
    for k in range(ND):
        for n, (x_T, w) in enumerate(passes):
            last = nc.tensor.matmul(out[:, :], x_T[:, k, :], w[:, k, :], start=(k == 0 and n == 0), stop=(k == ND - 1 and n == len(passes) - 1))
    return last


def turn_rows(nc, rows, out, ident):
    for k in range(ND):
        last = nc.tensor.transpose(out[:, k // 4, bass.ts(k % 4, P)], rows[:, bass.ts(k, P)], ident[:, :])
    return last


def turn_hidden(nc, m, ident):
    for k in range(CHUNK // P):
        last = nc.tensor.transpose(m.hT_ps[:, bass.ts(k, P)], m.hid[:, bass.ts(k, P)], ident[:, :])
    return last


def down_product(nc, w2, m, start, stop):
    for h in range(2):
        for k in range(CHUNK // P):
            last = nc.tensor.matmul(m.y_ps[:, h, :], m.hid_T[:, k, :], w2[:, k, bass.ts(h, BANK)],
                                    start=(start and k == 0), stop=(stop and k == CHUNK // P - 1))
    return last


def expert_phase(nc, name, n_steps, weights, idx_all, src, ident, shared_x, y_rows=None, scale=None, add_to=None):
    n_chunks = n_steps * PER_STEP
    n_groups = n_steps if shared_x else n_chunks
    with ExpertStore(nc, name, 1 if shared_x else 2, weights) as m:
        nx = m.n_x

        def group(i, c):
            return i if shared_x else PER_STEP * i + c

        with nc.Block() as block:
            @block.sync
            def _(sp):
                def load_w2(i, c):
                    b = c % 2
                    sp.wait_ge(m.y_ready, PER_STEP * i + c - 1)
                    sp.dma_start(weights.w2[b][:, :, :], weights.w2_of(i, c)).then_inc(weights.w2_loaded[b], 16)

                def step(i):
                    for c in range(PER_STEP):
                        q, b = PER_STEP * i + c, c % 2
                        if not (first(i) and c < 2):
                            sp.wait_ge(m.gate_ready, q - 1)
                            sp.dma_start(weights.w1[b][:, :, :], weights.w1_of(i, c)).then_inc(weights.w1_loaded[b], 16)
                            sp.wait_ge(m.up_ready, q - 1)
                            sp.dma_start(weights.w3[b][:, :, :], weights.w3_of(i, c)).then_inc(weights.w3_loaded[b], 16)
                        if not (first(i) and c < 3):
                            load_w2(*((i, c - 1) if c else (i - 1, PER_STEP - 1)))

                repeat(sp, n_steps, step)
                load_w2(n_steps - 1, PER_STEP - 1)

            @block.gpsimd
            def _(pool):
                def gather(g, b, nth):
                    if not (isinstance(g, int) and g < nx):
                        pool.wait_ge(m.x_turned, g - nx + 1)
                    pool.tensor_copy(m.idx[:, :], idx_all[:, tile(g)]).then_inc(m.idx_ready, 1)
                    pool.wait_ge(m.idx_ready, nth)
                    pool.sem_inc(m.lists_taken, 1)
                    pool.indirect_dma_start(out=m.rows[b][:, :], out_offset=None, in_=src,
                                            in_offset=bass.IndirectOffsetOnAxis(ap=m.idx[:, 0:1], axis=0)).then_inc(m.rows_loaded[b], 16)

                if not shared_x:
                    def step(i):
                        for c in range(PER_STEP):
                            g = PER_STEP * i + c
                            if not (first(i) and c == 0):
                                pool.wait_ge(m.rows_loaded[(c - 1) % 2], 16 * (2 * i + (c + 1) // 2))
                            gather(g, c % 2, g + 1)
                    repeat(pool, n_steps, step)
                    return

                def scatter(g, b, nth, n_same):
                    pool.wait_ge(m.y_read, g + 1)
                    pool.tensor_copy(m.idx[:, :], idx_all[:, tile(g)]).then_inc(m.idx_ready, 1)
                    pool.wait_ge(m.idx_ready, nth)
                    pool.sem_inc(m.lists_taken, 1)
                    pool.indirect_dma_start(out=add_to, out_offset=bass.IndirectOffsetOnAxis(ap=m.idx[:, 0:1], axis=0),
                                            in_=m.y[b][:, :], in_offset=None, compute_op=ALU.add).then_inc(m.y_stored[b], 16)
                    pool.wait_ge(m.y_stored[b], 16 * n_same)

                gather(0, 0, 1)
                pool.wait_ge(m.rows_loaded[0], 16)
                gather(1, 0, 2)
                pool.wait_ge(m.rows_loaded[0], 32)

                with pool.Fori(0, n_steps // 2 - 1) as i:
                    for b in range(2):
                        scatter(2 * i + b, b, 4 * i + 2 * b + 3, i + 1)
                        gather(2 * i + b + 2, 0, 4 * i + 2 * b + 4)
                        pool.wait_ge(m.rows_loaded[0], 16 * (2 * i + b + 3))
                for b in range(2):
                    scatter(n_steps - 2 + b, b, 2 * n_steps - 1 + b, n_steps // 2)

            @block.tensor
            def _(pe):
                def turn_x(g, b, nth):
                    pe.wait_ge(m.rows_loaded[b], 16 * nth)
                    if not (isinstance(g, int) and g == 0):
                        pe.wait_ge(m.xT_ready, g)
                    turn_rows(nc, m.rows[b], m.xT_ps, ident).then_inc(m.x_turned, 1)

                def turn_hid(q):
                    pe.wait_ge(m.hid_ready, q + 1)
                    turn_hidden(nc, m, ident).then_inc(m.hid_turned, 1)

                def down(q, i, c):
                    pe.wait_ge(weights.w2_loaded[c % 2], 16 * (2 * i + c // 2 + 1))
                    pe.wait_ge(m.hidT_ready, q + 1)
                    start, stop = not shared_x or c == 0, not shared_x or c == PER_STEP - 1
                    if start:
                        g = i if shared_x else q
                        if not (isinstance(g, int) and g == 0):
                            pe.wait_ge(m.y_read, g)
                    down_product(nc, weights.w2[c % 2], m, start, stop).then_inc(m.y_ready, 1)

                def step(i):
                    for c in range(PER_STEP):
                        q, b = PER_STEP * i + c, c % 2
                        x = m.x[b % nx]
                        before = None if first(i) and c == 0 else (q - 1, i if c else i - 1, (c - 1) % PER_STEP)
                        pe.wait_ge(m.x_split, group(i, c) + 1)
                        pe.wait_ge(m.w_split, 2 * q + 1)
                        if before:
                            pe.wait_ge(m.silu_ready, q)
                        up_product(nc, three_passes(x, m.w1[b]), m.gate_ps).then_inc(m.gate_ready, 1)
                        if before:
                            turn_hid(before[0])
                        pe.wait_ge(m.w_split, 2 * q + 2)
                        up_product(nc, three_passes(x, m.w3[b]), m.up_ps).then_inc(m.up_ready, 1)
                        if not shared_x:
                            if c < PER_STEP - 1 or not (isinstance(i, int) and i == n_steps - 1):
                                turn_x(q + 1, (c + 1) % 2, 2 * i + (c + 1) // 2 + 1)
                        elif c == PER_STEP - 1 and not (isinstance(i, int) and i == n_steps - 1):
                            turn_x(i + 1, 0, i + 2)
                        if before:
                            down(*before)

                turn_x(0, 0, 1)
                step(0)
                with pe.Fori(1, n_steps - 1) as i:
                    step(i)
                step(n_steps - 1)
                turn_hid(n_chunks - 1)
                down(n_chunks - 1, n_steps - 1, PER_STEP - 1)

            @block.scalar
            def _(act):
                def copy_x(g, b):
                    act.wait_ge(m.x_turned, g + 1)
                    act.activation(m.x_T[b][:, :, :], m.xT_ps[:, :, :].rearrange("p a (k s) -> p (a k) s", s=SLOTS), ACT.Copy).then_inc(m.xT_ready, 1)

                def store_y(q, b):
                    act.wait_ge(m.y_read, q + 1)
                    act.dma_start(y_rows[bass.ds(q * SLOTS, SLOTS), :], m.y[b][:, :]).then_inc(m.y_stored[b], 16)

                def copy_hid(q):
                    act.wait_ge(m.hid_turned, q + 1)
                    act.activation(m.hid_T[:, :, :], m.hT_ps[:, :].rearrange("p (k s) -> p k s", s=SLOTS), ACT.Copy).then_inc(m.hidT_ready, 1)

                def step(i):
                    for c in range(PER_STEP):
                        q = PER_STEP * i + c
                        last = isinstance(i, int) and i == n_steps - 1
                        act.wait_ge(m.gate_ready, q + 1)
                        if not (first(i) and c == 0):
                            act.wait_ge(m.hid_ready, q)
                        act.activation(m.silu[:, :], m.gate_ps[:, :], ACT.Silu).then_inc(m.silu_ready, 1)
                        if not (first(i) and c == 0):
                            copy_hid(q - 1)
                        if not shared_x and not (last and c == PER_STEP - 1):
                            copy_x(q + 1, (c + 1) % 2)
                        if not shared_x and not (first(i) and c < 2):
                            store_y(q - 2, c % 2)
                        if shared_x and c == PER_STEP - 1 and not last:
                            copy_x(i + 1, 0)

                copy_x(0, 0)
                step(0)
                with act.Fori(1, n_steps - 1) as i:
                    step(i)
                step(n_steps - 1)
                copy_hid(n_chunks - 1)
                if not shared_x:
                    for q in range(n_chunks - 2, n_chunks):
                        store_y(q, q % 2)
                    for b in range(2):
                        act.wait_ge(m.y_stored[b], 16 * n_chunks // 2)

            @block.vector
            def _(dve):
                def split_w(i, c, which=(0, 1)):
                    q, b = PER_STEP * i + c, c % 2
                    for n in which:
                        w, loaded, used = ((m.w1, weights.w1_loaded, m.gate_ready), (m.w3, weights.w3_loaded, m.up_ready))[n]
                        dve.wait_ge(loaded[b], 16 * (2 * i + c // 2 + 1))
                        if not (first(i) and c < 2):
                            dve.wait_ge(used, q - 1)
                        split(dve, w[b], WHOLE, m.w_rounded, 2 * q + n + 1, m.w_split)

                def split_x(g, b):
                    dve.wait_ge(m.xT_ready, g + 1)
                    split(dve, m.x[b], WHOLE, m.x_rounded, g + 1, m.x_split)

                def split_next_w(i, c):
                    if c < PER_STEP - 1:
                        split_w(i, c + 1)
                    elif not (isinstance(i, int) and i == n_steps - 1):
                        split_w(i + 1, 0)

                split_w(0, 0, (0,))
                split_x(0, 0)
                split_w(0, 0, (1,))

                def hidden(q):
                    dve.wait_ge(m.silu_ready, q + 1)
                    dve.wait_ge(m.up_ready, q + 1)
                    if not (isinstance(q, int) and q == 0):
                        dve.wait_ge(m.hid_turned, q)
                    dve.tensor_tensor(m.hid[:, :], m.up_ps[:, :], m.silu[:, :], ALU.mult).then_inc(m.hid_ready, 1)

                def results(g, q, b, nth):
                    dve.wait_ge(m.y_ready, q + 1)
                    if not (isinstance(nth, int) and nth == 1):
                        dve.wait_ge(m.y_stored[b], 16 * (nth - 1))
                    y = m.y_ps[:, :, :].rearrange("p a n -> p (a n)")
                    if scale is None:
                        dve.tensor_copy(m.y[b][:, :], y).then_inc(m.y_read, 1)
                    else:
                        dve.tensor_scalar(m.y[b][:, :], y, scale[:, tile(g)], None, ALU.mult).then_inc(m.y_read, 1)

                if shared_x:
                    def two_steps(i):
                        for b in range(2):
                            g = 2 * i + b
                            for c in range(PER_STEP):
                                split_next_w(g, c)
                                hidden(PER_STEP * g + c)
                                if c == PER_STEP - 1 and not (isinstance(g, int) and g == n_steps - 1):
                                    split_x(g + 1, 0)
                                if c == 0 and not (first(i) and b == 0):
                                    results(g - 1, PER_STEP * g - 1, 1 - b, i + b)
                    two_steps(0)
                    two_steps(1)
                    with dve.Fori(2, n_steps // 2 - 1) as i:
                        two_steps(i)
                    two_steps(n_steps // 2 - 1)
                    results(n_steps - 1, n_chunks - 1, 1, n_steps // 2)
                else:
                    def step(i):
                        for c in range(PER_STEP):
                            q = PER_STEP * i + c
                            split_next_w(i, c)
                            hidden(q)
                            if not (isinstance(q, int) and q == n_chunks - 1):
                                split_x(q + 1, (c + 1) % 2)
                            if not (first(i) and c == 0):
                                results(q - 1, q - 1, (c - 1) % 2, 2 * i + (c + 1) // 2)
                    step(0)
                    with dve.Fori(1, n_steps - 1) as i:
                        step(i)
                    step(n_steps - 1)
                    results(n_chunks - 1, n_chunks - 1, 1, n_chunks // 2)


def overflow_phase(nc, w1, w3, w2, tables, src, y_rows, ident):
    idx_all, over_exp, n_over = tables["idx_all"], tables["over_exp"], tables["n_over"]
    with ExpertWeights(nc, "over_w", 1, None, None, None) as w, ExpertStore(nc, "over", 1) as m:
        w1_v, w3_v = (x.rearrange("e (k p) f -> e p k f", p=P) for x in (w1, w3))
        w2_v = w2.rearrange("e (k p) d -> e p k d", p=P)

        def where_needed(engine, body, after=None):
            n = engine.value_load(n_over[0:1, 0:1], min_val=0, max_val=N_OVER)
            with engine.If(n > 0):
                repeat(engine, N_OVER, body)
                if after:
                    after()

        with nc.Block() as block:
            @block.sync
            def _(sp):
                def load(j):
                    e = sp.value_load(over_exp[0:1, tile(j)], min_val=0, max_val=N_EXP - 1)
                    if not first(j):
                        sp.wait_ge(m.y_ready, j)
                        sp.wait_ge(w.w1_loaded[0], 16)
                    sp.dma_start(w.w1[0][:, :, :], w1_v[tile(e), :, :, :].rearrange("o p k f -> (o p) k f")).then_inc(w.w1_loaded[0], 16)
                    sp.dma_start(w.w3[0][:, :, :], w3_v[tile(e), :, :, :].rearrange("o p k f -> (o p) k f")).then_inc(w.w3_loaded[0], 16)
                    sp.dma_start(w.w2[0][:, :, :], w2_v[tile(e), :, :, :].rearrange("o p k f -> (o p) k f")).then_inc(w.w2_loaded[0], 16)
                    sp.wait_ge(m.y_read, j + 1)
                    sp.dma_start(y_rows[bass.ds((j + N_EXP) * SLOTS, SLOTS), :], m.y[0][:, :]).then_inc(m.y_stored[0], 16)
                where_needed(sp, load, lambda: sp.wait_ge(m.y_stored[0], 16 * N_OVER))

            @block.gpsimd
            def _(pool):

                def gather(j):
                    if not first(j):
                        pool.wait_ge(m.x_turned, j)
                    pool.tensor_copy(m.idx[:, :], idx_all[:, tile(j + N_EXP)]).then_inc(m.idx_ready, 1)
                    pool.wait_ge(m.idx_ready, j + 1)
                    pool.sem_inc(m.lists_taken, 1)
                    pool.indirect_dma_start(out=m.rows[0][:, :], out_offset=None, in_=src,
                                            in_offset=bass.IndirectOffsetOnAxis(ap=m.idx[:, 0:1], axis=0)).then_inc(m.rows_loaded[0], 16)
                    pool.wait_ge(m.rows_loaded[0], 16 * (j + 1))
                where_needed(pool, gather)

            @block.tensor
            def _(pe):
                def products(j):
                    pe.wait_ge(m.rows_loaded[0], 16 * (j + 1))
                    turn_rows(nc, m.rows[0], m.xT_ps, ident).then_inc(m.x_turned, 1)
                    pe.wait_ge(m.xT_ready, j + 1)
                    pe.wait_ge(w.w1_loaded[0], 16 * (j + 1))
                    up_product(nc, [(m.x_T[0], w.w1[0])], m.gate_ps).then_inc(m.gate_ready, 1)
                    pe.wait_ge(w.w3_loaded[0], 16 * (j + 1))
                    up_product(nc, [(m.x_T[0], w.w3[0])], m.up_ps).then_inc(m.up_ready, 1)
                    pe.wait_ge(m.hid_ready, j + 1)
                    turn_hidden(nc, m, ident).then_inc(m.hid_turned, 1)
                    pe.wait_ge(m.hidT_ready, j + 1)
                    pe.wait_ge(w.w2_loaded[0], 16 * (j + 1))
                    if not first(j):
                        pe.wait_ge(m.y_read, j)
                    down_product(nc, w.w2[0], m, True, True).then_inc(m.y_ready, 1)
                where_needed(pe, products)

            @block.scalar
            def _(act):
                def middle(j):
                    act.wait_ge(m.x_turned, j + 1)
                    act.activation(m.x_T[0][:, :, :], m.xT_ps[:, :, :].rearrange("p a (k s) -> p (a k) s", s=SLOTS), ACT.Copy).then_inc(m.xT_ready, 1)
                    act.wait_ge(m.gate_ready, j + 1)
                    act.activation(m.silu[:, :], m.gate_ps[:, :], ACT.Silu).then_inc(m.silu_ready, 1)
                    act.wait_ge(m.hid_turned, j + 1)
                    act.activation(m.hid_T[:, :, :], m.hT_ps[:, :].rearrange("p (k s) -> p k s", s=SLOTS), ACT.Copy).then_inc(m.hidT_ready, 1)
                where_needed(act, middle)

            @block.vector
            def _(dve):
                def products(j):
                    dve.wait_ge(m.silu_ready, j + 1)
                    dve.wait_ge(m.up_ready, j + 1)
                    dve.tensor_tensor(m.hid[:, :], m.up_ps[:, :], m.silu[:, :], ALU.mult).then_inc(m.hid_ready, 1)
                    dve.wait_ge(m.y_ready, j + 1)
                    if not first(j):
                        dve.wait_ge(m.y_stored[0], 16 * j)
                    dve.tensor_copy(m.y[0][:, :], m.y_ps[:, :, :].rearrange("p a n -> p (a n)")).then_inc(m.y_read, 1)
                where_needed(dve, products)


def combine_phase(nc, x1, y_rows, tables, gain1, gain2, ident, x2, h_T, network):
    gates, dest = tables["gates"], tables["dest"]
    N_Y = 4
    NETWORK_AFTER = [0, 3]
    with Store(nc, "combine") as m:
        x = [m.sb(f"x{b}", [P, D]) for b in range(2)]
        y = [[m.sb(f"y{j}_{b}", [P, D]) for b in range(N_Y)] for j in range(2)]
        n1 = [m.sb(f"n1_{b}", [P, D]) for b in range(2)]
        n2 = [m.sb(f"n2_{b}", [P, D]) for b in range(2)]
        sq = [m.sb(f"sq{j}", [P, D]) for j in range(2)]
        g = [m.sb(f"g{j}", [P, D]) for j in range(2)]
        ssum = m.sb("ssum", [P, 2 * NT])
        rms = m.sb("rms", [P, 2 * NT])
        rstd = m.sb("rstd", [P, 2 * NT])
        eps = m.sb("eps", [P, 1])
        turned = [m.ps(f"turned{b}", [P, 2, BANK]) for b in range(2)]
        g_loaded = m.sem("g_loaded")
        x_loaded = [m.sem(f"x_loaded{b}") for b in range(2)]
        y_loaded = [m.sem(f"y_loaded{b}") for b in range(N_Y)]
        step = m.sem("step")
        added = m.sem("added")
        sum_ready = [m.sem(f"sum_ready{j}") for j in range(2)]
        rms_ready = [m.sem(f"rms_ready{j}") for j in range(2)]
        n1_ready = m.sem("n1_ready")
        n2_ready = m.sem("n2_ready")
        n2_turned = m.sem("n2_turned")
        copied = m.sem("copied")
        rounded = m.sem("rounded")
        h_split = m.sem("h_split")
        stored = [m.sem(f"stored{b}") for b in range(2)]
        with nc.Block() as block:
            @block.sync
            def _(sp):
                for t in range(NT):
                    b = t % 2
                    if t >= 2:
                        sp.wait_ge(n1_ready, t - 1)
                    sp.dma_start(x[b][:, :], x1[bass.ts(t, P), :]).then_inc(x_loaded[b], 16)
                    if t == 0:
                        for j, gain in enumerate((gain1, gain2)):
                            sp.dma_start(g[j][:, :], row(gain).partition_broadcast(P)).then_inc(g_loaded, 16)
                        network.load(sp)

            @block.gpsimd
            def _(pool):
                for t in range(NT):
                    b = t % N_Y
                    if t >= N_Y:
                        pool.wait_ge(added, t - N_Y + 1)
                    for j in range(2):
                        pool.indirect_dma_start(out=y[j][b][:, :], out_offset=None, in_=y_rows,
                                                in_offset=bass.IndirectOffsetOnAxis(ap=dest[:, 2 * t + j:2 * t + j + 1], axis=0)).then_inc(y_loaded[b], 16)

            @block.vector
            def _(dve):
                c = Chain(dve, step)
                c.then(dve.memset(eps[:, :], EPS))
                dve.wait_ge(g_loaded, 32)

                def add(t):
                    b = t % 2
                    dve.wait_ge(x_loaded[b], 16 * (t // 2 + 1))
                    dve.wait_ge(y_loaded[t % N_Y], 32 * (t // N_Y + 1))
                    c.then(dve.scalar_tensor_tensor(x[b][:, :], y[0][t % N_Y][:, :], gates[:, 0, t:t + 1], x[b][:, :], ALU.mult, ALU.add))
                    dve.scalar_tensor_tensor(x[b][:, :], y[1][t % N_Y][:, :], gates[:, 1, t:t + 1], x[b][:, :], ALU.mult, ALU.add).then_inc(added, 1)

                def norm(src, j, t, out, ready):
                    n = 2 * t + j
                    dve.wait_ge(rms_ready[j], t + 1)
                    c.then(dve.reciprocal(rstd[:, n:n + 1], rms[:, n:n + 1]))
                    if t >= 2:
                        dve.wait_ge(stored[t % 2], 16 * (t // 2)) if j == 0 else dve.wait_ge(n2_turned, t - 1)
                    dve.scalar_tensor_tensor(out[:, :], src[:, :], rstd[:, n:n + 1], g[j][:, :], ALU.mult, ALU.mult).then_inc(ready, 1)

                def split_turned(t):
                    dve.wait_ge(copied, t + 1)
                    split(dve, h_T, (slice(None), slice(None), bass.ts(t, P)), rounded, t + 1, h_split)

                add(0)
                for t in range(NT):
                    b = t % 2
                    if t + 1 < NT:
                        add(t + 1)
                    norm(x[b], 0, t, n1[b], n1_ready)
                    if t:
                        split_turned(t - 1)
                    dve.wait_ge(n1_ready, t + 1)
                    norm(n1[b], 1, t, n2[b], n2_ready)
                    if t in NETWORK_AFTER:
                        network.arguments(c, NETWORK_AFTER.index(t))
                split_turned(NT - 1)

            @block.scalar
            def _(act):
                act.wait_ge(step, 1)

                def root(src, j, t, ready):
                    n = 2 * t + j
                    act.wait_ge(ready, t + 1)
                    act.activation(sq[j][:, :], src[:, :], ACT.Square, accum_out=ssum[:, n:n + 1]).then_inc(sum_ready[j], 1)
                    act.wait_ge(sum_ready[j], t + 1)
                    act.activation(rms[:, n:n + 1], ssum[:, n:n + 1], ACT.Sqrt, scale=1.0 / D, bias=eps[:, :]).then_inc(rms_ready[j], 1)

                def copy_turned(t):
                    act.wait_ge(n2_turned, t + 1)
                    act.activation(h_T.whole[:, :, bass.ts(t, P)], turned[t % 2][:, :, :].rearrange("p a (k q) -> p (a k) q", q=P), ACT.Copy).then_inc(copied, 1)

                root(x[0], 0, 0, added)
                for t in range(NT):
                    b = t % 2
                    if t + 1 < NT:
                        root(x[1 - b], 0, t + 1, added)
                    if t:
                        copy_turned(t - 1)
                    act.wait_ge(n1_ready, t + 1)
                    act.dma_start(x2[bass.ts(t, P), :], n1[b][:, :]).then_inc(stored[b], 16)
                    root(n1[b], 1, t, n1_ready)
                    if t in NETWORK_AFTER:
                        network.sines(act, NETWORK_AFTER.index(t))
                copy_turned(NT - 1)
                for b in range(2):
                    act.wait_ge(stored[b], 16 * (NT // 2))

            @block.tensor
            def _(pe):
                network.products(pe, 0)
                for t in range(NT):
                    b = t % 2
                    pe.wait_ge(n2_ready, t + 1)
                    if t >= 2:
                        pe.wait_ge(copied, t - 1)
                    turn_rows(nc, n2[b], turned[b], ident).then_inc(n2_turned, 1)
                    if t == NETWORK_AFTER[0] + 1:
                        network.products(pe, 1)


LRU_W, LRU_H, LRU_D, LRU_TAPS, LRU_C = 1024, 16, 64, 4, 8.0
HY_W, HY_ORDER, HY_TAPS = 1024, 2, 3
N_LRU = LRU_W // P
COL_AX, COL_AGATE = 0, LRU_W
COL_HY = 2 * LRU_W
COL_GA = COL_HY + (HY_ORDER + 1) * HY_W
COL_GB = COL_GA + D
LOG1P_TERMS = 9


def wide_product(nc, out, w, rhs_T, tiles=range(ND)):
    for h in range(2):
        for k in tiles:
            for n, (lhs, rhs) in enumerate(three_passes(w, rhs_T)):
                last = nc.tensor.matmul(out[:, h, :], lhs[:, k, :], rhs[:, k, bass.ts(h, BANK)],
                                        start=(k == 0 and n == 0), stop=(k == ND - 1 and n == 2))
    return last


def lru_phase(nc, h_T, w_in, conv_w, conv_b, w_r, b_r, w_i, b_i, lam, ident, ya_T):
    R_CONVB, R_BR, R_BI, R_LAM = (LRU_TAPS * N_LRU, (LRU_TAPS + 1) * N_LRU, (LRU_TAPS + 3) * N_LRU, (LRU_TAPS + 5) * N_LRU)
    N_ROWS = (LRU_TAPS + 7) * N_LRU
    PAD_L, PAD = LRU_TAPS // 2, LRU_TAPS - 1
    NB = range(2)
    with Store(nc, "lru") as m:
        w = [[m.parts(f"w{n}{b}", [P, ND, P]) for b in NB] for n in "xg"]
        w_gate = [m.sb(f"w_gate{b}", [P, 2, 2, P]) for b in NB]
        vec_rows = m.sb("vec_rows", [N_ROWS, P])
        vec = m.sb("vec", [P, N_ROWS])
        rate = m.sb("rate", [P, 2 * N_LRU])
        rate_neg = m.sb("rate_neg", [P, 2 * N_LRU])
        u = m.sb("u", [P, 2 * N_LRU])
        s = m.sb("s", [P, 2 * N_LRU])
        s2 = m.sb("s2", [P, 2 * N_LRU])
        poly = m.sb("poly", [P, 2 * N_LRU])
        a_x = [m.sb(f"a_x{b}", [P, T + PAD]) for b in NB]
        xa = [m.sb(f"xa{b}", [P, T]) for b in NB]
        a_gate = [m.sb(f"a_gate{b}", [P, T]) for b in NB]
        r = [[m.sb(f"r{b}{d}", [P, T]) for d in NB] for b in NB]
        x_in = [[m.sb(f"x_in{b}{d}", [P, T]) for d in NB] for b in NB]
        a = [[m.sb(f"a{b}{d}", [P, T]) for d in NB] for b in NB]
        h = [m.sb(f"h{d}", [P, T]) for d in NB]
        a_sq = h
        ya = [m.sb(f"ya{b}", [P, T]) for b in NB]
        ax_ps = m.ps("ax_ps", [P, 2, BANK])
        ag_ps = m.ps("ag_ps", [P, 2, BANK])
        gate_ps = m.ps("gate_ps", [P, 2, 2, BANK])
        cleared = m.sem("cleared")
        vec_loaded = m.sem("vec_loaded")
        vec_turned = m.sem("vec_turned")
        vec_ready = m.sem("vec_ready")
        u_ready = m.sem("u_ready")
        u_made = m.sem("u_made")
        rate_ready = m.sem("rate_ready")
        step = m.sem("step")
        w_loaded = [m.sem(f"w_loaded{b}") for b in NB]
        gate_loaded = [m.sem(f"gate_loaded{b}") for b in NB]
        proj_made = m.sem("proj_made")
        ax_copied = m.sem("ax_copied")
        gelu_done = m.sem("gelu_done")
        conv_step = m.sem("conv_step")
        xa_ready = m.sem("xa_ready")
        gates_made = m.sem("gates_made")
        sig_ready = m.sem("sig_ready")
        tanh_ready = m.sem("tanh_ready")
        x_in_ready = m.sem("x_in_ready")
        sq_ready = m.sem("sq_ready")
        rest_ready = m.sem("rest_ready")
        factor_ready = m.sem("factor_ready")
        scan_step = m.sem("scan_step")
        sum_ready = m.sem("sum_ready")
        ya_ready = m.sem("ya_ready")
        rounded = m.sem("rounded")
        w_split = m.sem("w_split")
        taken = m.sem("taken")
        ya_stored = [m.sem(f"ya_stored{b}") for b in NB]
        w_k = w_in.rearrange("(k p) n -> p k n", p=P)

        def col(j, n=0):
            return vec[:, bass.ds(j + n, 1)]

        with nc.Block() as block:
            @block.gpsimd
            def _(pool):
                for b in NB:
                    pool.memset(a_x[b][:, :], 0.0).then_inc(cleared, 1)
                    pool.memset(w_gate[b][:, :, :, :], 0.0).then_inc(cleared, 1)
                with pool.Fori(0, N_LRU // 2) as i:
                    for b in NB:
                        j = 2 * i + b
                        pool.wait_ge(ya_ready, j + 1)
                        pool.sem_inc(taken, 1)
                        pool.dma_start(ya_T[bass.ds(j * P, P), :], ya[b][:, :]).then_inc(ya_stored[b], 16)
                for b in NB:
                    pool.wait_ge(ya_stored[b], 16 * (N_LRU // 2))

            @block.sync
            def _(sp):
                def load_vectors():
                    for n, src in ((0, conv_w.rearrange("k (t p) -> (k t) p", p=P)), (R_CONVB, conv_b.rearrange("(t p) -> t p", p=P)),
                                   (R_BR, b_r.rearrange("d (t p) -> (d t) p", p=P)), (R_BI, b_i.rearrange("d (t p) -> (d t) p", p=P)),
                                   (R_LAM, lam.rearrange("d (t p) -> (d t) p", p=P))):
                        sp.dma_start(vec_rows[n:n + src.shape[0], :], src).then_inc(vec_loaded, 16)
                    sp.wait_ge(cleared, 4)

                def load(i):
                    for b in NB:
                        j = 2 * i + b
                        if not first(i):
                            sp.wait_ge(proj_made, 4 * i + 2 * b - 2)
                        for n, at in enumerate((COL_AX, COL_AGATE)):
                            sp.dma_start(w[n][b].whole[:, :, :], w_k[:, :, bass.ds(j * P + at, P)]).then_inc(w_loaded[b], 16)
                        if first(i) and b == 0:
                            load_vectors()
                        if not first(i):
                            sp.wait_ge(gates_made, 4 * i + 2 * b - 2)
                        for g, src in enumerate((w_r, w_i)):
                            for e in range(2):
                                half = slice(e * LRU_D, (e + 1) * LRU_D)
                                sp.dma_start(w_gate[b][half, g, :, half],
                                             src[:, bass.ds(2 * j + e, 1), :, :].rearrange("d o p n -> (o p) d n")).then_inc(gate_loaded[b], 16)
                repeat(sp, N_LRU // 2, load)

            @block.tensor
            def _(pe):
                def project(j, i, b):
                    for n, (out, read) in enumerate(((ax_ps, ax_copied), (ag_ps, gelu_done))):
                        pe.wait_ge(w_split, 2 * j + n + 1)
                        if not first(j):
                            pe.wait_ge(read, j)
                        wide_product(nc, out, w[n][b], h_T).then_inc(proj_made, 1)
                    if first(j):
                        pe.wait_ge(vec_loaded, 16 * 5)
                        nc.tensor.transpose(gate_ps[:, 0, 0, 0:N_ROWS], vec_rows[:, :], ident[0:N_ROWS, 0:N_ROWS]).then_inc(vec_turned, 1)

                def gates(j, i, b):
                    pe.wait_ge(xa_ready, j + 1)
                    pe.wait_ge(gate_loaded[b], 64 * (i + 1))
                    for d in NB:
                        if d or not first(j):
                            pe.wait_ge(sig_ready, 2 * (2 * j + d))
                        for g in range(2):
                            for t in range(2):
                                last = nc.tensor.matmul(gate_ps[:, g, t, :], w_gate[b][:, g, d, :], xa[b][:, bass.ts(t, BANK)], start=True, stop=True)
                        last.then_inc(gates_made, 1)

                def two_tiles(i):
                    project(2 * i, i, 0)
                    if not first(i):
                        gates(2 * i - 1, i - 1, 1)
                    project(2 * i + 1, i, 1)
                    gates(2 * i, i, 0)
                repeat(pe, N_LRU // 2, two_tiles)
                gates(N_LRU - 1, N_LRU // 2 - 1, 1)

            @block.scalar
            def _(act):
                act.wait_ge(cleared, 4)

                def inputs(j, i, b):
                    act.wait_ge(proj_made, 2 * j + 1)
                    if not first(i):
                        act.wait_ge(xa_ready, j - 1)
                    act.activation(a_x[b][:, PAD_L:PAD_L + T], ax_ps[:, :, :].rearrange("p a n -> p (a n)"), ACT.Copy).then_inc(ax_copied, 1)
                    act.wait_ge(proj_made, 2 * j + 2)
                    if not first(i):
                        act.wait_ge(ya_ready, j - 1)
                    act.activation(a_gate[b][:, :], ag_ps[:, :, :].rearrange("p a n -> p (a n)"), ACT.Gelu_apprx_tanh).then_inc(gelu_done, 1)
                    if first(j):
                        act.wait_ge(u_ready, 1)
                        act.activation(u[:, :], u[:, :], ACT.Exp).then_inc(u_made, 1)
                        act.wait_ge(rate_ready, 1)

                def gates(j, i, b):
                    for d in NB:
                        act.wait_ge(gates_made, 2 * j + d + 1)
                        for g, (out, n) in enumerate(((r, R_BR), (x_in, R_BI))):
                            act.activation(out[b][d][:, :], gate_ps[:, g, :, :].rearrange("p a n -> p (a n)"), ACT.Sigmoid,
                                           bias=col(j, n + d * N_LRU)).then_inc(sig_ready, 1)
                    act.wait_ge(sig_ready, 4 * j + 4)
                    for d in NB:
                        act.activation(a[b][d][:, :], r[b][d][:, :], ACT.Exp, scale=rate_neg[:, bass.ds(j + d * N_LRU, 1)])
                    for d in NB:
                        act.activation(r[b][d][:, :], r[b][d][:, :], ACT.Tanh, scale=rate[:, bass.ds(j + d * N_LRU, 1)]).then_inc(tanh_ready, 1)
                    for d in NB:
                        act.wait_ge(rest_ready, 2 * j + d + 1)
                        act.activation(r[b][d][:, :], r[b][d][:, :], ACT.Sqrt).then_inc(factor_ready, 1)

                def two_tiles(i):
                    inputs(2 * i, i, 0)
                    if not first(i):
                        gates(2 * i - 1, i - 1, 1)
                    inputs(2 * i + 1, i, 1)
                    gates(2 * i, i, 0)
                repeat(act, N_LRU // 2, two_tiles)
                gates(N_LRU - 1, N_LRU // 2 - 1, 1)

            @block.vector
            def _(dve):
                def split_w(j, i, b):
                    dve.wait_ge(w_loaded[b], 32 * (i + 1))
                    for n in range(2):
                        split(dve, w[n][b], WHOLE, rounded, 2 * j + n + 1, w_split)

                split_w(0, 0, 0)
                split_w(1, 0, 1)
                c = Chain(dve, step)
                dve.wait_ge(vec_turned, 1)
                dve.tensor_copy(vec[:, :], gate_ps[:, 0, 0, 0:N_ROWS]).then_inc(vec_ready, 1)
                dve.wait_ge(vec_ready, 1)
                lam_v = vec[:, R_LAM:R_LAM + 2 * N_LRU]
                c.then(dve.tensor_scalar(rate_neg[:, :], lam_v, -1.0, None, ALU.mult))
                dve.tensor_tensor(u[:, :], lam_v, rate_neg[:, :], ALU.min).then_inc(u_ready, 1)
                c.then(dve.tensor_scalar(rate[:, :], rate_neg[:, :], 0.0, None, ALU.max))
                dve.wait_ge(u_made, 1)
                c.then(dve.tensor_scalar(s[:, :], u[:, :], 2.0, None, ALU.add))
                c.then(dve.reciprocal(s[:, :], s[:, :]))
                c.then(dve.tensor_tensor(s[:, :], s[:, :], u[:, :], ALU.mult))
                c.then(dve.tensor_tensor(s2[:, :], s[:, :], s[:, :], ALU.mult))
                for n in reversed(range(LOG1P_TERMS)):
                    term = 2.0 / (2 * n + 1)
                    if n == LOG1P_TERMS - 1:
                        c.then(dve.tensor_scalar(poly[:, :], s2[:, :], 0.0, term, ALU.mult, ALU.add))
                    else:
                        c.then(dve.tensor_tensor(poly[:, :], poly[:, :], s2[:, :], ALU.mult))
                        c.then(dve.tensor_scalar(poly[:, :], poly[:, :], term, None, ALU.add))
                c.then(dve.tensor_tensor(poly[:, :], poly[:, :], s[:, :], ALU.mult))
                c.then(dve.tensor_tensor(rate[:, :], rate[:, :], poly[:, :], ALU.add))
                c.then(dve.tensor_scalar(rate[:, :], rate[:, :], LRU_C, None, ALU.mult))
                dve.tensor_scalar(rate_neg[:, :], rate[:, :], -1.0, None, ALU.mult).then_inc(rate_ready, 1)

                def conv(j, i, b):
                    dve.wait_ge(ax_copied, j + 1)
                    if not first(i):
                        dve.wait_ge(gates_made, 2 * j - 2)
                    dve.tensor_scalar(xa[b][:, :], a_x[b][:, 0:T], col(j), col(j, R_CONVB), ALU.mult, ALU.add).then_inc(conv_step, 1)
                    for k in range(1, LRU_TAPS):
                        dve.wait_ge(conv_step, (LRU_TAPS - 1) * j + k)
                        dve.scalar_tensor_tensor(xa[b][:, :], a_x[b][:, k:k + T], col(j, k * N_LRU), xa[b][:, :],
                                                 ALU.mult, ALU.add).then_inc(xa_ready if k == LRU_TAPS - 1 else conv_step, 1)

                def scan(j, i, b):
                    dve.wait_ge(xa_ready, j + 1)
                    for d in NB:
                        dve.wait_ge(sig_ready, 4 * j + 2 * d + 2)
                        dve.tensor_tensor(x_in[b][d][:, :], x_in[b][d][:, :], xa[b][:, :], ALU.mult).then_inc(x_in_ready, 1)
                    if not first(j):
                        dve.wait_ge(ya_ready, j)
                    for d in NB:
                        dve.wait_ge(tanh_ready, 2 * j + d + 1)
                        dve.tensor_tensor(a_sq[d][:, :], a[b][d][:, :], a[b][d][:, :], ALU.mult).then_inc(sq_ready, 1)
                    for d in NB:
                        dve.wait_ge(sq_ready, 2 * j + d + 1)
                        dve.scalar_tensor_tensor(r[b][d][:, :], a_sq[d][:, :], 1.0, r[b][d][:, :], ALU.add, ALU.mult).then_inc(rest_ready, 1)
                    for d in NB:
                        rest = slice(1 - d, T - d)
                        dve.wait_ge(factor_ready, 2 * j + d + 1)
                        dve.wait_ge(x_in_ready, 2 * j + d + 1)
                        dve.tensor_tensor(x_in[b][d][:, rest], x_in[b][d][:, rest], r[b][d][:, rest], ALU.mult).then_inc(scan_step, 1)
                    for d in NB:
                        dve.wait_ge(scan_step, 4 * j + d + 1)
                        order = slice(None, None, -1 if d else 1)
                        dve.tensor_tensor_scan(h[d][:, order], a[b][d][:, order], x_in[b][d][:, order], 0.0, ALU.mult, ALU.add).then_inc(scan_step, 1)
                    dve.wait_ge(scan_step, 4 * j + 4)
                    dve.tensor_tensor(h[0][:, :], h[0][:, :], h[1][:, :], ALU.add).then_inc(sum_ready, 1)
                    dve.wait_ge(gelu_done, j + 1)
                    dve.wait_ge(sum_ready, j + 1)
                    if not (isinstance(i, int) and i == 0):
                        dve.wait_ge(ya_stored[b], 16 * i)
                    dve.tensor_tensor(ya[b][:, :], h[0][:, :], a_gate[b][:, :], ALU.mult).then_inc(ya_ready, 1)

                def split_next(j, i, b):
                    dve.wait_ge(proj_made, 2 * j - 2)
                    split_w(j, i, b)

                def two_tiles(i):
                    last = isinstance(i, int) and i == N_LRU // 2 - 1
                    conv(2 * i, i, 0)
                    if not first(i):
                        split_next(2 * i + 1, i, 1)
                        scan(2 * i - 1, i - 1, 1)
                    conv(2 * i + 1, i, 1)
                    if not last:
                        split_next(2 * i + 2, i + 1, 0)
                    scan(2 * i, i, 0)
                two_tiles(0)
                two_tiles(1)
                with dve.Fori(2, N_LRU // 2 - 1) as i:
                    two_tiles(i)
                two_tiles(N_LRU // 2 - 1)
                scan(N_LRU - 1, N_LRU // 2 - 1, 1)


def hyena_inputs_phase(nc, h_T, w_in, conv_w, conv_b, ident, v_x1, x2_T):
    N_NAT, N_ALL = 2 * HY_W // P, 3 * HY_W // P
    R_BIAS = HY_TAPS * N_ALL
    N_ROWS = (HY_TAPS + 1) * N_ALL
    PAD_L, PAD = HY_TAPS // 2, HY_TAPS - 1
    NB = range(2)
    with Store(nc, "hyin") as m:
        w = [m.parts(f"w{b}", [P, ND, P]) for b in NB]
        vec_rows = m.sb("vec_rows", [N_ROWS, P])
        vec = m.sb("vec", [P, N_ROWS])
        raw = [m.sb(f"raw{b}", [P, T + PAD]) for b in NB]
        conv = [m.sb(f"conv{b}", [P, T]) for b in NB]
        rows = [m.sb(f"rows{b}", [P, NT, P]) for b in NB]
        proj_ps = [m.ps(f"proj{b}", [P, 2, BANK]) for b in NB]
        turned_ps = [m.ps(f"turned{b}", [P, 2, BANK]) for b in NB]
        cleared = m.sem("cleared")
        vec_loaded = m.sem("vec_loaded")
        vec_turned = m.sem("vec_turned")
        vec_ready = m.sem("vec_ready")
        w_loaded = [m.sem(f"w_loaded{b}") for b in NB]
        rounded = m.sem("rounded")
        w_split = m.sem("w_split")
        proj_made = m.sem("proj_made")
        raw_ready = m.sem("raw_ready")
        tap_done = m.sem("tap_done")
        conv_ready = m.sem("conv_ready")
        turned = m.sem("turned")
        rows_ready = m.sem("rows_ready")
        taken = m.sem("taken")
        stored = [m.sem(f"stored{b}") for b in NB]
        w_k = w_in.rearrange("(k p) n -> p k n", p=P)
        nat = v_x1.rearrange("(t p) c -> p t c", p=P)

        def loops(engine, body):
            body(0, True)
            with engine.Fori(1, N_NAT // 2) as i:
                body(i, True)
            with engine.Fori(N_NAT // 2, N_ALL // 2) as i:
                body(i, False)

        with nc.Block() as block:
            @block.gpsimd
            def _(pool):
                for b in NB:
                    pool.memset(raw[b][:, :], 0.0).then_inc(cleared, 1)

                def store(i, turn):
                    for b in NB:
                        j = 2 * i + b
                        if turn:
                            pool.wait_ge(rows_ready, j + 1)
                            pool.sem_inc(taken, 1)
                            pool.dma_start(nat[:, :, bass.ds(j * P, P)], rows[b][:, :, :]).then_inc(stored[b], 16)
                        else:
                            pool.wait_ge(conv_ready, j + 1)
                            pool.sem_inc(taken, 1)
                            pool.dma_start(x2_T[bass.ds((j - N_NAT) * P, P), :], conv[b][:, :]).then_inc(stored[b], 16)
                loops(pool, store)
                for b in NB:
                    pool.wait_ge(stored[b], 16 * (N_ALL // 2))

            @block.sync
            def _(sp):
                def load(i):
                    for b in NB:
                        j = 2 * i + b
                        if not first(i):
                            sp.wait_ge(proj_made, j - 1)
                        sp.dma_start(w[b].whole[:, :, :], w_k[:, :, bass.ds(j * P + COL_HY, P)]).then_inc(w_loaded[b], 16)
                        if first(i) and b == 0:
                            sp.dma_start(vec_rows[0:R_BIAS, :], conv_w.rearrange("k (t p) -> (k t) p", p=P)).then_inc(vec_loaded, 16)
                            sp.dma_start(vec_rows[R_BIAS:, :], conv_b.rearrange("(t p) -> t p", p=P)).then_inc(vec_loaded, 16)
                repeat(sp, N_ALL // 2, load)

            @block.tensor
            def _(pe):
                def turn(j, b):
                    pe.wait_ge(conv_ready, j + 1)
                    if not (isinstance(j, int) and j < 2):
                        pe.wait_ge(rows_ready, j - 1)
                    turn_rows(nc, conv[b], turned_ps[b], ident).then_inc(turned, 1)

                def two_tiles(i, turning):
                    for b in NB:
                        j = 2 * i + b
                        pe.wait_ge(w_split, j + 1)
                        if not first(i):
                            pe.wait_ge(raw_ready, j - 1)
                        wide_product(nc, proj_ps[b], w[b], h_T).then_inc(proj_made, 1)
                        if first(j):
                            pe.wait_ge(vec_loaded, 32)
                            nc.tensor.transpose(turned_ps[1][:, 0, 0:N_ROWS], vec_rows[:, :], ident[0:N_ROWS, 0:N_ROWS]).then_inc(vec_turned, 1)
                        if turning and not (first(i) and b == 0):
                            turn(j - 1, 1 - b)

                two_tiles(0, True)
                with pe.Fori(1, N_NAT // 2) as i:
                    two_tiles(i, True)
                turn(N_NAT - 1, 1)
                with pe.Fori(N_NAT // 2, N_ALL // 2) as i:
                    two_tiles(i, False)

            @block.scalar
            def _(act):
                act.wait_ge(cleared, 2)

                def copy_rows(j, i, b):
                    act.wait_ge(turned, j + 1)
                    if not first(i):
                        act.wait_ge(stored[b], 16 * i)
                    act.activation(rows[b][:, :, :], turned_ps[b][:, :, :].rearrange("p a (k c) -> p (a k) c", c=P), ACT.Copy).then_inc(rows_ready, 1)

                def two_tiles(i, turning):
                    for b in NB:
                        j = 2 * i + b
                        act.wait_ge(proj_made, j + 1)
                        if not first(i):
                            act.wait_ge(conv_ready, j - 1)
                        act.activation(raw[b][:, PAD_L:PAD_L + T], proj_ps[b][:, :, :].rearrange("p a n -> p (a n)"), ACT.Copy).then_inc(raw_ready, 1)
                        if turning and not (first(i) and b == 0):
                            copy_rows(j - 1, i if b else i - 1, 1 - b)

                two_tiles(0, True)
                two_tiles(1, True)
                with act.Fori(2, N_NAT // 2) as i:
                    two_tiles(i, True)
                copy_rows(N_NAT - 1, N_NAT // 2 - 1, 1)
                with act.Fori(N_NAT // 2, N_ALL // 2) as i:
                    two_tiles(i, False)

            @block.vector
            def _(dve):
                def split_w(j, i, b):
                    dve.wait_ge(w_loaded[b], 16 * (i + 1))
                    if not (isinstance(j, int) and j < 2):
                        dve.wait_ge(proj_made, j - 1)
                    split(dve, w[b], WHOLE, rounded, j + 1, w_split)

                split_w(0, 0, 0)

                def two_tiles(i, turning):
                    for b in NB:
                        j = 2 * i + b
                        if not (isinstance(j, int) and j == N_ALL - 1):
                            split_w(j + 1, i + b, 1 - b)
                        if first(j):
                            dve.wait_ge(vec_turned, 1)
                            dve.tensor_copy(vec[:, :], turned_ps[1][:, 0, 0:N_ROWS]).then_inc(vec_ready, 1)
                            dve.wait_ge(vec_ready, 1)
                        dve.wait_ge(raw_ready, j + 1)
                        if not first(i):
                            if turning:
                                dve.wait_ge(turned, j - 1)
                            else:
                                dve.wait_ge(stored[b], 16 * i)
                        dve.tensor_scalar(conv[b][:, :], raw[b][:, 0:T], vec[:, bass.ds(j, 1)], vec[:, bass.ds(j + R_BIAS, 1)],
                                          ALU.mult, ALU.add).then_inc(tap_done, 1)
                        for k in range(1, HY_TAPS):
                            dve.wait_ge(tap_done, (HY_TAPS - 1) * j + k)
                            dve.scalar_tensor_tensor(conv[b][:, :], raw[b][:, k:k + T], vec[:, bass.ds(j + k * N_ALL, 1)], conv[b][:, :],
                                                     ALU.mult, ALU.add).then_inc(conv_ready if k == HY_TAPS - 1 else tap_done, 1)
                two_tiles(0, True)
                with dve.Fori(1, N_NAT // 2) as i:
                    two_tiles(i, True)
                with dve.Fori(N_NAT // 2, N_ALL // 2 - 1) as i:
                    two_tiles(i, False)
                two_tiles(N_ALL // 2 - 1, False)


def gates_phase(nc, h_T, ya_T, w_in, w_a_out, part_T, gate_T):
    NB = range(2)
    with Store(nc, "gates") as m:
        w = [[m.parts(f"w{n}{b}", [P, ND, P]) for n in ("ga", "gb", "a")] for b in NB]
        ya = m.parts("ya", [P, N_LRU, T])
        sig_a = [m.sb(f"sig_a{b}", [P, T]) for b in NB]
        sig_b = [m.sb(f"sig_b{b}", [P, T]) for b in NB]
        part = [m.sb(f"part{b}", [P, T]) for b in NB]
        ga_ps = m.ps("ga_ps", [P, 2, BANK])
        gb_ps = m.ps("gb_ps", [P, 2, BANK])
        a_ps = m.ps("a_ps", [P, 2, BANK])
        w_loaded = [m.sem(f"w_loaded{b}") for b in NB]
        ya_loaded = [m.sem(f"ya_loaded{h}") for h in range(2)]
        rounded = m.sem("rounded")
        w_split = m.sem("w_split")
        ya_split = m.sem("ya_split")
        made = m.sem("made")
        sig_ready = m.sem("sig_ready")
        part_ready = m.sem("part_ready")
        taken = m.sem("taken")
        sig_stored = [m.sem(f"sig_stored{b}") for b in NB]
        part_stored = [m.sem(f"part_stored{b}") for b in NB]
        srcs = [(w_in.rearrange("(k p) n -> p k n", p=P), COL_GA), (w_in.rearrange("(k p) n -> p k n", p=P), COL_GB),
                (w_a_out.rearrange("(k p) n -> p k n", p=P), 0)]
        with nc.Block() as block:
            @block.sync
            def _(sp):
                def load(i):
                    for b in NB:
                        j = 2 * i + b
                        if not first(i):
                            sp.wait_ge(made, 6 * i + 3 * b - 3)
                        for n, (src, at) in enumerate(srcs):
                            sp.dma_start(w[b][n].whole[:, :, :], src[:, :, bass.ds(j * P + at, P)]).then_inc(w_loaded[b], 16)
                        if first(i) and b == 0:
                            for h in range(2):
                                sp.dma_start(ya.whole[:, :, bass.ts(h, BANK)],
                                             ya_T.rearrange("(k p) t -> p k t", p=P)[:, :, bass.ts(h, BANK)]).then_inc(ya_loaded[h], 16)
                repeat(sp, ND // 2, load)

            @block.gpsimd
            def _(pool):
                with pool.Fori(0, ND // 2) as i:
                    for b in NB:
                        j = 2 * i + b
                        pool.wait_ge(sig_ready, 2 * j + 2)
                        pool.sem_inc(taken, 1)
                        pool.dma_start(gate_T[bass.ds(j * P, P), :], sig_b[b][:, :]).then_inc(sig_stored[b], 16)
                        pool.wait_ge(part_ready, j + 1)
                        pool.sem_inc(taken, 1)
                        pool.dma_start(part_T[bass.ds(j * P, P), :], part[b][:, :]).then_inc(part_stored[b], 16)
                for b in NB:
                    pool.wait_ge(sig_stored[b], 16 * (ND // 2))
                    pool.wait_ge(part_stored[b], 16 * (ND // 2))

            @block.tensor
            def _(pe):
                def two_tiles(i):
                    for b in NB:
                        j = 2 * i + b
                        for n, (out, rhs) in enumerate(((ga_ps, h_T), (gb_ps, h_T), (a_ps, ya))):
                            pe.wait_ge(w_split, 3 * j + n + 1)
                            if n == 2:
                                pe.wait_ge(ya_split, 2)
                            if not first(j):
                                pe.wait_ge(*((sig_ready, 2 * j + n - 1), (sig_ready, 2 * j + n - 1), (part_ready, j))[n])
                            wide_product(nc, out, w[b][n], rhs).then_inc(made, 1)
                repeat(pe, ND // 2, two_tiles)

            @block.scalar
            def _(act):
                def two_tiles(i):
                    for b in NB:
                        j = 2 * i + b
                        act.wait_ge(made, 3 * j + 1)
                        if not first(i):
                            act.wait_ge(part_ready, j - 1)
                        act.activation(sig_a[b][:, :], ga_ps[:, :, :].rearrange("p a n -> p (a n)"), ACT.Sigmoid).then_inc(sig_ready, 1)
                        act.wait_ge(made, 3 * j + 2)
                        if not first(i):
                            act.wait_ge(sig_stored[b], 16 * i)
                        act.activation(sig_b[b][:, :], gb_ps[:, :, :].rearrange("p a n -> p (a n)"), ACT.Sigmoid).then_inc(sig_ready, 1)
                repeat(act, ND // 2, two_tiles)

            @block.vector
            def _(dve):
                def split_w(j, i, b):
                    dve.wait_ge(w_loaded[b], 48 * (i + 1))
                    for n in range(3):
                        if not (isinstance(j, int) and j < 2):
                            dve.wait_ge(made, 3 * j + n - 5)
                        split(dve, w[b][n], WHOLE, rounded, 3 * j + n + (1 if first(j) else 3), w_split)

                split_w(0, 0, 0)
                for h in range(2):
                    dve.wait_ge(ya_loaded[h], 16)
                    split(dve, ya, (slice(None), slice(None), bass.ts(h, BANK)), rounded, 4 + h, ya_split)

                def two_tiles(i):
                    for b in NB:
                        j = 2 * i + b
                        if not (isinstance(j, int) and j == ND - 1):
                            split_w(j + 1, i + b, 1 - b)
                        dve.wait_ge(sig_ready, 2 * j + 1)
                        dve.wait_ge(made, 3 * j + 3)
                        if not first(i):
                            dve.wait_ge(part_stored[b], 16 * i)
                        dve.tensor_tensor(part[b][:, :], a_ps[:, :, :].rearrange("p a n -> p (a n)"), sig_a[b][:, :], ALU.mult).then_inc(part_ready, 1)
                two_tiles(0)
                with dve.Fori(1, ND // 2 - 1) as i:
                    two_tiles(i)
                two_tiles(ND // 2 - 1)


def merge_phase(nc, z_T, w_b_out, part_T, gate_T, merged_T):
    NB = range(2)
    with Store(nc, "merge") as m:
        z = m.parts("z", [P, ND, T])
        w = [m.parts(f"w{b}", [P, ND, P]) for b in NB]
        part = [m.sb(f"part{b}", [P, T]) for b in NB]
        gate = [m.sb(f"gate{b}", [P, T]) for b in NB]
        prod = [m.sb(f"prod{b}", [P, T]) for b in NB]
        b_ps = [m.ps(f"b_ps{b}", [P, 2, BANK]) for b in NB]
        z_loaded = [m.sem(f"z_loaded{k}") for k in range(ND)]
        rounded = m.sem("rounded")
        z_split = m.sem("z_split")
        w_split = m.sem("w_split")
        w_loaded = [m.sem(f"w_loaded{b}") for b in NB]
        parts_loaded = [m.sem(f"parts_loaded{b}") for b in NB]
        made = m.sem("made")
        prod_ready = m.sem("prod_ready")
        merged_ready = m.sem("merged_ready")
        w_k = w_b_out.rearrange("(k p) n -> p k n", p=P)
        with nc.Block() as block:
            @block.sync
            def _(sp):
                def load(i):
                    for b in NB:
                        j = 2 * i + b
                        if not first(i):
                            sp.wait_ge(made, j - 1)
                        sp.dma_start(w[b].whole[:, :, :], w_k[:, :, bass.ds(j * P, P)]).then_inc(w_loaded[b], 16)
                        if first(i) and b == 0:
                            for k in range(ND):
                                sp.dma_start(z.whole[:, k, :], z_T[bass.ts(k, P), :]).then_inc(z_loaded[k], 16)
                        if not first(i):
                            sp.wait_ge(merged_ready, j - 1)
                        sp.dma_start(gate[b][:, :], gate_T[bass.ds(j * P, P), :]).then_inc(parts_loaded[b], 16)
                        sp.dma_start(part[b][:, :], part_T[bass.ds(j * P, P), :]).then_inc(parts_loaded[b], 16)
                repeat(sp, ND // 2, load)

            @block.tensor
            def _(pe):
                def two_tiles(i):
                    for b in NB:
                        j = 2 * i + b
                        pe.wait_ge(w_split, j + 1)
                        if not first(i):
                            pe.wait_ge(prod_ready, j - 1)
                        if first(i) and b == 0:
                            for k in range(ND):
                                pe.wait_ge(z_split, k + 1)
                                last = wide_product(nc, b_ps[b], w[b], z, [k])
                            last.then_inc(made, 1)
                        else:
                            wide_product(nc, b_ps[b], w[b], z).then_inc(made, 1)
                repeat(pe, ND // 2, two_tiles)

            @block.vector
            def _(dve):
                def split_w(j, i, b):
                    dve.wait_ge(w_loaded[b], 16 * (i + 1))
                    if not (isinstance(j, int) and j < 2):
                        dve.wait_ge(made, j - 1)
                    split(dve, w[b], WHOLE, rounded, j + 1 + (0 if first(j) else ND), w_split)

                split_w(0, 0, 0)
                for k in range(ND):
                    dve.wait_ge(z_loaded[k], 16)
                    split(dve, z, (slice(None), k), rounded, 2 + k, z_split)

                def two_tiles(i):
                    for b in NB:
                        j = 2 * i + b
                        if not (isinstance(j, int) and j == ND - 1):
                            split_w(j + 1, i + b, 1 - b)
                        dve.wait_ge(parts_loaded[b], 32 * (i + 1))
                        dve.wait_ge(made, j + 1)
                        dve.tensor_tensor(prod[b][:, :], b_ps[b][:, :, :].rearrange("p a n -> p (a n)"), gate[b][:, :], ALU.mult).then_inc(prod_ready, 1)
                        dve.wait_ge(prod_ready, j + 1)
                        dve.tensor_tensor(merged_T[:, tile(j), :].rearrange("p o t -> p (o t)"), prod[b][:, :], part[b][:, :], ALU.add).then_inc(merged_ready, 1)
                two_tiles(0)
                with dve.Fori(1, ND // 2 - 1) as i:
                    two_tiles(i)
                two_tiles(ND // 2 - 1)


FILT_EMB, FILT_HID = 33, 64
FILT_BANDS = (FILT_EMB - 1) // 2
DECAY_FAST, DECAY_SLOW, DECAY_TARGET = 0.3, 1.5, 1e-2
TWO_PI = (6.28125, 0.0019350051879882812, 3.01991598196781e-07)
SIN_MAX = 3.1415925
TO_WHOLE = 1.5 * 2 ** 23
HB = 256
NHB = T // HB
HJ = HB // P
HF = HB // P
HC = BANK
COS, SIN, SIN_NEG = range(3)


def filter_positions():
    f4 = np.float32
    lag = np.linspace(0.0, 1.0, T, dtype=f4)[:, None]
    w = f4(2.0 * np.pi / T) * np.arange(T, dtype=f4)[:, None]
    f = np.linspace(1e-4, FILT_BANDS - 1, FILT_BANDS, dtype=f4)[None, :]
    return np.ascontiguousarray(np.concatenate([lag, np.cos(w * f), -np.sin(w * f)], axis=-1).T.astype(f4))


def filter_decay():
    f4 = np.float32
    lag = np.linspace(0.0, 1.0, T, dtype=f4)[:, None]
    rates = np.abs(np.linspace(np.log(DECAY_TARGET) / DECAY_SLOW, np.log(DECAY_TARGET) / DECAY_FAST, HY_W, dtype=f4))
    return np.ascontiguousarray(np.exp(-lag * rates[None, :]).astype(f4))


def block_angles():
    f = np.stack([np.arange(P) * HF + n for n in range(HF)])
    return np.pi * np.arange(HB)[:, None, None] * (2 * f[None] + 1) / (2 * HB)


def block_transform():
    angle = block_angles()
    kinds = np.stack([np.cos(angle), np.sin(angle), -np.sin(angle)], axis=1)
    return np.ascontiguousarray(kinds.reshape(HJ, P, 3, HF, P).transpose(1, 0, 2, 3, 4).astype(np.float32))


def block_inverse():
    angle = block_angles().transpose(2, 1, 0)
    return np.ascontiguousarray((np.stack([np.cos(angle), -np.sin(angle)], axis=2) / HB).astype(np.float32))


class FilterNetwork(Store):

    def __init__(self, nc, positions, w1, b1, w2, b2, freq, hid_T):
        super().__init__(nc, "filter")
        self.positions, self.layers, self.freq_src, self.hid_T = positions, ((w1, b1), (w2, b2)), freq, hid_T

    def __enter__(m):
        super().__enter__()
        H = FILT_HID
        m.pos = m.sb("pos", [FILT_EMB, T])
        m.w = [m.sb("w1", [FILT_EMB, H]), m.sb("w2", [H, H])]
        m.b = [m.sb(f"b{n}", [H, 1]) for n in range(2)]
        m.fr = [m.sb(f"freq{n}", [H, 1]) for n in range(2)]
        m.arg = m.sb("arg", [H, T])
        m.turns = m.sb("turns", [H, T])
        m.hid1 = m.sb("hid1", [H, T])
        m.acc = m.ps("acc", [P, 2, BANK])
        m.loaded = m.sem("loaded")
        m.made = m.sem("made")
        m.arg_ready = m.sem("arg_ready")
        m.hid_ready = m.sem("hid_ready")
        return m

    def load(m, sp):
        sp.dma_start(m.pos[:, :], m.positions).then_inc(m.loaded, 16)
        for n, (wn, bn) in enumerate(m.layers):
            sp.dma_start(m.w[n][:, :], wn).then_inc(m.loaded, 16)
            with m.nc.allow_non_contiguous_dma(reason="a number per partition"):
                sp.dma_start(m.b[n][:, :], bn.rearrange("(p o) -> p o", o=1)).then_inc(m.loaded, 16)
                sp.dma_start(m.fr[n][:, :], m.freq_src[n:n + 1, :].rearrange("o p -> p o")).then_inc(m.loaded, 16)


    def products(m, pe, n):
        if n == 0:
            pe.wait_ge(m.loaded, 16 * 7)
        else:
            pe.wait_ge(m.hid_ready, 1)
        for t in range(2):
            last = m.nc.tensor.matmul(m.acc[0:FILT_HID, t, :], m.w[n][:, :], (m.hid1 if n else m.pos)[:, bass.ts(t, BANK)], start=True, stop=True)
        last.then_inc(m.made, 1)

    def arguments(m, c, n):
        dve = c.engine
        if n == 0:
            dve.wait_ge(m.loaded, 16 * 7)
        else:
            dve.wait_ge(m.hid_ready, 1)
        dve.wait_ge(m.made, n + 1)
        c.then(dve.tensor_scalar(m.arg[:, :], m.acc[0:FILT_HID, :, :].rearrange("p a n -> p (a n)"), m.b[n][:, :], m.fr[n][:, :], ALU.add, ALU.mult))
        c.then(dve.tensor_scalar(m.turns[:, :], m.arg[:, :], 1.0 / (2.0 * np.pi), TO_WHOLE, ALU.mult, ALU.add))
        c.then(dve.tensor_scalar(m.turns[:, :], m.turns[:, :], -TO_WHOLE, None, ALU.add))
        for part in TWO_PI:
            c.then(dve.scalar_tensor_tensor(m.arg[:, :], m.turns[:, :], -part, m.arg[:, :], ALU.mult, ALU.add))
        dve.tensor_scalar(m.arg[:, :], m.arg[:, :], -SIN_MAX, SIN_MAX, ALU.max, ALU.min).then_inc(m.arg_ready, 1)

    def sines(m, act, n):
        act.wait_ge(m.arg_ready, n + 1)
        act.activation(m.hid_T[0:FILT_HID, :] if n else m.hid1[:, :], m.arg[:, :], ACT.Sin).then_inc(m.hid_ready, 1)


def hyena_phase(nc, v_x1, x2_T, hid_T, w3, bias, decay, transform, inverse, z1, z_T):
    PASSES = [(o, h) for o in range(HY_ORDER) for h in range(HY_W // HC)]
    NP = len(PASSES)
    SHIFTS = range(1 - NHB, NHB)
    FWD, BWD = range(2)
    LAST = NHB - 1
    N_DECAY = 4

    program = [("F", 0, 0), ("T", 0, (BWD, 3)), ("T", 0, (BWD, 2)), ("U", 0, 3), ("T", 0, (BWD, 1)), ("U", 0, 2), ("T", 0, (BWD, 0)),
               ("U", 0, 1), ("T", 0, (FWD, 0)), ("U", 0, 0)]
    for n in range(NP):
        if n:
            program += [("T", n, (BWD, b)) for b in (3, 2, 1)]
            program += [("Y", n - 1, 2), ("U", n, 3), ("T", n, (BWD, 0)), ("U", n, 2), ("T", n, (FWD, 0)), ("U", n, 1), ("Y", n - 1, 3), ("U", n, 0)]
        program += [("T", n, (FWD, 1)), ("Y", n, 0), ("T", n, (FWD, 2)), ("T", n, (FWD, 3))]
        program += ([("F", n + 1, 0)] if n + 1 < NP else []) + [("Y", n, 1)]
    program += [("Y", NP - 1, 2), ("Y", NP - 1, 3)]
    moved = {what: n for n, what in enumerate(w for w in program if w[0] in "UT")}
    turned_back = {what: n for n, what in enumerate(w for w in program if w[0] == "Y")}
    def pair(n, m_, i):
        return NHB * NHB * n + NHB * m_ + NHB - i

    def shift(n, d):
        return len(SHIFTS) * n + d + NHB

    with Store(nc, "hyena") as m:
        tr = m.sb("tr", [P, HJ, 3, HF, P])
        inv = m.sb("inv", [P, HF, 2, HB])
        w3_sb = m.sb("w3", [P, 2, HC])
        bias_sb = m.sb("bias", [1, HC])
        decay_sb = [m.sb(f"decay{b}", [P, HC]) for b in range(N_DECAY)]
        filt = m.sb("filt", [P, 2, NT, HC])
        u = [m.sb(f"u{b}", [P, HJ, HC]) for b in range(2)]
        U = [m.sb(f"U{i}", [P, 2, HF * HC]) for i in range(NHB)]
        K = {d: m.sb(f"K{d + NHB}", [P, 2, HF * HC]) for d in SHIFTS}
        last_T = m.sb("last_T", [P, 2, HF * HC])
        T_at = {(BWD, b): K[-b] for b in range(NHB)} | {(FWD, b): K[b + 1] for b in range(LAST)} | {(FWD, LAST): last_T}
        Y = [m.sb(f"Y{b}", [P, 2, HF * HC]) for b in range(2)]
        by_re = m.sb("by_re", [P, 2, HF * HC])
        by_im = m.sb("by_im", [P, 2, HF * HC])
        z = [m.sb(f"z{b}", [P, HJ * HC]) for b in range(2)]
        tr_ps = [m.ps(f"tr_ps{c}", [P, HF * HC]) for c in range(2)]
        inv_ps = m.ps("inv_ps", [P, HJ * HC])
        filt_ps = [m.ps(f"filt_ps{b}", [P, HC]) for b in range(2)]
        tables_loaded = m.sem("tables_loaded")
        w3_loaded = m.sem("w3_loaded")
        decay_loaded = [m.sem(f"decay_loaded{b}") for b in range(N_DECAY)]
        u_loaded = [m.sem(f"u_loaded{b}") for b in range(2)]
        gate_loaded = [m.sem(f"gate_loaded{b}") for b in range(2)]
        rest_cleared = m.sem("rest_cleared")
        filt_made = m.sem("filt_made")
        filt_ready = m.sem("filt_ready")
        ends_set = m.sem("ends_set")
        tr_made = m.sem("tr_made")
        tr_copied = m.sem("tr_copied")
        K_made = m.sem("K_made")
        re_made = m.sem("re_made")
        im_made = m.sem("im_made")
        sum_step = m.sem("sum_step")
        pair_added = m.sem("pair_added")
        inv_made = m.sem("inv_made")
        z_ready = m.sem("z_ready")
        z_stored = [m.sem(f"z_stored{b}") for b in range(2)]
        N_F = 2 * NT
        ENDS = 2

        def u_src(n, i):
            o, h = PASSES[n]
            rows = (z1 if o else v_x1)[bass.ts(i, HB), bass.ts(h, HC)]
            return rows.rearrange("(j p) c -> p j c", p=P)

        def z_place(n, m_):
            o, h = PASSES[n]
            if o == 0:
                return z1[bass.ts(m_, HB), bass.ts(h, HC)].rearrange("(j p) c -> p j c", p=P), dict(j=HJ)
            return z_T[bass.ts(h, HC), bass.ts(m_, HB)].rearrange("(j p) t -> p j t", p=P), dict(j=HC // P)

        def gate_src(n, m_):
            o, h = PASSES[n]
            if o == 0:
                return v_x1[bass.ts(m_, HB), bass.ds(HY_W + h * HC, HC)].rearrange("(j p) c -> p j c", p=P)
            return x2_T[bass.ts(h, HC), bass.ts(m_, HB)].rearrange("(j p) t -> p j t", p=P)

        def both(x, c):
            return x[:, c, :].unsqueeze(1).to_broadcast([P, 2, HF * HC])

        with nc.Block() as block:
            @block.sync
            def _(sp):
                n_u = 0
                for what, n, at in program:
                    o, h = PASSES[n]
                    if what == "F":
                        if n:
                            sp.wait_ge(filt_made, N_F * n)
                            sp.wait_ge(ends_set, ENDS * n)
                        cols = w3[:, bass.ds(o * 2 * HY_W, 2 * HY_W)].rearrange("k (d c) -> k d c", d=2)
                        sp.dma_start(w3_sb[0:FILT_HID, :, :], cols[:, :, bass.ts(h, HC)]).then_inc(w3_loaded, 16)
                        sp.dma_start(bias_sb[:, :], bias[o:o + 1, bass.ts(h, HC)]).then_inc(w3_loaded, 16)
                        for t in range(NT):
                            if n == 0 and t == N_DECAY:
                                sp.dma_start(tr[:, :, :, :, :], transform).then_inc(tables_loaded, 16)
                                sp.dma_start(inv[:, :, :, :], inverse).then_inc(tables_loaded, 16)
                            if NT * n + t >= N_DECAY:
                                sp.wait_ge(filt_ready, N_F * n + 2 * (t - N_DECAY) + 2)
                            sp.dma_start(decay_sb[t % N_DECAY][:, :], decay[bass.ts(t, P), bass.ts(h, HC)]).then_inc(decay_loaded[t % N_DECAY], 16)
                    elif what == "U":
                        if n_u >= 2:
                            before = [w for w in program if w[0] == "U"][n_u - 2]
                            sp.wait_ge(tr_made, 2 * moved[before] + 2)
                        if o:
                            done = turned_back["Y", n - 2, at] // 2 + 1
                            sp.wait_ge(z_stored[turned_back["Y", n - 2, at] % 2], 16 * done)
                        sp.dma_start(u[n_u % 2][:, :, :], u_src(n, at)).then_inc(u_loaded[n_u % 2], 16)
                        n_u += 1
                    elif what == "Y":
                        e = turned_back[what, n, at]
                        if e >= 2:
                            sp.wait_ge(z_stored[e % 2], 16 * (e // 2))
                        src = gate_src(n, at)
                        sp.dma_start(z[e % 2][:, :].rearrange("p (j x) -> p j x", j=src.shape[1]), src).then_inc(gate_loaded[e % 2], 16)

            @block.gpsimd
            def _(pool):
                pool.memset(hid_T[FILT_HID:P, :], 0.0).then_inc(rest_cleared, 1)
                pool.memset(w3_sb[FILT_HID:P, :, :], 0.0).then_inc(rest_cleared, 1)

                def store(n, m_):
                    e = turned_back["Y", n, m_]
                    dst, split = z_place(n, m_)
                    pool.wait_ge(z_ready, e + 1)
                    pool.dma_start(dst, z[e % 2][:, :].rearrange("p (j x) -> p j x", **split)).then_inc(z_stored[e % 2], 16)

                def combine(n, d, c):
                    after = T_at[(BWD, -d - 1) if d < 0 else (FWD, d)][:, 1 - c, :]
                    own = K[d][:, c, :]
                    if c == 0:
                        pool.wait_ge(tr_copied, 2 * moved["T", n, (BWD, -d - 1) if d < 0 else (FWD, d)] + 2)
                        if shift(n, d) > 1:
                            pool.wait_ge(K_made, shift(n, d) - 1)
                    if d == 0:
                        step = pool.tensor_tensor(own, own, after, ALU.add)
                    else:
                        for f in range(HF):
                            x, y = own[:, bass.ts(f, HC)], after[:, bass.ts(f, HC)]
                            step = pool.tensor_tensor(x, *((x, y) if d < 0 else (y, x)), ALU.add if (c == f) == (d < 0) else ALU.subtract)
                    if c == 1:
                        step.then_inc(K_made, 1)

                blocks = [(n, m_) for n in range(NP) for m_ in range(NHB)]
                AHEAD = {(3, 3): (-3, 0), (3, 2): (-3, 1), (3, 1): (-2, 0), (3, 0): (-2, 1)}
                JUST = {(0, 3): (-1, 0), (0, 2): (-1, 1), (0, 1): (0, 0), (0, 0): (0, 1), (1, 2): (1, 0), (1, 1): (1, 1),
                        (2, 3): (2, 0), (2, 2): (2, 1), (2, 1): (3, 0), (2, 0): (3, 1)}
                for d in (-3, -2):
                    for c in range(2):
                        combine(0, d, c)
                for g, (n, m_) in enumerate(blocks):
                    for i in reversed(range(NHB)):
                        if (m_, i) in JUST:
                            combine(n, *JUST[m_, i])
                        elif (m_, i) in AHEAD and n + 1 < NP:
                            combine(n + 1, *AHEAD[m_, i])
                        d = m_ - i
                        pool.wait_ge(tr_copied, 2 * moved["U", n, i] + 2)
                        pool.wait_ge(K_made, shift(n, d))
                        if pair(n, m_, i) > 1:
                            pool.wait_ge(pair_added, pair(n, m_, i) - 1)
                        pool.tensor_tensor(by_im[:, :, :], K[d][:, ::-1, :], both(U[i], 1), ALU.mult).then_inc(im_made, 1)
                        if i == NHB - 1 and g >= 2:
                            store(*blocks[g - 2])
                for at in blocks[-2:]:
                    store(*at)
                for b in range(2):
                    pool.wait_ge(z_stored[b], 16 * len(turned_back) // 2)

            @block.tensor
            def _(pe):
                pe.wait_ge(rest_cleared, 2)
                n_u = 0
                for step, (what, n, at) in enumerate(program):
                    o, h = PASSES[n]
                    if step == 1:
                        pe.wait_ge(tables_loaded, 32)
                    if what == "F":
                        pe.wait_ge(w3_loaded, 32 * (n + 1))
                        for t in range(NT):
                            for d in range(2):
                                f = N_F * n + 2 * t + d
                                if f >= 2:
                                    pe.wait_ge(filt_ready, f - 1)
                                nc.tensor.matmul(filt_ps[d][:, :], hid_T[:, bass.ts(t, P)], w3_sb[:, d, :], start=True, stop=True).then_inc(filt_made, 1)
                        continue
                    if what == "Y":
                        e = turned_back[what, n, at]
                        y = Y[at % 2]
                        pe.wait_ge(pair_added, pair(n, at, 0))
                        if e:
                            pe.wait_ge(z_ready, e)
                        terms = [(c, f) for c in range(2) for f in range(HF)]
                        for j in range(HJ if o == 0 else HC // P):
                            for c, f in terms:
                                if o == 0:
                                    out, lhsT, rhs = inv_ps[:, bass.ts(j, HC)], inv[:, f, c, bass.ts(j, P)], y[:, c, bass.ts(f, HC)]
                                else:
                                    out, lhsT, rhs = inv_ps[:, bass.ts(j, HB)], y[:, c, bass.ds(f * HC + j * P, P)], inv[:, f, c, :]
                                last = nc.tensor.matmul(out, lhsT, rhs, start=((c, f) == terms[0]), stop=((c, f) == terms[-1]))
                        last.then_inc(inv_made, 1)
                        continue
                    q = moved[what, n, at]
                    if what == "U":
                        pe.wait_ge(u_loaded[n_u % 2], 16 * (n_u // 2 + 1))
                        kinds, src = (COS, SIN_NEG), u[n_u % 2][:, :, :]
                        n_u += 1
                    else:
                        pe.wait_ge(filt_ready, N_F * (n + 1))
                        pe.wait_ge(ends_set, ENDS * (n + 1))
                        d, blk = at
                        kinds, src = (COS, SIN if d == BWD else SIN_NEG), filt[:, d, bass.ts(blk, HJ), :]
                    for c in range(2):
                        if q:
                            pe.wait_ge(tr_copied, 2 * q + c - 1)
                        for f in range(HF):
                            for j in range(HJ):
                                last = nc.tensor.matmul(tr_ps[c][:, bass.ts(f, HC)], tr[:, j, kinds[c], f, :], src[:, j, :],
                                                        start=(j == 0), stop=(j == HJ - 1))
                        last.then_inc(tr_made, 1)

            @block.scalar
            def _(act):
                for (what, n, at), q in moved.items():
                    for c in range(2):
                        act.wait_ge(tr_made, 2 * q + c + 1)
                        if n and c == 0:
                            if what == "U":
                                act.wait_ge(pair_added, pair(n - 1, LAST, at))
                            elif at == (FWD, LAST):
                                act.wait_ge(K_made, shift(n - 1, LAST))
                            else:
                                d = at[1] + 1 if at[0] == FWD else -at[1]
                                act.wait_ge(pair_added, pair(n - 1, min(LAST, LAST + d), LAST - max(d, 0)))
                        dst = U[at][:, c, :] if what == "U" else T_at[at][:, 1 - c if at[0] == FWD else c, :]
                        act.activation(dst, tr_ps[c][:, :], ACT.Copy).then_inc(tr_copied, 1)

            @block.vector
            def _(dve):
                n_sum = 0
                FILTERS_AFTER = {(1, 1): (0,), (1, 0): (1, 2, 3)}

                def filters(n, quarter):
                    if n and quarter == 0:
                        dve.wait_ge(tr_made, 2 * moved["T", n - 1, (FWD, LAST)] + 2)
                    for t in range(NT // 4 * quarter, NT // 4 * (quarter + 1)):
                        dve.wait_ge(decay_loaded[t % N_DECAY], 16 * (NT // N_DECAY * n + t // N_DECAY + 1))
                        for d in range(2):
                            f = N_F * n + 2 * t + d
                            dve.wait_ge(filt_made, f + 1)
                            dve.tensor_tensor(filt[:, d, t, :], filt_ps[d][:, :], decay_sb[t % N_DECAY][:, :], ALU.mult).then_inc(filt_ready, 1)
                    if quarter == 3:
                        dve.wait_ge(filt_ready, N_F * (n + 1))
                        dve.wait_ge(w3_loaded, 32 * (n + 1))
                        dve.tensor_tensor(filt[0:1, FWD, 0, :], filt[0:1, FWD, 0, :], bias_sb[:, :], ALU.add).then_inc(ends_set, 1)
                        dve.memset(filt[0:1, BWD, 0, :], 0.0).then_inc(ends_set, 1)

                def results(n, m_):
                    e = turned_back["Y", n, m_]
                    dve.wait_ge(inv_made, e + 1)
                    dve.wait_ge(gate_loaded[e % 2], 16 * (e // 2 + 1))
                    dve.tensor_tensor(z[e % 2][:, :], inv_ps[:, :], z[e % 2][:, :], ALU.mult).then_inc(z_ready, 1)

                for quarter in range(4):
                    filters(0, quarter)
                for n in range(NP):
                    for m_ in range(NHB):
                        y = Y[m_ % 2]
                        if NHB * n + m_ >= 2:
                            before = ("Y", n, m_ - 2) if m_ >= 2 else ("Y", n - 1, m_ + NHB - 2)
                            dve.wait_ge(inv_made, turned_back[before] + 1)
                        for i in reversed(range(NHB)):
                            d = m_ - i
                            start = i == NHB - 1
                            dve.wait_ge(tr_copied, 2 * moved["U", n, i] + 2)
                            dve.wait_ge(K_made, shift(n, d))
                            dve.tensor_tensor((y if start else by_re)[:, :, :], K[d][:, :, :], both(U[i], 0), ALU.mult).then_inc(re_made, 1)
                            dve.wait_ge(re_made, pair(n, m_, i))
                            if not start:
                                dve.tensor_tensor(y[:, :, :], y[:, :, :], by_re[:, :, :], ALU.add).then_inc(sum_step, 1)
                                n_sum += 1
                                dve.wait_ge(sum_step, n_sum)
                            dve.wait_ge(im_made, pair(n, m_, i))
                            dve.tensor_tensor(y[:, 0, :], y[:, 0, :], by_im[:, 0, :], ALU.subtract)
                            dve.tensor_tensor(y[:, 1, :], y[:, 1, :], by_im[:, 1, :], ALU.add).then_inc(pair_added, 1)
                            dve.wait_ge(pair_added, pair(n, m_, i))
                            if n + 1 < NP:
                                for quarter in FILTERS_AFTER.get((m_, i), ()):
                                    filters(n + 1, quarter)
                        if m_ == 0 and n:
                            results(n - 1, NHB - 1)
                        if m_:
                            results(n, m_ - 1)
                results(NP - 1, NHB - 1)


N_EXP2, F_EXP2 = 16, 2 * D
CAP = 2 * T // N_EXP2
MAX_AT_ONCE = 8
TAKEN = -1.0


def expert_choice_phase(nc, h_T, inputs, ident, idx, scale, next_weights):
    NE = N_EXP2
    with Store(nc, "choice") as m:
        w = inputs.w
        aff = m.sb("aff", [P, NT, NE])
        best = m.sb("best", [P, NT])
        total = m.sb("total", [P, NT])
        left = m.sb("left", [NE, T])
        top = m.sb("top", [NE, MAX_AT_ONCE])
        chosen = m.sb("chosen", [NE, T])
        ones_T = m.sb("ones_T", [NE, T])
        place = m.sb("place", [NE, T])
        place_t = m.sb("place_t", [P, NT, NE])
        slot = m.sb("slot", [P, CAP])
        number = m.sb("number", [P, NT, NE])
        nothing = m.sb("nothing", [P, NT, NE])
        N_WHAT = 4
        what = m.sb("what", [P, NT, NE, N_WHAT], F32R)
        aff_upper = m.sb("aff_upper", [P, NT, NE])
        hot = [m.sb(f"hot{b}", [P, NT, CAP], F32R) for b in range(2)]
        parts = m.sb("parts", [P, NE, N_WHAT])
        logit_ps = m.ps("logit_ps", [P, NT, NE])
        aff_ps = m.ps("aff_ps", [NE, T])
        place_ps = m.ps("place_ps", [P, NT, NE])
        list_ps = m.ps("list_ps", [P, NE, N_WHAT])
        made = m.sem("made")
        logits_ready = m.sem("logits_ready")
        diff_ready = m.sem("diff_ready")
        exp_ready = m.sem("exp_ready")
        aff_ready = m.sem("aff_ready")
        aff_turned = m.sem("aff_turned")
        place_ready = m.sem("place_ready")
        place_turned = m.sem("place_turned")
        hot_ready = m.sem("hot_ready")
        hot_used = m.sem("hot_used")
        step = m.sem("step")

        def over_e(x):
            return x.unsqueeze(2).to_broadcast([P, NT, NE])

        add_logits(m, NE)
        with nc.Block() as block:
            @block.sync
            def _(sp):
                next_weights.load_first(sp)

            @block.gpsimd
            def _(pool):
                pool.iota(slot[:, :], pattern=[[1, CAP]], base=0, channel_multiplier=0, allow_small_or_imprecise_dtypes=True).then_inc(made, 1)
                pool.iota(number[:, :, :], pattern=[[P, NT], [0, NE]], base=0, channel_multiplier=1, allow_small_or_imprecise_dtypes=True).then_inc(made, 1)
                pool.memset(ones_T[:, :], 1.0).then_inc(made, 1)
                pool.memset(nothing[:, :, :], 0.0).then_inc(made, 1)

            @block.tensor
            def _(pe):
                pe.wait_ge(inputs.loaded, inputs.all_loaded)
                router_logits(nc, pe, m, h_T, w, logit_ps, ident, logits_ready)
                pe.wait_ge(aff_ready, 1)
                for t in range(NT):
                    last = nc.tensor.transpose(aff_ps[:, bass.ts(t, P)], aff[:, t, :], ident[:, :])
                last.then_inc(aff_turned, 1)
                pe.wait_ge(place_ready, 1)
                for t in range(NT):
                    last = nc.tensor.transpose(place_ps[:, t, :], place[:, bass.ts(t, P)], ident[0:NE, 0:NE])
                last.then_inc(place_turned, 1)
                for e in range(NE):
                    pe.wait_ge(hot_ready, e + 1)
                    for t in range(NT):
                        last = nc.tensor.matmul(list_ps[:, e, :], hot[e % 2][:, t, :], what[:, t, e, :], start=(t == 0), stop=(t == NT - 1))
                    last.then_inc(hot_used, 1)

            @block.scalar
            def _(act):
                copy_logits(act, m)
                act.wait_ge(diff_ready, 1)
                act.activation(aff[:, :, :], aff[:, :, :], ACT.Exp).then_inc(exp_ready, 1)

            @block.vector
            def _(dve):
                c = Chain(dve, step)
                dve.wait_ge(made, 4)
                dve.wait_ge(logits_ready, 1)
                c.then(dve.reduce_max(best[:, :], logit_ps[:, :, :], axis=AXX))
                dve.tensor_tensor(aff[:, :, :], logit_ps[:, :, :], over_e(best[:, :]), ALU.subtract).then_inc(diff_ready, 1)
                dve.wait_ge(exp_ready, 1)
                c.then(dve.reduce_sum(total[:, :], aff[:, :, :], axis=AXX))
                c.then(dve.reciprocal(total[:, :], total[:, :]))
                dve.tensor_tensor(aff[:, :, :], aff[:, :, :], over_e(total[:, :]), ALU.mult).then_inc(aff_ready, 1)
                dve.wait_ge(aff_ready, 1)
                c.then(dve.tensor_copy(what[:, :, :, 0], number[:, :, :]))
                c.then(dve.tensor_copy(what[:, :, :, 1], aff[:, :, :]))
                c.then(dve.tensor_copy(aff_upper[:, :, :], what[:, :, :, 1].bitcast(F32)))
                c.then(dve.tensor_tensor(what[:, :, :, 2], aff[:, :, :], aff_upper[:, :, :], ALU.subtract))
                c.then(dve.tensor_copy(what[:, :, :, 3], nothing[:, :, :]))
                dve.wait_ge(aff_turned, 1)
                c.then(dve.tensor_copy(left[:, :], aff_ps[:, :]))
                for n in range(CAP // MAX_AT_ONCE):
                    c.then(dve.max(top[:, :], left[:, :]))
                    c.then(dve.match_replace(left[:, :], top[:, :], left[:, :], TAKEN))
                c.then(dve.tensor_scalar(chosen[:, :], left[:, :], TAKEN, None, ALU.is_equal))
                c.then(dve.tensor_tensor_scan(place[:, :], ones_T[:, :], chosen[:, :], 0.0, ALU.mult, ALU.add))
                c.then(dve.tensor_tensor(place[:, :], place[:, :], chosen[:, :], ALU.mult))
                dve.tensor_scalar(place[:, :], place[:, :], 1.0, None, ALU.subtract).then_inc(place_ready, 1)
                dve.wait_ge(place_turned, 1)
                c.then(dve.tensor_copy(place_t[:, :, :], place_ps[:, :, :]))
                for e in range(NE):
                    if e >= 2:
                        dve.wait_ge(hot_used, e - 1)
                    dve.tensor_tensor(hot[e % 2][:, :, :], slot[:, :].unsqueeze(1).to_broadcast([P, NT, CAP]),
                                      place_t[:, :, e:e + 1].to_broadcast([P, NT, CAP]), ALU.is_equal).then_inc(hot_ready, 1)
                dve.wait_ge(hot_used, NE)
                c.then(dve.tensor_copy(parts[:, :, :], list_ps[:, :, :]))
                c.then(dve.tensor_copy(idx[:, :], parts[:, :, 0]))
                c.then(dve.tensor_tensor(scale[:, :], parts[:, :, 1], parts[:, :, 2], ALU.add))


INPUTS = ("x", "norm1_g", "w_in", "gla_gate_w2", "gla_gate_b", "gla_norm_g", "w_out", "norm2_g", "router_group_w", "router_group_b",
          "router_expert_w", "router_expert_b", "expert_w1", "expert_w3", "expert_w2", "final_norm_g", "g_mix_2", "w_in_2", "conv_a_w_2",
          "conv_a_b_2", "lru_w_r_2", "lru_b_r_2", "lru_w_i_2", "lru_b_i_2", "lru_lambda_2", "w_a_out_2", "conv_b_w_2", "conv_b_b_2",
          "filt_w1_2", "filt_b1_2", "filt_w2_2", "filt_b2_2", "filt_w3_2", "filt_freq_2", "filt_bias_2", "w_b_out_2", "w_o_2", "g_ffn_2",
          "w_router_2", "w_gate_2", "w_up_2", "w_down_2", "g_final_2")


def constants():
    return {"gla_masks": gla_level_masks(), "att_bias": attention_bias(), "filt_positions": filter_positions(), "filt_decay": filter_decay(),
            "block_transform": block_transform(), "block_inverse": block_inverse()}


def build_program(nc, a, out):
    def dram(name, shape, dt=F32):
        return nc.dram_tensor(f"tmp_{name}", shape, dt, kind="Internal").ap()

    x1, h2, x2, h3, total = (dram(n, [T, D]) for n in ("x1", "h2", "x2", "h3", "total"))
    row_tok = dram("row_tok", [N_BLK * SLOTS, 1], I32)
    y_rows = dram("y_rows", [N_BLK * SLOTS, D])
    ya_T = dram("ya_T", [LRU_W, T])
    v_x1, x2_T, z1, z_T = dram("v_x1", [T, 2 * HY_W]), dram("x2_T", [HY_W, T]), dram("z1", [T, HY_W]), dram("z_T", [HY_W, T])
    part_T, gate_T = dram("part_T", [D, T]), dram("gate_T", [D, T])

    ident = nc.alloc_sbuf_tensor("ident", [P, P], F32)
    ones_col = nc.alloc_sbuf_tensor("ones_col", [P, 1], F32)
    tables = {"gates": nc.alloc_sbuf_tensor("gates", [P, 2, NT], F32), "dest": nc.alloc_sbuf_tensor("dest", [P, 2 * NT], I32),
              "idx_all": nc.alloc_sbuf_tensor("idx_all", [P, N_BLK], I32), "over_exp": nc.alloc_sbuf_tensor("over_exp", [1, N_OVER], I32),
              "n_over": nc.alloc_sbuf_tensor("n_over", [1, 1], I32)}
    idx2 = nc.alloc_sbuf_tensor("idx2", [P, N_EXP2], I32)
    scale2 = nc.alloc_sbuf_tensor("scale2", [P, N_EXP2], F32)
    Store.used = []
    setup_constants(nc, ident, ones_col)

    with Store(nc, "mixer") as s:
        o_T = s.sb("o_T", [P, ND, T])
        with Store(nc, "mixer_in") as s_in:
            n_T = s_in.sb("n_T", [P, ND, T])
            norm_phase(nc, "norm1", a["x"], a["norm1_g"], ident, transposed=n_T)
            gla_phase(nc, n_T, a["w_in"], a["gla_gate_w2"], a["gla_gate_b"], a["gla_norm_g"], a["gla_masks"], ident, o_T)
            attention_phase(nc, n_T, a["w_in"], a["att_bias"], ident, o_T)
        h2_T = s.sb("h2_T", [P, ND, T])
        routing = RouterInputs(nc, "routing", (a["router_group_w"], a["router_expert_w"]), (a["router_group_b"], a["router_expert_b"])).open()
        residual_norm_phase(nc, "out1", o_T, a["w_out"], a["x"], [x1], a["norm2_g"], ident, h2, h2_T, routing)

        def expert(name):
            view = a[name].rearrange("e (k p) n -> e p k n", p=P)
            return lambda i, c: view[bass.ds(i * PER_STEP + c, 1), :, :, :].rearrange("o p k n -> (o p) k n")
        weights1 = ExpertWeights(nc, "moe1_w", 2, expert("expert_w1"), expert("expert_w3"), expert("expert_w2")).open()
        router_phase(nc, h2_T, routing, ident, tables, row_tok, y_rows, weights1)
    expert_phase(nc, "moe1", N_EXP // PER_STEP, weights1, tables["idx_all"], h2, ident, False, y_rows=y_rows)
    weights1.close()
    routing.close()
    overflow_phase(nc, a["expert_w1"], a["expert_w3"], a["expert_w2"], tables, h2, y_rows, ident)

    Store.give_back_semaphores(nc)

    filters = Store(nc, "filters", side="right").open()
    hid_T = filters.sb("hid_T", [P, T])
    with Store(nc, "block2") as s:
        h_T = s.parts("h_T", [P, ND, T])
        with FilterNetwork(nc, a["filt_positions"], a["filt_w1_2"], a["filt_b1_2"], a["filt_w2_2"], a["filt_b2_2"], a["filt_freq_2"], hid_T) as network:
            combine_phase(nc, x1, y_rows, tables, a["final_norm_g"], a["g_mix_2"], ident, x2, h_T, network)
        lru_phase(nc, h_T, a["w_in_2"], a["conv_a_w_2"], a["conv_a_b_2"], a["lru_w_r_2"], a["lru_b_r_2"], a["lru_w_i_2"], a["lru_b_i_2"],
                  a["lru_lambda_2"], ident, ya_T)
        hyena_inputs_phase(nc, h_T, a["w_in_2"], a["conv_b_w_2"], a["conv_b_b_2"], ident, v_x1, x2_T)
        gates_phase(nc, h_T, ya_T, a["w_in_2"], a["w_a_out_2"], part_T, gate_T)
    hyena_phase(nc, v_x1, x2_T, hid_T, a["filt_w3_2"], a["filt_bias_2"], a["filt_decay"], a["block_transform"], a["block_inverse"], z1, z_T)
    filters.close()
    with Store(nc, "merged") as s:
        merged_T = s.sb("merged_T", [P, ND, T])
        merge_phase(nc, z_T, a["w_b_out_2"], part_T, gate_T, merged_T)
        Store.give_back_semaphores(nc)
        h3_T = s.sb("h3_T", [P, ND, T])
        choosing = RouterInputs(nc, "choosing", (a["w_router_2"],), ()).open()
        residual_norm_phase(nc, "out2", merged_T, a["w_o_2"], x2, [total], a["g_ffn_2"], ident, h3, h3_T, choosing)

        def columns(name):
            view = a[name].rearrange("e (k p) f -> e p k f", p=P)
            return lambda i, c: view[bass.ds(i, 1), :, :, bass.ts(c, CHUNK)].rearrange("o p k f -> (o p) k f")

        def rows(name):
            view = a[name].rearrange("e (k p) d -> e p k d", p=P)
            return lambda i, c: view[bass.ds(i, 1), :, bass.ts(c, CHUNK // P), :].rearrange("o p k d -> (o p) k d")
        weights2 = ExpertWeights(nc, "moe2_w", 2, columns("w_gate_2"), columns("w_up_2"), rows("w_down_2")).open()
        expert_choice_phase(nc, h3_T, choosing, ident, idx2, scale2, weights2)
    expert_phase(nc, "moe2", N_EXP2, weights2, idx2, h3, ident, True, scale=scale2, add_to=total)
    weights2.close()
    choosing.close()
    norm_phase(nc, "norm4", total, a["g_final_2"], ident, natural=out)


def kernel(**inputs):
    import concourse.bacc as bacc
    from concourse.bass_utils import run_bass_kernel_spmd

    nc = bacc.Bacc("TRN2", target_bir_lowering=False, num_devices=1)
    arrays, views = {}, {}
    for name, array in [(n, inputs[n]) for n in INPUTS] + list(constants().items()):
        array = np.ascontiguousarray(array)
        if array.ndim > 1 and array.shape[0] == 1:
            array = array.reshape(array.shape[1:])
        arrays[f"in_{name}_dram"] = array
        views[name] = nc.dram_tensor(f"in_{name}_dram", array.shape, mybir.dt.from_np(array.dtype), kind="ExternalInput").ap()
    out = nc.dram_tensor("out_0_dram", (1, T, D), F32, kind="ExternalOutput").ap()
    build_program(nc, views, out.rearrange("o t d -> (o t) d"))
    results = run_bass_kernel_spmd(nc, [arrays], core_ids=[0])
    return results.results[0]["out_0_dram"]
```
